# Optimizing a Trainium2 kernel written in Bass

```python
import jax
import jax.numpy as jnp
from jax import lax
import numpy as np
import math
import jax, jax.numpy as jnp

D_MODEL = 1024
BATCH = 1
SEQ = 512
DEPTH = 1

D_MIX = D_MODEL
RWKV_WIDTH = D_MIX // 2
RWKV_HEAD_DIM = 64
RWKV_HEADS = RWKV_WIDTH // RWKV_HEAD_DIM
DECAY_LORA = 64
ICLR_LORA = 64
GATE_LORA = 128
GLA_V_WIDTH = D_MIX - RWKV_WIDTH
GLA_HEADS = 4
GLA_DV = GLA_V_WIDTH // GLA_HEADS
GLA_DK = GLA_DV // 2
GLA_K_WIDTH = GLA_HEADS * GLA_DK
GLA_GATE_LORA = 16
GLA_TAU = 16.0
GLA_CHUNK = 16
N_GROUPS = 4
EXPERTS_PER_GROUP = 8
N_EXPERTS = N_GROUPS * EXPERTS_PER_GROUP
TOP_K = 2
D_EXPERT = 512
MOE_BLOCK = 128
RMS_EPS = 1e-6
RWKV_GN_EPS = 64e-5

RWKV_SPLITS = (RWKV_WIDTH, RWKV_WIDTH, RWKV_WIDTH, DECAY_LORA, DECAY_LORA, ICLR_LORA, ICLR_LORA, GATE_LORA)
GLA_SPLITS = (GLA_K_WIDTH, GLA_K_WIDTH, GLA_V_WIDTH, GLA_GATE_LORA, GLA_GATE_LORA, GLA_V_WIDTH)
RWKV_COLS = sum(RWKV_SPLITS)
D_IN_PROJ = RWKV_COLS + sum(GLA_SPLITS)


def _split(p, sizes):
    return jnp.split(p, np.cumsum(sizes)[:-1].tolist(), axis=-1)

def rmsnorm(x, w):
    xf = x.astype(jnp.float32)
    y = xf * lax.rsqrt(jnp.mean(xf * xf, axis=-1, keepdims=True) + RMS_EPS)
    return (y * w.astype(jnp.float32)).astype(x.dtype)

def centred_shift(p):
    prev = jnp.pad(p[:, :-1], ((0, 0), (1, 0), (0, 0)))
    nxt = jnp.pad(p[:, 1:], ((0, 0), (0, 1), (0, 0)))
    return 0.5 * (prev + nxt)

def rwkv7_bidir_scan(r, w, k, v, kk, b):
    def to_dir(z):
        z = jnp.stack([z[0], jnp.flip(z[1], axis=1)])
        return jnp.moveaxis(z, 2, 0)

    def both(z):
        return to_dir(jnp.stack([z, z]))

    xs = (both(r), to_dir(w), to_dir(k), both(v), both(kk), to_dir(b))
    bsz, _, h, n = r.shape
    s0 = jnp.zeros((2, bsz, h, n, n), jnp.float32)

    def step(s, inp):
        r_t, w_t, k_t, v_t, kk_t, b_t = inp
        sa = jnp.einsum('dbhvk,dbhk->dbhv', s, -kk_t)
        s = s * w_t[..., None, :] + sa[..., None] * b_t[..., None, :] + v_t[..., None] * k_t[..., None, :]
        return s, jnp.einsum('dbhvk,dbhk->dbhv', s, r_t)

    _, ys = lax.scan(step, s0, xs)
    ys = jnp.moveaxis(ys, 0, 2)
    return ys[0] + jnp.flip(ys[1], axis=1)

def rwkv7_mixer(p, mu, w0_f, w2_f, w0_b, w2_b, a0_f, a2_f, a0_b, a2_b, g2, k_k, k_a, r_k, ln_w, ln_b):
    p = p.astype(jnp.float32)
    p = p + mu * (centred_shift(p) - p)
    r, k, v, wl_f, wl_b, al_f, al_b, gl = _split(p, RWKV_SPLITS)

    def decay(w0, wl, w2):
        logw = -jax.nn.softplus(-(w0 + jnp.tanh(wl) @ w2)) - 0.5
        return jnp.exp(-jnp.exp(logw))

    def heads(z):
        return z.reshape(z.shape[:-1] + (RWKV_HEADS, RWKV_HEAD_DIM))

    w = jnp.stack([decay(w0_f, wl_f, w2_f), decay(w0_b, wl_b, w2_b)])
    a = jax.nn.sigmoid(jnp.stack([a0_f + al_f @ a2_f, a0_b + al_b @ a2_b]))
    g = jax.nn.sigmoid(gl) @ g2
    kk = heads(k * k_k)
    kk = kk / jnp.maximum(jnp.sqrt(jnp.sum(kk * kk, axis=-1, keepdims=True)), 1e-12)
    k_dir = k * (1.0 + (a - 1.0) * k_a)
    b = kk * heads(a)
    rh, vh = heads(r), heads(v)
    y = rwkv7_bidir_scan(rh, heads(w), heads(k_dir), vh, kk, b)
    mean = jnp.mean(y, axis=-1, keepdims=True)
    var = jnp.var(y, axis=-1, keepdims=True)
    y = (y - mean) * lax.rsqrt(var + RWKV_GN_EPS)
    y = y.reshape(y.shape[:-2] + (RWKV_WIDTH,)) * ln_w + ln_b
    bonus = jnp.sum(rh * heads(k_dir[0] + k_dir[1]) * r_k, axis=-1, keepdims=True) * vh
    return (y + bonus.reshape(y.shape)) * g

def gla_chunked(q, k, v, g):
    bsz, h, t, dk = q.shape
    dv = v.shape[-1]
    c = GLA_CHUNK
    n = t // c
    q, k, g = (z.reshape(bsz, h, n, c, dk) for z in (q, k, g))
    v = v.reshape(bsz, h, n, c, dv)
    bc = jnp.cumsum(g, axis=3)
    causal = jnp.tril(jnp.ones((c, c), dtype=bool))
    diff = bc[..., :, None, :] - bc[..., None, :, :]
    dec = jnp.exp(jnp.where(causal[:, :, None], diff, -jnp.inf))
    att = jnp.einsum('bhnid,bhnjd,bhnijd->bhnij', q, k, dec)
    o = jnp.einsum('bhnij,bhnjv->bhniv', att, v)
    b_last = bc[..., -1, :]
    u = jnp.einsum('bhncd,bhncv->nbhdv', k * jnp.exp(b_last[..., None, :] - bc), v)

    def step(s, inp):
        u_n, d_n = inp
        return s * d_n[..., None] + u_n, s

    s0 = jnp.zeros((bsz, h, dk, dv), jnp.float32)
    _, s_in = lax.scan(step, s0, (u, jnp.moveaxis(jnp.exp(b_last), 2, 0)))
    o = o + jnp.einsum('bhncd,nbhdv->bhncv', q * jnp.exp(bc), s_in)
    return o.reshape(bsz, h, t, dv)

def gla_mixer(p, gw2_f, gb_f, gw2_b, gb_b, norm_w):
    p = p.astype(jnp.float32)
    bsz, t, _ = p.shape
    q, k, v, gl_f, gl_b, og = _split(p, GLA_SPLITS)

    def heads(z, d):
        return jnp.moveaxis(z.reshape(z.shape[:-1] + (GLA_HEADS, d)), 2, 1)

    q = heads(q, GLA_DK) * (GLA_DK ** -0.5)
    k = heads(k, GLA_DK)
    v = heads(v, GLA_DV)
    g_f = heads(jax.nn.log_sigmoid(gl_f @ gw2_f + gb_f) / GLA_TAU, GLA_DK)
    g_b = heads(jax.nn.log_sigmoid(gl_b @ gw2_b + gb_b) / GLA_TAU, GLA_DK)

    def flip(z):
        return jnp.flip(z, axis=2)

    o = gla_chunked(q, k, v, g_f) + flip(gla_chunked(flip(q), flip(k), flip(v), flip(g_b)))
    o = o * lax.rsqrt(jnp.mean(o * o, axis=-1, keepdims=True) + RMS_EPS)
    o = jnp.moveaxis(o, 1, 2).reshape(bsz, t, GLA_V_WIDTH)
    return o * norm_w * jax.nn.silu(og)

def hier_moe(h, w_coarse, b_coarse, w_fine, b_fine, w_gate, w_up, w_down):
    bsz, t, d = h.shape
    n_tok = bsz * t
    hf = h.reshape(n_tok, d)
    tok_idx = jnp.arange(n_tok)
    coarse = (hf @ w_coarse + b_coarse).astype(jnp.float32)
    pc = jax.nn.softmax(coarse, axis=-1)
    gsel = jnp.argmax(coarse, axis=-1)
    pg = pc[tok_idx, gsel]
    fine = (hf @ w_fine + b_fine).astype(jnp.float32).reshape(n_tok, N_GROUPS, EXPERTS_PER_GROUP)
    pf = jax.nn.softmax(fine[tok_idx, gsel], axis=-1)
    top_p, top_e = lax.top_k(pf, TOP_K)
    comb = pg[:, None] * top_p / jnp.sum(top_p, axis=-1, keepdims=True)
    eid = (gsel[:, None] * EXPERTS_PER_GROUP + top_e).reshape(-1).astype(jnp.int32)
    n_asg = n_tok * TOP_K
    tok = jnp.repeat(tok_idx, TOP_K).astype(jnp.int32)
    wts = comb.reshape(-1)
    order = jnp.argsort(eid, stable=True)
    se, st, sw = eid[order], tok[order], wts[order]
    counts = jnp.bincount(eid, length=N_EXPERTS).astype(jnp.int32)
    starts = jnp.cumsum(counts) - counts
    padded = ((counts + MOE_BLOCK - 1) // MOE_BLOCK) * MOE_BLOCK
    pends = jnp.cumsum(padded)
    pstarts = pends - padded
    dest = pstarts[se] + jnp.arange(n_asg, dtype=jnp.int32) - starts[se]
    n_blocks = -(-n_asg // MOE_BLOCK) + N_EXPERTS
    n_rows = n_blocks * MOE_BLOCK
    row_tok = jnp.zeros((n_rows,), jnp.int32).at[dest].set(st)
    row_w = jnp.zeros((n_rows,), jnp.float32).at[dest].set(sw)
    block_e = jnp.minimum(jnp.searchsorted(pends, jnp.arange(n_blocks, dtype=jnp.int32) * MOE_BLOCK, side='right'), N_EXPERTS - 1)
    xs = hf[row_tok].reshape(n_blocks, MOE_BLOCK, d)

    def expert_block(args):
        xb, e = args
        return (jax.nn.silu(xb @ w_gate[e]) * (xb @ w_up[e])) @ w_down[e]

    ys = lax.map(expert_block, (xs, block_e)).reshape(n_rows, d)
    out = jax.ops.segment_sum(ys * row_w[:, None].astype(ys.dtype), row_tok, num_segments=n_tok)
    return out.reshape(bsz, t, d)

def first_inputs(seed: int = 0) -> dict:
    key = jax.random.key(seed)
    ks = iter(jax.random.split(key, 40))

    def nrm(shape, scale):
        return jax.random.normal(next(ks), shape, jnp.float32) * scale

    def unif(shape, lo, hi):
        return jax.random.uniform(next(ks), shape, jnp.float32, lo, hi)

    L, D = DEPTH, D_MODEL
    return {
        'x': nrm((BATCH, SEQ, D), 1.0),
        'ln1_w': 1.0 + nrm((L, D), 0.05),
        'w_in': nrm((L, D, D_IN_PROJ), D ** -0.5),
        'rw_mu': unif((L, RWKV_COLS), 0.0, 1.0),
        'rw_w0_f': unif((L, RWKV_WIDTH), -6.0, -1.0),
        'rw_w2_f': nrm((L, DECAY_LORA, RWKV_WIDTH), 0.1),
        'rw_w0_b': unif((L, RWKV_WIDTH), -6.0, -1.0),
        'rw_w2_b': nrm((L, DECAY_LORA, RWKV_WIDTH), 0.1),
        'rw_a0_f': nrm((L, RWKV_WIDTH), 0.1),
        'rw_a2_f': nrm((L, ICLR_LORA, RWKV_WIDTH), 0.5 * ICLR_LORA ** -0.5),
        'rw_a0_b': nrm((L, RWKV_WIDTH), 0.1),
        'rw_a2_b': nrm((L, ICLR_LORA, RWKV_WIDTH), 0.5 * ICLR_LORA ** -0.5),
        'rw_g2': nrm((L, GATE_LORA, RWKV_WIDTH), GATE_LORA ** -0.5),
        'rw_k_k': 0.85 + nrm((L, RWKV_WIDTH), 0.05),
        'rw_k_a': 1.0 + nrm((L, RWKV_WIDTH), 0.05),
        'rw_r_k': nrm((L, RWKV_HEADS, RWKV_HEAD_DIM), 0.1),
        'rw_ln_w': 1.0 + nrm((L, RWKV_WIDTH), 0.05),
        'rw_ln_b': nrm((L, RWKV_WIDTH), 0.01),
        'gla_gw2_f': nrm((L, GLA_GATE_LORA, GLA_K_WIDTH), GLA_GATE_LORA ** -0.5),
        'gla_gb_f': 2.0 + nrm((L, GLA_K_WIDTH), 0.5),
        'gla_gw2_b': nrm((L, GLA_GATE_LORA, GLA_K_WIDTH), GLA_GATE_LORA ** -0.5),
        'gla_gb_b': 2.0 + nrm((L, GLA_K_WIDTH), 0.5),
        'gla_norm_w': 1.0 + nrm((L, GLA_V_WIDTH), 0.05),
        'w_out': nrm((L, D_MIX, D), D_MIX ** -0.5),
        'ln2_w': 1.0 + nrm((L, D), 0.05),
        'moe_w_coarse': nrm((L, D, N_GROUPS), D ** -0.5),
        'moe_b_coarse': nrm((L, N_GROUPS), 0.01),
        'moe_w_fine': nrm((L, D, N_EXPERTS), D ** -0.5),
        'moe_b_fine': nrm((L, N_EXPERTS), 0.01),
        'moe_w_gate': nrm((L, N_EXPERTS, D, D_EXPERT), D ** -0.5),
        'moe_w_up': nrm((L, N_EXPERTS, D, D_EXPERT), D ** -0.5),
        'moe_w_down': nrm((L, N_EXPERTS, D_EXPERT, D), D_EXPERT ** -0.5),
        'ln_f_w': 1.0 + nrm((D,), 0.05),
    }

def first_block(x, ln1_w, w_in, rw_mu, rw_w0_f, rw_w2_f, rw_w0_b, rw_w2_b, rw_a0_f, rw_a2_f, rw_a0_b, rw_a2_b, rw_g2, rw_k_k, rw_k_a, rw_r_k, rw_ln_w, rw_ln_b, gla_gw2_f, gla_gb_f, gla_gw2_b, gla_gb_b, gla_norm_w, w_out, ln2_w, moe_w_coarse, moe_b_coarse, moe_w_fine, moe_b_fine, moe_w_gate, moe_w_up, moe_w_down, ln_f_w):
    for l in range(DEPTH):
        h = rmsnorm(x, ln1_w[l])
        p = h @ w_in[l]
        y_rw = rwkv7_mixer(p[..., :RWKV_COLS], rw_mu[l], rw_w0_f[l], rw_w2_f[l], rw_w0_b[l], rw_w2_b[l],
                           rw_a0_f[l], rw_a2_f[l], rw_a0_b[l], rw_a2_b[l], rw_g2[l], rw_k_k[l], rw_k_a[l],
                           rw_r_k[l], rw_ln_w[l], rw_ln_b[l])
        y_gla = gla_mixer(p[..., RWKV_COLS:], gla_gw2_f[l], gla_gb_f[l], gla_gw2_b[l], gla_gb_b[l], gla_norm_w[l])
        mix = jnp.concatenate([y_rw, y_gla], axis=-1).astype(x.dtype)
        x = x + mix @ w_out[l]
        x = x + hier_moe(rmsnorm(x, ln2_w[l]), moe_w_coarse[l], moe_b_coarse[l], moe_w_fine[l], moe_b_fine[l],
                         moe_w_gate[l], moe_w_up[l], moe_w_down[l])
    return rmsnorm(x, ln_f_w)


DEPTH_2 = 2

GRID_W = 64
CTX_LEN = 256
N_EVEN = (DEPTH_2 + 1) // 2
N_ODD = DEPTH_2 // 2
RNN_WIDTH = D_MODEL // 2
LRU_HEADS = 8
LRU_HEAD_DIM = RNN_WIDTH // LRU_HEADS
LRU_CONV = 4
LRU_C = 8.0
LRU_A_MIN = 0.9
LRU_A_MAX = 0.999
HYENA_WIDTH = D_MODEL // 2
HYENA_ORDER = 2
HYENA_SHORT_CONV = 3
FILTER_EMB = 33
FILTER_HIDDEN = 64
HYENA_DECAY_TARGET = 1e-2
HYENA_FAST_PCT = 0.3
HYENA_SLOW_PCT = 1.5
HYENA_SHIFT = 0.05
IN_WIDTH = 2 * RNN_WIDTH + (HYENA_ORDER + 1) * HYENA_WIDTH
CONF_KERNEL = 31
N_EXPERTS_2 = 16
EC_CAPACITY = 2
EXPERT_FF = 1024
N_MOD = 6
EPS = 1e-6


def _rmsnorm(x, g):
    xf = x.astype(jnp.float32)
    y = xf * lax.rsqrt(jnp.mean(xf * xf, axis=-1, keepdims=True) + EPS)
    return (y * g.astype(jnp.float32)).astype(x.dtype)

def _layernorm(x, g, b):
    xf = x.astype(jnp.float32)
    mu = jnp.mean(xf, axis=-1, keepdims=True)
    var = jnp.mean(jnp.square(xf - mu), axis=-1, keepdims=True)
    y = (xf - mu) * lax.rsqrt(var + EPS) * g.astype(jnp.float32) + b.astype(jnp.float32)
    return y.astype(x.dtype)

def _adaln(cvec, w_mod, b_mod, n_chunks):
    m = jax.nn.silu(cvec) @ w_mod[:, :n_chunks * D_MODEL] + b_mod[:n_chunks * D_MODEL]
    return [m[:, None, j * D_MODEL:(j + 1) * D_MODEL] for j in range(n_chunks)]

def _modulate(h, shift, scale):
    return h * (1 + scale) + shift

def _dwconv1d(x, w, b):
    k = w.shape[0]
    y = lax.conv_general_dilated(x, w[:, None, :], window_strides=(1,),
                                 padding=[((k - 1) // 2, k // 2)],
                                 dimension_numbers=('NWC', 'WIO', 'NWC'),
                                 feature_group_count=x.shape[-1])
    return y + b

def _dwconv_vertical(x, w, b, rows):
    bsz, n, ch = x.shape
    k = w.shape[0]
    grid = x.reshape(bsz, rows, GRID_W, ch)
    y = lax.conv_general_dilated(grid, w[:, None, None, :], window_strides=(1, 1),
                                 padding=[((k - 1) // 2, k // 2), (0, 0)],
                                 dimension_numbers=('NHWC', 'HWIO', 'NHWC'),
                                 feature_group_count=ch)
    return y.reshape(bsz, n, ch) + b

def _lin_combine(left, right):
    a_l, b_l = left
    a_r, b_r = right
    return a_l * a_r, a_r * b_l + b_r

def _rglru(xa_raw, p, h0):
    f32 = jnp.float32
    xa = _dwconv1d(xa_raw, p['conv_a_w'], p['conv_a_b'])
    bsz, n, _ = xa.shape
    xh = xa.reshape(bsz, n, LRU_HEADS, LRU_HEAD_DIM)

    def gate(w, b):
        z = jnp.einsum('bnhi,khij->kbnhj', xh, w).reshape(2, bsz, n, RNN_WIDTH)
        return jax.nn.sigmoid((z + b[:, None, None, :]).astype(f32))

    r = gate(p['lru_wr'], p['lru_br'])
    i = gate(p['lru_wi'], p['lru_bi'])
    log_a = -LRU_C * r * jax.nn.softplus(-p['lru_lam'].astype(f32))[:, None, None, :]
    a = jnp.exp(log_a)
    u = jnp.sqrt(-jnp.expm1(2.0 * log_a)) * i * xa.astype(f32)[None]
    a = jnp.stack([a[0], jnp.flip(a[1], axis=1)])
    u = jnp.stack([u[0], jnp.flip(u[1], axis=1)])
    a_cum, h = lax.associative_scan(_lin_combine, (a, u), axis=2)
    h = h + a_cum * h0[:, :, None, :]
    return h, h[:, :, -1]

def _hyena_filters_fft(n, p):
    f32 = jnp.float32
    t = jnp.linspace(0.0, 1.0, n, dtype=f32)[:, None]
    bands = (FILTER_EMB - 1) // 2
    w = (2.0 * math.pi / n) * jnp.arange(n, dtype=f32)[:, None]
    f = jnp.linspace(1e-4, bands - 1, bands, dtype=f32)[None, :]
    z = jnp.concatenate([t, jnp.cos(f * w), -jnp.sin(f * w)], axis=-1)
    freq = p['filt_freq'].astype(f32)
    hid = jnp.sin(freq[0] * (z @ p['filt_w1'].astype(f32) + p['filt_b1'].astype(f32)))
    hid = jnp.sin(freq[1] * (hid @ p['filt_w2'].astype(f32) + p['filt_b2'].astype(f32)))
    filt = (hid @ p['filt_w3'].astype(f32) + p['filt_b3'].astype(f32))
    filt = filt.reshape(n, HYENA_ORDER, 2, HYENA_WIDTH)
    deltas = jnp.abs(jnp.linspace(math.log(HYENA_DECAY_TARGET) / HYENA_SLOW_PCT,
                                  math.log(HYENA_DECAY_TARGET) / HYENA_FAST_PCT,
                                  HYENA_WIDTH, dtype=f32))
    window = jnp.exp(-t * deltas[None, :]) + HYENA_SHIFT
    filt = filt * window[:, None, None, :]
    fwd, bwd = filt[:, :, 0], filt[:, :, 1]
    kern = jnp.concatenate([fwd, jnp.zeros((1, HYENA_ORDER, HYENA_WIDTH), f32), bwd[:0:-1]], axis=0)
    return jnp.fft.rfft(kern, axis=0)

def _fftconv(u, kf, bias):
    n = u.shape[1]
    uf = u.astype(jnp.float32)
    y = jnp.fft.irfft(jnp.fft.rfft(uf, n=2 * n, axis=1) * kf[None], n=2 * n, axis=1)[:, :n]
    return (y + uf * bias.astype(jnp.float32)).astype(u.dtype)

def _even_mixer(h, p, h0):
    proj = h @ p['w_in']
    gate = proj[..., :RNN_WIDTH]
    xa_raw = proj[..., RNN_WIDTH:2 * RNN_WIDTH]
    hy = proj[..., 2 * RNN_WIDTH:]
    hs, h_last = _rglru(xa_raw, p, h0)
    y_a = jax.nn.gelu(gate) * (hs[0] + jnp.flip(hs[1], axis=1)).astype(h.dtype)
    u = _dwconv1d(hy, p['conv_b_w'], p['conv_b_b'])
    v, *gates = jnp.split(u, HYENA_ORDER + 1, axis=-1)
    kf = _hyena_filters_fft(h.shape[1], p)
    z = v
    for o in range(HYENA_ORDER):
        z = gates[o] * _fftconv(z, kf[:, o], p['filt_bias'][o])
    return jnp.concatenate([y_a, z], axis=-1) @ p['w_out'], h_last

def _conformer_conv(h, p, rows):
    u = h @ p['cf_w1'] + p['cf_b1']
    u = u[..., :D_MODEL] * jax.nn.sigmoid(u[..., D_MODEL:])
    if rows is None:
        u = _dwconv1d(u, p['cf_dw_w'], p['cf_dw_b'])
    else:
        u = _dwconv_vertical(u, p['cf_dw_w'], p['cf_dw_b'], rows)
    u = jax.nn.silu(_layernorm(u, p['cf_ln_g'], p['cf_ln_b']))
    return u @ p['cf_w2'] + p['cf_b2']

def _ec_moe(h, router, w1, w3, w2):
    bsz, n, _ = h.shape
    cap = EC_CAPACITY * n // N_EXPERTS_2
    probs = jax.nn.softmax(jnp.einsum('bnd,de->ben', h, router).astype(jnp.float32), axis=1)
    gates, idx = lax.top_k(probs, cap)
    bidx = jnp.arange(bsz)[:, None, None]
    xs = h[bidx, idx]
    a = jnp.einsum('becd,edf->becf', xs, w1)
    g = jnp.einsum('becd,edf->becf', xs, w3)
    y = jnp.einsum('becf,efd->becd', jax.nn.silu(a) * g, w2) * gates[..., None].astype(h.dtype)
    return jnp.zeros_like(h).at[bidx, idx].add(y)

def second_inputs(seed: int = 0) -> dict:
    key = jax.random.key(seed)
    ks = iter(jax.random.split(key, 48))
    f32 = jnp.float32
    D = D_MODEL

    def nrm(shape, scale):
        return jax.random.normal(next(ks), shape, f32) * scale

    x = nrm((BATCH, SEQ, D), 1.0)
    c = nrm((BATCH, D), 1.0)
    ctx = nrm((BATCH, CTX_LEN, D), 1.0)
    c_ctx = nrm((D,), 1.0)
    norm1_g = 1.0 + nrm((DEPTH_2, D), 0.1)
    norm2_g = 1.0 + nrm((DEPTH_2, D), 0.1)
    w_mod = nrm((DEPTH_2, D, N_MOD * D), 0.5 * D ** -0.5)
    b_mod = nrm((DEPTH_2, N_MOD * D), 0.01)
    w_in = nrm((N_EVEN, D, IN_WIDTH), D ** -0.5)
    conv_a_w = nrm((N_EVEN, LRU_CONV, RNN_WIDTH), LRU_CONV ** -0.5)
    conv_a_b = nrm((N_EVEN, RNN_WIDTH), 0.01)
    lru_wr = nrm((N_EVEN, 2, LRU_HEADS, LRU_HEAD_DIM, LRU_HEAD_DIM), LRU_HEAD_DIM ** -0.5)
    lru_br = nrm((N_EVEN, 2, RNN_WIDTH), 0.01)
    lru_wi = nrm((N_EVEN, 2, LRU_HEADS, LRU_HEAD_DIM, LRU_HEAD_DIM), LRU_HEAD_DIM ** -0.5)
    lru_bi = nrm((N_EVEN, 2, RNN_WIDTH), 0.01)
    lo, hi = LRU_A_MIN ** (1.0 / LRU_C), LRU_A_MAX ** (1.0 / LRU_C)
    ua = jax.random.uniform(next(ks), (N_EVEN, 2, RNN_WIDTH), f32, lo, hi)
    lru_lam = jnp.log(ua) - jnp.log1p(-ua)
    conv_b_w = nrm((N_EVEN, HYENA_SHORT_CONV, (HYENA_ORDER + 1) * HYENA_WIDTH), HYENA_SHORT_CONV ** -0.5)
    conv_b_b = nrm((N_EVEN, (HYENA_ORDER + 1) * HYENA_WIDTH), 0.01)
    filt_w1 = nrm((N_EVEN, FILTER_EMB, FILTER_HIDDEN), FILTER_EMB ** -0.5)
    filt_b1 = nrm((N_EVEN, FILTER_HIDDEN), 0.1)
    filt_w2 = nrm((N_EVEN, FILTER_HIDDEN, FILTER_HIDDEN), FILTER_HIDDEN ** -0.5)
    filt_b2 = nrm((N_EVEN, FILTER_HIDDEN), 0.1)
    filt_w3 = nrm((N_EVEN, FILTER_HIDDEN, HYENA_ORDER * 2 * HYENA_WIDTH), 0.1 * FILTER_HIDDEN ** -0.5)
    filt_b3 = nrm((N_EVEN, HYENA_ORDER * 2 * HYENA_WIDTH), 0.01)
    filt_freq = 1.0 + nrm((N_EVEN, 2, FILTER_HIDDEN), 0.1)
    filt_bias = nrm((N_EVEN, HYENA_ORDER, HYENA_WIDTH), 0.5)
    w_out = nrm((N_EVEN, RNN_WIDTH + HYENA_WIDTH, D), (RNN_WIDTH + HYENA_WIDTH) ** -0.5)
    cf_w1 = nrm((N_ODD, D, 2 * D), D ** -0.5)
    cf_b1 = nrm((N_ODD, 2 * D), 0.01)
    cf_dw_w = nrm((N_ODD, CONF_KERNEL, D), CONF_KERNEL ** -0.5)
    cf_dw_b = nrm((N_ODD, D), 0.01)
    cf_ln_g = 1.0 + nrm((N_ODD, D), 0.1)
    cf_ln_b = nrm((N_ODD, D), 0.01)
    cf_w2 = nrm((N_ODD, D, D), D ** -0.5)
    cf_b2 = nrm((N_ODD, D), 0.01)
    router = nrm((DEPTH_2, D, N_EXPERTS_2), D ** -0.5)
    exp_w1 = nrm((DEPTH_2, N_EXPERTS_2, D, EXPERT_FF), D ** -0.5)
    exp_w3 = nrm((DEPTH_2, N_EXPERTS_2, D, EXPERT_FF), D ** -0.5)
    exp_w2 = nrm((DEPTH_2, N_EXPERTS_2, EXPERT_FF, D), EXPERT_FF ** -0.5)
    final_g = 1.0 + nrm((D,), 0.1)
    return {"x": x, "c": c, "ctx": ctx, "c_ctx": c_ctx,
            "norm1_g": norm1_g, "norm2_g": norm2_g, "w_mod": w_mod, "b_mod": b_mod,
            "w_in": w_in, "conv_a_w": conv_a_w, "conv_a_b": conv_a_b,
            "lru_wr": lru_wr, "lru_br": lru_br, "lru_wi": lru_wi, "lru_bi": lru_bi, "lru_lam": lru_lam,
            "conv_b_w": conv_b_w, "conv_b_b": conv_b_b,
            "filt_w1": filt_w1, "filt_b1": filt_b1, "filt_w2": filt_w2, "filt_b2": filt_b2,
            "filt_w3": filt_w3, "filt_b3": filt_b3, "filt_freq": filt_freq, "filt_bias": filt_bias,
            "w_out": w_out,
            "cf_w1": cf_w1, "cf_b1": cf_b1, "cf_dw_w": cf_dw_w, "cf_dw_b": cf_dw_b,
            "cf_ln_g": cf_ln_g, "cf_ln_b": cf_ln_b, "cf_w2": cf_w2, "cf_b2": cf_b2,
            "router": router, "exp_w1": exp_w1, "exp_w3": exp_w3, "exp_w2": exp_w2,
            "final_g": final_g}

def second_block(x, c, ctx, c_ctx, norm1_g, norm2_g, w_mod, b_mod,
              w_in, conv_a_w, conv_a_b, lru_wr, lru_br, lru_wi, lru_bi, lru_lam,
              conv_b_w, conv_b_b, filt_w1, filt_b1, filt_w2, filt_b2, filt_w3, filt_b3,
              filt_freq, filt_bias, w_out,
              cf_w1, cf_b1, cf_dw_w, cf_dw_b, cf_ln_g, cf_ln_b, cf_w2, cf_b2,
              router, exp_w1, exp_w3, exp_w2, final_g):
    n_lat = x.shape[1]
    rows = n_lat // GRID_W
    last_ctx_layer = ((DEPTH_2 - 1) // 2) * 2
    xl, xc = x, ctx
    for l in range(DEPTH_2):
        carry_ctx = l < last_ctx_layer
        sh1, sc1, g1, sh2, sc2, g2 = _adaln(c, w_mod[l], b_mod[l], N_MOD)
        hl = _modulate(_rmsnorm(xl, norm1_g[l]), sh1, sc1)
        if l % 2 == 0 or carry_ctx:
            cm = _adaln(c_ctx[None], w_mod[l], b_mod[l], N_MOD if carry_ctx else 2)
            hc = _modulate(_rmsnorm(xc, norm1_g[l]), cm[0], cm[1])
        if l % 2 == 0:
            e = l // 2
            pe = {'w_in': w_in[e], 'conv_a_w': conv_a_w[e], 'conv_a_b': conv_a_b[e],
                  'lru_wr': lru_wr[e], 'lru_br': lru_br[e], 'lru_wi': lru_wi[e], 'lru_bi': lru_bi[e],
                  'lru_lam': lru_lam[e], 'conv_b_w': conv_b_w[e], 'conv_b_b': conv_b_b[e],
                  'filt_w1': filt_w1[e], 'filt_b1': filt_b1[e], 'filt_w2': filt_w2[e],
                  'filt_b2': filt_b2[e], 'filt_w3': filt_w3[e], 'filt_b3': filt_b3[e],
                  'filt_freq': filt_freq[e], 'filt_bias': filt_bias[e], 'w_out': w_out[e]}
            h0_ctx = jnp.zeros((2, xc.shape[0], RNN_WIDTH), jnp.float32)
            if carry_ctx:
                yc, ctx_state = _even_mixer(hc, pe, h0_ctx)
            else:
                _, ctx_state = _rglru(hc @ pe['w_in'][:, RNN_WIDTH:2 * RNN_WIDTH], pe, h0_ctx)
            yl, _ = _even_mixer(hl, pe, ctx_state)
        else:
            o = l // 2
            po = {'cf_w1': cf_w1[o], 'cf_b1': cf_b1[o], 'cf_dw_w': cf_dw_w[o], 'cf_dw_b': cf_dw_b[o],
                  'cf_ln_g': cf_ln_g[o], 'cf_ln_b': cf_ln_b[o], 'cf_w2': cf_w2[o], 'cf_b2': cf_b2[o]}
            yl = _conformer_conv(hl, po, rows)
            if carry_ctx:
                yc = _conformer_conv(hc, po, None)
        xl = xl + g1 * yl
        xl = xl + g2 * _ec_moe(_modulate(_rmsnorm(xl, norm2_g[l]), sh2, sc2),
                               router[l], exp_w1[l], exp_w3[l], exp_w2[l])
        if carry_ctx:
            xc = xc + cm[2] * yc
            xc = xc + cm[5] * _ec_moe(_modulate(_rmsnorm(xc, norm2_g[l]), cm[3], cm[4]),
                                      router[l], exp_w1[l], exp_w3[l], exp_w2[l])
    return _rmsnorm(xl, final_g)


def setup_inputs(seed=0):
    out = dict(first_inputs(seed))
    for name, value in second_inputs(seed + 1).items():
        if name != "x":
            out[name + "_2"] = value
    return out


def reference(
    x, ln1_w, w_in, rw_mu, rw_w0_f, rw_w2_f, rw_w0_b, rw_w2_b, rw_a0_f, rw_a2_f, rw_a0_b,
    rw_a2_b, rw_g2, rw_k_k, rw_k_a, rw_r_k, rw_ln_w, rw_ln_b, gla_gw2_f, gla_gb_f, gla_gw2_b,
    gla_gb_b, gla_norm_w, w_out, ln2_w, moe_w_coarse, moe_b_coarse, moe_w_fine, moe_b_fine,
    moe_w_gate, moe_w_up, moe_w_down, ln_f_w, c_2, ctx_2, c_ctx_2, norm1_g_2, norm2_g_2,
    w_mod_2, b_mod_2, w_in_2, conv_a_w_2, conv_a_b_2, lru_wr_2, lru_br_2, lru_wi_2, lru_bi_2,
    lru_lam_2, conv_b_w_2, conv_b_b_2, filt_w1_2, filt_b1_2, filt_w2_2, filt_b2_2, filt_w3_2,
    filt_b3_2, filt_freq_2, filt_bias_2, w_out_2, cf_w1_2, cf_b1_2, cf_dw_w_2, cf_dw_b_2,
    cf_ln_g_2, cf_ln_b_2, cf_w2_2, cf_b2_2, router_2, exp_w1_2, exp_w3_2, exp_w2_2, final_g_2,
):
    x = first_block(
        x, ln1_w, w_in, rw_mu, rw_w0_f, rw_w2_f, rw_w0_b, rw_w2_b, rw_a0_f, rw_a2_f, rw_a0_b,
        rw_a2_b, rw_g2, rw_k_k, rw_k_a, rw_r_k, rw_ln_w, rw_ln_b, gla_gw2_f, gla_gb_f,
        gla_gw2_b, gla_gb_b, gla_norm_w, w_out, ln2_w, moe_w_coarse, moe_b_coarse, moe_w_fine,
        moe_b_fine, moe_w_gate, moe_w_up, moe_w_down, ln_f_w,
    )
    return second_block(
        x, c_2, ctx_2, c_ctx_2, norm1_g_2, norm2_g_2, w_mod_2, b_mod_2, w_in_2, conv_a_w_2,
        conv_a_b_2, lru_wr_2, lru_br_2, lru_wi_2, lru_bi_2, lru_lam_2, conv_b_w_2, conv_b_b_2,
        filt_w1_2, filt_b1_2, filt_w2_2, filt_b2_2, filt_w3_2, filt_b3_2, filt_freq_2,
        filt_bias_2, w_out_2, cf_w1_2, cf_b1_2, cf_dw_w_2, cf_dw_b_2, cf_ln_g_2, cf_ln_b_2,
        cf_w2_2, cf_b2_2, router_2, exp_w1_2, exp_w3_2, exp_w2_2, final_g_2,
    )


_drawn_inputs = setup_inputs


def setup_inputs(seed=0):
    import zlib

    import numpy as np

    out = dict(_drawn_inputs(seed))
    spreads = {}
    factors = {'rw_a0_f': 2.746,
     'rw_a0_b': 2.721,
     'rw_ln_b': 4.363,
     'moe_b_coarse': 6.249,
     'moe_b_fine': 4.809,
     'conv_a_b_2': 3.578,
     'lru_br_2': 64.0,
     'lru_bi_2': 40.948,
     'conv_b_b_2': 8.0,
     'filt_freq_2': 2.812,
     'cf_b1_2': 8.0,
     'cf_dw_b_2': 8.0,
     'cf_ln_g_2': 2.759,
     'cf_ln_b_2': 32.71,
     'cf_b2_2': 24.053,
     'rw_w2_f': 3.108,
     'rw_w2_b': 2.674,
     'norm2_g_2': 2.678}
    for name, (base, spread) in spreads.items():
        noise = np.random.default_rng([zlib.crc32(name.encode()), seed]).standard_normal(out[name].shape)
        drawn = base * np.exp(spread * noise) if base else spread * noise
        out[name] = jnp.asarray(drawn.astype(out[name].dtype))
    for name, factor in factors.items():
        out[name] = (out[name] * factor).astype(out[name].dtype)
    return out
```

```python
import math
from contextlib import ExitStack

import numpy as np
import concourse.bass as bass
from concourse import mybir

ALU = mybir.AluOpType
ACT = mybir.ActivationFunctionType
F32 = mybir.dt.float32
I32 = mybir.dt.int32
U32 = mybir.dt.uint32
AX = mybir.AxisListType

P = 128
D = 1024
KD = D // P
T = 512
KT = T // P
RMS_EPS = 1e-6
RW = 512
CT = RW // P
RW_HD = 64
RW_GN_EPS = 64e-5
RW_COLS = 1920
GLA_DK = 64
GLA_TAU = 16.0
GLA_SUB = 32
GLA_CLAMP = 80.0
LEVELS = 7
N_GROUPS, PER_GROUP = 4, 8
N_EXP1 = N_GROUPS * PER_GROUP
SLOTS = 64
PAIRS = 4
MORE1 = -(-T // SLOTS) - 1
N_OVER = max(k for k in range(2 * T) if k * (SLOTS + 1) <= 2 * T)
FILTER_EMB, FILTER_HIDDEN, HYENA_WIDTH, HYENA_ORDER = 33, 64, 512, 2
HYENA_DECAY_TARGET, HYENA_FAST_PCT, HYENA_SLOW_PCT, HYENA_SHIFT = 1e-2, 0.3, 1.5, 0.05
ROUND = 1.5 * 2.0 ** 23
TURN_HI = 6.28125
TURN_LO = 2.0 * math.pi - 6.28125
PI_IN = 3.1415925
LRU_C = 8.0
CTX = 256
GRID_W = 64
CONF_TAPS = 31
N_EXP2, FF2, CAP2 = 16, 1024, 64
RING = 6


class Signal:

    def __init__(self, sem):
        self.sem, self.n = sem, 0

    def up(self, by=1):
        self.n += by
        return self.sem, by


class Columns:

    def __init__(self):
        self.start, self.parts, self.n = {}, [], 0

    def add(self, name, a):
        a = np.asarray(a, np.float32)
        if a.shape[0] < P:
            a = np.concatenate([a, np.zeros((P - a.shape[0], a.shape[1]), np.float32)])
        self.start[name] = self.n
        self.parts.append(a)
        self.n += a.shape[1]

    def array(self):
        return np.ascontiguousarray(np.concatenate(self.parts, axis=1))


def pack_vectors(a):
    cols = Columns()

    def put(name, v, rows=P):
        v = np.asarray(v).reshape(-1, rows).T
        cols.add(name, v)

    for name in ("ln1_w", "rw_mu", "rw_w0_f", "rw_w0_b", "rw_a0_f", "rw_a0_b", "rw_k_k", "rw_k_a", "rw_r_k",
                 "rw_ln_w", "rw_ln_b", "gla_gb_f", "gla_gb_b", "gla_norm_w", "ln2_w", "ln_f_w",
                 "norm1_g_2", "norm2_g_2", "final_g_2", "conv_a_w_2", "conv_a_b_2", "lru_br_2", "lru_bi_2",
                 "lru_lam_2", "conv_b_w_2", "conv_b_b_2", "filt_bias_2", "cf_b1_2", "cf_dw_w_2", "cf_dw_b_2",
                 "cf_ln_g_2", "cf_ln_b_2", "cf_b2_2", "b_mod_2", "c_2", "c_ctx_2"):
        put(name, a[name])
    for name in ("filt_b1_2", "filt_b2_2", "filt_freq_2"):
        put(name, a[name], 64)
    put("moe_b_coarse", a["moe_b_coarse"], 4)
    put("moe_b_fine", a["moe_b_fine"], 32)
    return cols


def shape_constants():
    cols = Columns()
    i = np.arange(P)
    row, col = i[:, None], i[None, :]
    cols.add("ident", row == col)
    cols.add("ones", np.ones((P, P)))
    cols.add("head_ones", row // RW_HD == col // RW_HD)
    cols.add("before", row < col)
    cols.add("slots", np.tile(np.arange(SLOTS), (P, 1)))
    cols.add("experts", np.tile(np.arange(N_EXP1), (P, 1)))
    cols.add("overflows", np.tile(np.arange(N_OVER), (P, 1)))
    cols.add("first4", np.tile(np.arange(4, 0, -1), (P, 1)))
    cols.add("first8", np.tile(np.arange(8, 0, -1), (P, 1)))
    cols.add("quarter_rows", np.stack([i % 32 == 0, i % 32 == 1], axis=1))
    cols.add("base_end", np.zeros((P, 1)))
    cols.add("strict", np.concatenate([row < col, row > col], axis=1))
    cols.add("incl", np.concatenate([row <= col, row >= col], axis=1))
    levels = []
    for back in (False, True):
        for s in (2 ** l for l in range(LEVELS)):
            lower = (row // (2 * s) == col // (2 * s)) & (row // s > col // s)
            levels.append(lower.T if back else lower)
    cols.add("levels", np.concatenate(levels, axis=1))
    return cols


def hyena_tables():
    t = np.linspace(0.0, 1.0, T, dtype=np.float32)[:, None]
    bands = (FILTER_EMB - 1) // 2
    w = np.float32(2.0 * math.pi / T) * np.arange(T, dtype=np.float32)[:, None]
    f = np.linspace(1e-4, bands - 1, bands, dtype=np.float32)[None, :]
    z = np.concatenate([t, np.cos(f * w), -np.sin(f * w)], axis=-1).astype(np.float32)
    deltas = np.abs(np.linspace(math.log(HYENA_DECAY_TARGET) / HYENA_SLOW_PCT, math.log(HYENA_DECAY_TARGET) / HYENA_FAST_PCT,
                                HYENA_WIDTH, dtype=np.float32))
    window = (np.exp(-t * deltas[None, :]) + np.float32(HYENA_SHIFT)).astype(np.float32)
    angle = 2.0 * math.pi * ((2 * np.arange(T)[None, :] + 1) * np.arange(T)[:, None] % (4 * T)) / (4 * T)
    spectrum = np.concatenate([np.cos(angle), np.sin(angle)], axis=1).astype(np.float32)
    inverse = (np.concatenate([np.cos(angle).T, np.sin(angle).T], axis=0) / T).astype(np.float32)
    return {"hy_z": np.ascontiguousarray(z.T), "hy_window": window, "hy_spectrum": spectrum, "hy_inverse": inverse}


def build(nc, A, out, vec_at, const_at):
    ctx = ExitStack()
    with ctx:
        def signal(name):
            return Signal(ctx.enter_context(nc.semaphore(name)))

        names = {}

        def sbuf(stack, name, shape, dt=F32):
            names[name] = names.get(name, 0) + 1
            if names[name] > 1:
                name = f"{name}_{names[name]}"
            return stack.enter_context(nc.sbuf_tensor("s_" + name, shape, dt))

        ps = ctx.enter_context(nc.psum_tensor("ps", [P, 8, 512], F32))
        xT = sbuf(ctx, "xT", [P, KD, T])
        n_vec = A["vectors"].shape[1]
        vec = sbuf(ctx, "vec", [P, n_vec])
        base = sbuf(ctx, "base", [P, const_at["base_end"]])

        def table(name, n):
            return base[:, const_at[name]:const_at[name] + n]

        ident, ones, head_ones, before = (table(n, P) for n in ("ident", "ones", "head_ones", "before"))
        slots, experts, overflows = table("slots", SLOTS), table("experts", N_EXP1), table("overflows", N_OVER)
        first4, first8 = table("first4", 4), table("first8", 8)

        def vcol(name, k, n=1):
            at = vec_at[name] + k
            return vec[:, at:at + n]

        inputs_in = signal("inputs_in")
        w_in = [signal("w_in0"), signal("w_in1")]
        mm_done = signal("mm_done")
        act_evac = signal("act_evac")
        dve_evac = signal("dve_evac")
        dve_step = signal("dve_step")
        act_step = signal("act_step")
        dve_out = signal("dve_out")
        act_out = signal("act_out")
        pool_out = signal("pool_out")
        stored = signal("stored")

        def vlink(ins):
            ins.then_inc(*dve_step.up())
            nc.vector.wait_ge(dve_step.sem, dve_step.n)

        def alink(ins):
            ins.then_inc(*act_step.up())
            nc.scalar.wait_ge(act_step.sem, act_step.n)

        def bcast(ap, n):
            return ap.unsqueeze(1).to_broadcast([ap.shape[0], n, ap.shape[1]])

        def load_and_transpose(dram, dst, n_tok, first):
            n_t = n_tok // P
            with ExitStack() as st:
                rows = sbuf(st, "rows", [P, n_t, D])
                m0, a0, v0, l0 = mm_done.n, act_evac.n, dve_evac.n, inputs_in.n
                n_loads = 3 if first else 1
                with nc.Block() as block:
                    @block.sync
                    def _(sp):
                        if first:
                            sp.dma_start(base[:], A["consts"][:, 0:const_at["base_end"]]).then_inc(*inputs_in.up(16))
                            sp.dma_start(vec[:], A["vectors"]).then_inc(*inputs_in.up(16))
                        sp.dma_start(rows[:], dram.rearrange("(t p) d -> p t d", p=P)).then_inc(*inputs_in.up(16))

                    @block.tensor
                    def _(pe):
                        pe.wait_ge(inputs_in.sem, l0 + 16 * n_loads)
                        for d in range(KD):
                            for t in range(n_t):
                                last = nc.tensor.transpose(ps[:, d, t * P:(t + 1) * P], rows[:, t, d * P:(d + 1) * P], ident)
                            last.then_inc(*mm_done.up())

                    @block.scalar
                    def _(act):
                        for d in range(0, KD, 2):
                            act.wait_ge(mm_done.sem, m0 + d + 1)
                            nc.scalar.activation(dst[:, d, :], ps[:, d, 0:n_tok], ACT.Copy)

                    @block.vector
                    def _(dve):
                        for d in range(1, KD, 2):
                            dve.wait_ge(mm_done.sem, m0 + d + 1)
                            nc.vector.tensor_copy(dst[:, d, :], ps[:, d, 0:n_tok])

        def rms_norm(src, dst, n_tok, weight, shift=None, sq=None):
            sq = dst if sq is None else sq
            with ExitStack() as st:
                rt = sbuf(st, "rt", [P, 2, n_tok])
                m0, v0, a0 = mm_done.n, dve_out.n, act_out.n
                sums = ps[:, 0, 0:n_tok]
                with nc.Block() as block:
                    @block.tensor
                    def _(pe):
                        for k in range(KD):
                            if k % 2 == 0:
                                pe.wait_ge(dve_out.sem, v0 + k // 2 + 1)
                            else:
                                pe.wait_ge(act_out.sem, a0 + k // 2 + 1)
                            last = nc.tensor.matmul(sums, ones, sq[:, k, :], start=(k == 0), stop=(k == KD - 1))
                        last.then_inc(*mm_done.up())

                    @block.scalar
                    def _(act):
                        for k in range(1, KD, 2):
                            nc.scalar.activation(sq[:, k, :], src[:, k, :], ACT.Square).then_inc(*act_out.up())
                        act.wait_ge(dve_out.sem, v0 + KD // 2 + 1)
                        nc.scalar.activation(rt[:, 1, :], rt[:, 0, :], ACT.Sqrt).then_inc(*act_out.up())
                        if shift is not None:
                            for k in range(KD):
                                act.wait_ge(dve_out.sem, v0 + KD // 2 + 2 + k)
                                nc.scalar.activation(dst[:, k, :], dst[:, k, :], ACT.Identity, bias=shift(k))

                    @block.vector
                    def _(dve):
                        for k in range(0, KD, 2):
                            nc.vector.tensor_tensor(sq[:, k, :], src[:, k, :], src[:, k, :], ALU.mult).then_inc(*dve_out.up())
                        dve.wait_ge(mm_done.sem, m0 + 1)
                        nc.vector.tensor_scalar(rt[:, 0, :], sums, 1.0 / D, RMS_EPS, ALU.mult, ALU.add).then_inc(*dve_out.up())
                        dve.wait_ge(act_out.sem, a0 + KD // 2 + 1)
                        vlink(nc.vector.reciprocal(rt[:, 0, :], rt[:, 1, :]))
                        for k in range(KD):
                            nc.vector.scalar_tensor_tensor(dst[:, k, :], src[:, k, :], weight(k), rt[:, 0, :], ALU.mult, ALU.mult).then_inc(*dve_out.up())

        def project_first(hT, proj, gla_q, gla_k, gla_v, gla_gl, gla_og):
            w = A["w_in"].rearrange("(k p) n -> p k n", p=P)
            groups = [(c, min(512, RW_COLS - c)) for c in range(0, RW_COLS, 512)]
            groups += [(RW_COLS, 512), (RW_COLS + 512, 512), (RW_COLS + 1024, 32), (RW_COLS + 1056, 512)]
            tiles = []
            for g, (c0, n) in enumerate(groups):
                for j in range(0, n, P):
                    m = min(P, n - j)
                    if g < 4:
                        tiles.append((g, j, m, "rwkv", (c0 + j) // P))
                    else:
                        tiles.append((g, j, m, ("qk", "v", "gl", "og")[g - 4], j // P))
            n_rw = RW_COLS // P
            with ExitStack() as st:
                wb = sbuf(st, "wb", [P, 2, KD, 512])
                pad = sbuf(st, "pad", [P, 3, T + 2])
                tmp = sbuf(st, "tmp", [P, T])
                m0, a0, v0, p0 = mm_done.n, act_evac.n, dve_out.n, pool_out.n
                w0 = [w_in[0].n, w_in[1].n]
                end_of = [max(i for i, t in enumerate(tiles) if t[0] == g) + 1 for g in range(len(groups))]
                with nc.Block() as block:
                    @block.sync
                    def _(sp):
                        for g, (c0, n) in enumerate(groups):
                            if g >= 2:
                                sp.wait_ge(mm_done.sem, m0 + end_of[g - 2])
                            sp.dma_start(wb[:, g % 2, :, 0:n], w[:, :, c0:c0 + n]).then_inc(*w_in[g % 2].up(16))

                    @block.gpsimd
                    def _(pool):
                        nc.gpsimd.memset(pad[:], 0.0).then_inc(*pool_out.up())

                    @block.tensor
                    def _(pe):
                        for i, (g, j, m, kind, idx) in enumerate(tiles):
                            if i == 0 or tiles[i - 1][0] != g:
                                pe.wait_ge(w_in[g % 2].sem, w0[g % 2] + 16 * (g // 2 + 1))
                            if i >= 8:
                                pe.wait_ge(act_evac.sem, a0 + i - 7)
                            for k in range(KD):
                                if kind == "v":
                                    last = nc.tensor.matmul(ps[:, i % 8, :], hT[:, k, idx * P:(idx + 1) * P], wb[:, g % 2, k, :],
                                                            start=(k == 0), stop=(k == KD - 1))
                                else:
                                    last = nc.tensor.matmul(ps[0:m, i % 8, :], wb[:, g % 2, k, j:j + m], hT[:, k, :],
                                                            start=(k == 0), stop=(k == KD - 1))
                            last.then_inc(*mm_done.up())

                    @block.scalar
                    def _(act):
                        act.wait_ge(pool_out.sem, p0 + 1)
                        for i, (g, j, m, kind, idx) in enumerate(tiles):
                            act.wait_ge(mm_done.sem, m0 + i + 1)
                            src = ps[0:m, i % 8, :]
                            if kind == "rwkv":
                                if i >= 3:
                                    act.wait_ge(dve_out.sem, v0 + i - 2)
                                ins = nc.scalar.activation(pad[:, i % 3, 1:T + 1], src, ACT.Copy)
                            elif kind == "qk":
                                dst = gla_q if idx < 2 else gla_k
                                ins = nc.scalar.activation(dst[:, idx % 2, :], src, ACT.Copy, scale=GLA_DK ** -0.5 if idx < 2 else 1.0)
                            elif kind == "v":
                                ins = nc.scalar.activation(gla_v[:, idx, :], src, ACT.Copy)
                            elif kind == "gl":
                                ins = nc.scalar.activation(gla_gl[0:m, :], src, ACT.Copy)
                            else:
                                ins = nc.scalar.activation(gla_og[:, idx, :], src, ACT.Silu)
                            ins.then_inc(*act_evac.up())

                    @block.vector
                    def _(dve):
                        for i in range(n_rw):
                            dve.wait_ge(act_evac.sem, a0 + i + 1)
                            p = pad[:, i % 3, 1:T + 1]
                            if i > 0:
                                dve.wait_ge(dve_out.sem, v0 + i)
                            vlink(nc.vector.tensor_tensor(tmp[:], pad[:, i % 3, 0:T], pad[:, i % 3, 2:T + 2], ALU.add))
                            vlink(nc.vector.scalar_tensor_tensor(tmp[:], tmp[:], 0.5, p, ALU.mult, ALU.subtract))
                            nc.vector.scalar_tensor_tensor(proj[:, i, :], tmp[:], vcol("rw_mu", i), p, ALU.mult, ALU.add).then_inc(*dve_out.up())

        def rwkv_keys(proj, kk, w2, a2, g2, lnk):
            r_, k_, v_ = proj[:, 0:4, :], proj[:, 4:8, :], proj[:, 8:12, :]
            with ExitStack() as st:
                sq = sbuf(st, "sq", [P, CT, T])
                m0, a0, v0, l0 = mm_done.n, act_out.n, dve_out.n, inputs_in.n
                with nc.Block() as block:
                    @block.sync
                    def _(sp):
                        sp.dma_start(w2[0:64, :], A["rw_w2_f"]).then_inc(*inputs_in.up(16))
                        sp.dma_start(w2[64:128, :], A["rw_w2_b"]).then_inc(*inputs_in.up(16))
                        sp.dma_start(a2[0:64, :], A["rw_a2_f"]).then_inc(*inputs_in.up(16))
                        sp.dma_start(a2[64:128, :], A["rw_a2_b"]).then_inc(*inputs_in.up(16))
                        sp.dma_start(g2[:], A["rw_g2"]).then_inc(*inputs_in.up(16))
                        sp.wait_ge(inputs_in.sem, l0 + 80)

                    @block.vector
                    def _(dve):
                        for c in range(CT):
                            vlink(nc.vector.tensor_scalar(kk[:, c, :], k_[:, c, :], vcol("rw_k_k", c), None, ALU.mult))
                            nc.vector.tensor_tensor(sq[:, c, :], kk[:, c, :], kk[:, c, :], ALU.mult).then_inc(*dve_out.up())
                        for c in range(CT):
                            dve.wait_ge(act_out.sem, a0 + c + 1)
                            vlink(nc.vector.tensor_scalar(sq[:, c, :], sq[:, c, :], 1e-12, None, ALU.max))
                            vlink(nc.vector.reciprocal(sq[:, c, :], sq[:, c, :]))
                            nc.vector.tensor_tensor(kk[:, c, :], kk[:, c, :], sq[:, c, :], ALU.mult)

                    @block.tensor
                    def _(pe):
                        for c in range(CT):
                            pe.wait_ge(dve_out.sem, v0 + c + 1)
                            nc.tensor.matmul(ps[:, c, :], head_ones, sq[:, c, :], start=True, stop=True).then_inc(*mm_done.up())

                    @block.scalar
                    def _(act):
                        for c in range(CT):
                            act.wait_ge(mm_done.sem, m0 + c + 1)
                            nc.scalar.activation(sq[:, c, :], ps[:, c, :], ACT.Sqrt).then_inc(*act_out.up())
                        nc.scalar.activation(proj[:, 14, :], proj[:, 14, :], ACT.Sigmoid)
                        nc.scalar.activation(proj[:, 12, :], proj[:, 12, :], ACT.Tanh)

        def rwkv_direction(back, proj, kk, w2, a2, kd_sum, bufs):
            r_, k_ = proj[:, 0:4, :], proj[:, 4:8, :]
            lw, cc, ex, a_, kd, qt, rt = bufs["lw"], bufs["cc"], bufs["ex"], bufs["a"], bufs["kd"], bufs["q"], bufs["r"]
            half, scale = bufs["half"], bufs["scale"]
            rows = slice(64, 128) if back else slice(0, 64)
            w0, ka0 = ("rw_w0_b", "rw_a0_b") if back else ("rw_w0_f", "rw_a0_f")

            def chunks(t):
                return t[:, :, :].rearrange("p c (n i) -> p (c n) i", i=P)

            def flat(t):
                return t[:, :, :].rearrange("p c n -> p (c n)")

            m0, a0, v0 = mm_done.n, act_out.n, dve_out.n
            with nc.Block() as block:
                @block.tensor
                def _(pe):
                    for j in range(2 * CT):
                        c, w, x = j % CT, (w2, a2)[j // CT], proj[rows, 12 + j // CT, :]
                        nc.tensor.matmul(ps[:, j, :], w[rows, c * P:(c + 1) * P], x, start=True, stop=True).then_inc(*mm_done.up())

                @block.scalar
                def _(act):
                    for j in range(2 * CT):
                        c, name, dst = j % CT, (w0, ka0)[j // CT], (lw, a_)[j // CT]
                        act.wait_ge(mm_done.sem, m0 + j + 1)
                        nc.scalar.activation(dst[:, c, :], ps[:, j, :], ACT.Sigmoid, bias=vcol(name, c)).then_inc(*act_out.up())
                    act.wait_ge(dve_out.sem, v0 + 1)
                    nc.scalar.activation(scale[:], half[:], ACT.Exp).then_inc(*act_out.up())
                    act.wait_ge(dve_out.sem, v0 + 2)
                    if back:
                        nc.scalar.activation(flat(ex), flat(lw), ACT.Exp, scale=-1.0).then_inc(*act_out.up())
                        alink(nc.scalar.activation(flat(cc), flat(cc), ACT.Exp, scale=-1.0))
                    else:
                        alink(nc.scalar.activation(flat(ex), flat(cc), ACT.Exp, scale=-1.0))
                        nc.scalar.activation(flat(cc), flat(cc), ACT.Exp).then_inc(*act_out.up())
                    act.wait_ge(act_step.sem, act_step.n)
                    if back:
                        act.wait_ge(act_out.sem, act_out.n)
                    nc.scalar.activation(flat(lw), flat(lw), ACT.Exp).then_inc(*act_out.up())

                @block.vector
                def _(dve):
                    dve.wait_ge(act_out.sem, a0 + CT)
                    vlink(nc.vector.tensor_scalar(flat(lw), flat(lw), -math.exp(-0.5), None, ALU.mult))
                    for c in range(CT):
                        for n in range(KT):
                            at = slice(n * P, (n + 1) * P)
                            ins = nc.vector.tensor_tensor_scan(cc[:, c, at], ones, lw[:, c, at], 0.0, ALU.mult, ALU.add)
                    vlink(ins)
                    totals = chunks(cc)[:, :, P - 1:P]
                    ins = nc.vector.tensor_scalar(half[:].unsqueeze(2), totals, 0.5, None, ALU.mult)
                    ins.then_inc(*dve_out.up())
                    dve.wait_ge(dve_out.sem, v0 + 1)
                    vlink(nc.vector.tensor_tensor(chunks(cc), chunks(cc), half[:].unsqueeze(2).to_broadcast([P, CT * KT, P]), ALU.subtract))
                    nc.vector.tensor_tensor(flat(lw), flat(cc), flat(lw), ALU.subtract).then_inc(*dve_out.up())
                    dve.wait_ge(act_out.sem, a0 + 2 * CT)
                    for c in range(CT):
                        ins = nc.vector.tensor_scalar(kd[:, c, :], a_[:, c, :], -1.0, vcol("rw_k_a", c), ALU.add, ALU.mult)
                    vlink(ins)
                    vlink(nc.vector.scalar_tensor_tensor(flat(kd), flat(kd), 1.0, flat(k_), ALU.add, ALU.mult))
                    if back:
                        nc.vector.tensor_tensor(flat(kd_sum), flat(kd_sum), flat(kd), ALU.add)
                    else:
                        nc.vector.tensor_copy(flat(kd_sum), flat(kd))
                    vlink(nc.vector.tensor_tensor(flat(a_), flat(a_), flat(kk), ALU.mult))
                    dve.wait_ge(act_out.sem, a0 + 2 * CT + 3)
                    dve.wait_ge(act_step.sem, act_step.n)
                    eq, er, eb = (cc, ex, lw) if back else (lw, cc, ex)
                    nc.vector.tensor_tensor(flat(qt), flat(kk), flat(eq), ALU.mult)
                    nc.vector.tensor_tensor(flat(rt), flat(r_), flat(er), ALU.mult)
                    nc.vector.tensor_tensor(flat(kd), flat(kd), flat(eb), ALU.mult)
                    nc.vector.tensor_tensor(flat(a_), flat(a_), flat(eb), ALU.mult)

        def to_tokens(pairs):
            m0 = mm_done.n
            a0 = act_evac.n
            v0 = dve_evac.n
            jobs = [(src, dst, n) for src, dst in pairs for n in range(KT)]
            with nc.Block() as block:
                @block.tensor
                def _(pe):
                    for j, (src, dst, n) in enumerate(jobs):
                        if j >= 8:
                            if j % 2:
                                pe.wait_ge(act_evac.sem, a0 + (j - 8) // 2 + 1)
                            else:
                                pe.wait_ge(dve_evac.sem, v0 + (j - 8) // 2 + 1)
                        n_c = src.shape[1]
                        for c in range(n_c):
                            last = nc.tensor.transpose(ps[:, j % 8, c * P:(c + 1) * P], src[:, c, n * P:(n + 1) * P], ident)
                        last.then_inc(*mm_done.up())

                @block.scalar
                def _(act):
                    for j, (src, dst, n) in enumerate(jobs):
                        if j % 2:
                            act.wait_ge(mm_done.sem, m0 + j + 1)
                            nc.scalar.activation(dst[:, n, :], ps[:, j % 8, 0:src.shape[1] * P], ACT.Copy).then_inc(*act_evac.up())

                @block.vector
                def _(dve):
                    for j, (src, dst, n) in enumerate(jobs):
                        if j % 2 == 0:
                            dve.wait_ge(mm_done.sem, m0 + j + 1)
                            nc.vector.tensor_copy(dst[:, n, :], ps[:, j % 8, 0:src.shape[1] * P]).then_inc(*dve_evac.up())

        def rwkv_scan(back, bufs, v_tok, y, masks):
            qt, rt, kt, bt = bufs["q"], bufs["r"], bufs["kd"], bufs["a"]
            b_tok, k_tok = bufs["b_tok"], bufs["k_tok"]
            scale = bufs["scale"]
            N, X, Z, U, BT, RB, RK = (bufs[n] for n in ("N", "X", "Z", "U", "BT", "RB", "RK"))
            rhs, sa, S, hop = bufs["rhs"], bufs["sa"], bufs["S"], bufs["hop"]
            d = 1 if back else 0
            strict = masks["strict"][:, d * P:(d + 1) * P]
            incl = masks["incl"][:, d * P:(d + 1) * P]

            def level(l, back_=back):
                at = (LEVELS * int(back_) + l) * P
                return masks["levels"][:, at:at + P]

            order = list(range(KT))[::-1] if back else list(range(KT))
            H4 = CT
            rows = (slice(0, 64), slice(64, 128))
            jobs = []
            for n in order:
                for par in range(2):
                    jobs += [(n, nm, par, 0) for nm in ("A", "N", "RB", "BT", "RK")]
                for l in range(1, LEVELS):
                    jobs += [(n, "U", par, l) for par in range(2)]
                    for par in range(2):
                        if l < LEVELS - 1:
                            jobs.append((n, "X", par, l))
                        jobs.append((n, "Z", par, l))
                jobs += [(n, "rhs", 0, 0), (n, "rhs", 1, 0), (n, "sa", 0, 0), (n, "y", 0, 0), (n, "y", 1, 0), (n, "S", 0, 0)]
            number = {job: i for i, job in enumerate(jobs)}
            m0, e0 = mm_done.n, dve_evac.n

            def four(bank):
                return ps[:, bank, :].rearrange("p (h i) -> p h i", h=H4)

            with nc.Block() as block:
                @block.tensor
                def _(pe):
                    free = [0]

                    def evacuated(job):
                        need = number[job] + 1
                        if need > free[0]:
                            free[0] = need
                            pe.wait_ge(dve_evac.sem, e0 + need)

                    for i, (n, nm, par, l) in enumerate(jobs):
                        at = slice(n * P, (n + 1) * P)
                        r = rows[par]
                        bank = ps[:, i % 8, :]
                        if i >= 8:
                            evacuated(jobs[i - 8])
                        mm = nc.tensor.matmul
                        if nm in ("A", "N", "RB", "BT", "RK"):
                            lhs, rhs_ = {"A": (qt, bt), "N": (bt, qt), "RB": (bt, rt), "BT": (kt, qt), "RK": (kt, rt)}[nm]
                            for h in range(H4):
                                last = mm(bank[:, h * P:(h + 1) * P], lhs[r, h, at], rhs_[r, h, at], start=True, stop=True)
                        elif nm == "U":
                            evacuated((n, "RK", par, 0) if l == 1 else (n, "X", par, l - 1))
                            for h in range(H4):
                                last = mm(bank[:, h * P:(h + 1) * P], N[:, par, h, :], X[:, par, h, :], start=True, stop=True)
                        elif nm == "X":
                            evacuated((n, "U", par, l))
                            for h in range(H4):
                                last = mm(bank[:, h * P:(h + 1) * P], Z[:, par, h, :], U[:, par, h, :], start=True, stop=True)
                        elif nm == "Z":
                            evacuated((n, "U", par, l))
                            for h in range(H4):
                                last = mm(bank[:, h * P:(h + 1) * P], U[:, par, h, :], Z[:, par, h, :], start=True, stop=True)
                        elif nm == "rhs":
                            evacuated((n, "RK", 1, 0))
                            if n != order[0]:
                                evacuated((order[order.index(n) - 1], "S", 0, 0))
                            for h in range(H4):
                                o = bank[:, h * 64:(h + 1) * 64]
                                mm(o, qt[r, h, at], S[r, h, :], start=True, stop=False)
                                last = mm(o, BT[:, par, h, :], v_tok[:, n, h * P + par * 64:h * P + par * 64 + 64], start=False, stop=True)
                        elif nm == "sa":
                            evacuated((n, "Z", 1, LEVELS - 1))
                            evacuated((n, "rhs", 1, 0))
                            for h in range(H4):
                                for q in range(2):
                                    last = mm(bank[:, (2 * h + q) * 64:(2 * h + q + 1) * 64], Z[:, q, h, :], rhs[:, q, h, :], start=True, stop=True)
                        elif nm == "y":
                            evacuated((n, "sa", 0, 0))
                            for h in range(H4):
                                o = bank[r, h * P:(h + 1) * P]
                                head = slice(h * P + par * 64, h * P + par * 64 + 64)
                                mm(o, S[r, h, :], rt[r, h, at], start=True, stop=False)
                                mm(o, sa[:, head], RB[:, par, h, :], start=False, stop=False)
                                last = mm(o, v_tok[:, n, head], RK[:, par, h, :], start=False, stop=True)
                        else:
                            for h in range(H4):
                                for q in range(2):
                                    o = bank[rows[q], h * 64:(h + 1) * 64]
                                    head = slice(h * P + q * 64, h * P + q * 64 + 64)
                                    mm(o, b_tok[:, n, head], sa[:, head], start=True, stop=False)
                                    last = mm(o, k_tok[:, n, head], v_tok[:, n, head], start=False, stop=True)
                        last.then_inc(*mm_done.up())

                @block.vector
                def _(dve):
                    sc = scale[:].rearrange("p (c n) -> p c n", n=KT)
                    for j, n in enumerate(order[:-1]):
                        nc.vector.tensor_tensor(hop[:, j, :], sc[:, :, n], sc[:, :, order[j + 1]], ALU.mult)
                    vlink(nc.vector.memset(S[:], 0.0))
                    for i, (n, nm, par, l) in enumerate(jobs):
                        dve.wait_ge(mm_done.sem, m0 + i + 1)
                        at = slice(n * P, (n + 1) * P)
                        r = rows[par]
                        bank = four(i % 8)
                        tt = nc.vector.tensor_tensor
                        if nm == "A":
                            vlink(tt(X[:, par], bank, bcast(level(0), H4), ALU.mult))
                            ins = tt(X[:, par], bcast(ident, H4), X[:, par], ALU.subtract)
                        elif nm == "N":
                            vlink(tt(N[:, par], bank, bcast(strict, H4), ALU.mult))
                            vlink(tt(Z[:, par], N[:, par], bcast(level(0, not back), H4), ALU.mult))
                            ins = tt(Z[:, par], bcast(ident, H4), Z[:, par], ALU.subtract)
                        elif nm in ("RB", "BT", "RK"):
                            ins = tt({"RB": RB, "BT": BT, "RK": RK}[nm][:, par], bank, bcast(strict if nm == "BT" else incl, H4), ALU.mult)
                        elif nm == "U":
                            ins = tt(U[:, par], bank, bcast(level(l), H4), ALU.mult)
                        elif nm in ("X", "Z"):
                            M = X if nm == "X" else Z
                            ins = tt(M[:, par], M[:, par], bank, ALU.subtract)
                        elif nm == "rhs":
                            ins = nc.vector.tensor_scalar(rhs[:, par], ps[:, i % 8, 0:256].rearrange("p (h v) -> p h v", h=H4), -1.0, None, ALU.mult)
                        elif nm == "sa":
                            ins = nc.vector.tensor_copy(sa[:], ps[:, i % 8, :])
                        elif nm == "y":
                            o = y[r, :, at]
                            if back:
                                ins = tt(o, o, bank[r], ALU.add)
                            else:
                                ins = nc.vector.tensor_copy(o, bank[r])
                        else:
                            j = order.index(n)
                            if j == KT - 1:
                                ins = nc.vector.tensor_copy(S[:], ps[:, i % 8, 0:256].rearrange("p (h v) -> p h v", h=H4))
                            else:
                                vlink(tt(S[:], S[:], ps[:, i % 8, 0:256].rearrange("p (h v) -> p h v", h=H4), ALU.add))
                                ins = tt(S[:], S[:], hop[:, j, :].unsqueeze(2).to_broadcast([P, CT, 64]), ALU.mult)
                        ins.then_inc(*dve_evac.up())
                        dve.wait_ge(dve_evac.sem, e0 + i + 1)

        def rwkv_output(proj, y, kd_sum, g2):
            r_, v_ = proj[:, 0:4, :], proj[:, 8:12, :]
            with ExitStack() as st:
                sq = sbuf(st, "gn_sq", [P, CT, T])
                m0, v0, a0 = mm_done.n, dve_out.n, act_out.n
                n_mm = 4 * CT
                with nc.Block() as block:
                    @block.tensor
                    def _(pe):
                        for c in range(CT):
                            nc.tensor.matmul(ps[:, c, :], head_ones, y[:, c, :], start=True, stop=True).then_inc(*mm_done.up())
                        for c in range(CT):
                            nc.tensor.matmul(ps[:, 4 + c, :], g2[:, c * P:(c + 1) * P], proj[:, 14, :], start=True, stop=True).then_inc(*mm_done.up())
                        for c in range(CT):
                            pe.wait_ge(dve_out.sem, v0 + c + 1)
                            nc.tensor.matmul(ps[:, c, :], head_ones, sq[:, c, :], start=True, stop=True).then_inc(*mm_done.up())
                        for c in range(CT):
                            pe.wait_ge(dve_out.sem, v0 + 2 * CT + c + 1)
                            nc.tensor.matmul(ps[:, c, :], head_ones, kd_sum[:, c, :], start=True, stop=True).then_inc(*mm_done.up())

                    @block.scalar
                    def _(act):
                        for c in range(CT):
                            act.wait_ge(dve_out.sem, v0 + CT + c + 1)
                            nc.scalar.activation(sq[:, c, :], sq[:, c, :], ACT.Sqrt).then_inc(*act_out.up())

                    @block.vector
                    def _(dve):
                        for c in range(CT):
                            dve.wait_ge(mm_done.sem, m0 + c + 1)
                            vlink(nc.vector.scalar_tensor_tensor(y[:, c, :], ps[:, c, :], -1.0 / RW_HD, y[:, c, :], ALU.mult, ALU.add))
                            nc.vector.tensor_tensor(sq[:, c, :], y[:, c, :], y[:, c, :], ALU.mult).then_inc(*dve_out.up())
                        for c in range(CT):
                            dve.wait_ge(mm_done.sem, m0 + 2 * CT + c + 1)
                            nc.vector.tensor_scalar(sq[:, c, :], ps[:, c, :], 1.0 / RW_HD, RW_GN_EPS, ALU.mult, ALU.add).then_inc(*dve_out.up())
                        for c in range(CT):
                            nc.vector.scalar_tensor_tensor(kd_sum[:, c, :], r_[:, c, :], vcol("rw_r_k", c), kd_sum[:, c, :], ALU.mult, ALU.mult).then_inc(*dve_out.up())
                        for c in range(CT):
                            dve.wait_ge(act_out.sem, a0 + c + 1)
                            vlink(nc.vector.reciprocal(sq[:, c, :], sq[:, c, :]))
                            vlink(nc.vector.tensor_tensor(y[:, c, :], y[:, c, :], sq[:, c, :], ALU.mult))
                            vlink(nc.vector.tensor_scalar(y[:, c, :], y[:, c, :], vcol("rw_ln_w", c), vcol("rw_ln_b", c), ALU.mult, ALU.add))
                            dve.wait_ge(mm_done.sem, m0 + 3 * CT + c + 1)
                            vlink(nc.vector.tensor_tensor(v_[:, c, :], ps[:, c, :], v_[:, c, :], ALU.mult))
                            vlink(nc.vector.tensor_tensor(y[:, c, :], y[:, c, :], v_[:, c, :], ALU.add))
                            nc.vector.tensor_tensor(y[:, c, :], ps[:, 4 + c, :], y[:, c, :], ALU.mult)

        def gla_mixer(q, k, v_tok, gl, og, o, masks):
            n_sub = P // GLA_SUB
            NT = 2
            C8 = NT * KT

            def flat(t):
                return t[:, :, :].rearrange("p c n -> p (c n)")

            def chunks(t):
                return t[:, :, :].rearrange("p c (n i) -> p (c n) i", i=P)

            with ExitStack() as st:
                gw2 = sbuf(st, "gw2", [32, 2, 256])
                z = sbuf(st, "gz", [P, NT, T])
                L = sbuf(st, "gL", [P, NT, T])
                e = sbuf(st, "ge", [P, NT, T])
                qs = sbuf(st, "g_qs", [P, NT, T])
                qc = sbuf(st, "g_qc", [P, NT, T])
                kc = sbuf(st, "g_kc", [P, NT, T])
                ks = sbuf(st, "g_ks", [P, n_sub, NT, T])
                kc_tok = sbuf(st, "g_kc_tok", [P, KT, NT * P])
                att = sbuf(st, "g_att", [P, 4, P])
                S = sbuf(st, "g_S", [P, NT, P])
                last_decay = sbuf(st, "g_last", [P, C8])
                l0 = inputs_in.n
                with nc.Block() as block:
                    @block.sync
                    def _(sp):
                        sp.dma_start(gw2[:], A["gla_gw2"]).then_inc(*inputs_in.up(16))
                        sp.wait_ge(inputs_in.sem, l0 + 16)
                for back in (False, True):
                    d = int(back)
                    incl = masks["incl"][:, d * P:(d + 1) * P]
                    order = list(range(KT))[::-1] if back else list(range(KT))
                    gb = "gla_gb_b" if back else "gla_gb_f"
                    m0, a0, v0 = mm_done.n, act_out.n, dve_out.n
                    with nc.Block() as block:
                        @block.tensor
                        def _(pe):
                            for c in range(NT):
                                nc.tensor.matmul(ps[:, c, :], gw2[:, d, c * P:(c + 1) * P], gl[:, :], start=True, stop=True).then_inc(*mm_done.up())

                        @block.scalar
                        def _(act):
                            act.wait_ge(dve_out.sem, v0 + 1)
                            alink(nc.scalar.activation(flat(e), flat(z), ACT.Abs))
                            alink(nc.scalar.activation(flat(e), flat(e), ACT.Exp, scale=-1.0))
                            nc.scalar.activation(flat(e), flat(e), ACT.Ln, bias=1.0).then_inc(*act_out.up())
                            act.wait_ge(dve_out.sem, v0 + 2)
                            alink(nc.scalar.activation(flat(z), flat(L), ACT.Exp))
                            nc.scalar.activation(last_decay[:].unsqueeze(2), chunks(z)[:, :, 0:1] if back else chunks(z)[:, :, P - 1:P], ACT.Copy).then_inc(*act_out.up())
                            act.wait_ge(dve_out.sem, v0 + 3)
                            nc.scalar.activation(flat(kc), flat(kc), ACT.Exp).then_inc(*act_out.up())
                            act.wait_ge(dve_out.sem, v0 + 4)
                            nc.scalar.activation(flat(qs), flat(qs), ACT.Exp).then_inc(*act_out.up())
                            for s in range(n_sub):
                                act.wait_ge(dve_out.sem, v0 + 5 + s)
                                nc.scalar.activation(flat(ks[:, s]), flat(ks[:, s]), ACT.Exp, scale=-1.0).then_inc(*act_out.up())

                        @block.vector
                        def _(dve):
                            for c in range(NT):
                                dve.wait_ge(mm_done.sem, m0 + c + 1)
                                ins = nc.vector.tensor_scalar(z[:, c, :], ps[:, c, :], vcol(gb, c), None, ALU.add)
                            ins.then_inc(*dve_out.up())
                            dve.wait_ge(act_out.sem, a0 + 1)
                            vlink(nc.vector.scalar_tensor_tensor(flat(z), flat(z), 0.0, flat(e), ALU.min, ALU.subtract))
                            vlink(nc.vector.tensor_scalar(flat(z), flat(z), 1.0 / GLA_TAU, None, ALU.mult))
                            for j in range(C8):
                                ins = nc.vector.tensor_tensor_scan(chunks(L)[:, j, :], ones, chunks(z)[:, j, :], 0.0, ALU.mult, ALU.add)
                            if back:
                                vlink(ins)
                                vlink(nc.vector.tensor_tensor(chunks(z), chunks(z), chunks(L)[:, :, P - 1:P].to_broadcast([P, C8, P]), ALU.add))
                                ins = nc.vector.tensor_tensor(flat(L), flat(z), flat(L), ALU.subtract)
                            ins.then_inc(*dve_out.up())
                            dve.wait_ge(dve_out.sem, v0 + 2)
                            total = chunks(L)[:, :, 0:1] if back else chunks(L)[:, :, P - 1:P]
                            nc.vector.tensor_tensor(chunks(kc), total.to_broadcast([P, C8, P]), chunks(L), ALU.subtract).then_inc(*dve_out.up())
                            for s in range(n_sub):
                                sub = slice(s * GLA_SUB, (s + 1) * GLA_SUB)
                                mid = s * GLA_SUB + GLA_SUB // 2
                                anchor = chunks(L)[:, :, mid:mid + 1]
                                ins = nc.vector.tensor_tensor(chunks(qs)[:, :, sub], chunks(L)[:, :, sub], anchor.to_broadcast([P, C8, GLA_SUB]), ALU.subtract)
                            vlink(ins)
                            nc.vector.tensor_scalar(flat(qs), flat(qs), GLA_CLAMP, None, ALU.min).then_inc(*dve_out.up())
                            for s in range(n_sub):
                                mid = s * GLA_SUB + GLA_SUB // 2
                                anchor = chunks(L)[:, :, mid:mid + 1]
                                vlink(nc.vector.tensor_tensor(chunks(ks[:, s]), chunks(L), anchor.to_broadcast([P, C8, P]), ALU.subtract))
                                nc.vector.tensor_scalar(flat(ks[:, s]), flat(ks[:, s]), -GLA_CLAMP, None, ALU.max).then_inc(*dve_out.up())
                            dve.wait_ge(act_out.sem, a0 + 4)
                            dve.wait_ge(act_step.sem, act_step.n)
                            nc.vector.tensor_tensor(flat(qc), flat(q), flat(z), ALU.mult)
                            nc.vector.tensor_tensor(flat(kc), flat(k), flat(kc), ALU.mult)
                            nc.vector.tensor_tensor(flat(qs), flat(q), flat(qs), ALU.mult)
                            for s in range(n_sub):
                                dve.wait_ge(act_out.sem, a0 + 5 + s)
                                nc.vector.tensor_tensor(flat(ks[:, s]), flat(k), flat(ks[:, s]), ALU.mult)
                    to_tokens([(kc, kc_tok)])
                    rows = (slice(0, 64), slice(64, 128))
                    jobs = []
                    for n in order:
                        jobs += [(n, "att", 0), (n, "att", 1), (n, "o", 0), (n, "o", 1), (n, "S", 0)]
                    number = {job: i for i, job in enumerate(jobs)}
                    m1, e1 = mm_done.n, dve_evac.n
                    with nc.Block() as block:
                        @block.tensor
                        def _(pe):
                            for i, (n, nm, par) in enumerate(jobs):
                                at = slice(n * P, (n + 1) * P)
                                r = rows[par]
                                bank = ps[:, i % 8, :]
                                if i >= 8:
                                    pe.wait_ge(dve_evac.sem, e1 + i - 7)
                                if nm == "att":
                                    for c in range(NT):
                                        for s in range(n_sub):
                                            sub = slice(n * P + s * GLA_SUB, n * P + (s + 1) * GLA_SUB)
                                            o0 = c * P + s * GLA_SUB
                                            last = nc.tensor.matmul(bank[:, o0:o0 + GLA_SUB], ks[r, s, c, at], qs[r, c, sub], start=True, stop=True)
                                elif nm == "o":
                                    pe.wait_ge(dve_evac.sem, e1 + number[(n, "att", 1)] + 1)
                                    if n != order[0]:
                                        pe.wait_ge(dve_evac.sem, e1 + number[(order[order.index(n) - 1], "S", 0)] + 1)
                                    for c in range(NT):
                                        h = 2 * c + par
                                        nc.tensor.matmul(bank[:, c * P:(c + 1) * P], S[r, c, :], qc[r, c, at], start=True, stop=False)
                                        last = nc.tensor.matmul(bank[:, c * P:(c + 1) * P], v_tok[:, n, h * P:(h + 1) * P], att[:, h, :], start=False, stop=True)
                                else:
                                    for c in range(NT):
                                        for q_ in range(2):
                                            h = 2 * c + q_
                                            last = nc.tensor.matmul(bank[rows[q_], c * P:(c + 1) * P], kc_tok[:, n, h * 64:(h + 1) * 64],
                                                                    v_tok[:, n, h * P:(h + 1) * P], start=True, stop=True)
                                last.then_inc(*mm_done.up())

                        @block.vector
                        def _(dve):
                            vlink(nc.vector.memset(S[:], 0.0))
                            ld = last_decay[:].rearrange("p (c n) -> p c n", n=KT)
                            for i, (n, nm, par) in enumerate(jobs):
                                at = slice(n * P, (n + 1) * P)
                                dve.wait_ge(mm_done.sem, m1 + i + 1)
                                two = ps[:, i % 8, 0:2 * P].rearrange("p (c i) -> p c i", c=NT)
                                if nm == "att":
                                    ins = nc.vector.tensor_tensor(att[:, par::2, :], two, bcast(incl, NT), ALU.mult)
                                elif nm == "o":
                                    dst = o[:, par::2, at]
                                    if back:
                                        ins = nc.vector.tensor_tensor(dst, dst, two, ALU.add)
                                    else:
                                        ins = nc.vector.tensor_copy(dst, two)
                                else:
                                    vlink(nc.vector.tensor_tensor(S[:], S[:], ld[:, :, n:n + 1].to_broadcast([P, NT, P]), ALU.mult))
                                    ins = nc.vector.tensor_tensor(S[:], S[:], two, ALU.add)
                                ins.then_inc(*dve_evac.up())
                                dve.wait_ge(dve_evac.sem, e1 + i + 1)
                m2, v2, a2 = mm_done.n, dve_out.n, act_out.n
                with nc.Block() as block:
                    @block.tensor
                    def _(pe):
                        for c in range(CT):
                            pe.wait_ge(dve_out.sem, v2 + c + 1)
                            nc.tensor.matmul(ps[:, c, :], ones, ks[:, c, 0, :], start=True, stop=True).then_inc(*mm_done.up())

                    @block.scalar
                    def _(act):
                        for c in range(CT):
                            act.wait_ge(dve_out.sem, v2 + CT + c + 1)
                            nc.scalar.activation(ks[:, c, 1, :], ks[:, c, 0, :], ACT.Sqrt).then_inc(*act_out.up())

                    @block.vector
                    def _(dve):
                        for c in range(CT):
                            nc.vector.tensor_tensor(ks[:, c, 0, :], o[:, c, :], o[:, c, :], ALU.mult).then_inc(*dve_out.up())
                        for c in range(CT):
                            dve.wait_ge(mm_done.sem, m2 + c + 1)
                            nc.vector.tensor_scalar(ks[:, c, 0, :], ps[:, c, :], 1.0 / P, RMS_EPS, ALU.mult, ALU.add).then_inc(*dve_out.up())
                        for c in range(CT):
                            dve.wait_ge(act_out.sem, a2 + c + 1)
                            vlink(nc.vector.reciprocal(ks[:, c, 1, :], ks[:, c, 1, :]))
                            vlink(nc.vector.scalar_tensor_tensor(o[:, c, :], o[:, c, :], vcol("gla_norm_w", c), ks[:, c, 1, :], ALU.mult, ALU.mult))
                            nc.vector.tensor_tensor(o[:, c, :], o[:, c, :], og[:, c, :], ALU.mult)
        def project_residual(w_dram, src, dst, gate=None, bias=None):
            w = w_dram.rearrange("(k p) n -> p k n", p=P)
            n_g = D // 512
            with ExitStack() as st:
                wb = sbuf(st, "wo" + str(mm_done.n), [P, n_g, KD, 512])
                tmp = sbuf(st, "wt" + str(mm_done.n), [P, 2, T])
                m0, v0 = mm_done.n, dve_evac.n
                w0 = [w_in[0].n, w_in[1].n]
                with nc.Block() as block:
                    @block.sync
                    def _(sp):
                        for g in range(n_g):
                            sp.dma_start(wb[:, g], w[:, :, g * 512:(g + 1) * 512]).then_inc(*w_in[g].up(16))

                    @block.tensor
                    def _(pe):
                        for m in range(KD):
                            if m % 4 == 0:
                                pe.wait_ge(w_in[m // 4].sem, w0[m // 4] + 16)
                            for k in range(KD):
                                last = nc.tensor.matmul(ps[:, m, :], wb[:, m // 4, k, (m % 4) * P:(m % 4 + 1) * P], src[:, k, :],
                                                        start=(k == 0), stop=(k == KD - 1))
                            last.then_inc(*mm_done.up())

                    @block.vector
                    def _(dve):
                        for m in range(KD):
                            dve.wait_ge(mm_done.sem, m0 + m + 1)
                            if gate is None:
                                nc.vector.tensor_tensor(dst[:, m, :], ps[:, m, :], dst[:, m, :], ALU.add)
                            elif bias is None:
                                nc.vector.scalar_tensor_tensor(dst[:, m, :], ps[:, m, :], gate(m), dst[:, m, :], ALU.mult, ALU.add)
                            else:
                                if m >= 2:
                                    dve.wait_ge(dve_evac.sem, v0 + m - 1)
                                vlink(nc.vector.tensor_scalar(tmp[:, m % 2, :], ps[:, m, :], bias(m), gate(m), ALU.add, ALU.mult))
                                nc.vector.tensor_tensor(dst[:, m, :], tmp[:, m % 2, :], dst[:, m, :], ALU.add).then_inc(*dve_evac.up())

        def rows_of(src, dst):
            m0, a0, v0 = mm_done.n, act_evac.n, dve_evac.n
            jobs = [(n, half) for n in range(KT) for half in range(2)]
            with nc.Block() as block:
                @block.tensor
                def _(pe):
                    for j, (n, half) in enumerate(jobs):
                        for c in range(4):
                            last = nc.tensor.transpose(ps[:, j, c * P:(c + 1) * P], src[:, half * 4 + c, n * P:(n + 1) * P], ident)
                        last.then_inc(*mm_done.up())

                @block.scalar
                def _(act):
                    for j, (n, half) in enumerate(jobs):
                        if half:
                            act.wait_ge(mm_done.sem, m0 + j + 1)
                            nc.scalar.activation(dst[:, n, 512:1024], ps[:, j, :], ACT.Copy)

                @block.vector
                def _(dve):
                    for j, (n, half) in enumerate(jobs):
                        if not half:
                            dve.wait_ge(mm_done.sem, m0 + j + 1)
                            nc.vector.tensor_copy(dst[:, n, 0:512], ps[:, j, :])

        def route_first(hT, rankm, wts, over_one, over_first, over_int):
            E, NG, NE = N_EXP1, N_GROUPS, PER_GROUP
            n_log = NG + E
            with ExitStack() as st:
                wr = sbuf(st, "w_route", [P, KD, n_log])
                br = sbuf(st, "b_route", [1, n_log])
                lg = sbuf(st, "logits", [P, KT, n_log])
                t4 = sbuf(st, "t4", [P, KT, NG])
                og = sbuf(st, "one_group", [P, KT, NG])
                prod = sbuf(st, "prod", [P, KT, NE, NG])
                fs = sbuf(st, "fine", [P, KT, NE])
                t8 = sbuf(st, "t8", [P, KT, NE])
                o1 = sbuf(st, "one_first", [P, KT, NE])
                o2 = sbuf(st, "one_second", [P, KT, NE])
                col = {n: sbuf(st, "col_" + n, [P, KT]) for n in ("m", "pg", "m1", "m2", "e2", "c1", "c2", "t")}
                E1 = sbuf(st, "E1", [P, KT, NG, NE])
                E2 = sbuf(st, "E2", [P, KT, NG, NE])
                M = sbuf(st, "Mboth", [P, KT, E])
                cnt = sbuf(st, "cnt", [P, E])
                nov = sbuf(st, "nov", [P, E])
                gt = sbuf(st, "gt", [P, E])
                cum = sbuf(st, "cum", [P, E])
                cux = sbuf(st, "cux", [P, E])
                ov = sbuf(st, "ov", [P, N_OVER, E])
                ofl = sbuf(st, "ofl", [P, N_OVER + 1])
                m0, a0, v0, l0 = mm_done.n, act_out.n, dve_out.n, inputs_in.n
                V = nc.vector

                def tt(o, a, b, op):
                    vlink(V.tensor_tensor(o, a, b, op))

                def over(ap, n):
                    return ap.unsqueeze(len(ap.shape)).to_broadcast(list(ap.shape) + [n])

                with nc.Block() as block:
                    @block.sync
                    def _(sp):
                        sp.dma_start(wr[:], A["moe_w_route"].rearrange("(k p) n -> p k n", p=P)).then_inc(*inputs_in.up(16))
                        sp.dma_start(br[:], A["moe_b_route"]).then_inc(*inputs_in.up(16))

                    @block.tensor
                    def _(pe):
                        pe.wait_ge(inputs_in.sem, l0 + 32)
                        for t in range(KT):
                            o = ps[:, 0, t * n_log:(t + 1) * n_log]
                            for k in range(KD):
                                nc.tensor.matmul(o, hT[:, k, t * P:(t + 1) * P], wr[:, k, :], start=(k == 0), stop=False)
                            last = nc.tensor.matmul(o, ones[0:1, :], br[:], start=False, stop=True)
                        last.then_inc(*mm_done.up())
                        pe.wait_ge(dve_out.sem, v0 + 3)
                        for t in range(KT):
                            o = ps[:, 1, t * E:(t + 1) * E]
                            for s in range(t + 1):
                                nc.tensor.matmul(o, before if s == t else ones, M[:, s, :], start=(s == 0), stop=(s == t))
                        for t in range(KT):
                            last = nc.tensor.matmul(ps[:, 2, 0:E], ones, M[:, t, :], start=(t == 0), stop=(t == KT - 1))
                        last.then_inc(*mm_done.up())

                    @block.scalar
                    def _(act):
                        act.wait_ge(dve_out.sem, v0 + 1)
                        nc.scalar.activation(t4[:], t4[:], ACT.Exp).then_inc(*act_out.up())
                        act.wait_ge(dve_out.sem, v0 + 2)
                        nc.scalar.activation(col["e2"][:], col["e2"][:], ACT.Exp).then_inc(*act_out.up())

                    @block.vector
                    def _(dve):
                        dve.wait_ge(mm_done.sem, m0 + 1)
                        vlink(V.tensor_copy(lg[:], ps[:, 0, 0:KT * n_log].rearrange("p (t n) -> p t n", t=KT)))
                        coarse = lg[:, :, 0:NG]
                        fine = lg[:, :, NG:].rearrange("p t (g e) -> p t e g", g=NG)
                        vlink(V.tensor_reduce(col["m"][:], coarse, AX.X, ALU.max))
                        V.tensor_tensor(t4[:], coarse, over(col["m"][:], NG), ALU.subtract).then_inc(*dve_out.up())
                        tt(og[:], coarse, over(col["m"][:], NG), ALU.is_equal)
                        tt(og[:], og[:], bcast(first4, KT), ALU.mult)
                        vlink(V.tensor_reduce(col["t"][:], og[:], AX.X, ALU.max))
                        tt(og[:], og[:], over(col["t"][:], NG), ALU.is_equal)
                        tt(prod[:], fine, og[:].unsqueeze(2).to_broadcast([P, KT, NE, NG]), ALU.mult)
                        vlink(V.tensor_reduce(fs[:], prod[:], AX.X, ALU.add))
                        for m, o in (("m1", o1), ("m2", o2)):
                            vlink(V.tensor_reduce(col[m][:], fs[:], AX.X, ALU.max))
                            tt(o[:], fs[:], over(col[m][:], NE), ALU.is_equal)
                            tt(o[:], o[:], bcast(first8, KT), ALU.mult)
                            vlink(V.tensor_reduce(col["t"][:], o[:], AX.X, ALU.max))
                            tt(o[:], o[:], over(col["t"][:], NE), ALU.is_equal)
                            if m == "m1":
                                vlink(V.tensor_scalar(t8[:], o1[:], -3e38, None, ALU.mult))
                                tt(fs[:], fs[:], t8[:], ALU.add)
                        V.tensor_tensor(col["e2"][:], col["m2"][:], col["m1"][:], ALU.subtract).then_inc(*dve_out.up())
                        for Eo, o in ((E1, o1), (E2, o2)):
                            tt(Eo[:], over(og[:], NE), o[:].unsqueeze(2).to_broadcast([P, KT, NG, NE]), ALU.mult)
                        e1, e2 = (x[:].rearrange("p t g e -> p t (g e)") for x in (E1, E2))
                        V.tensor_tensor(M[:], e1, e2, ALU.add).then_inc(*dve_out.up())
                        dve.wait_ge(act_out.sem, a0 + 2)
                        vlink(V.tensor_reduce(col["pg"][:], t4[:], AX.X, ALU.add))
                        vlink(V.reciprocal(col["pg"][:], col["pg"][:]))
                        vlink(V.tensor_scalar(col["c1"][:], col["e2"][:], 1.0, None, ALU.add))
                        vlink(V.reciprocal(col["c1"][:], col["c1"][:]))
                        tt(col["c1"][:], col["c1"][:], col["pg"][:], ALU.mult)
                        tt(col["c2"][:], col["c1"][:], col["e2"][:], ALU.mult)
                        tt(wts[:], e1, over(col["c1"][:], E), ALU.mult)
                        tt(e2, e2, over(col["c2"][:], E), ALU.mult)
                        tt(wts[:], wts[:], e2, ALU.add)
                        dve.wait_ge(mm_done.sem, m0 + 2)
                        vlink(V.scalar_tensor_tensor(rankm[:], ps[:, 1, 0:KT * E].rearrange("p (t e) -> p t e", t=KT), 1.0, M[:], ALU.add, ALU.mult))
                        vlink(V.tensor_scalar(rankm[:], rankm[:], -1.0, None, ALU.add))
                        vlink(V.tensor_copy(cnt[:], ps[:, 2, 0:E]))
                        vlink(V.tensor_scalar(nov[:], cnt[:], float(SLOTS), None, ALU.is_gt))
                        for j in range(2, MORE1 + 1):
                            vlink(V.tensor_scalar(gt[:], cnt[:], float(j * SLOTS), None, ALU.is_gt))
                            tt(nov[:], nov[:], gt[:], ALU.add)
                        vlink(V.tensor_tensor_scan(cum[:], ones[:, 0:E], nov[:], 0.0, ALU.mult, ALU.add))
                        tt(cux[:], cum[:], nov[:], ALU.subtract)
                        o_ax = overflows.unsqueeze(2).to_broadcast([P, N_OVER, E])
                        tt(over_one[:], bcast(cux[:], N_OVER), o_ax, ALU.is_le)
                        tt(ov[:], bcast(cum[:], N_OVER), o_ax, ALU.is_gt)
                        tt(over_one[:], over_one[:], ov[:], ALU.mult)
                        tt(ov[:], over_one[:], bcast(cux[:], N_OVER), ALU.mult)
                        vlink(V.tensor_reduce(over_first[:], ov[:], AX.X, ALU.add))
                        tt(over_first[:], overflows, over_first[:], ALU.subtract)
                        vlink(V.tensor_scalar(over_first[:], over_first[:], 1.0, float(SLOTS), ALU.add, ALU.mult))
                        tt(ov[:], over_one[:], bcast(experts, N_OVER), ALU.mult)
                        vlink(V.tensor_reduce(ofl[:, 0:N_OVER], ov[:], AX.X, ALU.add))
                        vlink(V.tensor_copy(ofl[:, N_OVER:], cum[:, E - 1:E]))
                        V.tensor_copy(over_int[:], ofl[:])

        def experts_pass(tag, h_tok, rankm, wts, n_exp, w_gate, w_up, w_down, ff, out_gate):
            n_groups = n_exp // (2 * PAIRS)
            halves = ff // 512
            steps = [(p, fh) for p in range(PAIRS) for fh in range(halves)]
            S = len(steps)
            GS = 2 * PAIRS * SLOTS
            wg = w_gate.rearrange("e (k p) f -> e p k f", p=P)
            wu = w_up.rearrange("e (k p) f -> e p k f", p=P)
            wd = w_down.rearrange("e (f p) d -> e p f d", p=P)
            units = []
            for s in range(S + 1):
                if s < S:
                    units += [("gate", s, 0), ("gate", s, 1), ("up", s, 0), ("up", s, 1)]
                if s > 0:
                    units += [("down", s - 1, 0), ("down", s - 1, 1)]
            U = len(units)
            unit_at = {u: i for i, u in enumerate(units)}
            assert U % RING == 0
            turns = U // RING
            jobs = [("gather", d) for d in range(KD)] + [("weights", p) for p in range(PAIRS)]
            for s in range(S + 1):
                if s < S:
                    jobs += [("gate", s), ("up", s)]
                if s > 0:
                    jobs += [("turn", s - 1), ("down", s - 1)]
            jobs += [("scatter", d) for d in range(KD)]
            job_at = {j: i + 1 for i, j in enumerate(jobs)}
            act_jobs = [("gather", d) for d in range(0, KD, 2)] + [("weights", p) for p in range(PAIRS)]
            dve_jobs = [("onehot", t) for t in range(KT)] + [("gather", d) for d in range(1, KD, 2)] + [("weighted", t) for t in range(KT)]
            for s in range(S + 1):
                if s < S:
                    act_jobs += [("silu", s)]
                    dve_jobs += [("hidden", s)]
                if s > 0:
                    dve_jobs += [("turned", s - 1)]
                    if steps[s - 1][1] == halves - 1:
                        act_jobs += [("y0", steps[s - 1][0]), ("y1", steps[s - 1][0])]
            dve_jobs += [("scatter", d) for d in range(KD)]
            act_at = {j: i + 1 for i, j in enumerate(act_jobs)}
            dve_at = {j: i + 1 for i, j in enumerate(dve_jobs)}
            NM, NA, NV = len(jobs), len(act_jobs), len(dve_jobs)

            with ExitStack() as st:
                ring = sbuf(st, tag + "_ring", [P, RING, 4096])
                G = sbuf(st, tag + "_G", [P, KT, GS])
                XG = sbuf(st, tag + "_XG", [P, KD, GS])
                GT = sbuf(st, tag + "_GT", [P, PAIRS, T])
                sil = sbuf(st, tag + "_sil", [P, 2, 512])
                hid = sbuf(st, tag + "_hid", [P, 2, 512])
                hidT = sbuf(st, tag + "_hidT", [P, 2, 4, P])
                unit_in = [signal(f"{tag}_unit_in{j}") for j in range(RING)]
                mm = signal(tag + "_mm")
                act_did = signal(tag + "_act")
                dve_did = signal(tag + "_dve")
                XG_p = XG[:].rearrange("p k (q s) -> p k q s", q=PAIRS)

                def ring_unit(name, s, x):
                    return ring[:, unit_at[(name, s, x)] % RING, :]

                with nc.Block() as block:
                    @block.sync
                    def _(sp):
                        sp.sem_inc(mm.sem, NM)
                        with sp.Fori(0, n_groups) as g:
                            for i, (name, s, x) in enumerate(units):
                                p, fh = steps[s]
                                e = g * (2 * PAIRS) + (2 * p + x)
                                old, old_s, _ = units[i - RING]
                                sp.wait_ge(mm.sem, (g + (1 if i >= RING else 0)) * NM + job_at[(old, old_s)])
                                if name == "down":
                                    src = wd[bass.ds(e, 1), :, fh * 4:(fh + 1) * 4, :].rearrange("e p f d -> p (e f) d")
                                    dst = ring_unit(name, s, x).rearrange("p (f d) -> p f d", f=4)
                                else:
                                    w = wg if name == "gate" else wu
                                    src = w[bass.ds(e, 1), :, :, fh * 512:(fh + 1) * 512].rearrange("e p k f -> p (e k) f")
                                    dst = ring_unit(name, s, x).rearrange("p (k f) -> p k f", k=KD)
                                sp.dma_start(dst, src).then_inc(unit_in[i % RING].sem, 16)

                    @block.tensor
                    def _(pe):
                        with pe.Fori(0, n_groups) as g:
                            def after_act(job):
                                pe.wait_ge(act_did.sem, g * NA + act_at[job])

                            def after_dve(job):
                                pe.wait_ge(dve_did.sem, g * NV + dve_at[job])

                            def unit(name, s, x):
                                i = unit_at[(name, s, x)]
                                pe.wait_ge(unit_in[i % RING].sem, (g * turns + (i // RING + 1)) * 16)

                            after_dve(("onehot", KT - 1))
                            for d in range(KD):
                                for t in range(KT):
                                    last = nc.tensor.matmul(ps[:, d, :], h_tok[:, t, d * P:(d + 1) * P], G[:, t, :], start=(t == 0), stop=(t == KT - 1))
                                last.then_inc(mm.sem, 1)
                            after_dve(("weighted", KT - 1))
                            after_act(("gather", KD - 2))
                            for p in range(PAIRS):
                                for t in range(KT):
                                    last = nc.tensor.transpose(ps[:, p, t * P:(t + 1) * P], G[:, t, p * P:(p + 1) * P], ident)
                                last.then_inc(mm.sem, 1)
                            after_act(("weights", PAIRS - 1))

                            def gate_up(s):
                                p, fh = steps[s]
                                for j, name in enumerate(("gate", "up")):
                                    bank = 2 * (s % 2) + j
                                    unit(name, s, 0)
                                    unit(name, s, 1)
                                    if s >= 2:
                                        after_dve(("hidden", s - 2))
                                    for k in range(KD):
                                        for x in range(2):
                                            c0 = p * P + x * SLOTS
                                            w = ring_unit(name, s, x)[:, k * 512:(k + 1) * 512]
                                            last = nc.tensor.matmul(ps[x * SLOTS:(x + 1) * SLOTS, bank, :], XG[:, k, c0:c0 + SLOTS], w,
                                                                    start=(k == 0), stop=(k == KD - 1))
                                    last.then_inc(mm.sem, 1)

                            def down(s):
                                p, fh = steps[s]
                                turn = 4 + 3 * (s % 2)
                                after_dve(("hidden", s))
                                for f in range(4):
                                    last = nc.tensor.transpose(ps[:, turn, f * P:(f + 1) * P], hid[:, s % 2, f * P:(f + 1) * P], ident)
                                last.then_inc(mm.sem, 1)
                                unit("down", s, 0)
                                unit("down", s, 1)
                                after_dve(("turned", s))
                                if fh == 0 and p > 0:
                                    after_act(("y1", p - 1))
                                for x in range(2):
                                    rows = slice(x * SLOTS, (x + 1) * SLOTS)
                                    w = ring_unit("down", s, x)
                                    for half in range(2):
                                        for f in range(4):
                                            last = nc.tensor.matmul(ps[rows, 5 + half, :], hidT[:, s % 2, f, rows],
                                                                    w[:, f * D + half * 512:f * D + half * 512 + 512],
                                                                    start=(fh == 0 and f == 0), stop=(fh == halves - 1 and f == 3))
                                last.then_inc(mm.sem, 1)

                            for s in range(S + 1):
                                if s < S:
                                    gate_up(s)
                                if s > 0:
                                    down(s - 1)
                            after_act(("y1", PAIRS - 1))
                            for d in range(KD):
                                for p in range(PAIRS):
                                    last = nc.tensor.matmul(ps[:, d, :], XG_p[:, d, p, :], GT[:, p, :], start=(p == 0), stop=(p == PAIRS - 1))
                                last.then_inc(mm.sem, 1)

                    @block.scalar
                    def _(act):
                        with act.Fori(0, n_groups) as g:
                            def after_pe(job):
                                act.wait_ge(mm.sem, (g + 1) * NM + job_at[job])

                            for job in act_jobs:
                                name, j = job
                                if name == "gather":
                                    after_pe(job)
                                    ins = nc.scalar.activation(XG[:, j, :], ps[:, j, :], ACT.Copy)
                                elif name == "weights":
                                    after_pe(job)
                                    ins = nc.scalar.activation(GT[:, j, :], ps[:, j, :], ACT.Copy)
                                elif name == "silu":
                                    after_pe(("gate", j))
                                    if j >= 2:
                                        act.wait_ge(dve_did.sem, g * NV + dve_at[("hidden", j - 2)])
                                    ins = nc.scalar.activation(sil[:, j % 2, :], ps[:, 2 * (j % 2), :], ACT.Silu)
                                else:
                                    half = int(name[1])
                                    after_pe(("down", j * halves + halves - 1))
                                    ins = nc.scalar.activation(XG_p[:, 4 * half:4 * half + 4, j, :], ps[:, 5 + half, :].rearrange("p (k c) -> p k c", k=4), ACT.Copy)
                                ins.then_inc(act_did.sem, 1)

                    @block.vector
                    def _(dve):
                        with dve.Fori(0, n_groups) as g:
                            def after_pe(job):
                                dve.wait_ge(mm.sem, (g + 1) * NM + job_at[job])

                            mine = g * (2 * PAIRS)
                            for job in dve_jobs:
                                name, j = job
                                if name == "onehot":
                                    r = rankm[:, j, bass.ds(mine, 2 * PAIRS)].unsqueeze(2).to_broadcast([P, 2 * PAIRS, SLOTS])
                                    ins = nc.vector.tensor_tensor(G[:, j, :].rearrange("p (e s) -> p e s", s=SLOTS), bcast(slots, 2 * PAIRS), r, ALU.is_equal)
                                elif name == "gather":
                                    after_pe(job)
                                    ins = nc.vector.tensor_copy(XG[:, j, :], ps[:, j, :])
                                elif name == "weighted":
                                    if j == 0:
                                        after_pe(("gather", KD - 1))
                                    w = wts[:, j, bass.ds(mine, 2 * PAIRS)].unsqueeze(2).to_broadcast([P, 2 * PAIRS, SLOTS])
                                    o = G[:, j, :].rearrange("p (e s) -> p e s", s=SLOTS)
                                    ins = nc.vector.tensor_tensor(o, o, w, ALU.mult)
                                elif name == "hidden":
                                    after_pe(("up", j))
                                    dve.wait_ge(act_did.sem, g * NA + act_at[("silu", j)])
                                    if j >= 2:
                                        after_pe(("turn", j - 2))
                                    ins = nc.vector.tensor_tensor(hid[:, j % 2, :], ps[:, 2 * (j % 2) + 1, :], sil[:, j % 2, :], ALU.mult)
                                elif name == "turned":
                                    after_pe(("turn", j))
                                    ins = nc.vector.tensor_copy(hidT[:, j % 2], ps[:, 4 + 3 * (j % 2), :].rearrange("p (f s) -> p f s", f=4))
                                else:
                                    after_pe(("scatter", j))
                                    if out_gate is None:
                                        ins = nc.vector.tensor_tensor(xT[:, j, :], ps[:, j, :], xT[:, j, :], ALU.add)
                                    else:
                                        ins = nc.vector.scalar_tensor_tensor(xT[:, j, :], ps[:, j, :], out_gate(j), xT[:, j, :], ALU.mult, ALU.add)
                                ins.then_inc(dve_did.sem, 1)

        def overflow_pass(h_tok, rankm, wts, over_one, over_first, over_int):
            wg = A["moe_w_gate"].rearrange("e (k p) f -> e p k f", p=P)
            wu = A["moe_w_up"].rearrange("e (k p) f -> e p k f", p=P)
            wd = A["moe_w_down"].rearrange("e (f p) d -> e p f d", p=P)
            with ExitStack() as st:
                wgb = sbuf(st, "ov_wg", [P, KD, 512])
                wub = sbuf(st, "ov_wu", [P, KD, 512])
                wdb = sbuf(st, "ov_wd", [P, 4, D])
                sel = sbuf(st, "ov_sel", [P, KT, N_EXP1])
                r_o = sbuf(st, "ov_r", [P, KT])
                w_o = sbuf(st, "ov_w", [P, KT])
                G = sbuf(st, "ov_G", [P, KT, P])
                X = sbuf(st, "ov_X", [P, KD, SLOTS])
                GT = sbuf(st, "ov_GT", [SLOTS, T])
                hid = sbuf(st, "ov_hid", [P, 512])
                hidT = sbuf(st, "ov_hidT", [P, 4, SLOTS])
                Y = sbuf(st, "ov_Y", [SLOTS, D])
                w_here = signal("ov_w_here")
                mm = signal("ov_mm")
                dve_did = signal("ov_dve")
                silu = signal("ov_silu")
                v_steps = ["sel", "r", "sel2", "w", "shift", "G0", "G1", "G2", "G3", "X", "W0", "W1", "W2", "W3", "GT", "hid", "hidT", "Y0", "Y1"]
                v_steps += [f"out{d}" for d in range(KD)]
                v_at = {n: i + 1 for i, n in enumerate(v_steps)}
                p_steps = ["gather", "gt", "gate", "up", "turn", "down"] + [f"out{d}" for d in range(KD)]
                p_at = {n: i + 1 for i, n in enumerate(p_steps)}
                NV, NP = len(v_steps), len(p_steps)

                with nc.Block() as block:
                    @block.gpsimd
                    def _(pool):
                        nc.gpsimd.memset(G[:], 0.0).then_inc(dve_did.sem, 1)
                        nc.gpsimd.memset(hid[:], 0.0).then_inc(mm.sem, 1)

                def blocks(eng):
                    return eng.value_load(over_int[0:1, N_OVER:N_OVER + 1], min_val=0, max_val=N_OVER)

                with nc.Block() as block:
                    @block.sync
                    def _(sp):
                        n = blocks(sp)
                        with sp.Fori(0, N_OVER) as o:
                            with sp.If(o < n):
                                e = sp.value_load(over_int[0:1, bass.ds(o, 1)], min_val=0, max_val=N_EXP1 - 1)
                                sp.wait_ge(mm.sem, o * NP + 1)
                                sp.dma_start(wgb[:], wg[bass.ds(e, 1)].rearrange("e p k f -> p (e k) f")).then_inc(w_here.sem, 16)
                                sp.dma_start(wub[:], wu[bass.ds(e, 1)].rearrange("e p k f -> p (e k) f")).then_inc(w_here.sem, 16)
                                sp.dma_start(wdb[:], wd[bass.ds(e, 1)].rearrange("e p f d -> p (e f) d")).then_inc(w_here.sem, 16)

                    @block.tensor
                    def _(pe):
                        n = blocks(pe)
                        with pe.Fori(0, N_OVER) as o:
                            with pe.If(o < n):
                                def after(step):
                                    pe.wait_ge(dve_did.sem, o * NV + v_at[step] + 1)

                                after("G3")
                                for d in range(KD):
                                    for t in range(KT):
                                        last = nc.tensor.matmul(ps[:, 0, d * SLOTS:(d + 1) * SLOTS], h_tok[:, t, d * P:(d + 1) * P], G[:, t, 0:SLOTS], start=(t == 0), stop=(t == KT - 1))
                                last.then_inc(mm.sem, 1)
                                after("W3")
                                for t in range(KT):
                                    last = nc.tensor.transpose(ps[:, 1, t * P:(t + 1) * P], G[:, t, :], ident)
                                last.then_inc(mm.sem, 1)
                                pe.wait_ge(w_here.sem, o * 48 + 48)
                                for bank, w in ((2, wgb), (3, wub)):
                                    for k in range(KD):
                                        last = nc.tensor.matmul(ps[0:SLOTS, bank, :], X[:, k, :], w[:, k, :], start=(k == 0), stop=(k == KD - 1))
                                    last.then_inc(mm.sem, 1)
                                after("hid")
                                for f in range(4):
                                    last = nc.tensor.transpose(ps[:, 4, f * P:(f + 1) * P], hid[:, f * P:(f + 1) * P], ident)
                                last.then_inc(mm.sem, 1)
                                after("hidT")
                                for half in range(2):
                                    for f in range(4):
                                        last = nc.tensor.matmul(ps[0:SLOTS, 5 + half, :], hidT[:, f, :], wdb[:, f, half * 512:(half + 1) * 512], start=(f == 0), stop=(f == 3))
                                last.then_inc(mm.sem, 1)
                                after("Y1")
                                for d in range(KD):
                                    nc.tensor.matmul(ps[:, d, :], Y[:, d * P:(d + 1) * P], GT[:], start=True, stop=True).then_inc(mm.sem, 1)

                    @block.scalar
                    def _(act):
                        n = blocks(act)
                        with act.Fori(0, N_OVER) as o:
                            with act.If(o < n):
                                act.wait_ge(mm.sem, o * NP + p_at["gate"] + 1)
                                act.wait_ge(dve_did.sem, o * NV + 1)
                                nc.scalar.activation(hid[0:SLOTS, :], ps[0:SLOTS, 2, :], ACT.Silu).then_inc(silu.sem, 1)

                    @block.vector
                    def _(dve):
                        n = blocks(dve)
                        with dve.Fori(0, N_OVER) as o:
                            with dve.If(o < n):
                                V = nc.vector

                                def done(step, ins):
                                    ins.then_inc(dve_did.sem, 1)
                                    if step != v_steps[-1]:
                                        dve.wait_ge(dve_did.sem, o * NV + v_at[step] + 1)

                                def after(step):
                                    dve.wait_ge(mm.sem, o * NP + p_at[step] + 1)

                                dve.wait_ge(dve_did.sem, o * NV + 1)
                                one = over_one[:, bass.ds(o, 1), :].to_broadcast([P, KT, N_EXP1])
                                done("sel", V.tensor_tensor(sel[:], rankm[:], one, ALU.mult))
                                done("r", V.tensor_reduce(r_o[:], sel[:], AX.X, ALU.add))
                                done("sel2", V.tensor_tensor(sel[:], wts[:], one, ALU.mult))
                                done("w", V.tensor_reduce(w_o[:], sel[:], AX.X, ALU.add))
                                done("shift", V.tensor_tensor(r_o[:], r_o[:], over_first[:, bass.ds(o, 1)].to_broadcast([P, KT]), ALU.subtract))
                                for t in range(KT):
                                    done(f"G{t}", V.tensor_scalar(G[:, t, 0:SLOTS], slots, r_o[:, t:t + 1], None, ALU.is_equal))
                                after("gather")
                                done("X", V.tensor_copy(X[:], ps[:, 0, :].rearrange("p (k s) -> p k s", k=KD)))
                                for t in range(KT):
                                    done(f"W{t}", V.tensor_scalar(G[:, t, 0:SLOTS], G[:, t, 0:SLOTS], w_o[:, t:t + 1], None, ALU.mult))
                                after("gt")
                                done("GT", V.tensor_copy(GT[:], ps[0:SLOTS, 1, :]))
                                after("up")
                                dve.wait_ge(silu.sem, o + 1)
                                done("hid", V.tensor_tensor(hid[0:SLOTS, :], ps[0:SLOTS, 3, :], hid[0:SLOTS, :], ALU.mult))
                                after("turn")
                                done("hidT", V.tensor_copy(hidT[:], ps[:, 4, :].rearrange("p (f s) -> p f s", f=4)[:, :, 0:SLOTS]))
                                after("down")
                                for half in range(2):
                                    done(f"Y{half}", V.tensor_copy(Y[:, half * 512:(half + 1) * 512], ps[0:SLOTS, 5 + half, :]))
                                for d in range(KD):
                                    after(f"out{d}")
                                    done(f"out{d}", V.tensor_tensor(xT[:, d, :], ps[:, d, :], xT[:, d, :], ALU.add))

        def modulation(l, mod, mod_c, scaled):
            w = A["w_mod_2"][l].rearrange("(k p) n -> p k n", p=P)
            n_g = 6 * D // 512
            n_buf = 4
            with ExitStack() as st:
                wb = sbuf(st, "mod_w", [P, n_buf, KD, 512])
                rows = sbuf(st, "mod_rows", [P, 2, 512])
                act_c = sbuf(st, "mod_c", [P, KD, 32])
                here = [signal(f"mod{l}_w{j}") for j in range(n_buf)]
                m0, v0, a0, p0 = mm_done.n, dve_out.n, act_out.n, pool_out.n
                picked = table("quarter_rows", 2)
                with nc.Block() as block:
                    @block.sync
                    def _(sp):
                        for g in range(n_g):
                            if g >= n_buf:
                                sp.wait_ge(mm_done.sem, m0 + 2 * (g - n_buf) + 1)
                            sp.dma_start(wb[:, g % n_buf], w[:, :, g * 512:(g + 1) * 512]).then_inc(*here[g % n_buf].up(16))

                    @block.gpsimd
                    def _(pool):
                        nc.gpsimd.memset(act_c[:], 0.0).then_inc(*pool_out.up())

                    @block.scalar
                    def _(act):
                        act.wait_ge(pool_out.sem, p0 + 1)
                        nc.scalar.activation(act_c[:, :, 0:1], vcol("c_2", 0, KD).unsqueeze(2), ACT.Silu).then_inc(*act_out.up())
                        nc.scalar.activation(act_c[:, :, 1:2], vcol("c_ctx_2", 0, KD).unsqueeze(2), ACT.Silu).then_inc(*act_out.up())

                    @block.tensor
                    def _(pe):
                        pe.wait_ge(act_out.sem, a0 + 2)

                        def columns(g):
                            pe.wait_ge(dve_out.sem, v0 + g + 1)
                            for j in range(4):
                                at = 2 * (4 * g + j)
                                last = nc.tensor.matmul(ps[:, 7, at:at + 2], rows[:, g % 2, j * P:(j + 1) * P], picked, start=True, stop=True)
                            last.then_inc(*mm_done.up())

                        for g in range(n_g):
                            pe.wait_ge(here[g % n_buf].sem, here[g % n_buf].n - 16 * ((n_g - 1 - g) // n_buf))
                            if g >= 2:
                                pe.wait_ge(dve_out.sem, v0 + g - 1)
                            for k in range(KD):
                                q = k % 4
                                last = nc.tensor.matmul(ps[32 * q:32 * q + 32, g % 2, :], act_c[:, k, :], wb[:, g % n_buf, k, :],
                                                        start=(k < 4), stop=(k >= 4))
                            last.then_inc(*mm_done.up())
                            if g > 0:
                                columns(g - 1)
                        columns(n_g - 1)

                    @block.vector
                    def _(dve):
                        for g in range(n_g):
                            dve.wait_ge(mm_done.sem, m0 + (1 if g == 0 else 2 * g))
                            if g >= 2:
                                dve.wait_ge(mm_done.sem, m0 + 2 * g - 1 if g < 3 else m0 + 2 * (g - 1) - 1)
                            nc.vector.tensor_copy(rows[:, g % 2, :], ps[:, g % 2, :]).then_inc(*dve_out.up())
                        dve.wait_ge(mm_done.sem, m0 + 2 * n_g)
                        got = ps[:, 7, 0:96].rearrange("p (c j) -> p c j", j=2)
                        bias = vcol("b_mod_2", 48 * l, 48)
                        vlink(nc.vector.tensor_tensor(mod[:], got[:, :, 0], bias, ALU.add))
                        for j, (norm, part) in enumerate((("norm1_g_2", 1), ("norm2_g_2", 4))):
                            nc.vector.scalar_tensor_tensor(scaled[:, j, :], mod[:, 8 * part:8 * part + 8], 1.0, vcol(norm, 8 * l, 8), ALU.add, ALU.mult)
                        if l == 0:
                            vlink(nc.vector.tensor_tensor(mod_c[:, 0:16], got[:, 0:16, 1], bias[:, 0:16], ALU.add))
                            nc.vector.scalar_tensor_tensor(mod_c[:, 16:24], mod_c[:, 8:16], 1.0, vcol("norm1_g_2", 0, 8), ALU.add, ALU.mult)

        def project_even(hT, n_tok, col_tiles, gate, xa, hy):
            w = A["w_in_2"].rearrange("(k p) n -> p k n", p=P)
            groups = [col_tiles[i:i + 4] for i in range(0, len(col_tiles), 4)]
            n = len(col_tiles)
            conv = [i for i in range(n) if col_tiles[i] >= 4]
            nth = {i: j for j, i in enumerate(conv)}
            with ExitStack() as st:
                wb = sbuf(st, "we", [P, 2, KD, 512])
                pad = sbuf(st, "pad_e", [P, 3, n_tok + 3])
                m0, a0, v0, p0 = mm_done.n, act_evac.n, dve_out.n, pool_out.n
                w0 = [w_in[0].n, w_in[1].n]
                with nc.Block() as block:
                    @block.sync
                    def _(sp):
                        for g, tiles in enumerate(groups):
                            if g >= 2:
                                sp.wait_ge(mm_done.sem, m0 + 4 * (g - 1))
                            sp.dma_start(wb[:, g % 2], w[:, :, tiles[0] * P:tiles[0] * P + 512]).then_inc(*w_in[g % 2].up(16))

                    @block.gpsimd
                    def _(pool):
                        nc.gpsimd.memset(pad[:], 0.0).then_inc(*pool_out.up())

                    @block.tensor
                    def _(pe):
                        for i in range(n):
                            g, j = i // 4, i % 4
                            if j == 0:
                                pe.wait_ge(w_in[g % 2].sem, w0[g % 2] + 16 * (g // 2 + 1))
                            if i >= 8:
                                pe.wait_ge(act_evac.sem, a0 + i - 7)
                            for k in range(KD):
                                last = nc.tensor.matmul(ps[:, i % 8, 0:n_tok], wb[:, g % 2, k, j * P:(j + 1) * P], hT[:, k, :],
                                                        start=(k == 0), stop=(k == KD - 1))
                            last.then_inc(*mm_done.up())

                    @block.scalar
                    def _(act):
                        act.wait_ge(pool_out.sem, p0 + 1)
                        for i, c in enumerate(col_tiles):
                            act.wait_ge(mm_done.sem, m0 + i + 1)
                            if c < 4:
                                ins = nc.scalar.activation(gate[:, c, :], ps[:, i % 8, 0:n_tok], ACT.Gelu_apprx_tanh)
                            else:
                                if nth[i] >= 3:
                                    act.wait_ge(dve_out.sem, v0 + nth[i] - 2)
                                ins = nc.scalar.activation(pad[:, nth[i] % 3, 1:n_tok + 1], ps[:, i % 8, 0:n_tok], ACT.Copy)
                            ins.then_inc(*act_evac.up())

                    @block.vector
                    def _(dve):
                        for i in conv:
                            c = col_tiles[i]
                            dve.wait_ge(act_evac.sem, a0 + i + 1)
                            if c < 8:
                                dst, taps, wt, bias, t0, n_t = xa[:, c - 4, :], 4, "conv_a_w_2", "conv_a_b_2", c - 4, 4
                            else:
                                dst, taps, wt, bias, t0, n_t = hy[:, c - 8, :], 3, "conv_b_w_2", "conv_b_b_2", c - 8, 12
                            b = nth[i] % 3
                            vlink(nc.vector.tensor_scalar(dst, pad[:, b, 0:n_tok], vcol(wt, t0), vcol(bias, t0), ALU.mult, ALU.add))
                            for k in range(1, taps):
                                ins = nc.vector.scalar_tensor_tensor(dst, pad[:, b, k:n_tok + k], vcol(wt, k * n_t + t0), dst, ALU.mult, ALU.add)
                                if k < taps - 1:
                                    vlink(ins)
                            ins.then_inc(*dve_out.up())

        def lru_rates(rate):
            with ExitStack() as st:
                e = sbuf(st, "rate_e", [P, 8])
                lam = vcol("lru_lam_2", 0, 8)
                a0 = act_out.n
                with nc.Block() as block:
                    @block.scalar
                    def _(act):
                        alink(nc.scalar.activation(e[:], lam, ACT.Abs))
                        alink(nc.scalar.activation(e[:], e[:], ACT.Exp, scale=-1.0))
                        nc.scalar.activation(e[:], e[:], ACT.Ln, bias=1.0).then_inc(*act_out.up())

                    @block.vector
                    def _(dve):
                        dve.wait_ge(act_out.sem, a0 + 1)
                        vlink(nc.vector.scalar_tensor_tensor(e[:], lam, 0.0, e[:], ALU.min, ALU.subtract))
                        nc.vector.tensor_scalar(rate[:, 0, :], e[:], LRU_C, None, ALU.mult)
                        nc.vector.tensor_scalar(rate[:, 1, :], e[:], -LRU_C, None, ALU.mult)

        def lru_scan(xa, n_tok, gates, rate, start, final, total):
            n_j = 2 * CT
            with ExitStack() as st:
                r = sbuf(st, "lru_r", [P, n_j, n_tok])
                i_ = sbuf(st, "lru_i", [P, n_j, n_tok])
                th = sbuf(st, "lru_th", [P, n_j, n_tok])
                h = sbuf(st, "lru_h", [P, n_j, n_tok])
                m0, a0, v0 = mm_done.n, act_out.n, dve_out.n
                with nc.Block() as block:
                    @block.tensor
                    def _(pe):
                        for q in range(2):
                            for j in range(n_j):
                                if q == 1:
                                    pe.wait_ge(act_out.sem, a0 + j + 1)
                                nc.tensor.matmul(ps[:, j, 0:n_tok], gates[:, q, j // CT, j % CT, :], xa[:, j % CT, :], start=True, stop=True).then_inc(*mm_done.up())

                    @block.scalar
                    def _(act):
                        for q, (dst, bias) in enumerate(((r, "lru_br_2"), (i_, "lru_bi_2"))):
                            for j in range(n_j):
                                act.wait_ge(mm_done.sem, m0 + q * n_j + j + 1)
                                nc.scalar.activation(dst[:, j, :], ps[:, j, 0:n_tok], ACT.Sigmoid, bias=vcol(bias, j)).then_inc(*act_out.up())
                        act.wait_ge(act_out.sem, act_out.n)
                        for j in range(n_j):
                            nc.scalar.activation(th[:, j, :], r[:, j, :], ACT.Tanh, scale=rate[:, 1, j:j + 1]).then_inc(*act_out.up())
                        act.wait_ge(act_out.sem, act_out.n)
                        for j in range(n_j):
                            nc.scalar.activation(r[:, j, :], r[:, j, :], ACT.Exp, scale=rate[:, 0, j:j + 1]).then_inc(*act_out.up())
                        for j in range(n_j):
                            act.wait_ge(dve_out.sem, v0 + j + 1)
                            nc.scalar.activation(th[:, j, :], th[:, j, :], ACT.Sqrt).then_inc(*act_out.up())

                    @block.vector
                    def _(dve):
                        for j in range(n_j):
                            dve.wait_ge(act_out.sem, a0 + 3 * n_j + j + 1)
                            vlink(nc.vector.tensor_tensor(h[:, j, :], r[:, j, :], r[:, j, :], ALU.mult))
                            nc.vector.scalar_tensor_tensor(th[:, j, :], h[:, j, :], 1.0, th[:, j, :], ALU.add, ALU.mult).then_inc(*dve_out.up())
                        for j in range(n_j):
                            vlink(nc.vector.tensor_tensor(i_[:, j, :], i_[:, j, :], xa[:, j % CT, :], ALU.mult))
                            dve.wait_ge(act_out.sem, a0 + 4 * n_j + j + 1)
                            vlink(nc.vector.tensor_tensor(i_[:, j, :], i_[:, j, :], th[:, j, :], ALU.mult))
                            s0 = 0.0 if start is None else start[:, j:j + 1]
                            way = slice(None, None, -1) if j >= CT else slice(None)
                            vlink(nc.vector.tensor_tensor_scan(h[:, j, way], r[:, j, way], i_[:, j, way], s0, ALU.mult, ALU.add))
                            if final is not None:
                                end = 0 if j >= CT else n_tok - 1
                                nc.vector.tensor_copy(final[:, j:j + 1], h[:, j, end:end + 1])
                            if total is not None and j >= CT:
                                c = j - CT
                                vlink(nc.vector.tensor_tensor(h[:, j, :], h[:, j, :], h[:, c, :], ALU.add))
                                nc.vector.tensor_tensor(total[:, c, :], total[:, c, :], h[:, j, :], ALU.mult)

        def hyena_filters(spec, Kc, Ks):
            with ExitStack() as st:
                z = sbuf(st, "f_z", [FILTER_EMB, T])
                w1 = sbuf(st, "f_w1", [FILTER_EMB, FILTER_HIDDEN])
                w2 = sbuf(st, "f_w2", [FILTER_HIDDEN, FILTER_HIDDEN])
                w3 = sbuf(st, "f_w3", [FILTER_HIDDEN + 1, 4 * HYENA_WIDTH])
                win = sbuf(st, "f_win", [P, KT, HYENA_WIDTH])
                x = sbuf(st, "f_x", [FILTER_HIDDEN, T])
                turns = sbuf(st, "f_turns", [FILTER_HIDDEN, T])
                hid = sbuf(st, "f_hid", [FILTER_HIDDEN + 1, T])
                both = sbuf(st, "f_both", [P, KT, 2, HYENA_WIDTH])
                fsum = sbuf(st, "f_sum", [P, KT, HYENA_WIDTH])
                fdiff = sbuf(st, "f_diff", [P, KT, HYENA_WIDTH])
                m0, a0, v0, l0, e0 = mm_done.n, act_out.n, dve_out.n, inputs_in.n, act_evac.n
                H = FILTER_HIDDEN
                with nc.Block() as block:
                    @block.sync
                    def _(sp):
                        for dst, src in ((z[:], A["hy_z"]), (w1[:], A["filt_w1_2"]), (w2[:], A["filt_w2_2"]), (w3[:], A["filt_w3_2"]),
                                         (win[:], A["hy_window"].rearrange("(t p) c -> p t c", p=P)),
                                         (spec[:], A["hy_spectrum"].rearrange("(t p) f -> p t f", p=P))):
                            sp.dma_start(dst, src).then_inc(*inputs_in.up(16))

                    @block.tensor
                    def _(pe):
                        pe.wait_ge(inputs_in.sem, l0 + 96)
                        nc.tensor.matmul(ps[0:H, 0, :], w1[:], z[:], start=True, stop=True).then_inc(*mm_done.up())
                        pe.wait_ge(act_out.sem, a0 + 1)
                        nc.tensor.matmul(ps[0:H, 1, :], w2[:], hid[0:H, :], start=True, stop=True).then_inc(*mm_done.up())
                        pe.wait_ge(act_out.sem, a0 + 2)
                        pe.wait_ge(dve_out.sem, v0 + 3)
                        for o in range(HYENA_ORDER):
                            if o > 0:
                                pe.wait_ge(act_evac.sem, e0 + 8 * o)
                            for t in range(KT):
                                for q in range(2):
                                    nc.tensor.matmul(ps[:, 2 * t + q, :], hid[:, t * P:(t + 1) * P], w3[:, (2 * o + q) * 512:(2 * o + q + 1) * 512],
                                                     start=True, stop=True).then_inc(*mm_done.up())
                            pe.wait_ge(dve_out.sem, v0 + 4 + o)
                            for q, src in enumerate((fsum, fdiff)):
                                for f in range(KT):
                                    for t in range(KT):
                                        last = nc.tensor.matmul(ps[:, 4 * q + f, :], spec[:, t, q * T + f * P:q * T + (f + 1) * P], src[:, t, :],
                                                                start=(t == 0), stop=(t == KT - 1))
                                    last.then_inc(*mm_done.up())

                    @block.scalar
                    def _(act):
                        for j in range(2):
                            act.wait_ge(dve_out.sem, v0 + j + 1)
                            nc.scalar.activation(hid[0:H, :], x[:], ACT.Sin).then_inc(*act_out.up())
                        for o in range(HYENA_ORDER):
                            for q, dst in enumerate((Kc, Ks)):
                                for f in range(KT):
                                    act.wait_ge(mm_done.sem, m0 + 2 + 16 * o + 8 + 4 * q + f + 1)
                                    nc.scalar.activation(dst[:, f, o, :], ps[:, 4 * q + f, :], ACT.Copy).then_inc(*act_evac.up())

                    @block.vector
                    def _(dve):
                        V = nc.vector
                        for j, bias in enumerate(("filt_b1_2", "filt_b2_2")):
                            dve.wait_ge(mm_done.sem, m0 + j + 1)
                            vlink(V.tensor_scalar(x[:], ps[0:H, j, :], vcol(bias, 0)[0:H], vcol("filt_freq_2", j)[0:H], ALU.add, ALU.mult))
                            vlink(V.tensor_scalar(turns[:], x[:], 1.0 / (2.0 * math.pi), ROUND, ALU.mult, ALU.add))
                            vlink(V.tensor_scalar(turns[:], turns[:], -ROUND, None, ALU.add))
                            vlink(V.scalar_tensor_tensor(x[:], turns[:], -TURN_HI, x[:], ALU.mult, ALU.add))
                            vlink(V.scalar_tensor_tensor(x[:], turns[:], -TURN_LO, x[:], ALU.mult, ALU.add))
                            V.tensor_scalar(x[:], x[:], -PI_IN, PI_IN, ALU.max, ALU.min).then_inc(*dve_out.up())
                            dve.wait_ge(act_out.sem, a0 + j + 1)
                        V.memset(hid[H:H + 1, :], 1.0).then_inc(*dve_out.up())
                        for o in range(HYENA_ORDER):
                            for t in range(KT):
                                for q in range(2):
                                    dve.wait_ge(mm_done.sem, m0 + 2 + 16 * o + 2 * t + q + 1)
                                    ins = V.tensor_tensor(both[:, t, q, :], ps[:, 2 * t + q, :], win[:, t, :], ALU.mult)
                            vlink(ins)
                            vlink(V.memset(both[0:1, 0, 1, :], 0.0))
                            if o > 0:
                                dve.wait_ge(mm_done.sem, m0 + 2 + 16 * o)
                            V.tensor_tensor(fsum[:], both[:, :, 0, :], both[:, :, 1, :], ALU.add)
                            vlink_n = V.tensor_tensor(fdiff[:], both[:, :, 0, :], both[:, :, 1, :], ALU.subtract)
                            vlink_n.then_inc(*dve_out.up())
                            dve.wait_ge(dve_out.sem, v0 + 4 + o)

        def hyena_conv(o, z, gates, spec, inv, Kc, Ks):
            with ExitStack() as st:
                z_tok = sbuf(st, "hz_tok", [P, KT, HYENA_WIDTH])
                Uc = sbuf(st, "hUc", [P, KT, HYENA_WIDTH])
                Us = sbuf(st, "hUs", [P, KT, HYENA_WIDTH])
                Y = sbuf(st, "hY", [P, 2 * KT, HYENA_WIDTH])
                t1 = sbuf(st, "ht1", [P, 2, HYENA_WIDTH])
                to_tokens([(z, z_tok)])
                m0, a0, v0, e0 = mm_done.n, act_evac.n, dve_out.n, dve_evac.n
                with nc.Block() as block:
                    @block.tensor
                    def _(pe):
                        for f in range(KT):
                            for q in range(2):
                                for t in range(KT):
                                    last = nc.tensor.matmul(ps[:, 2 * f + q, :], spec[:, t, q * T + f * P:q * T + (f + 1) * P], z_tok[:, t, :],
                                                            start=(t == 0), stop=(t == KT - 1))
                                last.then_inc(*mm_done.up())
                        pe.wait_ge(act_evac.sem, a0 + 2 * KT)
                        pe.wait_ge(dve_out.sem, v0 + KT)
                        for c in range(CT):
                            for f in range(2 * KT):
                                last = nc.tensor.matmul(ps[:, c, :], Y[:, f, c * P:(c + 1) * P], inv[:, f, :], start=(f == 0), stop=(f == 2 * KT - 1))
                            last.then_inc(*mm_done.up())

                    @block.scalar
                    def _(act):
                        for f in range(KT):
                            for q, dst in enumerate((Uc, Us)):
                                act.wait_ge(mm_done.sem, m0 + 2 * f + q + 1)
                                nc.scalar.activation(dst[:, f, :], ps[:, 2 * f + q, :], ACT.Copy).then_inc(*act_evac.up())

                    @block.vector
                    def _(dve):
                        V = nc.vector
                        for f in range(KT):
                            dve.wait_ge(act_evac.sem, a0 + 2 * f + 2)
                            if f > 0:
                                dve.wait_ge(dve_out.sem, v0 + f)
                            V.tensor_tensor(Y[:, f, :], Uc[:, f, :], Kc[:, f, o, :], ALU.mult)
                            V.tensor_tensor(t1[:, 0, :], Us[:, f, :], Ks[:, f, o, :], ALU.mult)
                            V.tensor_tensor(Y[:, KT + f, :], Uc[:, f, :], Ks[:, f, o, :], ALU.mult)
                            vlink(V.tensor_tensor(t1[:, 1, :], Us[:, f, :], Kc[:, f, o, :], ALU.mult))
                            V.tensor_tensor(Y[:, f, :], Y[:, f, :], t1[:, 0, :], ALU.subtract)
                            V.tensor_tensor(Y[:, KT + f, :], Y[:, KT + f, :], t1[:, 1, :], ALU.add).then_inc(*dve_out.up())
                        for c in range(CT):
                            dve.wait_ge(mm_done.sem, m0 + 2 * KT + c + 1)
                            vlink(V.scalar_tensor_tensor(z[:, c, :], z[:, c, :], vcol("filt_bias_2", 4 * o + c), ps[:, c, :], ALU.mult, ALU.add))
                            V.tensor_tensor(z[:, c, :], z[:, c, :], gates[:, 4 * o + c, :], ALU.mult)

        def route_choice(l, hT, rankm, wts):
            E = N_EXP2
            with ExitStack() as st:
                wr = sbuf(st, "c_wr", [P, KD, E])
                lg = sbuf(st, "c_lg", [P, KT, E])
                col = sbuf(st, "c_col", [P, KT])
                work = [sbuf(st, f"c_work{j}", [E, T]) for j in range(2)]
                top = sbuf(st, "c_top", [E, 8])
                sel = sbuf(st, "c_sel", [E, T])
                rk = sbuf(st, "c_rk", [E, T])
                m0, a0, v0, l0 = mm_done.n, act_out.n, dve_out.n, inputs_in.n
                with nc.Block() as block:
                    @block.sync
                    def _(sp):
                        sp.dma_start(wr[:], A["router_2"][l].rearrange("(k p) e -> p k e", p=P)).then_inc(*inputs_in.up(16))

                    @block.tensor
                    def _(pe):
                        pe.wait_ge(inputs_in.sem, l0 + 16)
                        for t in range(KT):
                            for k in range(KD):
                                last = nc.tensor.matmul(ps[:, 0, t * E:(t + 1) * E], hT[:, k, t * P:(t + 1) * P], wr[:, k, :], start=(k == 0), stop=(k == KD - 1))
                        last.then_inc(*mm_done.up())
                        pe.wait_ge(dve_out.sem, v0 + 2)
                        for t in range(KT):
                            last = nc.tensor.transpose(ps[0:E, 1, t * P:(t + 1) * P], wts[:, t, :], ident)
                        last.then_inc(*mm_done.up())
                        pe.wait_ge(dve_out.sem, v0 + 3)
                        for t in range(KT):
                            last = nc.tensor.transpose(ps[:, 2, t * E:(t + 1) * E], rk[:, t * P:(t + 1) * P], ident[0:E, 0:E])
                        last.then_inc(*mm_done.up())

                    @block.scalar
                    def _(act):
                        act.wait_ge(dve_out.sem, v0 + 1)
                        nc.scalar.activation(lg[:], lg[:], ACT.Exp).then_inc(*act_out.up())

                    @block.vector
                    def _(dve):
                        V = nc.vector
                        dve.wait_ge(mm_done.sem, m0 + 1)
                        logits = ps[:, 0, 0:KT * E].rearrange("p (t e) -> p t e", t=KT)
                        vlink(V.tensor_reduce(col[:], logits, AX.X, ALU.max))
                        V.tensor_tensor(lg[:], logits, col[:].unsqueeze(2).to_broadcast([P, KT, E]), ALU.subtract).then_inc(*dve_out.up())
                        dve.wait_ge(act_out.sem, a0 + 1)
                        vlink(V.tensor_reduce(col[:], lg[:], AX.X, ALU.add))
                        vlink(V.reciprocal(col[:], col[:]))
                        V.tensor_tensor(wts[:], lg[:], col[:].unsqueeze(2).to_broadcast([P, KT, E]), ALU.mult).then_inc(*dve_out.up())
                        dve.wait_ge(mm_done.sem, m0 + 2)
                        vlink(V.tensor_copy(work[0][:], ps[0:E, 1, :]))
                        for j in range(CAP2 // 8):
                            vlink(V.max(top[:], work[j % 2][:]))
                            vlink(V.match_replace(work[(j + 1) % 2][:], top[:], work[j % 2][:], -1.0))
                        vlink(V.tensor_scalar(sel[:], work[CAP2 // 8 % 2][:], 0.0, None, ALU.is_lt))
                        vlink(V.tensor_tensor_scan(rk[:], sel[:], sel[:], 0.0, ALU.add, ALU.max))
                        vlink(V.tensor_tensor(rk[:], rk[:], sel[:], ALU.mult))
                        V.tensor_scalar(rk[:], rk[:], -1.0, None, ALU.add).then_inc(*dve_out.up())
                        dve.wait_ge(mm_done.sem, m0 + 3)
                        V.tensor_copy(rankm[:], ps[:, 2, 0:KT * E].rearrange("p (t e) -> p t e", t=KT))

        def conformer_in(hT, u):
            w = A["cf_w1_2"].rearrange("(k p) n -> p k n", p=P)
            n_g = D // 256
            with ExitStack() as st:
                wb = sbuf(st, "wc", [P, 2, KD, 2, 256])
                sig = sbuf(st, "cf_sig", [P, 2, T])
                m0, a0, v0 = mm_done.n, act_out.n, dve_out.n
                w0 = [w_in[0].n, w_in[1].n]
                with nc.Block() as block:
                    @block.sync
                    def _(sp):
                        for g in range(n_g):
                            if g >= 2:
                                sp.wait_ge(mm_done.sem, m0 + 4 * (g - 1))
                            for half in range(2):
                                sp.dma_start(wb[:, g % 2, :, half, :], w[:, :, half * D + g * 256:half * D + (g + 1) * 256]).then_inc(*w_in[g % 2].up(16))

                    @block.tensor
                    def _(pe):
                        for m in range(KD):
                            g = m // 2
                            if m % 2 == 0:
                                pe.wait_ge(w_in[g % 2].sem, w0[g % 2] + 32 * (g // 2 + 1))
                            if m >= 4:
                                pe.wait_ge(dve_out.sem, v0 + m - 3)
                            for half in range(2):
                                for k in range(KD):
                                    last = nc.tensor.matmul(ps[:, 2 * (m % 4) + half, :], wb[:, g % 2, k, half, (m % 2) * P:(m % 2 + 1) * P], hT[:, k, :],
                                                            start=(k == 0), stop=(k == KD - 1))
                                last.then_inc(*mm_done.up())

                    @block.scalar
                    def _(act):
                        for m in range(KD):
                            act.wait_ge(mm_done.sem, m0 + 2 * m + 2)
                            if m >= 2:
                                act.wait_ge(dve_out.sem, v0 + m - 1)
                            nc.scalar.activation(sig[:, m % 2, :], ps[:, 2 * (m % 4) + 1, :], ACT.Sigmoid, bias=vcol("cf_b1_2", KD + m)).then_inc(*act_out.up())

                    @block.vector
                    def _(dve):
                        for m in range(KD):
                            dve.wait_ge(act_out.sem, a0 + m + 1)
                            nc.vector.scalar_tensor_tensor(u[:, m, :], ps[:, 2 * (m % 4), :], vcol("cf_b1_2", m), sig[:, m % 2, :], ALU.add, ALU.mult).then_inc(*dve_out.up())

        def conformer_conv(u, acc):
            rows = T // GRID_W
            mid = (CONF_TAPS - 1) // 2
            with ExitStack() as st:
                stat = sbuf(st, "cf_stat", [P, 2, T])
                m0, a0, v0 = mm_done.n, act_out.n, dve_out.n
                with nc.Block() as block:
                    @block.vector
                    def _(dve):
                        V = nc.vector
                        for c in range(KD):
                            def tap(k):
                                return vcol("cf_dw_w_2", k * KD + c)
                            vlink(V.tensor_scalar(acc[:, c, :], u[:, c, :], tap(mid), vcol("cf_dw_b_2", c), ALU.mult, ALU.add))
                            for d in range(1, rows):
                                n = (rows - d) * GRID_W
                                vlink(V.scalar_tensor_tensor(acc[:, c, 0:n], u[:, c, T - n:T], tap(mid + d), acc[:, c, 0:n], ALU.mult, ALU.add))
                                ins = V.scalar_tensor_tensor(acc[:, c, T - n:T], u[:, c, 0:n], tap(mid - d), acc[:, c, T - n:T], ALU.mult, ALU.add)
                                if d < rows - 1:
                                    vlink(ins)
                            ins.then_inc(*dve_out.up())
                        dve.wait_ge(mm_done.sem, m0 + 1)
                        vlink(V.tensor_scalar(stat[:, 0, :], ps[:, 0, :], 1.0 / D, None, ALU.mult))
                        for c in range(KD):
                            V.tensor_tensor(acc[:, c, :], acc[:, c, :], stat[:, 0, :], ALU.subtract).then_inc(*dve_out.up())
                        dve.wait_ge(mm_done.sem, m0 + 2)
                        V.tensor_scalar(stat[:, 1, :], ps[:, 1, :], 1.0 / D, RMS_EPS, ALU.mult, ALU.add).then_inc(*dve_out.up())
                        dve.wait_ge(act_out.sem, a0 + KD + 1)
                        vlink(V.reciprocal(stat[:, 0, :], stat[:, 0, :]))
                        for c in range(KD):
                            V.scalar_tensor_tensor(acc[:, c, :], acc[:, c, :], vcol("cf_ln_g_2", c), stat[:, 0, :], ALU.mult, ALU.mult).then_inc(*dve_out.up())

                    @block.tensor
                    def _(pe):
                        for c in range(KD):
                            pe.wait_ge(dve_out.sem, v0 + c + 1)
                            last = nc.tensor.matmul(ps[:, 0, :], ones, acc[:, c, :], start=(c == 0), stop=(c == KD - 1))
                        last.then_inc(*mm_done.up())
                        for c in range(KD):
                            pe.wait_ge(act_out.sem, a0 + c + 1)
                            last = nc.tensor.matmul(ps[:, 1, :], ones, u[:, c, :], start=(c == 0), stop=(c == KD - 1))
                        last.then_inc(*mm_done.up())

                    @block.scalar
                    def _(act):
                        for c in range(KD):
                            act.wait_ge(dve_out.sem, v0 + KD + c + 1)
                            nc.scalar.activation(u[:, c, :], acc[:, c, :], ACT.Square).then_inc(*act_out.up())
                        act.wait_ge(dve_out.sem, v0 + 2 * KD + 1)
                        nc.scalar.activation(stat[:, 0, :], stat[:, 1, :], ACT.Sqrt).then_inc(*act_out.up())
                        for c in range(KD):
                            act.wait_ge(dve_out.sem, v0 + 2 * KD + 2 + c)
                            nc.scalar.activation(acc[:, c, :], acc[:, c, :], ACT.Silu, bias=vcol("cf_ln_b_2", c))

        def store_result(src):
            with ExitStack() as st:
                rows = sbuf(st, "out_rows", [P, KT, D])
                rows_of(src, rows)
                s0 = stored.n
                with nc.Block() as block:
                    @block.sync
                    def _(sp):
                        sp.dma_start(out.rearrange("(t p) d -> p t d", p=P), rows[:]).then_inc(*stored.up(16))
                        sp.wait_ge(stored.sem, s0 + 16)
        load_and_transpose(A["x"], xT, T, True)
        with ExitStack() as blk1:
            mix = sbuf(blk1, "mix", [P, 2 * CT, T])
            with ExitStack() as mixers:
                mk = sbuf(mixers, "masks", [P, (4 + 2 * LEVELS) * P])
                masks = {"strict": mk[:, 0:2 * P], "incl": mk[:, 2 * P:4 * P], "levels": mk[:, 4 * P:]}
                proj = sbuf(mixers, "proj", [P, 15, T])
                l0 = inputs_in.n
                with nc.Block() as block:
                    @block.sync
                    def _(sp):
                        sp.dma_start(mk[:], A["consts"][:, const_at["base_end"] + 1:]).then_inc(*inputs_in.up(16))
                        sp.wait_ge(inputs_in.sem, l0 + 16)
                with ExitStack() as gla:
                    gla_q = sbuf(gla, "gla_q", [P, 2, T])
                    gla_k = sbuf(gla, "gla_k", [P, 2, T])
                    gla_v = sbuf(gla, "gla_v", [P, KT, 512])
                    gla_gl = sbuf(gla, "gla_gl", [32, T])
                    gla_og = sbuf(gla, "gla_og", [P, CT, T])
                    with ExitStack() as first:
                        hT = sbuf(first, "hT", [P, KD, T])
                        rms_norm(xT, hT, T, lambda k: vcol("ln1_w", k))
                        project_first(hT, proj, gla_q, gla_k, gla_v, gla_gl, gla_og)
                    gla_mixer(gla_q, gla_k, gla_v, gla_gl, gla_og, mix[:, CT:2 * CT, :], masks)
                with ExitStack() as rwkv:
                    w2 = sbuf(rwkv, "w2s", [P, RW])
                    a2 = sbuf(rwkv, "a2s", [P, RW])
                    g2 = sbuf(rwkv, "g2s", [P, RW])
                    kk = sbuf(rwkv, "rw_kk", [P, CT, T])
                    kd_sum = sbuf(rwkv, "rw_kd_sum", [P, CT, T])
                    v_tok = sbuf(rwkv, "rw_v_tok", [P, KT, RW])
                    rwkv_keys(proj, kk, w2, a2, g2, None)
                    to_tokens([(proj[:, 8:12, :], v_tok)])
                    with ExitStack() as scan:
                        bufs = {n: sbuf(scan, "rw_" + n, [P, CT, T]) for n in ("lw", "cc", "ex", "a", "kd", "q", "r")}
                        for n in ("half", "scale"):
                            bufs[n] = sbuf(scan, "rw_" + n, [P, CT * KT])
                        for n in ("N", "X", "Z", "U", "BT", "RB", "RK"):
                            bufs[n] = sbuf(scan, "rw_" + n, [P, 2, CT, P])
                        bufs["rhs"] = sbuf(scan, "rw_rhs", [P, 2, CT, 64])
                        bufs["sa"] = sbuf(scan, "rw_sa", [P, RW])
                        bufs["S"] = sbuf(scan, "rw_S", [P, CT, 64])
                        bufs["hop"] = sbuf(scan, "rw_hop", [P, KT, CT])
                        bufs["b_tok"], bufs["k_tok"] = bufs["lw"], bufs["cc"]
                        for back in (False, True):
                            rwkv_direction(back, proj, kk, w2, a2, kd_sum, bufs)
                            to_tokens([(bufs["a"], bufs["b_tok"]), (bufs["kd"], bufs["k_tok"])])
                            rwkv_scan(back, bufs, v_tok, mix[:, 0:CT, :], masks)
                    rwkv_output(proj, mix[:, 0:CT, :], kd_sum, g2)
            with ExitStack() as wo:
                project_residual(A["w_out"], mix, xT)
        with ExitStack() as moe:
            h_tok = sbuf(moe, "h_tok1", [P, KT, D])
            rankm = sbuf(moe, "rankm1", [P, KT, N_EXP1])
            wts = sbuf(moe, "wts1", [P, KT, N_EXP1])
            over_one = sbuf(moe, "over_one", [P, N_OVER, N_EXP1])
            over_first = sbuf(moe, "over_first", [P, N_OVER])
            over_int = sbuf(moe, "over_int", [P, N_OVER + 1], I32)
            with ExitStack() as route:
                hT2 = sbuf(route, "hT2", [P, KD, T])
                rms_norm(xT, hT2, T, lambda k: vcol("ln2_w", k))
                rows_of(hT2, h_tok)
                route_first(hT2, rankm, wts, over_one, over_first, over_int)
            experts_pass("m1", h_tok, rankm, wts, N_EXP1, A["moe_w_gate"], A["moe_w_up"], A["moe_w_down"], 512, None)
            overflow_pass(h_tok, rankm, wts, over_one, over_first, over_int)
        with ExitStack() as nrm:
            sq = sbuf(nrm, "sq_f1", [P, KD, T])
            rms_norm(xT, xT, T, lambda k: vcol("ln_f_w", k), sq=sq)
        with ExitStack() as blk2:
            mods = [sbuf(blk2, f"mod_l{l}", [P, 48]) for l in range(2)]
            mod_c = sbuf(blk2, "mod_ctx", [P, 24])
            scaled = [sbuf(blk2, f"scaled_l{l}", [P, 2, KD]) for l in range(2)]
            for l in range(2):
                modulation(l, mods[l], mod_c, scaled[l])

            def part(l, j):
                return lambda k: mods[l][:, 8 * j + k:8 * j + k + 1]

            def weight(l, j):
                return lambda k: scaled[l][:, j, k:k + 1]

            with ExitStack() as even:
                cat = sbuf(even, "cat", [P, 2 * CT, T])
                hy = sbuf(even, "hy", [P, 3 * CT, T])
                spec = sbuf(even, "spec", [P, KT, 2 * T])
                with ExitStack() as lru:
                    gates = sbuf(lru, "lru_w", [P, 2, 2, CT, P])
                    rate = sbuf(lru, "lru_rate", [P, 2, 8])
                    state = sbuf(lru, "lru_state", [P, 2 * CT])
                    xa = sbuf(lru, "xa", [P, CT, T])
                    l0 = inputs_in.n
                    with nc.Block() as block:
                        @block.sync
                        def _(sp):
                            sp.dma_start(gates[:], A["lru_gates"]).then_inc(*inputs_in.up(16))
                            sp.wait_ge(inputs_in.sem, l0 + 16)
                    lru_rates(rate)
                    with ExitStack() as ctx_part:
                        cT = sbuf(ctx_part, "cT", [P, KD, CTX])
                        hc = sbuf(ctx_part, "hc", [P, KD, CTX])
                        xc = sbuf(ctx_part, "xc", [P, CT, CTX])
                        load_and_transpose(A["ctx_2"], cT, CTX, False)
                        rms_norm(cT, hc, CTX, lambda k: mod_c[:, 16 + k:17 + k], lambda k: mod_c[:, k:k + 1])
                        project_even(hc, CTX, [4, 5, 6, 7], None, xc, None)
                        lru_scan(xc, CTX, gates, rate, None, state, None)
                    with ExitStack() as first:
                        hT = sbuf(first, "hT_l0", [P, KD, T])
                        rms_norm(xT, hT, T, weight(0, 0), part(0, 0))
                        project_even(hT, T, list(range(20)), cat[:, 0:CT, :], xa, hy)
                    lru_scan(xa, T, gates, rate, state, None, cat[:, 0:CT, :])
                with ExitStack() as hyena:
                    Kc = sbuf(hyena, "Kc", [P, KT, HYENA_ORDER, HYENA_WIDTH])
                    Ks = sbuf(hyena, "Ks", [P, KT, HYENA_ORDER, HYENA_WIDTH])
                    hyena_filters(spec, Kc, Ks)
                    inv = sbuf(hyena, "inv", [P, 2 * KT, T])
                    l0 = inputs_in.n
                    with nc.Block() as block:
                        @block.sync
                        def _(sp):
                            sp.dma_start(inv[:], A["hy_inverse"].rearrange("(f p) t -> p f t", p=P)).then_inc(*inputs_in.up(16))
                            sp.wait_ge(inputs_in.sem, l0 + 16)

                        @block.gpsimd
                        def _(pool):
                            nc.gpsimd.tensor_copy(cat[:, CT:2 * CT, :], hy[:, 0:CT, :])
                    for o in range(HYENA_ORDER):
                        hyena_conv(o, cat[:, CT:2 * CT, :], hy[:, CT:3 * CT, :], spec, inv, Kc, Ks)
                project_residual(A["w_out_2"], cat, xT, gate=part(0, 2))

            for l in range(2):
                if l == 1:
                    with ExitStack() as conf:
                        hT = sbuf(conf, "hT_l1", [P, KD, T])
                        u = sbuf(conf, "cf_u", [P, KD, T])
                        rms_norm(xT, hT, T, weight(1, 0), part(1, 0))
                        conformer_in(hT, u)
                        conformer_conv(u, hT)
                        project_residual(A["cf_w2_2"], hT, xT, gate=part(1, 2), bias=lambda k: vcol("cf_b2_2", k))
                with ExitStack() as moe:
                    h_tok = sbuf(moe, "h_tok_c", [P, KT, D])
                    rankm = sbuf(moe, "rankm_c", [P, KT, N_EXP2])
                    wts = sbuf(moe, "wts_c", [P, KT, N_EXP2])
                    with ExitStack() as route:
                        hT = sbuf(route, "hT_c", [P, KD, T])
                        rms_norm(xT, hT, T, weight(l, 1), part(l, 3))
                        rows_of(hT, h_tok)
                        route_choice(l, hT, rankm, wts)
                    experts_pass(f"c{l}", h_tok, rankm, wts, N_EXP2, A["exp_w1_2"][l], A["exp_w3_2"][l], A["exp_w2_2"][l], FF2, part(l, 5))
            with ExitStack() as last:
                fin = sbuf(last, "fin", [P, KD, T])
                rms_norm(xT, fin, T, lambda k: vcol("final_g_2", k))
                store_result(fin)


def layout(inputs):
    a = {k: np.ascontiguousarray(np.asarray(v)) for k, v in inputs.items()}
    vectors, consts = pack_vectors(a), shape_constants()
    gw2 = np.zeros((32, 2, 256), np.float32)
    gw2[0:16, 0], gw2[16:32, 1] = a["gla_gw2_f"][0], a["gla_gw2_b"][0]
    ins = {"vectors": vectors.array(), "consts": consts.array(), "gla_gw2": gw2, "x": a["x"][0], "w_in": a["w_in"][0]}
    for name in ("rw_w2_f", "rw_w2_b", "rw_a2_f", "rw_a2_b", "rw_g2", "w_out"):
        ins[name] = a[name][0]
    more_layout(a, ins)
    return ins, vectors.start, consts.start


def more_layout(a, ins):
    for name in ("moe_w_gate", "moe_w_up", "moe_w_down"):
        ins[name] = a[name][0]
    ins["moe_w_route"] = np.concatenate([a["moe_w_coarse"][0], a["moe_w_fine"][0]], axis=1)
    ins["moe_b_route"] = np.concatenate([a["moe_b_coarse"][0], a["moe_b_fine"][0]])[None]
    for name in ("ctx_2", "w_in_2", "w_out_2", "filt_w1_2", "filt_w2_2", "cf_w1_2", "cf_w2_2"):
        ins[name] = a[name][0]
    for name in ("w_mod_2", "router_2", "exp_w1_2", "exp_w3_2", "exp_w2_2"):
        ins[name] = a[name]
    ins["filt_w3_2"] = np.concatenate([a["filt_w3_2"][0], a["filt_b3_2"]], axis=0)
    gates = np.zeros((P, 2, 2, CT, P), np.float32)
    for j, name in enumerate(("lru_wr_2", "lru_wi_2")):
        for h in range(8):
            at = slice(64 * (h % 2), 64 * (h % 2) + 64)
            gates[at, j, :, h // 2, at] = a[name][0, :, h].transpose(1, 0, 2)
    ins["lru_gates"] = gates
    ins.update(hyena_tables())


def kernel(**inputs):
    import concourse.bacc as bacc
    from concourse.bass_utils import run_bass_kernel_spmd

    ins, vec_at, const_at = layout(inputs)
    nc = bacc.Bacc("TRN2", target_bir_lowering=False, num_devices=1)
    A = {name: nc.dram_tensor(f"in_{name}", v.shape, mybir.dt.from_np(v.dtype), kind="ExternalInput").ap() for name, v in ins.items()}
    out = nc.dram_tensor("out_0", (T, D), F32, kind="ExternalOutput").ap()
    build(nc, A, out, vec_at, const_at)
    result = run_bass_kernel_spmd(nc, [{f"in_{name}": v for name, v in ins.items()}], core_ids=[0])
    return result.results[0]["out_0"].reshape(1, T, D)
```

```python
import math
from contextlib import ExitStack

import numpy as np
import concourse.bass as bass
from concourse import mybir

ALU = mybir.AluOpType
ACT = mybir.ActivationFunctionType
F32 = mybir.dt.float32
F32R = mybir.dt.float32r
I32 = mybir.dt.int32
U32 = mybir.dt.uint32
AX = mybir.AxisListType

P = 128
D = 1024
KD = D // P
T = 512
KT = T // P
RMS_EPS = 1e-6
RW = 512
CT = RW // P
RW_HD = 64
RW_GN_EPS = 64e-5
RW_COLS = 1920
GLA_DK = 64
GLA_TAU = 16.0
GLA_SUB = 32
GLA_CLAMP = 80.0
LEVELS = 7
N_GROUPS, PER_GROUP = 4, 8
N_EXP1 = N_GROUPS * PER_GROUP
SLOTS = 64
PAIRS = 2
MORE1 = -(-T // SLOTS) - 1
N_OVER = max(k for k in range(2 * T) if k * (SLOTS + 1) <= 2 * T)
FILTER_EMB, FILTER_HIDDEN, HYENA_WIDTH, HYENA_ORDER = 33, 64, 512, 2
HYENA_DECAY_TARGET, HYENA_FAST_PCT, HYENA_SLOW_PCT, HYENA_SHIFT = 1e-2, 0.3, 1.5, 0.05
ROUND = 1.5 * 2.0 ** 23
TURN_HI = 6.28125
TURN_LO = 2.0 * math.pi - 6.28125
PI_IN = 3.1415925
LRU_C = 8.0
CTX = 256
GRID_W = 64
CONF_TAPS = 31
N_EXP2, FF2, CAP2 = 16, 1024, 64
RING = 6


class Signal:

    def __init__(self, sem):
        self.sem, self.n = sem, 0

    def up(self, by=1):
        self.n += by
        return self.sem, by


class Columns:

    def __init__(self):
        self.start, self.parts, self.n = {}, [], 0

    def add(self, name, a):
        a = np.asarray(a, np.float32)
        if a.shape[0] < P:
            a = np.concatenate([a, np.zeros((P - a.shape[0], a.shape[1]), np.float32)])
        self.start[name] = self.n
        self.parts.append(a)
        self.n += a.shape[1]

    def array(self):
        return np.ascontiguousarray(np.concatenate(self.parts, axis=1))


def pack_vectors(a):
    cols = Columns()

    def put(name, v, rows=P):
        v = np.asarray(v).reshape(-1, rows).T
        cols.add(name, v)

    for name in ("ln1_w", "rw_mu", "rw_w0_f", "rw_w0_b", "rw_a0_f", "rw_a0_b", "rw_k_k", "rw_k_a", "rw_r_k",
                 "rw_ln_w", "rw_ln_b", "gla_gb_f", "gla_gb_b", "gla_norm_w", "ln2_w", "ln_f_w",
                 "norm1_g_2", "norm2_g_2", "final_g_2", "conv_a_w_2", "conv_a_b_2", "lru_br_2", "lru_bi_2",
                 "lru_lam_2", "conv_b_w_2", "conv_b_b_2", "filt_bias_2", "cf_b1_2", "cf_dw_w_2", "cf_dw_b_2",
                 "cf_ln_g_2", "cf_ln_b_2", "cf_b2_2", "b_mod_2", "c_2", "c_ctx_2"):
        put(name, a[name])
    for name in ("filt_b1_2", "filt_b2_2", "filt_freq_2"):
        put(name, a[name], 64)
    put("moe_b_coarse", a["moe_b_coarse"], 4)
    put("moe_b_fine", a["moe_b_fine"], 32)
    return cols


def shape_constants():
    cols = Columns()
    i = np.arange(P)
    row, col = i[:, None], i[None, :]
    cols.add("ident", row == col)
    cols.add("ones", np.ones((P, P)))
    cols.add("head_ones", row // RW_HD == col // RW_HD)
    cols.add("before", row < col)
    cols.add("slots", np.tile(np.arange(SLOTS), (P, 1)))
    cols.add("experts", np.tile(np.arange(N_EXP1), (P, 1)))
    cols.add("overflows", np.tile(np.arange(N_OVER), (P, 1)))
    cols.add("first4", np.tile(np.arange(4, 0, -1), (P, 1)))
    cols.add("first8", np.tile(np.arange(8, 0, -1), (P, 1)))
    cols.add("quarter_rows", np.stack([i % 32 == 0, i % 32 == 1], axis=1))
    cols.add("base_end", np.zeros((P, 1)))
    cols.add("strict", np.concatenate([row < col, row > col], axis=1))
    cols.add("incl", np.concatenate([row <= col, row >= col], axis=1))
    levels = []
    for back in (False, True):
        for s in (2 ** l for l in range(LEVELS)):
            lower = (row // (2 * s) == col // (2 * s)) & (row // s > col // s)
            levels.append(lower.T if back else lower)
    cols.add("levels", np.concatenate(levels, axis=1))
    return cols


def hyena_tables():
    t = np.linspace(0.0, 1.0, T, dtype=np.float32)[:, None]
    bands = (FILTER_EMB - 1) // 2
    w = np.float32(2.0 * math.pi / T) * np.arange(T, dtype=np.float32)[:, None]
    f = np.linspace(1e-4, bands - 1, bands, dtype=np.float32)[None, :]
    z = np.concatenate([t, np.cos(f * w), -np.sin(f * w)], axis=-1).astype(np.float32)
    deltas = np.abs(np.linspace(math.log(HYENA_DECAY_TARGET) / HYENA_SLOW_PCT, math.log(HYENA_DECAY_TARGET) / HYENA_FAST_PCT,
                                HYENA_WIDTH, dtype=np.float32))
    window = (np.exp(-t * deltas[None, :]) + np.float32(HYENA_SHIFT)).astype(np.float32)
    angle = 2.0 * math.pi * ((2 * np.arange(T)[None, :] + 1) * np.arange(T)[:, None] % (4 * T)) / (4 * T)
    spectrum = np.concatenate([np.cos(angle), np.sin(angle)], axis=1).astype(np.float32)
    inverse = (np.concatenate([np.cos(angle).T, np.sin(angle).T], axis=0) / T).astype(np.float32)
    return {"hy_z": np.ascontiguousarray(z.T), "hy_window": window, "hy_spectrum": spectrum, "hy_inverse": inverse}


def build(nc, A, out, vec_at, const_at):
    ctx = ExitStack()
    with ctx:
        def signal(name):
            return Signal(ctx.enter_context(nc.semaphore(name)))

        names = {}

        def sbuf(stack, name, shape, dt=F32):
            names[name] = names.get(name, 0) + 1
            if names[name] > 1:
                name = f"{name}_{names[name]}"
            return stack.enter_context(nc.sbuf_tensor("s_" + name, shape, dt))

        ps = ctx.enter_context(nc.psum_tensor("ps", [P, 8, 512], F32))
        xT = sbuf(ctx, "xT", [P, KD, T])
        n_vec = A["vectors"].shape[1]
        vec = sbuf(ctx, "vec", [P, n_vec])
        base = sbuf(ctx, "base", [P, const_at["base_end"]])

        def table(name, n):
            return base[:, const_at[name]:const_at[name] + n]

        ident, ones, head_ones, before = (table(n, P) for n in ("ident", "ones", "head_ones", "before"))
        slots, experts, overflows = table("slots", SLOTS), table("experts", N_EXP1), table("overflows", N_OVER)
        first4, first8 = table("first4", 4), table("first8", 8)

        def vcol(name, k, n=1):
            at = vec_at[name] + k
            return vec[:, at:at + n]

        inputs_in = signal("inputs_in")
        w_in = [signal("w_in0"), signal("w_in1")]
        mm_done = signal("mm_done")
        act_evac = signal("act_evac")
        dve_evac = signal("dve_evac")
        dve_step = signal("dve_step")
        act_step = signal("act_step")
        dve_out = signal("dve_out")
        act_out = signal("act_out")
        pool_out = signal("pool_out")
        stored = signal("stored")

        def vlink(ins):
            ins.then_inc(*dve_step.up())
            nc.vector.wait_ge(dve_step.sem, dve_step.n)

        def alink(ins):
            ins.then_inc(*act_step.up())
            nc.scalar.wait_ge(act_step.sem, act_step.n)

        def bcast(ap, n):
            return ap.unsqueeze(1).to_broadcast([ap.shape[0], n, ap.shape[1]])

        def load_and_transpose(dram, dst, n_tok, first):
            n_t = n_tok // P
            with ExitStack() as st:
                rows = sbuf(st, "rows", [P, n_t, D])
                m0, a0, v0, l0 = mm_done.n, act_evac.n, dve_evac.n, inputs_in.n
                n_loads = 3 if first else 1
                with nc.Block() as block:
                    @block.sync
                    def _(sp):
                        if first:
                            sp.dma_start(base[:], A["consts"][:, 0:const_at["base_end"]]).then_inc(*inputs_in.up(16))
                            sp.dma_start(vec[:], A["vectors"]).then_inc(*inputs_in.up(16))
                        sp.dma_start(rows[:], dram.rearrange("(t p) d -> p t d", p=P)).then_inc(*inputs_in.up(16))

                    @block.tensor
                    def _(pe):
                        pe.wait_ge(inputs_in.sem, l0 + 16 * n_loads)
                        for d in range(KD):
                            for t in range(n_t):
                                last = nc.tensor.transpose(ps[:, d, t * P:(t + 1) * P], rows[:, t, d * P:(d + 1) * P], ident)
                            last.then_inc(*mm_done.up())

                    @block.scalar
                    def _(act):
                        for d in range(0, KD, 2):
                            act.wait_ge(mm_done.sem, m0 + d + 1)
                            nc.scalar.activation(dst[:, d, :], ps[:, d, 0:n_tok], ACT.Copy)

                    @block.vector
                    def _(dve):
                        for d in range(1, KD, 2):
                            dve.wait_ge(mm_done.sem, m0 + d + 1)
                            nc.vector.tensor_copy(dst[:, d, :], ps[:, d, 0:n_tok])

        def rms_norm(src, dst, n_tok, weight, shift=None, sq=None):
            sq = dst if sq is None else sq
            with ExitStack() as st:
                rt = sbuf(st, "rt", [P, 2, n_tok])
                m0, v0, a0 = mm_done.n, dve_out.n, act_out.n
                sums = ps[:, 0, 0:n_tok]
                with nc.Block() as block:
                    @block.tensor
                    def _(pe):
                        for k in range(KD):
                            if k % 2 == 0:
                                pe.wait_ge(dve_out.sem, v0 + k // 2 + 1)
                            else:
                                pe.wait_ge(act_out.sem, a0 + k // 2 + 1)
                            last = nc.tensor.matmul(sums, ones, sq[:, k, :], start=(k == 0), stop=(k == KD - 1))
                        last.then_inc(*mm_done.up())

                    @block.scalar
                    def _(act):
                        for k in range(1, KD, 2):
                            nc.scalar.activation(sq[:, k, :], src[:, k, :], ACT.Square).then_inc(*act_out.up())
                        act.wait_ge(dve_out.sem, v0 + KD // 2 + 1)
                        nc.scalar.activation(rt[:, 1, :], rt[:, 0, :], ACT.Sqrt).then_inc(*act_out.up())
                        if shift is not None:
                            for k in range(KD):
                                act.wait_ge(dve_out.sem, v0 + KD // 2 + 2 + k)
                                nc.scalar.activation(dst[:, k, :], dst[:, k, :], ACT.Identity, bias=shift(k))

                    @block.vector
                    def _(dve):
                        for k in range(0, KD, 2):
                            nc.vector.tensor_tensor(sq[:, k, :], src[:, k, :], src[:, k, :], ALU.mult).then_inc(*dve_out.up())
                        dve.wait_ge(mm_done.sem, m0 + 1)
                        nc.vector.tensor_scalar(rt[:, 0, :], sums, 1.0 / D, RMS_EPS, ALU.mult, ALU.add).then_inc(*dve_out.up())
                        dve.wait_ge(act_out.sem, a0 + KD // 2 + 1)
                        vlink(nc.vector.reciprocal(rt[:, 0, :], rt[:, 1, :]))
                        for k in range(KD):
                            nc.vector.scalar_tensor_tensor(dst[:, k, :], src[:, k, :], weight(k), rt[:, 0, :], ALU.mult, ALU.mult).then_inc(*dve_out.up())

        def project_first(hT, proj, gla_q, gla_k, gla_v, gla_gl, gla_og):
            w = A["w_in"].rearrange("(k p) n -> p k n", p=P)
            groups = [(c, min(512, RW_COLS - c)) for c in range(0, RW_COLS, 512)]
            groups += [(RW_COLS, 512), (RW_COLS + 512, 512), (RW_COLS + 1024, 32), (RW_COLS + 1056, 512)]
            tiles = []
            for g, (c0, n) in enumerate(groups):
                for j in range(0, n, P):
                    m = min(P, n - j)
                    if g < 4:
                        tiles.append((g, j, m, "rwkv", (c0 + j) // P))
                    else:
                        tiles.append((g, j, m, ("qk", "v", "gl", "og")[g - 4], j // P))
            n_rw = RW_COLS // P
            with ExitStack() as st:
                wb = sbuf(st, "wb", [P, 2, KD, 512])
                pad = sbuf(st, "pad", [P, 3, T + 2])
                tmp = sbuf(st, "tmp", [P, T])
                m0, a0, v0, p0 = mm_done.n, act_evac.n, dve_out.n, pool_out.n
                w0 = [w_in[0].n, w_in[1].n]
                end_of = [max(i for i, t in enumerate(tiles) if t[0] == g) + 1 for g in range(len(groups))]
                with nc.Block() as block:
                    @block.sync
                    def _(sp):
                        for g, (c0, n) in enumerate(groups):
                            if g >= 2:
                                sp.wait_ge(mm_done.sem, m0 + end_of[g - 2])
                            sp.dma_start(wb[:, g % 2, :, 0:n], w[:, :, c0:c0 + n]).then_inc(*w_in[g % 2].up(16))

                    @block.gpsimd
                    def _(pool):
                        nc.gpsimd.memset(pad[:], 0.0).then_inc(*pool_out.up())

                    @block.tensor
                    def _(pe):
                        for i, (g, j, m, kind, idx) in enumerate(tiles):
                            if i == 0 or tiles[i - 1][0] != g:
                                pe.wait_ge(w_in[g % 2].sem, w0[g % 2] + 16 * (g // 2 + 1))
                            if i >= 8:
                                pe.wait_ge(act_evac.sem, a0 + i - 7)
                            for k in range(KD):
                                if kind == "v":
                                    last = nc.tensor.matmul(ps[:, i % 8, :], hT[:, k, idx * P:(idx + 1) * P], wb[:, g % 2, k, :],
                                                            start=(k == 0), stop=(k == KD - 1))
                                else:
                                    last = nc.tensor.matmul(ps[0:m, i % 8, :], wb[:, g % 2, k, j:j + m], hT[:, k, :],
                                                            start=(k == 0), stop=(k == KD - 1))
                            last.then_inc(*mm_done.up())

                    @block.scalar
                    def _(act):
                        act.wait_ge(pool_out.sem, p0 + 1)
                        for i, (g, j, m, kind, idx) in enumerate(tiles):
                            act.wait_ge(mm_done.sem, m0 + i + 1)
                            src = ps[0:m, i % 8, :]
                            if kind == "rwkv":
                                if i >= 3:
                                    act.wait_ge(dve_out.sem, v0 + i - 2)
                                ins = nc.scalar.activation(pad[:, i % 3, 1:T + 1], src, ACT.Copy)
                            elif kind == "qk":
                                dst = gla_q if idx < 2 else gla_k
                                ins = nc.scalar.activation(dst[:, idx % 2, :], src, ACT.Copy, scale=GLA_DK ** -0.5 if idx < 2 else 1.0)
                            elif kind == "v":
                                ins = nc.scalar.activation(gla_v[:, idx, :], src, ACT.Copy)
                            elif kind == "gl":
                                ins = nc.scalar.activation(gla_gl[0:m, :], src, ACT.Copy)
                            else:
                                ins = nc.scalar.activation(gla_og[:, idx, :], src, ACT.Silu)
                            ins.then_inc(*act_evac.up())

                    @block.vector
                    def _(dve):
                        for i in range(n_rw):
                            dve.wait_ge(act_evac.sem, a0 + i + 1)
                            p = pad[:, i % 3, 1:T + 1]
                            if i > 0:
                                dve.wait_ge(dve_out.sem, v0 + i)
                            vlink(nc.vector.tensor_tensor(tmp[:], pad[:, i % 3, 0:T], pad[:, i % 3, 2:T + 2], ALU.add))
                            vlink(nc.vector.scalar_tensor_tensor(tmp[:], tmp[:], 0.5, p, ALU.mult, ALU.subtract))
                            nc.vector.scalar_tensor_tensor(proj[:, i, :], tmp[:], vcol("rw_mu", i), p, ALU.mult, ALU.add).then_inc(*dve_out.up())

        def rwkv_keys(proj, kk, w2, a2, g2, lnk):
            r_, k_, v_ = proj[:, 0:4, :], proj[:, 4:8, :], proj[:, 8:12, :]
            with ExitStack() as st:
                sq = sbuf(st, "sq", [P, CT, T])
                m0, a0, v0, l0 = mm_done.n, act_out.n, dve_out.n, inputs_in.n
                with nc.Block() as block:
                    @block.sync
                    def _(sp):
                        sp.dma_start(w2[0:64, :], A["rw_w2_f"]).then_inc(*inputs_in.up(16))
                        sp.dma_start(w2[64:128, :], A["rw_w2_b"]).then_inc(*inputs_in.up(16))
                        sp.dma_start(a2[0:64, :], A["rw_a2_f"]).then_inc(*inputs_in.up(16))
                        sp.dma_start(a2[64:128, :], A["rw_a2_b"]).then_inc(*inputs_in.up(16))
                        sp.dma_start(g2[:], A["rw_g2"]).then_inc(*inputs_in.up(16))
                        sp.wait_ge(inputs_in.sem, l0 + 80)

                    @block.vector
                    def _(dve):
                        for c in range(CT):
                            vlink(nc.vector.tensor_scalar(kk[:, c, :], k_[:, c, :], vcol("rw_k_k", c), None, ALU.mult))
                            nc.vector.tensor_tensor(sq[:, c, :], kk[:, c, :], kk[:, c, :], ALU.mult).then_inc(*dve_out.up())
                        for c in range(CT):
                            dve.wait_ge(act_out.sem, a0 + c + 1)
                            vlink(nc.vector.tensor_scalar(sq[:, c, :], sq[:, c, :], 1e-12, None, ALU.max))
                            vlink(nc.vector.reciprocal(sq[:, c, :], sq[:, c, :]))
                            nc.vector.tensor_tensor(kk[:, c, :], kk[:, c, :], sq[:, c, :], ALU.mult)

                    @block.tensor
                    def _(pe):
                        for c in range(CT):
                            pe.wait_ge(dve_out.sem, v0 + c + 1)
                            nc.tensor.matmul(ps[:, c, :], head_ones, sq[:, c, :], start=True, stop=True).then_inc(*mm_done.up())

                    @block.scalar
                    def _(act):
                        for c in range(CT):
                            act.wait_ge(mm_done.sem, m0 + c + 1)
                            nc.scalar.activation(sq[:, c, :], ps[:, c, :], ACT.Sqrt).then_inc(*act_out.up())
                        nc.scalar.activation(proj[:, 14, :], proj[:, 14, :], ACT.Sigmoid)
                        nc.scalar.activation(proj[:, 12, :], proj[:, 12, :], ACT.Tanh)

        def rwkv_direction(back, proj, kk, w2, a2, kd_sum, bufs):
            r_, k_ = proj[:, 0:4, :], proj[:, 4:8, :]
            lw, cc, ex, a_, kd, qt, rt = bufs["lw"], bufs["cc"], bufs["ex"], bufs["a"], bufs["kd"], bufs["q"], bufs["r"]
            half, scale = bufs["half"], bufs["scale"]
            rows = slice(64, 128) if back else slice(0, 64)
            w0, ka0 = ("rw_w0_b", "rw_a0_b") if back else ("rw_w0_f", "rw_a0_f")

            def chunks(t):
                return t[:, :, :].rearrange("p c (n i) -> p (c n) i", i=P)

            def flat(t):
                return t[:, :, :].rearrange("p c n -> p (c n)")

            m0, a0, v0 = mm_done.n, act_out.n, dve_out.n
            with nc.Block() as block:
                @block.tensor
                def _(pe):
                    for j in range(2 * CT):
                        c, w, x = j % CT, (w2, a2)[j // CT], proj[rows, 12 + j // CT, :]
                        nc.tensor.matmul(ps[:, j, :], w[rows, c * P:(c + 1) * P], x, start=True, stop=True).then_inc(*mm_done.up())

                @block.scalar
                def _(act):
                    for j in range(2 * CT):
                        c, name, dst = j % CT, (w0, ka0)[j // CT], (lw, a_)[j // CT]
                        act.wait_ge(mm_done.sem, m0 + j + 1)
                        nc.scalar.activation(dst[:, c, :], ps[:, j, :], ACT.Sigmoid, bias=vcol(name, c)).then_inc(*act_out.up())
                    act.wait_ge(dve_out.sem, v0 + 1)
                    nc.scalar.activation(scale[:], half[:], ACT.Exp).then_inc(*act_out.up())
                    act.wait_ge(dve_out.sem, v0 + 2)
                    if back:
                        nc.scalar.activation(flat(ex), flat(lw), ACT.Exp, scale=-1.0).then_inc(*act_out.up())
                        alink(nc.scalar.activation(flat(cc), flat(cc), ACT.Exp, scale=-1.0))
                    else:
                        alink(nc.scalar.activation(flat(ex), flat(cc), ACT.Exp, scale=-1.0))
                        nc.scalar.activation(flat(cc), flat(cc), ACT.Exp).then_inc(*act_out.up())
                    act.wait_ge(act_step.sem, act_step.n)
                    if back:
                        act.wait_ge(act_out.sem, act_out.n)
                    nc.scalar.activation(flat(lw), flat(lw), ACT.Exp).then_inc(*act_out.up())

                @block.vector
                def _(dve):
                    dve.wait_ge(act_out.sem, a0 + CT)
                    vlink(nc.vector.tensor_scalar(flat(lw), flat(lw), -math.exp(-0.5), None, ALU.mult))
                    for c in range(CT):
                        for n in range(KT):
                            at = slice(n * P, (n + 1) * P)
                            ins = nc.vector.tensor_tensor_scan(cc[:, c, at], ones, lw[:, c, at], 0.0, ALU.mult, ALU.add)
                    vlink(ins)
                    totals = chunks(cc)[:, :, P - 1:P]
                    ins = nc.vector.tensor_scalar(half[:].unsqueeze(2), totals, 0.5, None, ALU.mult)
                    ins.then_inc(*dve_out.up())
                    dve.wait_ge(dve_out.sem, v0 + 1)
                    vlink(nc.vector.tensor_tensor(chunks(cc), chunks(cc), half[:].unsqueeze(2).to_broadcast([P, CT * KT, P]), ALU.subtract))
                    nc.vector.tensor_tensor(flat(lw), flat(cc), flat(lw), ALU.subtract).then_inc(*dve_out.up())
                    dve.wait_ge(act_out.sem, a0 + 2 * CT)
                    for c in range(CT):
                        ins = nc.vector.tensor_scalar(kd[:, c, :], a_[:, c, :], -1.0, vcol("rw_k_a", c), ALU.add, ALU.mult)
                    vlink(ins)
                    vlink(nc.vector.scalar_tensor_tensor(flat(kd), flat(kd), 1.0, flat(k_), ALU.add, ALU.mult))
                    if back:
                        nc.vector.tensor_tensor(flat(kd_sum), flat(kd_sum), flat(kd), ALU.add)
                    else:
                        nc.vector.tensor_copy(flat(kd_sum), flat(kd))
                    vlink(nc.vector.tensor_tensor(flat(a_), flat(a_), flat(kk), ALU.mult))
                    dve.wait_ge(act_out.sem, a0 + 2 * CT + 3)
                    dve.wait_ge(act_step.sem, act_step.n)
                    eq, er, eb = (cc, ex, lw) if back else (lw, cc, ex)
                    nc.vector.tensor_tensor(flat(qt), flat(kk), flat(eq), ALU.mult)
                    nc.vector.tensor_tensor(flat(rt), flat(r_), flat(er), ALU.mult)
                    nc.vector.tensor_tensor(flat(kd), flat(kd), flat(eb), ALU.mult)
                    nc.vector.tensor_tensor(flat(a_), flat(a_), flat(eb), ALU.mult)

        def to_tokens(pairs):
            m0 = mm_done.n
            a0 = act_evac.n
            v0 = dve_evac.n
            jobs = [(src, dst, n) for src, dst in pairs for n in range(KT)]
            with nc.Block() as block:
                @block.tensor
                def _(pe):
                    for j, (src, dst, n) in enumerate(jobs):
                        if j >= 8:
                            if j % 2:
                                pe.wait_ge(act_evac.sem, a0 + (j - 8) // 2 + 1)
                            else:
                                pe.wait_ge(dve_evac.sem, v0 + (j - 8) // 2 + 1)
                        n_c = src.shape[1]
                        for c in range(n_c):
                            last = nc.tensor.transpose(ps[:, j % 8, c * P:(c + 1) * P], src[:, c, n * P:(n + 1) * P], ident)
                        last.then_inc(*mm_done.up())

                @block.scalar
                def _(act):
                    for j, (src, dst, n) in enumerate(jobs):
                        if j % 2:
                            act.wait_ge(mm_done.sem, m0 + j + 1)
                            nc.scalar.activation(dst[:, n, :], ps[:, j % 8, 0:src.shape[1] * P], ACT.Copy).then_inc(*act_evac.up())

                @block.vector
                def _(dve):
                    for j, (src, dst, n) in enumerate(jobs):
                        if j % 2 == 0:
                            dve.wait_ge(mm_done.sem, m0 + j + 1)
                            nc.vector.tensor_copy(dst[:, n, :], ps[:, j % 8, 0:src.shape[1] * P]).then_inc(*dve_evac.up())

        def rwkv_scan(back, bufs, v_tok, y, masks):
            qt, rt, kt, bt = bufs["q"], bufs["r"], bufs["kd"], bufs["a"]
            b_tok, k_tok = bufs["b_tok"], bufs["k_tok"]
            scale = bufs["scale"]
            N, X, Z, U, BT, RB, RK = (bufs[n] for n in ("N", "X", "Z", "U", "BT", "RB", "RK"))
            rhs, sa, S, hop = bufs["rhs"], bufs["sa"], bufs["S"], bufs["hop"]
            d = 1 if back else 0
            strict = masks["strict"][:, d * P:(d + 1) * P]
            incl = masks["incl"][:, d * P:(d + 1) * P]

            def level(l, back_=back):
                at = (LEVELS * int(back_) + l) * P
                return masks["levels"][:, at:at + P]

            order = list(range(KT))[::-1] if back else list(range(KT))
            H4 = CT
            rows = (slice(0, 64), slice(64, 128))
            jobs = []
            for n in order:
                for par in range(2):
                    jobs += [(n, nm, par, 0) for nm in ("A", "N", "RB", "BT", "RK")]
                for l in range(1, LEVELS):
                    jobs += [(n, "U", par, l) for par in range(2)]
                    for par in range(2):
                        if l < LEVELS - 1:
                            jobs.append((n, "X", par, l))
                        jobs.append((n, "Z", par, l))
                jobs += [(n, "rhs", 0, 0), (n, "rhs", 1, 0), (n, "sa", 0, 0), (n, "y", 0, 0), (n, "y", 1, 0), (n, "S", 0, 0)]
            number = {job: i for i, job in enumerate(jobs)}
            m0, e0 = mm_done.n, dve_evac.n

            def four(bank):
                return ps[:, bank, :].rearrange("p (h i) -> p h i", h=H4)

            with nc.Block() as block:
                @block.tensor
                def _(pe):
                    free = [0]

                    def evacuated(job):
                        need = number[job] + 1
                        if need > free[0]:
                            free[0] = need
                            pe.wait_ge(dve_evac.sem, e0 + need)

                    for i, (n, nm, par, l) in enumerate(jobs):
                        at = slice(n * P, (n + 1) * P)
                        r = rows[par]
                        bank = ps[:, i % 8, :]
                        if i >= 8:
                            evacuated(jobs[i - 8])
                        mm = nc.tensor.matmul
                        if nm in ("A", "N", "RB", "BT", "RK"):
                            lhs, rhs_ = {"A": (qt, bt), "N": (bt, qt), "RB": (bt, rt), "BT": (kt, qt), "RK": (kt, rt)}[nm]
                            for h in range(H4):
                                last = mm(bank[:, h * P:(h + 1) * P], lhs[r, h, at], rhs_[r, h, at], start=True, stop=True)
                        elif nm == "U":
                            evacuated((n, "RK", par, 0) if l == 1 else (n, "X", par, l - 1))
                            for h in range(H4):
                                last = mm(bank[:, h * P:(h + 1) * P], N[:, par, h, :], X[:, par, h, :], start=True, stop=True)
                        elif nm == "X":
                            evacuated((n, "U", par, l))
                            for h in range(H4):
                                last = mm(bank[:, h * P:(h + 1) * P], Z[:, par, h, :], U[:, par, h, :], start=True, stop=True)
                        elif nm == "Z":
                            evacuated((n, "U", par, l))
                            for h in range(H4):
                                last = mm(bank[:, h * P:(h + 1) * P], U[:, par, h, :], Z[:, par, h, :], start=True, stop=True)
                        elif nm == "rhs":
                            evacuated((n, "RK", 1, 0))
                            if n != order[0]:
                                evacuated((order[order.index(n) - 1], "S", 0, 0))
                            for h in range(H4):
                                o = bank[:, h * 64:(h + 1) * 64]
                                mm(o, qt[r, h, at], S[r, h, :], start=True, stop=False)
                                last = mm(o, BT[:, par, h, :], v_tok[:, n, h * P + par * 64:h * P + par * 64 + 64], start=False, stop=True)
                        elif nm == "sa":
                            evacuated((n, "Z", 1, LEVELS - 1))
                            evacuated((n, "rhs", 1, 0))
                            for h in range(H4):
                                for q in range(2):
                                    last = mm(bank[:, (2 * h + q) * 64:(2 * h + q + 1) * 64], Z[:, q, h, :], rhs[:, q, h, :], start=True, stop=True)
                        elif nm == "y":
                            evacuated((n, "sa", 0, 0))
                            for h in range(H4):
                                o = bank[r, h * P:(h + 1) * P]
                                head = slice(h * P + par * 64, h * P + par * 64 + 64)
                                mm(o, S[r, h, :], rt[r, h, at], start=True, stop=False)
                                mm(o, sa[:, head], RB[:, par, h, :], start=False, stop=False)
                                last = mm(o, v_tok[:, n, head], RK[:, par, h, :], start=False, stop=True)
                        else:
                            for h in range(H4):
                                for q in range(2):
                                    o = bank[rows[q], h * 64:(h + 1) * 64]
                                    head = slice(h * P + q * 64, h * P + q * 64 + 64)
                                    mm(o, b_tok[:, n, head], sa[:, head], start=True, stop=False)
                                    last = mm(o, k_tok[:, n, head], v_tok[:, n, head], start=False, stop=True)
                        last.then_inc(*mm_done.up())

                @block.vector
                def _(dve):
                    sc = scale[:].rearrange("p (c n) -> p c n", n=KT)
                    for j, n in enumerate(order[:-1]):
                        nc.vector.tensor_tensor(hop[:, j, :], sc[:, :, n], sc[:, :, order[j + 1]], ALU.mult)
                    vlink(nc.vector.memset(S[:], 0.0))
                    for i, (n, nm, par, l) in enumerate(jobs):
                        dve.wait_ge(mm_done.sem, m0 + i + 1)
                        at = slice(n * P, (n + 1) * P)
                        r = rows[par]
                        bank = four(i % 8)
                        tt = nc.vector.tensor_tensor
                        if nm == "A":
                            vlink(tt(X[:, par], bank, bcast(level(0), H4), ALU.mult))
                            ins = tt(X[:, par], bcast(ident, H4), X[:, par], ALU.subtract)
                        elif nm == "N":
                            vlink(tt(N[:, par], bank, bcast(strict, H4), ALU.mult))
                            vlink(tt(Z[:, par], N[:, par], bcast(level(0, not back), H4), ALU.mult))
                            ins = tt(Z[:, par], bcast(ident, H4), Z[:, par], ALU.subtract)
                        elif nm in ("RB", "BT", "RK"):
                            ins = tt({"RB": RB, "BT": BT, "RK": RK}[nm][:, par], bank, bcast(strict if nm == "BT" else incl, H4), ALU.mult)
                        elif nm == "U":
                            ins = tt(U[:, par], bank, bcast(level(l), H4), ALU.mult)
                        elif nm in ("X", "Z"):
                            M = X if nm == "X" else Z
                            ins = tt(M[:, par], M[:, par], bank, ALU.subtract)
                        elif nm == "rhs":
                            ins = nc.vector.tensor_scalar(rhs[:, par], ps[:, i % 8, 0:256].rearrange("p (h v) -> p h v", h=H4), -1.0, None, ALU.mult)
                        elif nm == "sa":
                            ins = nc.vector.tensor_copy(sa[:], ps[:, i % 8, :])
                        elif nm == "y":
                            o = y[r, :, at]
                            if back:
                                ins = tt(o, o, bank[r], ALU.add)
                            else:
                                ins = nc.vector.tensor_copy(o, bank[r])
                        else:
                            j = order.index(n)
                            if j == KT - 1:
                                ins = nc.vector.tensor_copy(S[:], ps[:, i % 8, 0:256].rearrange("p (h v) -> p h v", h=H4))
                            else:
                                vlink(tt(S[:], S[:], ps[:, i % 8, 0:256].rearrange("p (h v) -> p h v", h=H4), ALU.add))
                                ins = tt(S[:], S[:], hop[:, j, :].unsqueeze(2).to_broadcast([P, CT, 64]), ALU.mult)
                        ins.then_inc(*dve_evac.up())
                        dve.wait_ge(dve_evac.sem, e0 + i + 1)

        def rwkv_output(proj, y, kd_sum, g2):
            r_, v_ = proj[:, 0:4, :], proj[:, 8:12, :]
            with ExitStack() as st:
                sq = sbuf(st, "gn_sq", [P, CT, T])
                m0, v0, a0 = mm_done.n, dve_out.n, act_out.n
                n_mm = 4 * CT
                with nc.Block() as block:
                    @block.tensor
                    def _(pe):
                        for c in range(CT):
                            nc.tensor.matmul(ps[:, c, :], head_ones, y[:, c, :], start=True, stop=True).then_inc(*mm_done.up())
                        for c in range(CT):
                            nc.tensor.matmul(ps[:, 4 + c, :], g2[:, c * P:(c + 1) * P], proj[:, 14, :], start=True, stop=True).then_inc(*mm_done.up())
                        for c in range(CT):
                            pe.wait_ge(dve_out.sem, v0 + c + 1)
                            nc.tensor.matmul(ps[:, c, :], head_ones, sq[:, c, :], start=True, stop=True).then_inc(*mm_done.up())
                        for c in range(CT):
                            pe.wait_ge(dve_out.sem, v0 + 2 * CT + c + 1)
                            nc.tensor.matmul(ps[:, c, :], head_ones, kd_sum[:, c, :], start=True, stop=True).then_inc(*mm_done.up())

                    @block.scalar
                    def _(act):
                        for c in range(CT):
                            act.wait_ge(dve_out.sem, v0 + CT + c + 1)
                            nc.scalar.activation(sq[:, c, :], sq[:, c, :], ACT.Sqrt).then_inc(*act_out.up())

                    @block.vector
                    def _(dve):
                        for c in range(CT):
                            dve.wait_ge(mm_done.sem, m0 + c + 1)
                            vlink(nc.vector.scalar_tensor_tensor(y[:, c, :], ps[:, c, :], -1.0 / RW_HD, y[:, c, :], ALU.mult, ALU.add))
                            nc.vector.tensor_tensor(sq[:, c, :], y[:, c, :], y[:, c, :], ALU.mult).then_inc(*dve_out.up())
                        for c in range(CT):
                            dve.wait_ge(mm_done.sem, m0 + 2 * CT + c + 1)
                            nc.vector.tensor_scalar(sq[:, c, :], ps[:, c, :], 1.0 / RW_HD, RW_GN_EPS, ALU.mult, ALU.add).then_inc(*dve_out.up())
                        for c in range(CT):
                            nc.vector.scalar_tensor_tensor(kd_sum[:, c, :], r_[:, c, :], vcol("rw_r_k", c), kd_sum[:, c, :], ALU.mult, ALU.mult).then_inc(*dve_out.up())
                        for c in range(CT):
                            dve.wait_ge(act_out.sem, a0 + c + 1)
                            vlink(nc.vector.reciprocal(sq[:, c, :], sq[:, c, :]))
                            vlink(nc.vector.tensor_tensor(y[:, c, :], y[:, c, :], sq[:, c, :], ALU.mult))
                            vlink(nc.vector.tensor_scalar(y[:, c, :], y[:, c, :], vcol("rw_ln_w", c), vcol("rw_ln_b", c), ALU.mult, ALU.add))
                            dve.wait_ge(mm_done.sem, m0 + 3 * CT + c + 1)
                            vlink(nc.vector.tensor_tensor(v_[:, c, :], ps[:, c, :], v_[:, c, :], ALU.mult))
                            vlink(nc.vector.tensor_tensor(y[:, c, :], y[:, c, :], v_[:, c, :], ALU.add))
                            nc.vector.tensor_tensor(y[:, c, :], ps[:, 4 + c, :], y[:, c, :], ALU.mult)

        def gla_mixer(q, k, v_tok, gl, og, o, masks):
            n_sub = P // GLA_SUB
            NT = 2
            C8 = NT * KT

            def flat(t):
                return t[:, :, :].rearrange("p c n -> p (c n)")

            def chunks(t):
                return t[:, :, :].rearrange("p c (n i) -> p (c n) i", i=P)

            with ExitStack() as st:
                gw2 = sbuf(st, "gw2", [32, 2, 256])
                z = sbuf(st, "gz", [P, NT, T])
                L = sbuf(st, "gL", [P, NT, T])
                e = sbuf(st, "ge", [P, NT, T])
                qs = sbuf(st, "g_qs", [P, NT, T])
                qc = sbuf(st, "g_qc", [P, NT, T])
                kc = sbuf(st, "g_kc", [P, NT, T])
                ks = sbuf(st, "g_ks", [P, n_sub, NT, T])
                kc_tok = sbuf(st, "g_kc_tok", [P, KT, NT * P])
                att = sbuf(st, "g_att", [P, 4, P])
                S = sbuf(st, "g_S", [P, NT, P])
                last_decay = sbuf(st, "g_last", [P, C8])
                l0 = inputs_in.n
                with nc.Block() as block:
                    @block.sync
                    def _(sp):
                        sp.dma_start(gw2[:], A["gla_gw2"]).then_inc(*inputs_in.up(16))
                        sp.wait_ge(inputs_in.sem, l0 + 16)
                for back in (False, True):
                    d = int(back)
                    incl = masks["incl"][:, d * P:(d + 1) * P]
                    order = list(range(KT))[::-1] if back else list(range(KT))
                    gb = "gla_gb_b" if back else "gla_gb_f"
                    m0, a0, v0 = mm_done.n, act_out.n, dve_out.n
                    with nc.Block() as block:
                        @block.tensor
                        def _(pe):
                            for c in range(NT):
                                nc.tensor.matmul(ps[:, c, :], gw2[:, d, c * P:(c + 1) * P], gl[:, :], start=True, stop=True).then_inc(*mm_done.up())

                        @block.scalar
                        def _(act):
                            act.wait_ge(dve_out.sem, v0 + 1)
                            alink(nc.scalar.activation(flat(e), flat(z), ACT.Abs))
                            alink(nc.scalar.activation(flat(e), flat(e), ACT.Exp, scale=-1.0))
                            nc.scalar.activation(flat(e), flat(e), ACT.Ln, bias=1.0).then_inc(*act_out.up())
                            act.wait_ge(dve_out.sem, v0 + 2)
                            alink(nc.scalar.activation(flat(z), flat(L), ACT.Exp))
                            nc.scalar.activation(last_decay[:].unsqueeze(2), chunks(z)[:, :, 0:1] if back else chunks(z)[:, :, P - 1:P], ACT.Copy).then_inc(*act_out.up())
                            act.wait_ge(dve_out.sem, v0 + 3)
                            nc.scalar.activation(flat(kc), flat(kc), ACT.Exp).then_inc(*act_out.up())
                            act.wait_ge(dve_out.sem, v0 + 4)
                            nc.scalar.activation(flat(qs), flat(qs), ACT.Exp).then_inc(*act_out.up())
                            for s in range(n_sub):
                                act.wait_ge(dve_out.sem, v0 + 5 + s)
                                nc.scalar.activation(flat(ks[:, s]), flat(ks[:, s]), ACT.Exp, scale=-1.0).then_inc(*act_out.up())

                        @block.vector
                        def _(dve):
                            for c in range(NT):
                                dve.wait_ge(mm_done.sem, m0 + c + 1)
                                ins = nc.vector.tensor_scalar(z[:, c, :], ps[:, c, :], vcol(gb, c), None, ALU.add)
                            ins.then_inc(*dve_out.up())
                            dve.wait_ge(act_out.sem, a0 + 1)
                            vlink(nc.vector.scalar_tensor_tensor(flat(z), flat(z), 0.0, flat(e), ALU.min, ALU.subtract))
                            vlink(nc.vector.tensor_scalar(flat(z), flat(z), 1.0 / GLA_TAU, None, ALU.mult))
                            for j in range(C8):
                                ins = nc.vector.tensor_tensor_scan(chunks(L)[:, j, :], ones, chunks(z)[:, j, :], 0.0, ALU.mult, ALU.add)
                            if back:
                                vlink(ins)
                                vlink(nc.vector.tensor_tensor(chunks(z), chunks(z), chunks(L)[:, :, P - 1:P].to_broadcast([P, C8, P]), ALU.add))
                                ins = nc.vector.tensor_tensor(flat(L), flat(z), flat(L), ALU.subtract)
                            ins.then_inc(*dve_out.up())
                            dve.wait_ge(dve_out.sem, v0 + 2)
                            total = chunks(L)[:, :, 0:1] if back else chunks(L)[:, :, P - 1:P]
                            nc.vector.tensor_tensor(chunks(kc), total.to_broadcast([P, C8, P]), chunks(L), ALU.subtract).then_inc(*dve_out.up())
                            for s in range(n_sub):
                                sub = slice(s * GLA_SUB, (s + 1) * GLA_SUB)
                                mid = s * GLA_SUB + GLA_SUB // 2
                                anchor = chunks(L)[:, :, mid:mid + 1]
                                ins = nc.vector.tensor_tensor(chunks(qs)[:, :, sub], chunks(L)[:, :, sub], anchor.to_broadcast([P, C8, GLA_SUB]), ALU.subtract)
                            vlink(ins)
                            nc.vector.tensor_scalar(flat(qs), flat(qs), GLA_CLAMP, None, ALU.min).then_inc(*dve_out.up())
                            for s in range(n_sub):
                                mid = s * GLA_SUB + GLA_SUB // 2
                                anchor = chunks(L)[:, :, mid:mid + 1]
                                vlink(nc.vector.tensor_tensor(chunks(ks[:, s]), chunks(L), anchor.to_broadcast([P, C8, P]), ALU.subtract))
                                nc.vector.tensor_scalar(flat(ks[:, s]), flat(ks[:, s]), -GLA_CLAMP, None, ALU.max).then_inc(*dve_out.up())
                            dve.wait_ge(act_out.sem, a0 + 4)
                            dve.wait_ge(act_step.sem, act_step.n)
                            nc.vector.tensor_tensor(flat(qc), flat(q), flat(z), ALU.mult)
                            nc.vector.tensor_tensor(flat(kc), flat(k), flat(kc), ALU.mult)
                            nc.vector.tensor_tensor(flat(qs), flat(q), flat(qs), ALU.mult)
                            for s in range(n_sub):
                                dve.wait_ge(act_out.sem, a0 + 5 + s)
                                nc.vector.tensor_tensor(flat(ks[:, s]), flat(k), flat(ks[:, s]), ALU.mult)
                    to_tokens([(kc, kc_tok)])
                    rows = (slice(0, 64), slice(64, 128))
                    jobs = []
                    for n in order:
                        jobs += [(n, "att", 0), (n, "att", 1), (n, "o", 0), (n, "o", 1), (n, "S", 0)]
                    number = {job: i for i, job in enumerate(jobs)}
                    m1, e1 = mm_done.n, dve_evac.n
                    with nc.Block() as block:
                        @block.tensor
                        def _(pe):
                            for i, (n, nm, par) in enumerate(jobs):
                                at = slice(n * P, (n + 1) * P)
                                r = rows[par]
                                bank = ps[:, i % 8, :]
                                if i >= 8:
                                    pe.wait_ge(dve_evac.sem, e1 + i - 7)
                                if nm == "att":
                                    for c in range(NT):
                                        for s in range(n_sub):
                                            sub = slice(n * P + s * GLA_SUB, n * P + (s + 1) * GLA_SUB)
                                            o0 = c * P + s * GLA_SUB
                                            last = nc.tensor.matmul(bank[:, o0:o0 + GLA_SUB], ks[r, s, c, at], qs[r, c, sub], start=True, stop=True)
                                elif nm == "o":
                                    pe.wait_ge(dve_evac.sem, e1 + number[(n, "att", 1)] + 1)
                                    if n != order[0]:
                                        pe.wait_ge(dve_evac.sem, e1 + number[(order[order.index(n) - 1], "S", 0)] + 1)
                                    for c in range(NT):
                                        h = 2 * c + par
                                        nc.tensor.matmul(bank[:, c * P:(c + 1) * P], S[r, c, :], qc[r, c, at], start=True, stop=False)
                                        last = nc.tensor.matmul(bank[:, c * P:(c + 1) * P], v_tok[:, n, h * P:(h + 1) * P], att[:, h, :], start=False, stop=True)
                                else:
                                    for c in range(NT):
                                        for q_ in range(2):
                                            h = 2 * c + q_
                                            last = nc.tensor.matmul(bank[rows[q_], c * P:(c + 1) * P], kc_tok[:, n, h * 64:(h + 1) * 64],
                                                                    v_tok[:, n, h * P:(h + 1) * P], start=True, stop=True)
                                last.then_inc(*mm_done.up())

                        @block.vector
                        def _(dve):
                            vlink(nc.vector.memset(S[:], 0.0))
                            ld = last_decay[:].rearrange("p (c n) -> p c n", n=KT)
                            for i, (n, nm, par) in enumerate(jobs):
                                at = slice(n * P, (n + 1) * P)
                                dve.wait_ge(mm_done.sem, m1 + i + 1)
                                two = ps[:, i % 8, 0:2 * P].rearrange("p (c i) -> p c i", c=NT)
                                if nm == "att":
                                    ins = nc.vector.tensor_tensor(att[:, par::2, :], two, bcast(incl, NT), ALU.mult)
                                elif nm == "o":
                                    dst = o[:, par::2, at]
                                    if back:
                                        ins = nc.vector.tensor_tensor(dst, dst, two, ALU.add)
                                    else:
                                        ins = nc.vector.tensor_copy(dst, two)
                                else:
                                    vlink(nc.vector.tensor_tensor(S[:], S[:], ld[:, :, n:n + 1].to_broadcast([P, NT, P]), ALU.mult))
                                    ins = nc.vector.tensor_tensor(S[:], S[:], two, ALU.add)
                                ins.then_inc(*dve_evac.up())
                                dve.wait_ge(dve_evac.sem, e1 + i + 1)
                m2, v2, a2 = mm_done.n, dve_out.n, act_out.n
                with nc.Block() as block:
                    @block.tensor
                    def _(pe):
                        for c in range(CT):
                            pe.wait_ge(dve_out.sem, v2 + c + 1)
                            nc.tensor.matmul(ps[:, c, :], ones, ks[:, c, 0, :], start=True, stop=True).then_inc(*mm_done.up())

                    @block.scalar
                    def _(act):
                        for c in range(CT):
                            act.wait_ge(dve_out.sem, v2 + CT + c + 1)
                            nc.scalar.activation(ks[:, c, 1, :], ks[:, c, 0, :], ACT.Sqrt).then_inc(*act_out.up())

                    @block.vector
                    def _(dve):
                        for c in range(CT):
                            nc.vector.tensor_tensor(ks[:, c, 0, :], o[:, c, :], o[:, c, :], ALU.mult).then_inc(*dve_out.up())
                        for c in range(CT):
                            dve.wait_ge(mm_done.sem, m2 + c + 1)
                            nc.vector.tensor_scalar(ks[:, c, 0, :], ps[:, c, :], 1.0 / P, RMS_EPS, ALU.mult, ALU.add).then_inc(*dve_out.up())
                        for c in range(CT):
                            dve.wait_ge(act_out.sem, a2 + c + 1)
                            vlink(nc.vector.reciprocal(ks[:, c, 1, :], ks[:, c, 1, :]))
                            vlink(nc.vector.scalar_tensor_tensor(o[:, c, :], o[:, c, :], vcol("gla_norm_w", c), ks[:, c, 1, :], ALU.mult, ALU.mult))
                            nc.vector.tensor_tensor(o[:, c, :], o[:, c, :], og[:, c, :], ALU.mult)
        def project_residual(w_dram, src, dst, gate=None, bias=None):
            w = w_dram.rearrange("(k p) n -> p k n", p=P)
            n_g = D // 512
            with ExitStack() as st:
                wb = sbuf(st, "wo" + str(mm_done.n), [P, n_g, KD, 512])
                tmp = sbuf(st, "wt" + str(mm_done.n), [P, 2, T])
                m0, v0 = mm_done.n, dve_evac.n
                w0 = [w_in[0].n, w_in[1].n]
                with nc.Block() as block:
                    @block.sync
                    def _(sp):
                        for g in range(n_g):
                            sp.dma_start(wb[:, g], w[:, :, g * 512:(g + 1) * 512]).then_inc(*w_in[g].up(16))

                    @block.tensor
                    def _(pe):
                        for m in range(KD):
                            if m % 4 == 0:
                                pe.wait_ge(w_in[m // 4].sem, w0[m // 4] + 16)
                            for k in range(KD):
                                last = nc.tensor.matmul(ps[:, m, :], wb[:, m // 4, k, (m % 4) * P:(m % 4 + 1) * P], src[:, k, :],
                                                        start=(k == 0), stop=(k == KD - 1))
                            last.then_inc(*mm_done.up())

                    @block.vector
                    def _(dve):
                        for m in range(KD):
                            dve.wait_ge(mm_done.sem, m0 + m + 1)
                            if gate is None:
                                nc.vector.tensor_tensor(dst[:, m, :], ps[:, m, :], dst[:, m, :], ALU.add)
                            elif bias is None:
                                nc.vector.scalar_tensor_tensor(dst[:, m, :], ps[:, m, :], gate(m), dst[:, m, :], ALU.mult, ALU.add)
                            else:
                                if m >= 2:
                                    dve.wait_ge(dve_evac.sem, v0 + m - 1)
                                vlink(nc.vector.tensor_scalar(tmp[:, m % 2, :], ps[:, m, :], bias(m), gate(m), ALU.add, ALU.mult))
                                nc.vector.tensor_tensor(dst[:, m, :], tmp[:, m % 2, :], dst[:, m, :], ALU.add).then_inc(*dve_evac.up())

        def rows_of(src, hi, lo):
            m0, a0 = mm_done.n, act_out.n
            jobs = [(n, half) for n in range(KT) for half in range(2)]
            with nc.Block() as block:
                @block.tensor
                def _(pe):
                    for j, (n, half) in enumerate(jobs):
                        for c in range(4):
                            last = nc.tensor.transpose(ps[:, j, c * P:(c + 1) * P], src[:, half * 4 + c, n * P:(n + 1) * P], ident)
                        last.then_inc(*mm_done.up())

                @block.scalar
                def _(act):
                    for j, (n, half) in enumerate(jobs):
                        act.wait_ge(mm_done.sem, m0 + j + 1)
                        nc.scalar.activation(hi[:, n, half * 512:(half + 1) * 512], ps[:, j, :], ACT.Copy).then_inc(*act_out.up())

                @block.vector
                def _(dve):
                    for j, (n, half) in enumerate(jobs):
                        at = slice(half * 512, (half + 1) * 512)
                        dve.wait_ge(act_out.sem, a0 + j + 1)
                        nc.vector.tensor_tensor(lo[:, n, at], ps[:, j, :], hi[:, n, at].bitcast(F32), ALU.subtract)

        def route_first(hT, rankm, wts, over_one, over_first, over_int, load_ahead):
            E, NG, NE = N_EXP1, N_GROUPS, PER_GROUP
            n_log = NG + E
            with ExitStack() as st:
                wr = sbuf(st, "w_route", [P, KD, n_log])
                br = sbuf(st, "b_route", [1, n_log])
                lg = sbuf(st, "logits", [P, KT, n_log])
                t4 = sbuf(st, "t4", [P, KT, NG])
                og = sbuf(st, "one_group", [P, KT, NG])
                prod = sbuf(st, "prod", [P, KT, NE, NG])
                fs = sbuf(st, "fine", [P, KT, NE])
                t8 = sbuf(st, "t8", [P, KT, NE])
                o1 = sbuf(st, "one_first", [P, KT, NE])
                o2 = sbuf(st, "one_second", [P, KT, NE])
                col = {n: sbuf(st, "col_" + n, [P, KT]) for n in ("m", "pg", "m1", "m2", "e2", "c1", "c2", "t")}
                E1 = sbuf(st, "E1", [P, KT, NG, NE])
                E2 = sbuf(st, "E2", [P, KT, NG, NE])
                M = sbuf(st, "Mboth", [P, KT, E])
                cnt = sbuf(st, "cnt", [P, E])
                nov = sbuf(st, "nov", [P, E])
                gt = sbuf(st, "gt", [P, E])
                cum = sbuf(st, "cum", [P, E])
                cux = sbuf(st, "cux", [P, E])
                ov = sbuf(st, "ov", [P, N_OVER, E])
                ofl = sbuf(st, "ofl", [P, N_OVER + 1])
                m0, a0, v0, l0 = mm_done.n, act_out.n, dve_out.n, inputs_in.n
                V = nc.vector

                def tt(o, a, b, op):
                    vlink(V.tensor_tensor(o, a, b, op))

                def over(ap, n):
                    return ap.unsqueeze(len(ap.shape)).to_broadcast(list(ap.shape) + [n])

                with nc.Block() as block:
                    @block.sync
                    def _(sp):
                        sp.dma_start(wr[:], A["moe_w_route"].rearrange("(k p) n -> p k n", p=P)).then_inc(*inputs_in.up(16))
                        sp.dma_start(br[:], A["moe_b_route"]).then_inc(*inputs_in.up(16))
                        load_ahead(sp)

                    @block.tensor
                    def _(pe):
                        pe.wait_ge(inputs_in.sem, l0 + 32)
                        for t in range(KT):
                            o = ps[:, 0, t * n_log:(t + 1) * n_log]
                            for k in range(KD):
                                nc.tensor.matmul(o, hT[:, k, t * P:(t + 1) * P], wr[:, k, :], start=(k == 0), stop=False)
                            last = nc.tensor.matmul(o, ones[0:1, :], br[:], start=False, stop=True)
                        last.then_inc(*mm_done.up())
                        pe.wait_ge(dve_out.sem, v0 + 3)
                        for t in range(KT):
                            o = ps[:, 1, t * E:(t + 1) * E]
                            for s in range(t + 1):
                                nc.tensor.matmul(o, before if s == t else ones, M[:, s, :], start=(s == 0), stop=(s == t))
                        for t in range(KT):
                            last = nc.tensor.matmul(ps[:, 2, 0:E], ones, M[:, t, :], start=(t == 0), stop=(t == KT - 1))
                        last.then_inc(*mm_done.up())

                    @block.scalar
                    def _(act):
                        act.wait_ge(dve_out.sem, v0 + 1)
                        nc.scalar.activation(t4[:], t4[:], ACT.Exp).then_inc(*act_out.up())
                        act.wait_ge(dve_out.sem, v0 + 2)
                        nc.scalar.activation(col["e2"][:], col["e2"][:], ACT.Exp).then_inc(*act_out.up())

                    @block.vector
                    def _(dve):
                        dve.wait_ge(mm_done.sem, m0 + 1)
                        vlink(V.tensor_copy(lg[:], ps[:, 0, 0:KT * n_log].rearrange("p (t n) -> p t n", t=KT)))
                        coarse = lg[:, :, 0:NG]
                        fine = lg[:, :, NG:].rearrange("p t (g e) -> p t e g", g=NG)
                        vlink(V.tensor_reduce(col["m"][:], coarse, AX.X, ALU.max))
                        V.tensor_tensor(t4[:], coarse, over(col["m"][:], NG), ALU.subtract).then_inc(*dve_out.up())
                        tt(og[:], coarse, over(col["m"][:], NG), ALU.is_equal)
                        tt(og[:], og[:], bcast(first4, KT), ALU.mult)
                        vlink(V.tensor_reduce(col["t"][:], og[:], AX.X, ALU.max))
                        tt(og[:], og[:], over(col["t"][:], NG), ALU.is_equal)
                        tt(prod[:], fine, og[:].unsqueeze(2).to_broadcast([P, KT, NE, NG]), ALU.mult)
                        vlink(V.tensor_reduce(fs[:], prod[:], AX.X, ALU.add))
                        for m, o in (("m1", o1), ("m2", o2)):
                            vlink(V.tensor_reduce(col[m][:], fs[:], AX.X, ALU.max))
                            tt(o[:], fs[:], over(col[m][:], NE), ALU.is_equal)
                            tt(o[:], o[:], bcast(first8, KT), ALU.mult)
                            vlink(V.tensor_reduce(col["t"][:], o[:], AX.X, ALU.max))
                            tt(o[:], o[:], over(col["t"][:], NE), ALU.is_equal)
                            if m == "m1":
                                vlink(V.tensor_scalar(t8[:], o1[:], -3e38, None, ALU.mult))
                                tt(fs[:], fs[:], t8[:], ALU.add)
                        V.tensor_tensor(col["e2"][:], col["m2"][:], col["m1"][:], ALU.subtract).then_inc(*dve_out.up())
                        for Eo, o in ((E1, o1), (E2, o2)):
                            tt(Eo[:], over(og[:], NE), o[:].unsqueeze(2).to_broadcast([P, KT, NG, NE]), ALU.mult)
                        e1, e2 = (x[:].rearrange("p t g e -> p t (g e)") for x in (E1, E2))
                        V.tensor_tensor(M[:], e1, e2, ALU.add).then_inc(*dve_out.up())
                        dve.wait_ge(act_out.sem, a0 + 2)
                        vlink(V.tensor_reduce(col["pg"][:], t4[:], AX.X, ALU.add))
                        vlink(V.reciprocal(col["pg"][:], col["pg"][:]))
                        vlink(V.tensor_scalar(col["c1"][:], col["e2"][:], 1.0, None, ALU.add))
                        vlink(V.reciprocal(col["c1"][:], col["c1"][:]))
                        tt(col["c1"][:], col["c1"][:], col["pg"][:], ALU.mult)
                        tt(col["c2"][:], col["c1"][:], col["e2"][:], ALU.mult)
                        tt(wts[:], e1, over(col["c1"][:], E), ALU.mult)
                        tt(e2, e2, over(col["c2"][:], E), ALU.mult)
                        tt(wts[:], wts[:], e2, ALU.add)
                        dve.wait_ge(mm_done.sem, m0 + 2)
                        vlink(V.scalar_tensor_tensor(rankm[:], ps[:, 1, 0:KT * E].rearrange("p (t e) -> p t e", t=KT), 1.0, M[:], ALU.add, ALU.mult))
                        vlink(V.tensor_scalar(rankm[:], rankm[:], -1.0, None, ALU.add))
                        vlink(V.tensor_copy(cnt[:], ps[:, 2, 0:E]))
                        vlink(V.tensor_scalar(nov[:], cnt[:], float(SLOTS), None, ALU.is_gt))
                        for j in range(2, MORE1 + 1):
                            vlink(V.tensor_scalar(gt[:], cnt[:], float(j * SLOTS), None, ALU.is_gt))
                            tt(nov[:], nov[:], gt[:], ALU.add)
                        vlink(V.tensor_tensor_scan(cum[:], ones[:, 0:E], nov[:], 0.0, ALU.mult, ALU.add))
                        tt(cux[:], cum[:], nov[:], ALU.subtract)
                        o_ax = overflows.unsqueeze(2).to_broadcast([P, N_OVER, E])
                        tt(over_one[:], bcast(cux[:], N_OVER), o_ax, ALU.is_le)
                        tt(ov[:], bcast(cum[:], N_OVER), o_ax, ALU.is_gt)
                        tt(over_one[:], over_one[:], ov[:], ALU.mult)
                        tt(ov[:], over_one[:], bcast(cux[:], N_OVER), ALU.mult)
                        vlink(V.tensor_reduce(over_first[:], ov[:], AX.X, ALU.add))
                        tt(over_first[:], overflows, over_first[:], ALU.subtract)
                        vlink(V.tensor_scalar(over_first[:], over_first[:], 1.0, float(SLOTS), ALU.add, ALU.mult))
                        tt(ov[:], over_one[:], bcast(experts, N_OVER), ALU.mult)
                        vlink(V.tensor_reduce(ofl[:, 0:N_OVER], ov[:], AX.X, ALU.add))
                        vlink(V.tensor_copy(ofl[:, N_OVER:], cum[:, E - 1:E]))
                        V.tensor_copy(over_int[:], ofl[:])

        def experts_pass(moe, tag, h_hi, h_lo, rankm, wts, n_exp, w_gate, w_up, w_down, ff, out_gate):
            n_groups = n_exp // (2 * PAIRS)
            halves = ff // 512
            steps = [(p, fh) for p in range(PAIRS) for fh in range(halves)]
            S = len(steps)
            GS = 2 * PAIRS * SLOTS
            per_bank = 512 // GS
            gather_banks = [5, 6, 7, 2]
            n_gb = KD // per_bank
            scatter_banks = 3
            wg = w_gate.rearrange("e (k p) f -> e p k f", p=P)
            wu = w_up.rearrange("e (k p) f -> e p k f", p=P)
            wd = w_down.rearrange("e (f p) d -> e p f d", p=P)
            units = [(name, s, x) for s in range(S) for name in ("gate", "up", "down") for x in range(2)]
            U = len(units)
            unit_at = {u: i for i, u in enumerate(units)}
            assert U % RING == 0
            turns = U // RING

            def scattered(fh):
                n = KD // halves
                first = min(scatter_banks, n // 2)
                tiles = list(range(fh * n, (fh + 1) * n))
                return tiles[:first], tiles[first:]

            jobs, act_jobs, dve_jobs = [], [], []
            for s, (p, fh) in enumerate(steps):
                early, late = scattered(fh)
                ends = fh == halves - 1
                jobs += [("gate", s), ("up", s)] + [("scatter", p, d) for d in early] + [("turn", s)] + [("scatter", p, d) for d in late]
                jobs += [("slot_to_token", p), ("slot_weight", p)] if ends else []
                jobs += [("down", s)]
                act_jobs += [("silu", s), ("turned", s)]
                act_jobs += [("slot_to_token", p), ("hi", p, 0), ("hi", p, 1)] if ends else []
                dve_jobs += [("hidden", s)] + [("add", p, d) for d in early + late]
                dve_jobs += [("slot_weight", p)] if ends else []
                if s == S - 1:
                    jobs += [("gather", b) for b in range(n_gb)]
                    act_jobs += [("gather", b) for b in range(0, n_gb, 2)]
                    dve_jobs += [("onehot", 0), ("weighted", 0)]
                dve_jobs += [("lo", p, 0), ("lo", p, 1)] if ends else []
                if s == S - 1:
                    dve_jobs += [("gather", b) for b in range(1, n_gb, 2)]
            job_at = {j: i + 1 for i, j in enumerate(jobs)}
            act_at = {j: i + 1 for i, j in enumerate(act_jobs)}
            dve_at = {j: i + 1 for i, j in enumerate(dve_jobs)}
            NM, NA, NV = len(jobs), len(act_jobs), len(dve_jobs)
            M0, A0, V0 = n_gb, n_gb // 2, n_gb // 2 + 2

            ring = sbuf(moe, tag + "_ring", [P, RING, 4096])
            G = sbuf(moe, tag + "_G", [P, KT, GS], F32R)
            Gw = sbuf(moe, tag + "_Gw", [P, KT, GS])
            XG = sbuf(moe, tag + "_XG", [P, KD, GS])
            GT = sbuf(moe, tag + "_GT", [P, T], F32R)
            w_slot = sbuf(moe, tag + "_w_slot", [P, 1])
            Y_hi = sbuf(moe, tag + "_Y_hi", [P, D], F32R)
            Y_lo = sbuf(moe, tag + "_Y_lo", [P, D], F32R)
            sil = sbuf(moe, tag + "_sil", [P, 512])
            hid = sbuf(moe, tag + "_hid", [P, 512])
            hidT = sbuf(moe, tag + "_hidT", [P, 4, P])
            unit_in = [signal(f"{tag}_unit_in{j}") for j in range(RING)]
            mm = signal(tag + "_mm")
            act_did = signal(tag + "_act")
            dve_did = signal(tag + "_dve")
            zeroed = signal(tag + "_zeroed")

            def load(sp, i, first_expert):
                name, s, x = units[i]
                p, fh = steps[s]
                e = first_expert + (2 * p + x)
                unit = ring[:, i % RING, :]
                if name == "down":
                    src = wd[bass.ds(e, 1), :, fh * 4:(fh + 1) * 4, :].rearrange("e p f d -> p (e f) d")
                    dst = unit.rearrange("p (f d) -> p f d", f=4)
                else:
                    w = wg if name == "gate" else wu
                    src = w[bass.ds(e, 1), :, :, fh * 512:(fh + 1) * 512].rearrange("e p k f -> p (e k) f")
                    dst = unit.rearrange("p (k f) -> p k f", k=KD)
                sp.dma_start(dst, src).then_inc(unit_in[i % RING].sem, 16)

            def load_ahead(sp):
                for i in range(RING):
                    load(sp, i, 0)

            def one_hots(mine, written):
                r = rankm[:, :, bass.ds(mine, 2 * PAIRS)].unsqueeze(3).to_broadcast([P, KT, 2 * PAIRS, SLOTS])
                s = slots.unsqueeze(1).unsqueeze(1).to_broadcast([P, KT, 2 * PAIRS, SLOTS])
                w = wts[:, :, bass.ds(mine, 2 * PAIRS)].unsqueeze(3).to_broadcast([P, KT, 2 * PAIRS, SLOTS])
                four = [x[:].rearrange("p t (e s) -> p t e s", s=SLOTS) for x in (G, Gw)]
                for t in range(KT):
                    ins = nc.vector.tensor_tensor(four[0][:, t], s[:, t], r[:, t], ALU.is_equal)
                ins.then_inc(dve_did.sem, 1)
                written()
                for t in range(KT):
                    ins = nc.vector.tensor_tensor(four[1][:, t], four[0][:, t].bitcast(F32), w[:, t], ALU.mult)
                ins.then_inc(dve_did.sem, 1)

            def gather():
                for b in range(n_gb):
                    for i in range(per_bank):
                        d = b * per_bank + i
                        parts = [(h, t) for h in (h_hi, h_lo) for t in range(KT)]
                        for j, (h, t) in enumerate(parts):
                            last = nc.tensor.matmul(ps[:, gather_banks[b], i * GS:(i + 1) * GS], h[:, t, d * P:(d + 1) * P], G[:, t, :],
                                                    start=(j == 0), stop=(j == len(parts) - 1))
                    last.then_inc(mm.sem, 1)

            def gathered(b):
                return (XG[:, b * per_bank:(b + 1) * per_bank, :], ps[:, gather_banks[b], :].rearrange("p (d s) -> p d s", s=GS))

            def scatter(p, d):
                bank = 5 + d % scatter_banks
                nc.tensor.matmul(ps[:, bank, :], Y_hi[:, d * P:(d + 1) * P], GT[:], start=True, stop=False)
                nc.tensor.matmul(ps[:, bank, :], Y_lo[:, d * P:(d + 1) * P], GT[:], start=False, stop=True).then_inc(mm.sem, 1)

            def add_output(d):
                bank = 5 + d % scatter_banks
                if out_gate is None:
                    ins = nc.vector.tensor_tensor(xT[:, d, :], ps[:, bank, :], xT[:, d, :], ALU.add)
                else:
                    ins = nc.vector.scalar_tensor_tensor(xT[:, d, :], ps[:, bank, :], out_gate(d), xT[:, d, :], ALU.mult, ALU.add)
                ins.then_inc(dve_did.sem, 1)

            def run():
                with nc.Block() as block:
                    @block.sync
                    def _(sp):
                        def refill(j, g):
                            i, later = (j + RING) % U, (j + RING) // U
                            name, s, _ = units[j]
                            sp.wait_ge(mm.sem, M0 + g * NM + job_at[(name, s)])
                            load(sp, i, (g + later) * (2 * PAIRS))

                        with sp.Fori(0, n_groups - 1) as g:
                            for j in range(U):
                                refill(j, g)
                        for j in range(U - RING):
                            refill(j, n_groups - 1)

                    @block.gpsimd
                    def _(pool):
                        nc.gpsimd.memset(Y_hi[:].bitcast(F32), 0.0).then_inc(zeroed.sem, 1)
                        nc.gpsimd.memset(Y_lo[:].bitcast(F32), 0.0).then_inc(zeroed.sem, 1)
                        nc.gpsimd.memset(GT[:].bitcast(F32), 0.0).then_inc(zeroed.sem, 1)
                        nc.gpsimd.memset(rankm[:, :, n_exp:], -1.0).then_inc(zeroed.sem, 1)
                        nc.gpsimd.memset(wts[:, :, n_exp:], 0.0).then_inc(zeroed.sem, 1)

                    @block.tensor
                    def _(pe):
                        pe.wait_ge(dve_did.sem, 1)
                        gather()
                        pe.wait_ge(zeroed.sem, 3)
                        with pe.Fori(0, n_groups) as g:
                            def after_act(*job):
                                pe.wait_ge(act_did.sem, A0 + g * NA + act_at[job])

                            def after_dve(*job):
                                pe.wait_ge(dve_did.sem, V0 + g * NV + dve_at[job])

                            def unit(name, s, x):
                                i = unit_at[(name, s, x)]
                                pe.wait_ge(unit_in[i % RING].sem, (g * turns + (i // RING + 1)) * 16)
                                return ring[:, i % RING, :]

                            def scatter_tiles(p, tiles):
                                for d in tiles:
                                    if d == 0 and p > 0:
                                        after_act("hi", p - 1, 1)
                                        after_dve("lo", p - 1, 1)
                                    if d >= scatter_banks:
                                        after_dve("add", p, d - scatter_banks)
                                    elif p > 0:
                                        after_dve("add", p - 1, KD - 1)
                                    scatter(p, d)

                            for s, (p, fh) in enumerate(steps):
                                early, late = scattered(fh)
                                ends = fh == halves - 1
                                for bank, name in enumerate(("gate", "up")):
                                    w = [unit(name, s, x) for x in range(2)]
                                    if p > 0 and fh == 0:
                                        if name == "gate":
                                            after_dve("slot_weight", p - 1)
                                        else:
                                            after_act("slot_to_token", p - 1)
                                    for k in range(KD):
                                        if s == 0 and name == "gate" and k % per_bank == 0:
                                            b = k // per_bank
                                            if b % 2 == 0:
                                                pe.wait_ge(act_did.sem, g * NA + (b // 2 + 1))
                                            else:
                                                pe.wait_ge(dve_did.sem, g * NV + (2 + b // 2 + 1))
                                        for x in range(2):
                                            c0 = p * P + x * SLOTS
                                            last = nc.tensor.matmul(ps[x * SLOTS:(x + 1) * SLOTS, bank, :], XG[:, k, c0:c0 + SLOTS],
                                                                    w[x][:, k * 512:(k + 1) * 512], start=(k == 0), stop=(k == KD - 1))
                                    last.then_inc(mm.sem, 1)
                                scatter_tiles(p, early)
                                after_dve("hidden", s)
                                for f in range(4):
                                    last = nc.tensor.transpose(ps[:, 2, f * P:(f + 1) * P], hid[:, f * P:(f + 1) * P], ident)
                                last.then_inc(mm.sem, 1)
                                scatter_tiles(p, late)
                                if ends:
                                    for t in range(KT):
                                        last = nc.tensor.transpose(ps[:, 1, t * P:(t + 1) * P], G[:, t, p * P:(p + 1) * P].bitcast(F32), ident)
                                    last.then_inc(mm.sem, 1)
                                    for t in range(KT):
                                        last = nc.tensor.matmul(ps[:, 0, 0:1], Gw[:, t, p * P:(p + 1) * P], ones[:, 0:1], start=(t == 0), stop=(t == KT - 1))
                                    last.then_inc(mm.sem, 1)
                                w = [unit("down", s, x) for x in range(2)]
                                after_act("turned", s)
                                for x in range(2):
                                    rows = slice(x * SLOTS, (x + 1) * SLOTS)
                                    for half in range(2):
                                        for f in range(4):
                                            last = nc.tensor.matmul(ps[rows, 3 + half, :], hidT[:, f, rows], w[x][:, f * D + half * 512:f * D + half * 512 + 512],
                                                                    start=(fh == 0 and f == 0), stop=(ends and f == 3))
                                last.then_inc(mm.sem, 1)
                            after_dve("onehot", 0)
                            gather()
                        for d in range(KD):
                            if d >= scatter_banks:
                                pe.wait_ge(dve_did.sem, V0 + n_groups * NV + d - scatter_banks + 1)
                            else:
                                pe.wait_ge(act_did.sem, A0 + n_groups * NA)
                                pe.wait_ge(dve_did.sem, V0 + n_groups * NV)
                            scatter(0, d)

                    @block.scalar
                    def _(act):
                        for b in range(0, n_gb, 2):
                            act.wait_ge(mm.sem, b + 1)
                            to, bank = gathered(b)
                            nc.scalar.activation(to, bank, ACT.Copy).then_inc(act_did.sem, 1)
                        with act.Fori(0, n_groups) as g:
                            def after_pe(*job):
                                act.wait_ge(mm.sem, M0 + g * NM + job_at[job])

                            for job in act_jobs:
                                name, j = job[0:2]
                                if name == "silu":
                                    after_pe("gate", j)
                                    ins = nc.scalar.activation(sil[:], ps[:, 0, :], ACT.Silu)
                                elif name == "turned":
                                    after_pe("turn", j)
                                    ins = nc.scalar.activation(hidT[:], ps[:, 2, :].rearrange("p (f s) -> p f s", f=4), ACT.Copy)
                                elif name == "slot_to_token":
                                    after_pe(*job)
                                    ins = nc.scalar.activation(GT[:], ps[:, 1, :], ACT.Copy)
                                elif name == "hi":
                                    half = job[2]
                                    after_pe("down", j * halves + halves - 1)
                                    act.wait_ge(dve_did.sem, V0 + g * NV + dve_at[("slot_weight", j)])
                                    ins = nc.scalar.activation(Y_hi[:, half * 512:(half + 1) * 512], ps[:, 3 + half, :], ACT.Copy, scale=w_slot[:])
                                else:
                                    after_pe(*job)
                                    to, bank = gathered(j)
                                    ins = nc.scalar.activation(to, bank, ACT.Copy)
                                ins.then_inc(act_did.sem, 1)

                    @block.vector
                    def _(dve):
                        def own(n):
                            return lambda: dve.wait_ge(dve_did.sem, n)

                        one_hots(0, own(1))
                        for b in range(1, n_gb, 2):
                            dve.wait_ge(mm.sem, b + 1)
                            to, bank = gathered(b)
                            nc.vector.tensor_copy(to, bank).then_inc(dve_did.sem, 1)
                        dve.wait_ge(zeroed.sem, 5)
                        with dve.Fori(0, n_groups) as g:
                            def after_pe(*job):
                                dve.wait_ge(mm.sem, M0 + g * NM + job_at[job])

                            for job in dve_jobs:
                                name, j = job[0:2]
                                if name == "hidden":
                                    after_pe("up", j)
                                    dve.wait_ge(act_did.sem, A0 + g * NA + act_at[("silu", j)])
                                    nc.vector.tensor_tensor(hid[:], ps[:, 1, :], sil[:], ALU.mult).then_inc(dve_did.sem, 1)
                                elif name == "add":
                                    after_pe("scatter", j, job[2])
                                    add_output(job[2])
                                elif name == "slot_weight":
                                    after_pe(*job)
                                    nc.vector.tensor_copy(w_slot[:], ps[:, 0, 0:1]).then_inc(dve_did.sem, 1)
                                elif name == "onehot":
                                    one_hots(g * (2 * PAIRS) + 2 * PAIRS, own(V0 + g * NV + dve_at[job]))
                                elif name == "weighted":
                                    pass
                                elif name == "lo":
                                    half = job[2]
                                    dve.wait_ge(act_did.sem, A0 + g * NA + act_at[("hi", j, half)])
                                    at = slice(half * 512, (half + 1) * 512)
                                    nc.vector.scalar_tensor_tensor(Y_lo[:, at], ps[:, 3 + half, :], w_slot[:], Y_hi[:, at].bitcast(F32), ALU.mult, ALU.subtract).then_inc(dve_did.sem, 1)
                                else:
                                    after_pe(*job)
                                    to, bank = gathered(j)
                                    nc.vector.tensor_copy(to, bank).then_inc(dve_did.sem, 1)
                        for d in range(KD):
                            dve.wait_ge(mm.sem, M0 + n_groups * NM + d + 1)
                            add_output(d)

            return load_ahead, run

        def overflow_pass(h_hi, h_lo, rankm, wts, over_one, over_first, over_int):
            wg = A["moe_w_gate"].rearrange("e (k p) f -> e p k f", p=P)
            wu = A["moe_w_up"].rearrange("e (k p) f -> e p k f", p=P)
            wd = A["moe_w_down"].rearrange("e (f p) d -> e p f d", p=P)
            with ExitStack() as st:
                wgb = sbuf(st, "ov_wg", [P, KD, 512])
                wub = sbuf(st, "ov_wu", [P, KD, 512])
                wdb = sbuf(st, "ov_wd", [P, 4, D])
                sel = sbuf(st, "ov_sel", [P, KT, N_EXP1])
                r_o = sbuf(st, "ov_r", [P, KT])
                w_o = sbuf(st, "ov_w", [P, KT])
                G = sbuf(st, "ov_G", [P, KT, P])
                X = sbuf(st, "ov_X", [P, KD, SLOTS])
                GT = sbuf(st, "ov_GT", [SLOTS, T])
                hid = sbuf(st, "ov_hid", [P, 512])
                hidT = sbuf(st, "ov_hidT", [P, 4, SLOTS])
                Y = sbuf(st, "ov_Y", [SLOTS, D])
                w_here = signal("ov_w_here")
                mm = signal("ov_mm")
                dve_did = signal("ov_dve")
                silu = signal("ov_silu")
                v_steps = ["sel", "r", "sel2", "w", "shift", "G0", "G1", "G2", "G3", "X", "W0", "W1", "W2", "W3", "GT", "hid", "hidT", "Y0", "Y1"]
                v_steps += [f"out{d}" for d in range(KD)]
                v_at = {n: i + 1 for i, n in enumerate(v_steps)}
                p_steps = ["gather", "gt", "gate", "up", "turn", "down"] + [f"out{d}" for d in range(KD)]
                p_at = {n: i + 1 for i, n in enumerate(p_steps)}
                NV, NP = len(v_steps), len(p_steps)

                with nc.Block() as block:
                    @block.gpsimd
                    def _(pool):
                        nc.gpsimd.memset(G[:], 0.0).then_inc(dve_did.sem, 1)
                        nc.gpsimd.memset(hid[:], 0.0).then_inc(mm.sem, 1)

                def blocks(eng):
                    return eng.value_load(over_int[0:1, N_OVER:N_OVER + 1], min_val=0, max_val=N_OVER)

                with nc.Block() as block:
                    @block.sync
                    def _(sp):
                        n = blocks(sp)
                        with sp.Fori(0, N_OVER) as o:
                            with sp.If(o < n):
                                e = sp.value_load(over_int[0:1, bass.ds(o, 1)], min_val=0, max_val=N_EXP1 - 1)
                                sp.wait_ge(mm.sem, o * NP + 1)
                                sp.dma_start(wgb[:], wg[bass.ds(e, 1)].rearrange("e p k f -> p (e k) f")).then_inc(w_here.sem, 16)
                                sp.dma_start(wub[:], wu[bass.ds(e, 1)].rearrange("e p k f -> p (e k) f")).then_inc(w_here.sem, 16)
                                sp.dma_start(wdb[:], wd[bass.ds(e, 1)].rearrange("e p f d -> p (e f) d")).then_inc(w_here.sem, 16)

                    @block.tensor
                    def _(pe):
                        n = blocks(pe)
                        with pe.Fori(0, N_OVER) as o:
                            with pe.If(o < n):
                                def after(step):
                                    pe.wait_ge(dve_did.sem, o * NV + v_at[step] + 1)

                                after("G3")
                                for d in range(KD):
                                    parts = [(h, t) for h in (h_hi, h_lo) for t in range(KT)]
                                    for j, (h, t) in enumerate(parts):
                                        last = nc.tensor.matmul(ps[:, 0, d * SLOTS:(d + 1) * SLOTS], h[:, t, d * P:(d + 1) * P].bitcast(F32), G[:, t, 0:SLOTS],
                                                                start=(j == 0), stop=(j == len(parts) - 1))
                                last.then_inc(mm.sem, 1)
                                after("W3")
                                for t in range(KT):
                                    last = nc.tensor.transpose(ps[:, 1, t * P:(t + 1) * P], G[:, t, :], ident)
                                last.then_inc(mm.sem, 1)
                                pe.wait_ge(w_here.sem, o * 48 + 48)
                                for bank, w in ((2, wgb), (3, wub)):
                                    for k in range(KD):
                                        last = nc.tensor.matmul(ps[0:SLOTS, bank, :], X[:, k, :], w[:, k, :], start=(k == 0), stop=(k == KD - 1))
                                    last.then_inc(mm.sem, 1)
                                after("hid")
                                for f in range(4):
                                    last = nc.tensor.transpose(ps[:, 4, f * P:(f + 1) * P], hid[:, f * P:(f + 1) * P], ident)
                                last.then_inc(mm.sem, 1)
                                after("hidT")
                                for half in range(2):
                                    for f in range(4):
                                        last = nc.tensor.matmul(ps[0:SLOTS, 5 + half, :], hidT[:, f, :], wdb[:, f, half * 512:(half + 1) * 512], start=(f == 0), stop=(f == 3))
                                last.then_inc(mm.sem, 1)
                                after("Y1")
                                for d in range(KD):
                                    nc.tensor.matmul(ps[:, d, :], Y[:, d * P:(d + 1) * P], GT[:], start=True, stop=True).then_inc(mm.sem, 1)

                    @block.scalar
                    def _(act):
                        n = blocks(act)
                        with act.Fori(0, N_OVER) as o:
                            with act.If(o < n):
                                act.wait_ge(mm.sem, o * NP + p_at["gate"] + 1)
                                act.wait_ge(dve_did.sem, o * NV + 1)
                                nc.scalar.activation(hid[0:SLOTS, :], ps[0:SLOTS, 2, :], ACT.Silu).then_inc(silu.sem, 1)

                    @block.vector
                    def _(dve):
                        n = blocks(dve)
                        with dve.Fori(0, N_OVER) as o:
                            with dve.If(o < n):
                                V = nc.vector

                                def done(step, ins):
                                    ins.then_inc(dve_did.sem, 1)
                                    if step != v_steps[-1]:
                                        dve.wait_ge(dve_did.sem, o * NV + v_at[step] + 1)

                                def after(step):
                                    dve.wait_ge(mm.sem, o * NP + p_at[step] + 1)

                                dve.wait_ge(dve_did.sem, o * NV + 1)
                                one = over_one[:, bass.ds(o, 1), :].to_broadcast([P, KT, N_EXP1])
                                done("sel", V.tensor_tensor(sel[:], rankm[:], one, ALU.mult))
                                done("r", V.tensor_reduce(r_o[:], sel[:], AX.X, ALU.add))
                                done("sel2", V.tensor_tensor(sel[:], wts[:], one, ALU.mult))
                                done("w", V.tensor_reduce(w_o[:], sel[:], AX.X, ALU.add))
                                done("shift", V.tensor_tensor(r_o[:], r_o[:], over_first[:, bass.ds(o, 1)].to_broadcast([P, KT]), ALU.subtract))
                                for t in range(KT):
                                    done(f"G{t}", V.tensor_scalar(G[:, t, 0:SLOTS], slots, r_o[:, t:t + 1], None, ALU.is_equal))
                                after("gather")
                                done("X", V.tensor_copy(X[:], ps[:, 0, :].rearrange("p (k s) -> p k s", k=KD)))
                                for t in range(KT):
                                    done(f"W{t}", V.tensor_scalar(G[:, t, 0:SLOTS], G[:, t, 0:SLOTS], w_o[:, t:t + 1], None, ALU.mult))
                                after("gt")
                                done("GT", V.tensor_copy(GT[:], ps[0:SLOTS, 1, :]))
                                after("up")
                                dve.wait_ge(silu.sem, o + 1)
                                done("hid", V.tensor_tensor(hid[0:SLOTS, :], ps[0:SLOTS, 3, :], hid[0:SLOTS, :], ALU.mult))
                                after("turn")
                                done("hidT", V.tensor_copy(hidT[:], ps[:, 4, :].rearrange("p (f s) -> p f s", f=4)[:, :, 0:SLOTS]))
                                after("down")
                                for half in range(2):
                                    done(f"Y{half}", V.tensor_copy(Y[:, half * 512:(half + 1) * 512], ps[0:SLOTS, 5 + half, :]))
                                for d in range(KD):
                                    after(f"out{d}")
                                    done(f"out{d}", V.tensor_tensor(xT[:, d, :], ps[:, d, :], xT[:, d, :], ALU.add))

        def modulation(l, mod, mod_c, scaled):
            w = A["w_mod_2"][l].rearrange("(k p) n -> p k n", p=P)
            n_g = 6 * D // 512
            n_buf = 4
            with ExitStack() as st:
                wb = sbuf(st, "mod_w", [P, n_buf, KD, 512])
                rows = sbuf(st, "mod_rows", [P, 2, 512])
                act_c = sbuf(st, "mod_c", [P, KD, 32])
                here = [signal(f"mod{l}_w{j}") for j in range(n_buf)]
                m0, v0, a0, p0 = mm_done.n, dve_out.n, act_out.n, pool_out.n
                picked = table("quarter_rows", 2)
                with nc.Block() as block:
                    @block.sync
                    def _(sp):
                        for g in range(n_g):
                            if g >= n_buf:
                                sp.wait_ge(mm_done.sem, m0 + 2 * (g - n_buf) + 1)
                            sp.dma_start(wb[:, g % n_buf], w[:, :, g * 512:(g + 1) * 512]).then_inc(*here[g % n_buf].up(16))

                    @block.gpsimd
                    def _(pool):
                        nc.gpsimd.memset(act_c[:], 0.0).then_inc(*pool_out.up())

                    @block.scalar
                    def _(act):
                        act.wait_ge(pool_out.sem, p0 + 1)
                        nc.scalar.activation(act_c[:, :, 0:1], vcol("c_2", 0, KD).unsqueeze(2), ACT.Silu).then_inc(*act_out.up())
                        nc.scalar.activation(act_c[:, :, 1:2], vcol("c_ctx_2", 0, KD).unsqueeze(2), ACT.Silu).then_inc(*act_out.up())

                    @block.tensor
                    def _(pe):
                        pe.wait_ge(act_out.sem, a0 + 2)

                        def columns(g):
                            pe.wait_ge(dve_out.sem, v0 + g + 1)
                            for j in range(4):
                                at = 2 * (4 * g + j)
                                last = nc.tensor.matmul(ps[:, 7, at:at + 2], rows[:, g % 2, j * P:(j + 1) * P], picked, start=True, stop=True)
                            last.then_inc(*mm_done.up())

                        for g in range(n_g):
                            pe.wait_ge(here[g % n_buf].sem, here[g % n_buf].n - 16 * ((n_g - 1 - g) // n_buf))
                            if g >= 2:
                                pe.wait_ge(dve_out.sem, v0 + g - 1)
                            for k in range(KD):
                                q = k % 4
                                last = nc.tensor.matmul(ps[32 * q:32 * q + 32, g % 2, :], act_c[:, k, :], wb[:, g % n_buf, k, :],
                                                        start=(k < 4), stop=(k >= 4))
                            last.then_inc(*mm_done.up())
                            if g > 0:
                                columns(g - 1)
                        columns(n_g - 1)

                    @block.vector
                    def _(dve):
                        for g in range(n_g):
                            dve.wait_ge(mm_done.sem, m0 + (1 if g == 0 else 2 * g))
                            if g >= 2:
                                dve.wait_ge(mm_done.sem, m0 + 2 * g - 1 if g < 3 else m0 + 2 * (g - 1) - 1)
                            nc.vector.tensor_copy(rows[:, g % 2, :], ps[:, g % 2, :]).then_inc(*dve_out.up())
                        dve.wait_ge(mm_done.sem, m0 + 2 * n_g)
                        got = ps[:, 7, 0:96].rearrange("p (c j) -> p c j", j=2)
                        bias = vcol("b_mod_2", 48 * l, 48)
                        vlink(nc.vector.tensor_tensor(mod[:], got[:, :, 0], bias, ALU.add))
                        for j, (norm, part) in enumerate((("norm1_g_2", 1), ("norm2_g_2", 4))):
                            nc.vector.scalar_tensor_tensor(scaled[:, j, :], mod[:, 8 * part:8 * part + 8], 1.0, vcol(norm, 8 * l, 8), ALU.add, ALU.mult)
                        if l == 0:
                            vlink(nc.vector.tensor_tensor(mod_c[:, 0:16], got[:, 0:16, 1], bias[:, 0:16], ALU.add))
                            nc.vector.scalar_tensor_tensor(mod_c[:, 16:24], mod_c[:, 8:16], 1.0, vcol("norm1_g_2", 0, 8), ALU.add, ALU.mult)

        def project_even(hT, n_tok, col_tiles, gate, xa, hy):
            w = A["w_in_2"].rearrange("(k p) n -> p k n", p=P)
            groups = [col_tiles[i:i + 4] for i in range(0, len(col_tiles), 4)]
            n = len(col_tiles)
            conv = [i for i in range(n) if col_tiles[i] >= 4]
            nth = {i: j for j, i in enumerate(conv)}
            with ExitStack() as st:
                wb = sbuf(st, "we", [P, 2, KD, 512])
                pad = sbuf(st, "pad_e", [P, 3, n_tok + 3])
                m0, a0, v0, p0 = mm_done.n, act_evac.n, dve_out.n, pool_out.n
                w0 = [w_in[0].n, w_in[1].n]
                with nc.Block() as block:
                    @block.sync
                    def _(sp):
                        for g, tiles in enumerate(groups):
                            if g >= 2:
                                sp.wait_ge(mm_done.sem, m0 + 4 * (g - 1))
                            sp.dma_start(wb[:, g % 2], w[:, :, tiles[0] * P:tiles[0] * P + 512]).then_inc(*w_in[g % 2].up(16))

                    @block.gpsimd
                    def _(pool):
                        nc.gpsimd.memset(pad[:], 0.0).then_inc(*pool_out.up())

                    @block.tensor
                    def _(pe):
                        for i in range(n):
                            g, j = i // 4, i % 4
                            if j == 0:
                                pe.wait_ge(w_in[g % 2].sem, w0[g % 2] + 16 * (g // 2 + 1))
                            if i >= 8:
                                pe.wait_ge(act_evac.sem, a0 + i - 7)
                            for k in range(KD):
                                last = nc.tensor.matmul(ps[:, i % 8, 0:n_tok], wb[:, g % 2, k, j * P:(j + 1) * P], hT[:, k, :],
                                                        start=(k == 0), stop=(k == KD - 1))
                            last.then_inc(*mm_done.up())

                    @block.scalar
                    def _(act):
                        act.wait_ge(pool_out.sem, p0 + 1)
                        for i, c in enumerate(col_tiles):
                            act.wait_ge(mm_done.sem, m0 + i + 1)
                            if c < 4:
                                ins = nc.scalar.activation(gate[:, c, :], ps[:, i % 8, 0:n_tok], ACT.Gelu_apprx_tanh)
                            else:
                                if nth[i] >= 3:
                                    act.wait_ge(dve_out.sem, v0 + nth[i] - 2)
                                ins = nc.scalar.activation(pad[:, nth[i] % 3, 1:n_tok + 1], ps[:, i % 8, 0:n_tok], ACT.Copy)
                            ins.then_inc(*act_evac.up())

                    @block.vector
                    def _(dve):
                        for i in conv:
                            c = col_tiles[i]
                            dve.wait_ge(act_evac.sem, a0 + i + 1)
                            if c < 8:
                                dst, taps, wt, bias, t0, n_t = xa[:, c - 4, :], 4, "conv_a_w_2", "conv_a_b_2", c - 4, 4
                            else:
                                dst, taps, wt, bias, t0, n_t = hy[:, c - 8, :], 3, "conv_b_w_2", "conv_b_b_2", c - 8, 12
                            b = nth[i] % 3
                            vlink(nc.vector.tensor_scalar(dst, pad[:, b, 0:n_tok], vcol(wt, t0), vcol(bias, t0), ALU.mult, ALU.add))
                            for k in range(1, taps):
                                ins = nc.vector.scalar_tensor_tensor(dst, pad[:, b, k:n_tok + k], vcol(wt, k * n_t + t0), dst, ALU.mult, ALU.add)
                                if k < taps - 1:
                                    vlink(ins)
                            ins.then_inc(*dve_out.up())

        def lru_rates(rate):
            with ExitStack() as st:
                e = sbuf(st, "rate_e", [P, 8])
                lam = vcol("lru_lam_2", 0, 8)
                a0 = act_out.n
                with nc.Block() as block:
                    @block.scalar
                    def _(act):
                        alink(nc.scalar.activation(e[:], lam, ACT.Abs))
                        alink(nc.scalar.activation(e[:], e[:], ACT.Exp, scale=-1.0))
                        nc.scalar.activation(e[:], e[:], ACT.Ln, bias=1.0).then_inc(*act_out.up())

                    @block.vector
                    def _(dve):
                        dve.wait_ge(act_out.sem, a0 + 1)
                        vlink(nc.vector.scalar_tensor_tensor(e[:], lam, 0.0, e[:], ALU.min, ALU.subtract))
                        nc.vector.tensor_scalar(rate[:, 0, :], e[:], LRU_C, None, ALU.mult)
                        nc.vector.tensor_scalar(rate[:, 1, :], e[:], -LRU_C, None, ALU.mult)

        def lru_scan(xa, n_tok, gates, rate, start, final, total):
            n_j = 2 * CT
            with ExitStack() as st:
                r = sbuf(st, "lru_r", [P, n_j, n_tok])
                i_ = sbuf(st, "lru_i", [P, n_j, n_tok])
                th = sbuf(st, "lru_th", [P, n_j, n_tok])
                h = sbuf(st, "lru_h", [P, n_j, n_tok])
                m0, a0, v0 = mm_done.n, act_out.n, dve_out.n
                with nc.Block() as block:
                    @block.tensor
                    def _(pe):
                        for q in range(2):
                            for j in range(n_j):
                                if q == 1:
                                    pe.wait_ge(act_out.sem, a0 + j + 1)
                                nc.tensor.matmul(ps[:, j, 0:n_tok], gates[:, q, j // CT, j % CT, :], xa[:, j % CT, :], start=True, stop=True).then_inc(*mm_done.up())

                    @block.scalar
                    def _(act):
                        for q, (dst, bias) in enumerate(((r, "lru_br_2"), (i_, "lru_bi_2"))):
                            for j in range(n_j):
                                act.wait_ge(mm_done.sem, m0 + q * n_j + j + 1)
                                nc.scalar.activation(dst[:, j, :], ps[:, j, 0:n_tok], ACT.Sigmoid, bias=vcol(bias, j)).then_inc(*act_out.up())
                        act.wait_ge(act_out.sem, act_out.n)
                        for j in range(n_j):
                            nc.scalar.activation(th[:, j, :], r[:, j, :], ACT.Tanh, scale=rate[:, 1, j:j + 1]).then_inc(*act_out.up())
                        act.wait_ge(act_out.sem, act_out.n)
                        for j in range(n_j):
                            nc.scalar.activation(r[:, j, :], r[:, j, :], ACT.Exp, scale=rate[:, 0, j:j + 1]).then_inc(*act_out.up())
                        for j in range(n_j):
                            act.wait_ge(dve_out.sem, v0 + j + 1)
                            nc.scalar.activation(th[:, j, :], th[:, j, :], ACT.Sqrt).then_inc(*act_out.up())

                    @block.vector
                    def _(dve):
                        for j in range(n_j):
                            dve.wait_ge(act_out.sem, a0 + 3 * n_j + j + 1)
                            vlink(nc.vector.tensor_tensor(h[:, j, :], r[:, j, :], r[:, j, :], ALU.mult))
                            nc.vector.scalar_tensor_tensor(th[:, j, :], h[:, j, :], 1.0, th[:, j, :], ALU.add, ALU.mult).then_inc(*dve_out.up())
                        for j in range(n_j):
                            vlink(nc.vector.tensor_tensor(i_[:, j, :], i_[:, j, :], xa[:, j % CT, :], ALU.mult))
                            dve.wait_ge(act_out.sem, a0 + 4 * n_j + j + 1)
                            vlink(nc.vector.tensor_tensor(i_[:, j, :], i_[:, j, :], th[:, j, :], ALU.mult))
                            s0 = 0.0 if start is None else start[:, j:j + 1]
                            way = slice(None, None, -1) if j >= CT else slice(None)
                            vlink(nc.vector.tensor_tensor_scan(h[:, j, way], r[:, j, way], i_[:, j, way], s0, ALU.mult, ALU.add))
                            if final is not None:
                                end = 0 if j >= CT else n_tok - 1
                                nc.vector.tensor_copy(final[:, j:j + 1], h[:, j, end:end + 1])
                            if total is not None and j >= CT:
                                c = j - CT
                                vlink(nc.vector.tensor_tensor(h[:, j, :], h[:, j, :], h[:, c, :], ALU.add))
                                nc.vector.tensor_tensor(total[:, c, :], total[:, c, :], h[:, j, :], ALU.mult)

        def hyena_filters(spec, Kc, Ks):
            with ExitStack() as st:
                z = sbuf(st, "f_z", [FILTER_EMB, T])
                w1 = sbuf(st, "f_w1", [FILTER_EMB, FILTER_HIDDEN])
                w2 = sbuf(st, "f_w2", [FILTER_HIDDEN, FILTER_HIDDEN])
                w3 = sbuf(st, "f_w3", [FILTER_HIDDEN + 1, 4 * HYENA_WIDTH])
                win = sbuf(st, "f_win", [P, KT, HYENA_WIDTH])
                x = sbuf(st, "f_x", [FILTER_HIDDEN, T])
                turns = sbuf(st, "f_turns", [FILTER_HIDDEN, T])
                hid = sbuf(st, "f_hid", [FILTER_HIDDEN + 1, T])
                both = sbuf(st, "f_both", [P, KT, 2, HYENA_WIDTH])
                fsum = sbuf(st, "f_sum", [P, KT, HYENA_WIDTH])
                fdiff = sbuf(st, "f_diff", [P, KT, HYENA_WIDTH])
                m0, a0, v0, l0, e0 = mm_done.n, act_out.n, dve_out.n, inputs_in.n, act_evac.n
                H = FILTER_HIDDEN
                with nc.Block() as block:
                    @block.sync
                    def _(sp):
                        for dst, src in ((z[:], A["hy_z"]), (w1[:], A["filt_w1_2"]), (w2[:], A["filt_w2_2"]), (w3[:], A["filt_w3_2"]),
                                         (win[:], A["hy_window"].rearrange("(t p) c -> p t c", p=P)),
                                         (spec[:], A["hy_spectrum"].rearrange("(t p) f -> p t f", p=P))):
                            sp.dma_start(dst, src).then_inc(*inputs_in.up(16))

                    @block.tensor
                    def _(pe):
                        pe.wait_ge(inputs_in.sem, l0 + 96)
                        nc.tensor.matmul(ps[0:H, 0, :], w1[:], z[:], start=True, stop=True).then_inc(*mm_done.up())
                        pe.wait_ge(act_out.sem, a0 + 1)
                        nc.tensor.matmul(ps[0:H, 1, :], w2[:], hid[0:H, :], start=True, stop=True).then_inc(*mm_done.up())
                        pe.wait_ge(act_out.sem, a0 + 2)
                        pe.wait_ge(dve_out.sem, v0 + 3)
                        for o in range(HYENA_ORDER):
                            if o > 0:
                                pe.wait_ge(act_evac.sem, e0 + 8 * o)
                            for t in range(KT):
                                for q in range(2):
                                    nc.tensor.matmul(ps[:, 2 * t + q, :], hid[:, t * P:(t + 1) * P], w3[:, (2 * o + q) * 512:(2 * o + q + 1) * 512],
                                                     start=True, stop=True).then_inc(*mm_done.up())
                            pe.wait_ge(dve_out.sem, v0 + 4 + o)
                            for q, src in enumerate((fsum, fdiff)):
                                for f in range(KT):
                                    for t in range(KT):
                                        last = nc.tensor.matmul(ps[:, 4 * q + f, :], spec[:, t, q * T + f * P:q * T + (f + 1) * P], src[:, t, :],
                                                                start=(t == 0), stop=(t == KT - 1))
                                    last.then_inc(*mm_done.up())

                    @block.scalar
                    def _(act):
                        for j in range(2):
                            act.wait_ge(dve_out.sem, v0 + j + 1)
                            nc.scalar.activation(hid[0:H, :], x[:], ACT.Sin).then_inc(*act_out.up())
                        for o in range(HYENA_ORDER):
                            for q, dst in enumerate((Kc, Ks)):
                                for f in range(KT):
                                    act.wait_ge(mm_done.sem, m0 + 2 + 16 * o + 8 + 4 * q + f + 1)
                                    nc.scalar.activation(dst[:, f, o, :], ps[:, 4 * q + f, :], ACT.Copy).then_inc(*act_evac.up())

                    @block.vector
                    def _(dve):
                        V = nc.vector
                        for j, bias in enumerate(("filt_b1_2", "filt_b2_2")):
                            dve.wait_ge(mm_done.sem, m0 + j + 1)
                            vlink(V.tensor_scalar(x[:], ps[0:H, j, :], vcol(bias, 0)[0:H], vcol("filt_freq_2", j)[0:H], ALU.add, ALU.mult))
                            vlink(V.tensor_scalar(turns[:], x[:], 1.0 / (2.0 * math.pi), ROUND, ALU.mult, ALU.add))
                            vlink(V.tensor_scalar(turns[:], turns[:], -ROUND, None, ALU.add))
                            vlink(V.scalar_tensor_tensor(x[:], turns[:], -TURN_HI, x[:], ALU.mult, ALU.add))
                            vlink(V.scalar_tensor_tensor(x[:], turns[:], -TURN_LO, x[:], ALU.mult, ALU.add))
                            V.tensor_scalar(x[:], x[:], -PI_IN, PI_IN, ALU.max, ALU.min).then_inc(*dve_out.up())
                            dve.wait_ge(act_out.sem, a0 + j + 1)
                        V.memset(hid[H:H + 1, :], 1.0).then_inc(*dve_out.up())
                        for o in range(HYENA_ORDER):
                            for t in range(KT):
                                for q in range(2):
                                    dve.wait_ge(mm_done.sem, m0 + 2 + 16 * o + 2 * t + q + 1)
                                    ins = V.tensor_tensor(both[:, t, q, :], ps[:, 2 * t + q, :], win[:, t, :], ALU.mult)
                            vlink(ins)
                            vlink(V.memset(both[0:1, 0, 1, :], 0.0))
                            if o > 0:
                                dve.wait_ge(mm_done.sem, m0 + 2 + 16 * o)
                            V.tensor_tensor(fsum[:], both[:, :, 0, :], both[:, :, 1, :], ALU.add)
                            vlink_n = V.tensor_tensor(fdiff[:], both[:, :, 0, :], both[:, :, 1, :], ALU.subtract)
                            vlink_n.then_inc(*dve_out.up())
                            dve.wait_ge(dve_out.sem, v0 + 4 + o)

        def hyena_conv(o, z, gates, spec, inv, Kc, Ks):
            with ExitStack() as st:
                z_tok = sbuf(st, "hz_tok", [P, KT, HYENA_WIDTH])
                Uc = sbuf(st, "hUc", [P, KT, HYENA_WIDTH])
                Us = sbuf(st, "hUs", [P, KT, HYENA_WIDTH])
                Y = sbuf(st, "hY", [P, 2 * KT, HYENA_WIDTH])
                t1 = sbuf(st, "ht1", [P, 2, HYENA_WIDTH])
                to_tokens([(z, z_tok)])
                m0, a0, v0, e0 = mm_done.n, act_evac.n, dve_out.n, dve_evac.n
                with nc.Block() as block:
                    @block.tensor
                    def _(pe):
                        for f in range(KT):
                            for q in range(2):
                                for t in range(KT):
                                    last = nc.tensor.matmul(ps[:, 2 * f + q, :], spec[:, t, q * T + f * P:q * T + (f + 1) * P], z_tok[:, t, :],
                                                            start=(t == 0), stop=(t == KT - 1))
                                last.then_inc(*mm_done.up())
                        pe.wait_ge(act_evac.sem, a0 + 2 * KT)
                        pe.wait_ge(dve_out.sem, v0 + KT)
                        for c in range(CT):
                            for f in range(2 * KT):
                                last = nc.tensor.matmul(ps[:, c, :], Y[:, f, c * P:(c + 1) * P], inv[:, f, :], start=(f == 0), stop=(f == 2 * KT - 1))
                            last.then_inc(*mm_done.up())

                    @block.scalar
                    def _(act):
                        for f in range(KT):
                            for q, dst in enumerate((Uc, Us)):
                                act.wait_ge(mm_done.sem, m0 + 2 * f + q + 1)
                                nc.scalar.activation(dst[:, f, :], ps[:, 2 * f + q, :], ACT.Copy).then_inc(*act_evac.up())

                    @block.vector
                    def _(dve):
                        V = nc.vector
                        for f in range(KT):
                            dve.wait_ge(act_evac.sem, a0 + 2 * f + 2)
                            if f > 0:
                                dve.wait_ge(dve_out.sem, v0 + f)
                            V.tensor_tensor(Y[:, f, :], Uc[:, f, :], Kc[:, f, o, :], ALU.mult)
                            V.tensor_tensor(t1[:, 0, :], Us[:, f, :], Ks[:, f, o, :], ALU.mult)
                            V.tensor_tensor(Y[:, KT + f, :], Uc[:, f, :], Ks[:, f, o, :], ALU.mult)
                            vlink(V.tensor_tensor(t1[:, 1, :], Us[:, f, :], Kc[:, f, o, :], ALU.mult))
                            V.tensor_tensor(Y[:, f, :], Y[:, f, :], t1[:, 0, :], ALU.subtract)
                            V.tensor_tensor(Y[:, KT + f, :], Y[:, KT + f, :], t1[:, 1, :], ALU.add).then_inc(*dve_out.up())
                        for c in range(CT):
                            dve.wait_ge(mm_done.sem, m0 + 2 * KT + c + 1)
                            vlink(V.scalar_tensor_tensor(z[:, c, :], z[:, c, :], vcol("filt_bias_2", 4 * o + c), ps[:, c, :], ALU.mult, ALU.add))
                            V.tensor_tensor(z[:, c, :], z[:, c, :], gates[:, 4 * o + c, :], ALU.mult)

        def route_choice(l, hT, rankm, wts, load_ahead):
            E = N_EXP2
            with ExitStack() as st:
                wr = sbuf(st, "c_wr", [P, KD, E])
                lg = sbuf(st, "c_lg", [P, KT, E])
                col = sbuf(st, "c_col", [P, KT])
                work = [sbuf(st, f"c_work{j}", [E, T]) for j in range(2)]
                top = sbuf(st, "c_top", [E, 8])
                sel = sbuf(st, "c_sel", [E, T])
                rk = sbuf(st, "c_rk", [E, T])
                m0, a0, v0, l0 = mm_done.n, act_out.n, dve_out.n, inputs_in.n
                with nc.Block() as block:
                    @block.sync
                    def _(sp):
                        sp.dma_start(wr[:], A["router_2"][l].rearrange("(k p) e -> p k e", p=P)).then_inc(*inputs_in.up(16))
                        load_ahead(sp)

                    @block.tensor
                    def _(pe):
                        pe.wait_ge(inputs_in.sem, l0 + 16)
                        for t in range(KT):
                            for k in range(KD):
                                last = nc.tensor.matmul(ps[:, 0, t * E:(t + 1) * E], hT[:, k, t * P:(t + 1) * P], wr[:, k, :], start=(k == 0), stop=(k == KD - 1))
                        last.then_inc(*mm_done.up())
                        pe.wait_ge(dve_out.sem, v0 + 2)
                        for t in range(KT):
                            last = nc.tensor.transpose(ps[0:E, 1, t * P:(t + 1) * P], wts[:, t, :], ident)
                        last.then_inc(*mm_done.up())
                        pe.wait_ge(dve_out.sem, v0 + 3)
                        for t in range(KT):
                            last = nc.tensor.transpose(ps[:, 2, t * E:(t + 1) * E], rk[:, t * P:(t + 1) * P], ident[0:E, 0:E])
                        last.then_inc(*mm_done.up())

                    @block.scalar
                    def _(act):
                        act.wait_ge(dve_out.sem, v0 + 1)
                        nc.scalar.activation(lg[:], lg[:], ACT.Exp).then_inc(*act_out.up())

                    @block.vector
                    def _(dve):
                        V = nc.vector
                        dve.wait_ge(mm_done.sem, m0 + 1)
                        logits = ps[:, 0, 0:KT * E].rearrange("p (t e) -> p t e", t=KT)
                        vlink(V.tensor_reduce(col[:], logits, AX.X, ALU.max))
                        V.tensor_tensor(lg[:], logits, col[:].unsqueeze(2).to_broadcast([P, KT, E]), ALU.subtract).then_inc(*dve_out.up())
                        dve.wait_ge(act_out.sem, a0 + 1)
                        vlink(V.tensor_reduce(col[:], lg[:], AX.X, ALU.add))
                        vlink(V.reciprocal(col[:], col[:]))
                        V.tensor_tensor(wts[:], lg[:], col[:].unsqueeze(2).to_broadcast([P, KT, E]), ALU.mult).then_inc(*dve_out.up())
                        dve.wait_ge(mm_done.sem, m0 + 2)
                        vlink(V.tensor_copy(work[0][:], ps[0:E, 1, :]))
                        for j in range(CAP2 // 8):
                            vlink(V.max(top[:], work[j % 2][:]))
                            vlink(V.match_replace(work[(j + 1) % 2][:], top[:], work[j % 2][:], -1.0))
                        vlink(V.tensor_scalar(sel[:], work[CAP2 // 8 % 2][:], 0.0, None, ALU.is_lt))
                        vlink(V.tensor_tensor_scan(rk[:], sel[:], sel[:], 0.0, ALU.add, ALU.max))
                        vlink(V.tensor_tensor(rk[:], rk[:], sel[:], ALU.mult))
                        V.tensor_scalar(rk[:], rk[:], -1.0, None, ALU.add).then_inc(*dve_out.up())
                        dve.wait_ge(mm_done.sem, m0 + 3)
                        V.tensor_copy(rankm[:], ps[:, 2, 0:KT * E].rearrange("p (t e) -> p t e", t=KT))

        def conformer_in(hT, u):
            w = A["cf_w1_2"].rearrange("(k p) n -> p k n", p=P)
            n_g = D // 256
            with ExitStack() as st:
                wb = sbuf(st, "wc", [P, 2, KD, 2, 256])
                sig = sbuf(st, "cf_sig", [P, 2, T])
                m0, a0, v0 = mm_done.n, act_out.n, dve_out.n
                w0 = [w_in[0].n, w_in[1].n]
                with nc.Block() as block:
                    @block.sync
                    def _(sp):
                        for g in range(n_g):
                            if g >= 2:
                                sp.wait_ge(mm_done.sem, m0 + 4 * (g - 1))
                            for half in range(2):
                                sp.dma_start(wb[:, g % 2, :, half, :], w[:, :, half * D + g * 256:half * D + (g + 1) * 256]).then_inc(*w_in[g % 2].up(16))

                    @block.tensor
                    def _(pe):
                        for m in range(KD):
                            g = m // 2
                            if m % 2 == 0:
                                pe.wait_ge(w_in[g % 2].sem, w0[g % 2] + 32 * (g // 2 + 1))
                            if m >= 4:
                                pe.wait_ge(dve_out.sem, v0 + m - 3)
                            for half in range(2):
                                for k in range(KD):
                                    last = nc.tensor.matmul(ps[:, 2 * (m % 4) + half, :], wb[:, g % 2, k, half, (m % 2) * P:(m % 2 + 1) * P], hT[:, k, :],
                                                            start=(k == 0), stop=(k == KD - 1))
                                last.then_inc(*mm_done.up())

                    @block.scalar
                    def _(act):
                        for m in range(KD):
                            act.wait_ge(mm_done.sem, m0 + 2 * m + 2)
                            if m >= 2:
                                act.wait_ge(dve_out.sem, v0 + m - 1)
                            nc.scalar.activation(sig[:, m % 2, :], ps[:, 2 * (m % 4) + 1, :], ACT.Sigmoid, bias=vcol("cf_b1_2", KD + m)).then_inc(*act_out.up())

                    @block.vector
                    def _(dve):
                        for m in range(KD):
                            dve.wait_ge(act_out.sem, a0 + m + 1)
                            nc.vector.scalar_tensor_tensor(u[:, m, :], ps[:, 2 * (m % 4), :], vcol("cf_b1_2", m), sig[:, m % 2, :], ALU.add, ALU.mult).then_inc(*dve_out.up())

        def conformer_conv(u, acc):
            rows = T // GRID_W
            mid = (CONF_TAPS - 1) // 2
            with ExitStack() as st:
                stat = sbuf(st, "cf_stat", [P, 2, T])
                m0, a0, v0 = mm_done.n, act_out.n, dve_out.n
                with nc.Block() as block:
                    @block.vector
                    def _(dve):
                        V = nc.vector
                        for c in range(KD):
                            def tap(k):
                                return vcol("cf_dw_w_2", k * KD + c)
                            vlink(V.tensor_scalar(acc[:, c, :], u[:, c, :], tap(mid), vcol("cf_dw_b_2", c), ALU.mult, ALU.add))
                            for d in range(1, rows):
                                n = (rows - d) * GRID_W
                                vlink(V.scalar_tensor_tensor(acc[:, c, 0:n], u[:, c, T - n:T], tap(mid + d), acc[:, c, 0:n], ALU.mult, ALU.add))
                                ins = V.scalar_tensor_tensor(acc[:, c, T - n:T], u[:, c, 0:n], tap(mid - d), acc[:, c, T - n:T], ALU.mult, ALU.add)
                                if d < rows - 1:
                                    vlink(ins)
                            ins.then_inc(*dve_out.up())
                        dve.wait_ge(mm_done.sem, m0 + 1)
                        vlink(V.tensor_scalar(stat[:, 0, :], ps[:, 0, :], 1.0 / D, None, ALU.mult))
                        for c in range(KD):
                            V.tensor_tensor(acc[:, c, :], acc[:, c, :], stat[:, 0, :], ALU.subtract).then_inc(*dve_out.up())
                        dve.wait_ge(mm_done.sem, m0 + 2)
                        V.tensor_scalar(stat[:, 1, :], ps[:, 1, :], 1.0 / D, RMS_EPS, ALU.mult, ALU.add).then_inc(*dve_out.up())
                        dve.wait_ge(act_out.sem, a0 + KD + 1)
                        vlink(V.reciprocal(stat[:, 0, :], stat[:, 0, :]))
                        for c in range(KD):
                            V.scalar_tensor_tensor(acc[:, c, :], acc[:, c, :], vcol("cf_ln_g_2", c), stat[:, 0, :], ALU.mult, ALU.mult).then_inc(*dve_out.up())

                    @block.tensor
                    def _(pe):
                        for c in range(KD):
                            pe.wait_ge(dve_out.sem, v0 + c + 1)
                            last = nc.tensor.matmul(ps[:, 0, :], ones, acc[:, c, :], start=(c == 0), stop=(c == KD - 1))
                        last.then_inc(*mm_done.up())
                        for c in range(KD):
                            pe.wait_ge(act_out.sem, a0 + c + 1)
                            last = nc.tensor.matmul(ps[:, 1, :], ones, u[:, c, :], start=(c == 0), stop=(c == KD - 1))
                        last.then_inc(*mm_done.up())

                    @block.scalar
                    def _(act):
                        for c in range(KD):
                            act.wait_ge(dve_out.sem, v0 + KD + c + 1)
                            nc.scalar.activation(u[:, c, :], acc[:, c, :], ACT.Square).then_inc(*act_out.up())
                        act.wait_ge(dve_out.sem, v0 + 2 * KD + 1)
                        nc.scalar.activation(stat[:, 0, :], stat[:, 1, :], ACT.Sqrt).then_inc(*act_out.up())
                        for c in range(KD):
                            act.wait_ge(dve_out.sem, v0 + 2 * KD + 2 + c)
                            nc.scalar.activation(acc[:, c, :], acc[:, c, :], ACT.Silu, bias=vcol("cf_ln_b_2", c))

        def store_result(src):
            with ExitStack() as st:
                rows = sbuf(st, "out_rows", [P, KT, D])
                m0, a0, v0, s0 = mm_done.n, act_out.n, dve_out.n, stored.n
                with nc.Block() as block:
                    @block.sync
                    def _(sp):
                        for t in range(KT):
                            sp.wait_ge(dve_out.sem, v0 + t + 1)
                            sp.wait_ge(act_out.sem, a0 + t + 1)
                            sp.dma_start(out[t * P:(t + 1) * P, :], rows[:, t, :]).then_inc(*stored.up(16))
                        sp.wait_ge(stored.sem, s0 + 16 * KT)

                    @block.tensor
                    def _(pe):
                        for t in range(KT):
                            for half in range(2):
                                for c in range(4):
                                    last = nc.tensor.transpose(ps[:, 2 * t + half, c * P:(c + 1) * P], src[:, half * 4 + c, t * P:(t + 1) * P], ident)
                                last.then_inc(*mm_done.up())

                    @block.scalar
                    def _(act):
                        for t in range(KT):
                            act.wait_ge(mm_done.sem, m0 + 2 * t + 2)
                            nc.scalar.activation(rows[:, t, 512:1024], ps[:, 2 * t + 1, :], ACT.Copy).then_inc(*act_out.up())

                    @block.vector
                    def _(dve):
                        for t in range(KT):
                            dve.wait_ge(mm_done.sem, m0 + 2 * t + 1)
                            nc.vector.tensor_copy(rows[:, t, 0:512], ps[:, 2 * t, :]).then_inc(*dve_out.up())
        load_and_transpose(A["x"], xT, T, True)
        with ExitStack() as blk1:
            mix = sbuf(blk1, "mix", [P, 2 * CT, T])
            with ExitStack() as mixers:
                mk = sbuf(mixers, "masks", [P, (4 + 2 * LEVELS) * P])
                masks = {"strict": mk[:, 0:2 * P], "incl": mk[:, 2 * P:4 * P], "levels": mk[:, 4 * P:]}
                proj = sbuf(mixers, "proj", [P, 15, T])
                l0 = inputs_in.n
                with nc.Block() as block:
                    @block.sync
                    def _(sp):
                        sp.dma_start(mk[:], A["consts"][:, const_at["base_end"] + 1:]).then_inc(*inputs_in.up(16))
                        sp.wait_ge(inputs_in.sem, l0 + 16)
                with ExitStack() as gla:
                    gla_q = sbuf(gla, "gla_q", [P, 2, T])
                    gla_k = sbuf(gla, "gla_k", [P, 2, T])
                    gla_v = sbuf(gla, "gla_v", [P, KT, 512])
                    gla_gl = sbuf(gla, "gla_gl", [32, T])
                    gla_og = sbuf(gla, "gla_og", [P, CT, T])
                    with ExitStack() as first:
                        hT = sbuf(first, "hT", [P, KD, T])
                        rms_norm(xT, hT, T, lambda k: vcol("ln1_w", k))
                        project_first(hT, proj, gla_q, gla_k, gla_v, gla_gl, gla_og)
                    gla_mixer(gla_q, gla_k, gla_v, gla_gl, gla_og, mix[:, CT:2 * CT, :], masks)
                with ExitStack() as rwkv:
                    w2 = sbuf(rwkv, "w2s", [P, RW])
                    a2 = sbuf(rwkv, "a2s", [P, RW])
                    g2 = sbuf(rwkv, "g2s", [P, RW])
                    kk = sbuf(rwkv, "rw_kk", [P, CT, T])
                    kd_sum = sbuf(rwkv, "rw_kd_sum", [P, CT, T])
                    v_tok = sbuf(rwkv, "rw_v_tok", [P, KT, RW])
                    rwkv_keys(proj, kk, w2, a2, g2, None)
                    to_tokens([(proj[:, 8:12, :], v_tok)])
                    with ExitStack() as scan:
                        bufs = {n: sbuf(scan, "rw_" + n, [P, CT, T]) for n in ("lw", "cc", "ex", "a", "kd", "q", "r")}
                        for n in ("half", "scale"):
                            bufs[n] = sbuf(scan, "rw_" + n, [P, CT * KT])
                        for n in ("N", "X", "Z", "U", "BT", "RB", "RK"):
                            bufs[n] = sbuf(scan, "rw_" + n, [P, 2, CT, P])
                        bufs["rhs"] = sbuf(scan, "rw_rhs", [P, 2, CT, 64])
                        bufs["sa"] = sbuf(scan, "rw_sa", [P, RW])
                        bufs["S"] = sbuf(scan, "rw_S", [P, CT, 64])
                        bufs["hop"] = sbuf(scan, "rw_hop", [P, KT, CT])
                        bufs["b_tok"], bufs["k_tok"] = bufs["lw"], bufs["cc"]
                        for back in (False, True):
                            rwkv_direction(back, proj, kk, w2, a2, kd_sum, bufs)
                            to_tokens([(bufs["a"], bufs["b_tok"]), (bufs["kd"], bufs["k_tok"])])
                            rwkv_scan(back, bufs, v_tok, mix[:, 0:CT, :], masks)
                    rwkv_output(proj, mix[:, 0:CT, :], kd_sum, g2)
            with ExitStack() as wo:
                project_residual(A["w_out"], mix, xT)
        with ExitStack() as moe:
            h_hi = sbuf(moe, "h_hi1", [P, KT, D], F32R)
            h_lo = sbuf(moe, "h_lo1", [P, KT, D], F32R)
            rank_pad = sbuf(moe, "rankm1", [P, KT, N_EXP1 + 2 * PAIRS])
            wts_pad = sbuf(moe, "wts1", [P, KT, N_EXP1 + 2 * PAIRS])
            rankm, wts = rank_pad[:, :, 0:N_EXP1], wts_pad[:, :, 0:N_EXP1]
            over_one = sbuf(moe, "over_one", [P, N_OVER, N_EXP1])
            over_first = sbuf(moe, "over_first", [P, N_OVER])
            over_int = sbuf(moe, "over_int", [P, N_OVER + 1], I32)
            with ExitStack() as experts_part:
                load_ahead, run = experts_pass(experts_part, "m1", h_hi, h_lo, rank_pad, wts_pad, N_EXP1, A["moe_w_gate"], A["moe_w_up"], A["moe_w_down"], 512, None)
                with ExitStack() as route:
                    hT2 = sbuf(route, "hT2", [P, KD, T])
                    rms_norm(xT, hT2, T, lambda k: vcol("ln2_w", k))
                    rows_of(hT2, h_hi, h_lo)
                    route_first(hT2, rankm, wts, over_one, over_first, over_int, load_ahead)
                run()
            overflow_pass(h_hi, h_lo, rankm, wts, over_one, over_first, over_int)
        with ExitStack() as nrm:
            sq = sbuf(nrm, "sq_f1", [P, KD, T])
            rms_norm(xT, xT, T, lambda k: vcol("ln_f_w", k), sq=sq)
        with ExitStack() as blk2:
            mods = [sbuf(blk2, f"mod_l{l}", [P, 48]) for l in range(2)]
            mod_c = sbuf(blk2, "mod_ctx", [P, 24])
            scaled = [sbuf(blk2, f"scaled_l{l}", [P, 2, KD]) for l in range(2)]
            for l in range(2):
                modulation(l, mods[l], mod_c, scaled[l])

            def part(l, j):
                return lambda k: mods[l][:, 8 * j + k:8 * j + k + 1]

            def weight(l, j):
                return lambda k: scaled[l][:, j, k:k + 1]

            with ExitStack() as even:
                cat = sbuf(even, "cat", [P, 2 * CT, T])
                hy = sbuf(even, "hy", [P, 3 * CT, T])
                spec = sbuf(even, "spec", [P, KT, 2 * T])
                with ExitStack() as lru:
                    gates = sbuf(lru, "lru_w", [P, 2, 2, CT, P])
                    rate = sbuf(lru, "lru_rate", [P, 2, 8])
                    state = sbuf(lru, "lru_state", [P, 2 * CT])
                    xa = sbuf(lru, "xa", [P, CT, T])
                    l0 = inputs_in.n
                    with nc.Block() as block:
                        @block.sync
                        def _(sp):
                            sp.dma_start(gates[:], A["lru_gates"]).then_inc(*inputs_in.up(16))
                            sp.wait_ge(inputs_in.sem, l0 + 16)
                    lru_rates(rate)
                    with ExitStack() as ctx_part:
                        cT = sbuf(ctx_part, "cT", [P, KD, CTX])
                        hc = sbuf(ctx_part, "hc", [P, KD, CTX])
                        xc = sbuf(ctx_part, "xc", [P, CT, CTX])
                        load_and_transpose(A["ctx_2"], cT, CTX, False)
                        rms_norm(cT, hc, CTX, lambda k: mod_c[:, 16 + k:17 + k], lambda k: mod_c[:, k:k + 1])
                        project_even(hc, CTX, [4, 5, 6, 7], None, xc, None)
                        lru_scan(xc, CTX, gates, rate, None, state, None)
                    with ExitStack() as first:
                        hT = sbuf(first, "hT_l0", [P, KD, T])
                        rms_norm(xT, hT, T, weight(0, 0), part(0, 0))
                        project_even(hT, T, list(range(20)), cat[:, 0:CT, :], xa, hy)
                    lru_scan(xa, T, gates, rate, state, None, cat[:, 0:CT, :])
                with ExitStack() as hyena:
                    Kc = sbuf(hyena, "Kc", [P, KT, HYENA_ORDER, HYENA_WIDTH])
                    Ks = sbuf(hyena, "Ks", [P, KT, HYENA_ORDER, HYENA_WIDTH])
                    hyena_filters(spec, Kc, Ks)
                    inv = sbuf(hyena, "inv", [P, 2 * KT, T])
                    l0 = inputs_in.n
                    with nc.Block() as block:
                        @block.sync
                        def _(sp):
                            sp.dma_start(inv[:], A["hy_inverse"].rearrange("(f p) t -> p f t", p=P)).then_inc(*inputs_in.up(16))
                            sp.wait_ge(inputs_in.sem, l0 + 16)

                        @block.gpsimd
                        def _(pool):
                            nc.gpsimd.tensor_copy(cat[:, CT:2 * CT, :], hy[:, 0:CT, :])
                    for o in range(HYENA_ORDER):
                        hyena_conv(o, cat[:, CT:2 * CT, :], hy[:, CT:3 * CT, :], spec, inv, Kc, Ks)
                project_residual(A["w_out_2"], cat, xT, gate=part(0, 2))

            for l in range(2):
                if l == 1:
                    with ExitStack() as conf:
                        hT = sbuf(conf, "hT_l1", [P, KD, T])
                        u = sbuf(conf, "cf_u", [P, KD, T])
                        rms_norm(xT, hT, T, weight(1, 0), part(1, 0))
                        conformer_in(hT, u)
                        conformer_conv(u, hT)
                        project_residual(A["cf_w2_2"], hT, xT, gate=part(1, 2), bias=lambda k: vcol("cf_b2_2", k))
                with ExitStack() as moe:
                    h_hi = sbuf(moe, "h_hi_c", [P, KT, D], F32R)
                    h_lo = sbuf(moe, "h_lo_c", [P, KT, D], F32R)
                    rank_pad = sbuf(moe, "rankm_c", [P, KT, N_EXP2 + 2 * PAIRS])
                    wts_pad = sbuf(moe, "wts_c", [P, KT, N_EXP2 + 2 * PAIRS])
                    load_ahead, run = experts_pass(moe, f"c{l}", h_hi, h_lo, rank_pad, wts_pad, N_EXP2, A["exp_w1_2"][l], A["exp_w3_2"][l], A["exp_w2_2"][l], FF2, part(l, 5))
                    with ExitStack() as route:
                        hT = sbuf(route, "hT_c", [P, KD, T])
                        rms_norm(xT, hT, T, weight(l, 1), part(l, 3))
                        rows_of(hT, h_hi, h_lo)
                        route_choice(l, hT, rank_pad[:, :, 0:N_EXP2], wts_pad[:, :, 0:N_EXP2], load_ahead)
                    run()
            with ExitStack() as last:
                fin = sbuf(last, "fin", [P, KD, T])
                rms_norm(xT, fin, T, lambda k: vcol("final_g_2", k))
                store_result(fin)


def layout(inputs):
    a = {k: np.ascontiguousarray(np.asarray(v)) for k, v in inputs.items()}
    vectors, consts = pack_vectors(a), shape_constants()
    gw2 = np.zeros((32, 2, 256), np.float32)
    gw2[0:16, 0], gw2[16:32, 1] = a["gla_gw2_f"][0], a["gla_gw2_b"][0]
    ins = {"vectors": vectors.array(), "consts": consts.array(), "gla_gw2": gw2, "x": a["x"][0], "w_in": a["w_in"][0]}
    for name in ("rw_w2_f", "rw_w2_b", "rw_a2_f", "rw_a2_b", "rw_g2", "w_out"):
        ins[name] = a[name][0]
    more_layout(a, ins)
    return ins, vectors.start, consts.start


def more_layout(a, ins):
    for name in ("moe_w_gate", "moe_w_up", "moe_w_down"):
        ins[name] = a[name][0]
    ins["moe_w_route"] = np.concatenate([a["moe_w_coarse"][0], a["moe_w_fine"][0]], axis=1)
    ins["moe_b_route"] = np.concatenate([a["moe_b_coarse"][0], a["moe_b_fine"][0]])[None]
    for name in ("ctx_2", "w_in_2", "w_out_2", "filt_w1_2", "filt_w2_2", "cf_w1_2", "cf_w2_2"):
        ins[name] = a[name][0]
    for name in ("w_mod_2", "router_2", "exp_w1_2", "exp_w3_2", "exp_w2_2"):
        ins[name] = a[name]
    ins["filt_w3_2"] = np.concatenate([a["filt_w3_2"][0], a["filt_b3_2"]], axis=0)
    gates = np.zeros((P, 2, 2, CT, P), np.float32)
    for j, name in enumerate(("lru_wr_2", "lru_wi_2")):
        for h in range(8):
            at = slice(64 * (h % 2), 64 * (h % 2) + 64)
            gates[at, j, :, h // 2, at] = a[name][0, :, h].transpose(1, 0, 2)
    ins["lru_gates"] = gates
    ins.update(hyena_tables())


def kernel(**inputs):
    import concourse.bacc as bacc
    from concourse.bass_utils import run_bass_kernel_spmd

    ins, vec_at, const_at = layout(inputs)
    nc = bacc.Bacc("TRN2", target_bir_lowering=False, num_devices=1)
    A = {name: nc.dram_tensor(f"in_{name}", v.shape, mybir.dt.from_np(v.dtype), kind="ExternalInput").ap() for name, v in ins.items()}
    out = nc.dram_tensor("out_0", (T, D), F32, kind="ExternalOutput").ap()
    build(nc, A, out, vec_at, const_at)
    result = run_bass_kernel_spmd(nc, [{f"in_{name}": v for name, v in ins.items()}], core_ids=[0])
    return result.results[0]["out_0"].reshape(1, T, D)
```

```python
import math
from contextlib import ExitStack

import numpy as np
import concourse.bass as bass
from concourse import mybir

ALU = mybir.AluOpType
ACT = mybir.ActivationFunctionType
F32 = mybir.dt.float32
F32R = mybir.dt.float32r
I32 = mybir.dt.int32
U32 = mybir.dt.uint32
AX = mybir.AxisListType

P = 128
D = 1024
KD = D // P
T = 512
KT = T // P
RMS_EPS = 1e-6
RW = 512
CT = RW // P
RW_HD = 64
RW_GN_EPS = 64e-5
RW_COLS = 1920
GLA_DK = 64
GLA_TAU = 16.0
GLA_SUB = 32
GLA_CLAMP = 80.0
LEVELS = 7
N_GROUPS, PER_GROUP = 4, 8
N_EXP1 = N_GROUPS * PER_GROUP
SLOTS = 64
PAIRS = 2
MORE1 = -(-T // SLOTS) - 1
N_OVER = max(k for k in range(2 * T) if k * (SLOTS + 1) <= 2 * T)
FILTER_EMB, FILTER_HIDDEN, HYENA_WIDTH, HYENA_ORDER = 33, 64, 512, 2
HYENA_DECAY_TARGET, HYENA_FAST_PCT, HYENA_SLOW_PCT, HYENA_SHIFT = 1e-2, 0.3, 1.5, 0.05
ROUND = 1.5 * 2.0 ** 23
TURN_HI = 6.28125
TURN_LO = 2.0 * math.pi - 6.28125
PI_IN = 3.1415925
LRU_C = 8.0
CTX = 256
GRID_W = 64
CONF_TAPS = 31
N_EXP2, FF2, CAP2 = 16, 1024, 64
MOD_BUFS, MOD_K = 3, 2
MOD_BANK = 7
UNIT_COLS = 256
RING = 6


class Signal:

    def __init__(self, sem):
        self.sem, self.n = sem, 0

    def up(self, by=1):
        self.n += by
        return self.sem, by


class Columns:

    def __init__(self):
        self.start, self.parts, self.n = {}, [], 0

    def add(self, name, a):
        a = np.asarray(a, np.float32)
        if a.shape[0] < P:
            a = np.concatenate([a, np.zeros((P - a.shape[0], a.shape[1]), np.float32)])
        self.start[name] = self.n
        self.parts.append(a)
        self.n += a.shape[1]

    def array(self):
        return np.ascontiguousarray(np.concatenate(self.parts, axis=1))


def pack_vectors(a):
    cols = Columns()

    def put(name, v, rows=P):
        v = np.asarray(v).reshape(-1, rows).T
        cols.add(name, v)

    for name in ("ln1_w", "rw_mu", "rw_w0_f", "rw_w0_b", "rw_a0_f", "rw_a0_b", "rw_k_k", "rw_k_a", "rw_r_k",
                 "rw_ln_w", "rw_ln_b", "gla_gb_f", "gla_gb_b", "gla_norm_w", "ln2_w", "ln_f_w",
                 "norm1_g_2", "norm2_g_2", "final_g_2", "conv_a_w_2", "conv_a_b_2", "lru_br_2", "lru_bi_2",
                 "lru_lam_2", "conv_b_w_2", "conv_b_b_2", "filt_bias_2", "cf_b1_2", "cf_dw_w_2", "cf_dw_b_2",
                 "cf_ln_g_2", "cf_ln_b_2", "cf_b2_2", "b_mod_2", "c_2", "c_ctx_2"):
        put(name, a[name])
    for name in ("filt_b1_2", "filt_b2_2", "filt_freq_2"):
        put(name, a[name], 64)
    put("moe_b_coarse", a["moe_b_coarse"], 4)
    put("moe_b_fine", a["moe_b_fine"], 32)
    return cols


def shape_constants():
    cols = Columns()
    i = np.arange(P)
    row, col = i[:, None], i[None, :]
    cols.add("ident", row == col)
    cols.add("ones", np.ones((P, P)))
    cols.add("head_ones", row // RW_HD == col // RW_HD)
    cols.add("before", row < col)
    cols.add("slots", np.tile(np.arange(SLOTS), (P, 1)))
    cols.add("experts", np.tile(np.arange(N_EXP1), (P, 1)))
    cols.add("overflows", np.tile(np.arange(N_OVER), (P, 1)))
    cols.add("first4", np.tile(np.arange(4, 0, -1), (P, 1)))
    cols.add("first8", np.tile(np.arange(8, 0, -1), (P, 1)))
    cols.add("spread", ((row % 32 < 16) == (col < RW_HD)) / 16.0)
    cols.add("base_end", np.zeros((P, 1)))
    cols.add("strict", np.concatenate([row < col, row > col], axis=1))
    cols.add("incl", np.concatenate([row <= col, row >= col], axis=1))
    levels = []
    for back in (False, True):
        for s in (2 ** l for l in range(LEVELS)):
            lower = (row // (2 * s) == col // (2 * s)) & (row // s > col // s)
            levels.append(lower.T if back else lower)
    cols.add("levels", np.concatenate(levels, axis=1))
    return cols


def hyena_tables():
    t = np.linspace(0.0, 1.0, T, dtype=np.float32)[:, None]
    bands = (FILTER_EMB - 1) // 2
    w = np.float32(2.0 * math.pi / T) * np.arange(T, dtype=np.float32)[:, None]
    f = np.linspace(1e-4, bands - 1, bands, dtype=np.float32)[None, :]
    z = np.concatenate([t, np.cos(f * w), -np.sin(f * w)], axis=-1).astype(np.float32)
    deltas = np.abs(np.linspace(math.log(HYENA_DECAY_TARGET) / HYENA_SLOW_PCT, math.log(HYENA_DECAY_TARGET) / HYENA_FAST_PCT,
                                HYENA_WIDTH, dtype=np.float32))
    window = (np.exp(-t * deltas[None, :]) + np.float32(HYENA_SHIFT)).astype(np.float32)
    token = np.concatenate([np.arange(0, T, 2), np.arange(1, T, 2)])
    angle = 2.0 * math.pi * ((2 * np.arange(T // 2)[None, :] + 1) * token[:, None] % (4 * T)) / (4 * T)
    spectrum = np.concatenate([np.cos(angle), np.sin(angle)], axis=1).astype(np.float32)
    inverse = (np.concatenate([np.cos(angle).T, np.sin(angle).T], axis=0) / T).astype(np.float32)
    return {"hy_z": np.ascontiguousarray(z.T[:, token]), "hy_window": np.ascontiguousarray(window[token]), "hy_spectrum": spectrum, "hy_inverse": inverse}


def build(nc, A, out, vec_at, const_at):
    ctx = ExitStack()
    with ctx:
        def signal(name):
            return Signal(ctx.enter_context(nc.semaphore(name)))

        names = {}

        def sbuf(stack, name, shape, dt=F32):
            names[name] = names.get(name, 0) + 1
            if names[name] > 1:
                name = f"{name}_{names[name]}"
            return stack.enter_context(nc.sbuf_tensor("s_" + name, shape, dt))

        ps = ctx.enter_context(nc.psum_tensor("ps", [P, 8, 512], F32))
        xT = sbuf(ctx, "xT", [P, KD, T])
        n_vec = A["vectors"].shape[1]
        vec = sbuf(ctx, "vec", [P, n_vec])
        base = sbuf(ctx, "base", [P, const_at["base_end"]])

        def table(name, n):
            return base[:, const_at[name]:const_at[name] + n]

        ident, ones, head_ones, before, spread = (table(n, P) for n in ("ident", "ones", "head_ones", "before", "spread"))
        slots, experts, overflows = table("slots", SLOTS), table("experts", N_EXP1), table("overflows", N_OVER)
        first4, first8 = table("first4", 4), table("first8", 8)

        def vcol(name, k, n=1):
            at = vec_at[name] + k
            return vec[:, at:at + n]

        inputs_in = signal("inputs_in")
        w_in = [signal("w_in0"), signal("w_in1")]
        mm_done = signal("mm_done")
        act_evac = signal("act_evac")
        dve_evac = signal("dve_evac")
        dve_step = signal("dve_step")
        act_step = signal("act_step")
        dve_out = signal("dve_out")
        act_out = signal("act_out")
        pool_out = signal("pool_out")
        raw_in = [signal("raw_in0"), signal("raw_in1")]
        hi_done = signal("hi_done")
        lo_done = signal("lo_done")
        stored = signal("stored")

        def vlink(ins):
            ins.then_inc(*dve_step.up())
            nc.vector.wait_ge(dve_step.sem, dve_step.n)

        def alink(ins):
            ins.then_inc(*act_step.up())
            nc.scalar.wait_ge(act_step.sem, act_step.n)

        def bcast(ap, n):
            return ap.unsqueeze(1).to_broadcast([ap.shape[0], n, ap.shape[1]])

        class SplitWeights:

            def __init__(self, st, units):
                self.units, self.unit_end, self.early = units, None, False
                self.raw = sbuf(st, "w_raw", [P, 2, KD, UNIT_COLS])
                self.hi = sbuf(st, "w_hi", [P, 2, KD, UNIT_COLS], F32R)
                self.lo = sbuf(st, "w_lo", [P, 2, KD, UNIT_COLS], F32R)
                self.cols = [max(c + ap.shape[2] for c, ap in u) for u in units]
                self.h0, self.l0 = hi_done.n, lo_done.n
                self.here = []
                for i, u in enumerate(units):
                    raw_in[i % 2].n += 16 * len(u)
                    self.here.append(raw_in[i % 2].n)
                hi_done.n += len(units)
                lo_done.n += len(units)

            def load_unit(self, eng, i):
                if i >= len(self.units):
                    return
                if i >= 2:
                    eng.wait_ge(lo_done.sem, self.l0 + i - 1)
                for c, ap in self.units[i]:
                    eng.dma_start(self.raw[:, i % 2, :, c:c + ap.shape[2]], ap).then_inc(raw_in[i % 2].sem, 16)

            def load(self, eng, first, end=None):
                for i in range(first, len(self.units) if end is None else end):
                    self.load_unit(eng, i)

            def next_unit(self):
                return 2 if self.early else 0

            def split_hi(self, act, i):
                if i >= len(self.units):
                    return
                at = slice(0, self.cols[i])
                act.wait_ge(raw_in[i % 2].sem, self.here[i])
                if i >= 2:
                    act.wait_ge(mm_done.sem, self.unit_end[i - 2])
                nc.scalar.activation(self.hi[:, i % 2, :, at], self.raw[:, i % 2, :, at], ACT.Copy).then_inc(hi_done.sem, 1)

            def split_lo(self, pool, first, end=None):
                for i in range(first, len(self.units) if end is None else end):
                    at = slice(0, self.cols[i])
                    pool.wait_ge(hi_done.sem, self.h0 + i + 1)
                    nc.gpsimd.tensor_tensor(self.lo[:, i % 2, :, at], self.raw[:, i % 2, :, at], self.hi[:, i % 2, :, at].bitcast(F32), ALU.subtract).then_inc(lo_done.sem, 1)

            def ready(self, pe, i):
                pe.wait_ge(lo_done.sem, self.l0 + i + 1)

            def product(self, bank, i, c0, x, at, swap=False):
                w = (self.hi, self.lo)
                passes = [(k, a, b) for k in range(KD) for a, b in ((0, 0), (0, 1), (1, 0))]
                for j, (k, a, b) in enumerate(passes):
                    start, stop = j == 0, j == len(passes) - 1
                    if swap:
                        last = nc.tensor.matmul(bank, x[a][:, k, at], w[b][:, i % 2, k, 0:self.cols[i]], start=start, stop=stop)
                    else:
                        last = nc.tensor.matmul(bank, w[a][:, i % 2, k, c0:c0 + P], x[b][:, k, at], start=start, stop=stop)
                return last

        class Modulation:

            def __init__(self, st, l, mod, mod_c, scaled, n_tiles, vector_tile, tensor_tile):
                self.l, self.mod, self.mod_c, self.scaled = l, mod, mod_c, scaled
                self.jobs = [(g, 0) for g in range(6 * D // 512)] + ([(g, 1) for g in range(2 * D // 512)] if l == 0 else [])
                self.w = A["w_mod_2"][l].rearrange("(k p) n -> p k n", p=P)
                self.buf = sbuf(st, "mod_w", [P, MOD_BUFS, MOD_K, 512])
                self.acc = sbuf(st, "mod_acc", [P, 2, 512])
                self.c = sbuf(st, "mod_silu", [P, 2, KD])
                self.here = [signal(f"mod{l}_here{j}") for j in range(MOD_BUFS)]
                self.step = signal(f"mod{l}_step")
                self.summed = signal(f"mod{l}_summed")
                self.silu = signal(f"mod{l}_silu")
                self.vector_at, self.tensor_at = {}, {}
                for q in range(len(self.jobs)):
                    self.vector_at.setdefault(vector_tile(q), []).append(q)
                    self.tensor_at.setdefault(min(tensor_tile(q), n_tiles - 1), []).append(q)

            def load(self, sp):
                for q, (g, _) in enumerate(self.jobs):
                    for h in range(KD // MOD_K):
                        u = q * (KD // MOD_K) + h
                        if u >= MOD_BUFS:
                            sp.wait_ge(self.step.sem, (u - MOD_BUFS + 1) * MOD_K)
                        sp.dma_start(self.buf[:, u % MOD_BUFS], self.w[:, h * MOD_K:(h + 1) * MOD_K, g * 512:(g + 1) * 512]).then_inc(self.here[u % MOD_BUFS].sem, 16)

            def silu_of_c(self):
                for j, name in enumerate(("c_2", "c_ctx_2")):
                    nc.scalar.activation(self.c[:, j, :], vcol(name, 0, KD), ACT.Silu).then_inc(self.silu.sem, 1)

            def vector(self, dve, i):
                for q in self.vector_at.get(i, []):
                    _, which = self.jobs[q]
                    acc = self.acc[:, q % 2, :]
                    if q == 0:
                        dve.wait_ge(self.silu.sem, 2)
                    if q >= 2:
                        dve.wait_ge(self.summed.sem, q - 1)
                    for k in range(KD):
                        u = q * (KD // MOD_K) + k // MOD_K
                        if k % MOD_K == 0:
                            dve.wait_ge(self.here[u % MOD_BUFS].sem, 16 * (u // MOD_BUFS + 1))
                        w, c = self.buf[:, u % MOD_BUFS, k % MOD_K, :], self.c[:, which, k:k + 1]
                        if k == 0:
                            ins = nc.vector.tensor_scalar(acc, w, c, None, ALU.mult)
                        else:
                            dve.wait_ge(self.step.sem, q * KD + k)
                            ins = nc.vector.scalar_tensor_tensor(acc, w, c, acc, ALU.mult, ALU.add)
                        ins.then_inc(self.step.sem, 1)

            def tensor(self, pe, i):
                for q in self.tensor_at.get(i, []):
                    pe.wait_ge(self.step.sem, (q + 1) * KD)
                    for j in range(4):
                        last = nc.tensor.matmul(ps[:, MOD_BANK, 4 * q + j:4 * q + j + 1], self.acc[:, q % 2, j * P:(j + 1) * P], ones[:, 0:1], start=True, stop=True)
                    last.then_inc(self.summed.sem, 1)

            def finish(self, dve):
                l, mod, mod_c = self.l, self.mod, self.mod_c
                dve.wait_ge(self.summed.sem, len(self.jobs))
                bias = vcol("b_mod_2", 48 * l, 48)
                vlink(nc.vector.tensor_tensor(mod[:], ps[:, MOD_BANK, 0:48], bias, ALU.add))
                for j, (norm, part) in enumerate((("norm1_g_2", 1), ("norm2_g_2", 4))):
                    nc.vector.scalar_tensor_tensor(self.scaled[:, j, :], mod[:, 8 * part:8 * part + 8], 1.0, vcol(norm, 8 * l, 8), ALU.add, ALU.mult)
                if l == 0:
                    vlink(nc.vector.tensor_tensor(mod_c[:, 0:16], ps[:, MOD_BANK, 48:64], bias[:, 0:16], ALU.add))
                    nc.vector.scalar_tensor_tensor(mod_c[:, 16:24], mod_c[:, 8:16], 1.0, vcol("norm1_g_2", 0, 8), ALU.add, ALU.mult)

        def load_and_transpose(dram, dst, n_tok, first):
            n_t = n_tok // P
            with ExitStack() as st:
                rows = sbuf(st, "rows", [P, n_t, D])
                m0, a0, v0, l0 = mm_done.n, act_evac.n, dve_evac.n, inputs_in.n
                n_loads = 3 if first else 1
                with nc.Block() as block:
                    @block.sync
                    def _(sp):
                        if first:
                            sp.dma_start(base[:], A["consts"][:, 0:const_at["base_end"]]).then_inc(*inputs_in.up(16))
                            sp.dma_start(vec[:], A["vectors"]).then_inc(*inputs_in.up(16))
                        sp.dma_start(rows[:], dram.rearrange("(t p) d -> p t d", p=P)).then_inc(*inputs_in.up(16))

                    @block.tensor
                    def _(pe):
                        pe.wait_ge(inputs_in.sem, l0 + 16 * n_loads)
                        for d in range(KD):
                            for t in range(n_t):
                                last = nc.tensor.transpose(ps[:, d, t * P:(t + 1) * P], rows[:, t, d * P:(d + 1) * P], ident)
                            last.then_inc(*mm_done.up())

                    @block.scalar
                    def _(act):
                        for d in range(0, KD, 2):
                            act.wait_ge(mm_done.sem, m0 + d + 1)
                            nc.scalar.activation(dst[:, d, :], ps[:, d, 0:n_tok], ACT.Copy)

                    @block.vector
                    def _(dve):
                        for d in range(1, KD, 2):
                            dve.wait_ge(mm_done.sem, m0 + d + 1)
                            nc.vector.tensor_copy(dst[:, d, :], ps[:, d, 0:n_tok])

        def rms_norm(src, dst, n_tok, weight, shift=None, sq=None, parts=None, ahead=None):
            sq = dst if sq is None else sq
            with ExitStack() as st:
                rt = sbuf(st, "rt", [P, 2, n_tok])
                m0, v0, a0 = mm_done.n, dve_out.n, act_out.n
                sums = ps[:, 0, 0:n_tok]
                with nc.Block() as block:
                    @block.sync
                    def _(sp):
                        if ahead is not None:
                            ahead.load(sp, 0, 2)

                    @block.tensor
                    def _(pe):
                        for k in range(0, KD, 2):
                            pe.wait_ge(dve_out.sem, v0 + k // 2 + 1)
                            last = nc.tensor.matmul(sums, ones, sq[:, k, :], start=(k == 0), stop=(k == KD - 2))
                        last.then_inc(*mm_done.up())

                    @block.scalar
                    def _(act):
                        for k in range(1, KD, 2):
                            nc.scalar.activation(sq[:, k, :], src[:, k, :], ACT.Square).then_inc(*act_out.up())
                        if ahead is not None:
                            ahead.split_hi(act, 0)
                            ahead.split_hi(act, 1)
                        act.wait_ge(dve_out.sem, v0 + KD // 2 + 1)
                        nc.scalar.activation(rt[:, 1, :], rt[:, 0, :], ACT.Sqrt).then_inc(*act_out.up())
                        if shift is not None:
                            for k in range(KD):
                                act.wait_ge(dve_out.sem, v0 + KD // 2 + 2 + k)
                                if parts is not None:
                                    ins = nc.scalar.activation(parts[0][:, k, :], dst[:, k, :], ACT.Identity, bias=shift(k))
                                    if k % 2 == 1:
                                        ins.then_inc(*act_out.up())
                                        continue
                                    alink(ins)
                                nc.scalar.activation(dst[:, k, :], dst[:, k, :], ACT.Identity, bias=shift(k)).then_inc(*act_out.up())
                        elif parts is not None:
                            for k in range(KD):
                                act.wait_ge(dve_out.sem, v0 + KD // 2 + 2 + k)
                                nc.scalar.activation(parts[0][:, k, :], dst[:, k, :], ACT.Copy).then_inc(*act_out.up())

                    @block.vector
                    def _(dve):
                        for k in range(0, KD, 2):
                            vlink(nc.vector.tensor_tensor(sq[:, k, :], src[:, k, :], src[:, k, :], ALU.mult))
                            dve.wait_ge(act_out.sem, a0 + k // 2 + 1)
                            nc.vector.tensor_tensor(sq[:, k, :], sq[:, k, :], sq[:, k + 1, :], ALU.add).then_inc(*dve_out.up())
                        dve.wait_ge(mm_done.sem, m0 + 1)
                        nc.vector.tensor_scalar(rt[:, 0, :], sums, 1.0 / D, RMS_EPS, ALU.mult, ALU.add).then_inc(*dve_out.up())
                        dve.wait_ge(act_out.sem, a0 + KD // 2 + 1)
                        vlink(nc.vector.reciprocal(rt[:, 0, :], rt[:, 1, :]))
                        for k in range(KD):
                            nc.vector.scalar_tensor_tensor(dst[:, k, :], src[:, k, :], weight(k), rt[:, 0, :], ALU.mult, ALU.mult).then_inc(*dve_out.up())
                        if parts is not None:
                            for k in range(1, KD, 2):
                                dve.wait_ge(act_out.sem, a0 + KD // 2 + 2 + k)
                                if shift is None:
                                    nc.vector.tensor_tensor(parts[1][:, k, :], dst[:, k, :], parts[0][:, k, :].bitcast(F32), ALU.subtract)
                                else:
                                    nc.vector.scalar_tensor_tensor(parts[1][:, k, :], dst[:, k, :], shift(k), parts[0][:, k, :].bitcast(F32), ALU.add, ALU.subtract)

                    @block.gpsimd
                    def _(pool):
                        if ahead is not None:
                            ahead.split_lo(pool, 0, 2)
                            ahead.early = True
                        if parts is not None:
                            for k in range(0, KD, 2):
                                pool.wait_ge(act_out.sem, a0 + KD // 2 + 2 + k)
                                nc.gpsimd.tensor_tensor(parts[1][:, k, :], dst[:, k, :], parts[0][:, k, :].bitcast(F32), ALU.subtract)

        w_first = A["w_in"].rearrange("(k p) n -> p k n", p=P)
        q0, v_0, gl0, og0 = RW_COLS, RW_COLS + 512, RW_COLS + 1024, RW_COLS + 1056
        first_spans = [(c, min(UNIT_COLS, RW_COLS - c), "rwkv") for c in range(0, RW_COLS, UNIT_COLS)]
        first_spans += [(c0 + c, UNIT_COLS, kind) for c0, kind in ((q0, "qk"), (v_0, "v"), (og0, "og")) for c in range(0, 512, UNIT_COLS)]

        def first_weights(st):
            return SplitWeights(st, [[(0, w_first[:, :, c0:c0 + n])] for c0, n, _ in first_spans])

        def square_weights(st, w_dram):
            w = w_dram.rearrange("(k p) n -> p k n", p=P)
            return SplitWeights(st, [[(0, w[:, :, c:c + UNIT_COLS])] for c in range(0, D, UNIT_COLS)])

        def project_first(W, hT, parts, proj, gla_q, gla_k, gla_v, gla_gl, gla_og, side):
            w, spans = w_first, first_spans
            tiles = []
            for u, (c0, n, kind) in enumerate(spans):
                first = {"rwkv": 0, "qk": q0, "v": v_0, "og": og0}[kind]
                if kind == "v":
                    tiles += [(u, (c0 - first), kind, t) for t in range(KT)]
                else:
                    tiles += [(u, j, kind, (c0 - first + j) // P) for j in range(0, n, P)]
            n_t = len(tiles)
            tiles.append((len(spans), 0, "gl", 0))
            n_rw = RW_COLS // P
            with ExitStack() as st:
                pad = sbuf(st, "pad", [P, 3, T + 2])
                w_gl = sbuf(st, "w_gl", [P, KD, 32])
                m0, a0, v0, p0, l0 = mm_done.n, act_evac.n, dve_out.n, pool_out.n, inputs_in.n
                W.unit_end = [m0 + max(i for i, t in enumerate(tiles) if t[0] == u) + 1 for u in range(len(spans))]
                beside = (n_rw + 1) // 2
                M = Modulation(st, *side, len(tiles), lambda q: 2 * q if q < beside else n_rw, lambda q: 2 * q + 3 if q < beside else n_rw + 3 + 2 * (q - beside))
                with nc.Block() as block:
                    @block.sync
                    def _(sp):
                        M.load(sp)

                    @block.gpsimd
                    def _(pool):
                        nc.gpsimd.memset(pad[:], 0.0).then_inc(*pool_out.up())
                        W.split_lo(pool, W.next_unit())

                    @block.tensor
                    def _(pe):
                        for i, (u, j, kind, idx) in enumerate(tiles):
                            if i >= MOD_BANK:
                                pe.wait_ge(act_evac.sem, a0 + i - MOD_BANK + 1)
                            if kind == "gl":
                                pe.wait_ge(inputs_in.sem, l0 + 16)
                                for k in range(KD):
                                    last = nc.tensor.matmul(ps[0:32, i % MOD_BANK, :], w_gl[:, k, :], hT[:, k, :], start=(k == 0), stop=(k == KD - 1))
                            else:
                                if i == 0 or tiles[i - 1][0] != u:
                                    W.ready(pe, u)
                                if kind == "v":
                                    last = W.product(ps[:, i % MOD_BANK, 0:UNIT_COLS], u, 0, parts, slice(idx * P, (idx + 1) * P), swap=True)
                                else:
                                    last = W.product(ps[:, i % MOD_BANK, :], u, j, parts, slice(0, T))
                            last.then_inc(*mm_done.up())
                            M.tensor(pe, i)

                    @block.scalar
                    def _(act):
                        W.load(act, W.next_unit(), 2)
                        act.dma_start(w_gl[:], w[:, :, gl0:gl0 + 32]).then_inc(*inputs_in.up(16))
                        M.silu_of_c()
                        for u in range(W.next_unit(), 2):
                            W.split_hi(act, u)
                        W.load_unit(act, 2)
                        act.wait_ge(pool_out.sem, p0 + 1)
                        for i, (u, j, kind, idx) in enumerate(tiles):
                            act.wait_ge(mm_done.sem, m0 + i + 1)
                            src = ps[:, i % MOD_BANK, :]
                            if kind == "rwkv":
                                if i >= 3:
                                    act.wait_ge(dve_out.sem, v0 + i - 2)
                                ins = nc.scalar.activation(pad[:, i % 3, 1:T + 1], src, ACT.Copy)
                            elif kind == "qk":
                                dst = gla_q if idx < 2 else gla_k
                                ins = nc.scalar.activation(dst[:, idx % 2, :], src, ACT.Copy, scale=GLA_DK ** -0.5 if idx < 2 else 1.0)
                            elif kind == "v":
                                ins = nc.scalar.activation(gla_v[:, idx, j:j + UNIT_COLS], src[:, 0:UNIT_COLS], ACT.Copy)
                            elif kind == "gl":
                                ins = nc.scalar.activation(gla_gl[:, :], src[0:32], ACT.Copy)
                            else:
                                ins = nc.scalar.activation(gla_og[:, idx, :], src, ACT.Silu)
                            ins.then_inc(*act_evac.up())
                            if i + 1 == n_t or (i + 1 < n_t and tiles[i + 1][0] != u):
                                W.load_unit(act, u + 3)
                                W.split_hi(act, u + 2)

                    @block.vector
                    def _(dve):
                        for i in range(len(tiles)):
                            if i >= n_rw:
                                M.vector(dve, i)
                                continue
                            dve.wait_ge(act_evac.sem, a0 + i + 1)
                            p, dst = pad[:, i % 3, 1:T + 1], proj[:, i, :]
                            vlink(nc.vector.tensor_tensor(dst, pad[:, i % 3, 0:T], pad[:, i % 3, 2:T + 2], ALU.add))
                            vlink(nc.vector.scalar_tensor_tensor(dst, dst, 0.5, p, ALU.mult, ALU.subtract))
                            nc.vector.scalar_tensor_tensor(dst, dst, vcol("rw_mu", i), p, ALU.mult, ALU.add).then_inc(*dve_out.up())
                            M.vector(dve, i)
                        M.finish(dve)

        def rwkv_keys(proj, kk, w2, a2, g2, lnk):
            r_, k_, v_ = proj[:, 0:4, :], proj[:, 4:8, :], proj[:, 8:12, :]
            with ExitStack() as st:
                sq = sbuf(st, "sq", [P, CT, T])
                m0, a0, v0, l0 = mm_done.n, act_out.n, dve_out.n, inputs_in.n
                with nc.Block() as block:
                    @block.sync
                    def _(sp):
                        sp.dma_start(w2[0:64, :], A["rw_w2_f"]).then_inc(*inputs_in.up(16))
                        sp.dma_start(w2[64:128, :], A["rw_w2_b"]).then_inc(*inputs_in.up(16))
                        sp.dma_start(a2[0:64, :], A["rw_a2_f"]).then_inc(*inputs_in.up(16))
                        sp.dma_start(a2[64:128, :], A["rw_a2_b"]).then_inc(*inputs_in.up(16))
                        sp.dma_start(g2[:], A["rw_g2"]).then_inc(*inputs_in.up(16))
                        sp.wait_ge(inputs_in.sem, l0 + 80)

                    @block.vector
                    def _(dve):
                        for c in range(CT):
                            vlink(nc.vector.tensor_scalar(kk[:, c, :], k_[:, c, :], vcol("rw_k_k", c), None, ALU.mult))
                            nc.vector.tensor_tensor(sq[:, c, :], kk[:, c, :], kk[:, c, :], ALU.mult).then_inc(*dve_out.up())
                        dve.wait_ge(act_out.sem, a0 + 1)
                        vlink(nc.vector.tensor_scalar(sq[:, 0, :], sq[:, 0, :], 1e-12, None, ALU.max))
                        nc.vector.reciprocal(sq[:, 1, :], sq[:, 0, :]).then_inc(*dve_out.up())
                        for c in range(CT):
                            dve.wait_ge(mm_done.sem, m0 + 2 + c)
                            nc.vector.tensor_tensor(kk[:, c, :], kk[:, c, :], ps[:, 1 + c, :], ALU.mult)

                    @block.tensor
                    def _(pe):
                        for c in range(CT):
                            pe.wait_ge(dve_out.sem, v0 + c + 1)
                            last = nc.tensor.matmul(ps[32 * c:32 * c + 32, 0, :], head_ones[:, 0:P:4], sq[:, c, :], start=True, stop=True)
                        last.then_inc(*mm_done.up())
                        pe.wait_ge(dve_out.sem, v0 + CT + 1)
                        for c in range(CT):
                            r = slice(32 * c, 32 * c + 32)
                            nc.tensor.matmul(ps[:, 1 + c, :], spread[r, :], sq[r, 1, :], start=True, stop=True).then_inc(*mm_done.up())

                    @block.scalar
                    def _(act):
                        act.wait_ge(mm_done.sem, m0 + 1)
                        nc.scalar.activation(sq[:, 0, :], ps[:, 0, :], ACT.Sqrt).then_inc(*act_out.up())
                        nc.scalar.activation(proj[:, 14, :], proj[:, 14, :], ACT.Sigmoid)
                        nc.scalar.activation(proj[:, 12, :], proj[:, 12, :], ACT.Tanh)

        def rwkv_direction(back, proj, kk, w2, a2, kd_sum, bufs):
            r_, k_ = proj[:, 0:4, :], proj[:, 4:8, :]
            lw, cc, ex, a_, kd, qt, rt = bufs["lw"], bufs["cc"], bufs["ex"], bufs["a"], bufs["kd"], bufs["q"], bufs["r"]
            half, scale = bufs["half"], bufs["scale"]
            rows = slice(64, 128) if back else slice(0, 64)
            w0, ka0 = ("rw_w0_b", "rw_a0_b") if back else ("rw_w0_f", "rw_a0_f")

            def chunks(t):
                return t[:, :, :].rearrange("p c (n i) -> p (c n) i", i=P)

            def flat(t):
                return t[:, :, :].rearrange("p c n -> p (c n)")

            m0, a0, v0, p0 = mm_done.n, act_out.n, dve_out.n, pool_out.n
            with nc.Block() as block:
                @block.tensor
                def _(pe):
                    for j in range(2 * CT):
                        c, w, x = j % CT, (w2, a2)[j // CT], proj[rows, 12 + j // CT, :]
                        nc.tensor.matmul(ps[:, j, :], w[rows, c * P:(c + 1) * P], x, start=True, stop=True).then_inc(*mm_done.up())

                @block.scalar
                def _(act):
                    for j in range(2 * CT):
                        c, name, dst = j % CT, (w0, ka0)[j // CT], (lw, a_)[j // CT]
                        act.wait_ge(mm_done.sem, m0 + j + 1)
                        nc.scalar.activation(dst[:, c, :], ps[:, j, :], ACT.Sigmoid, bias=vcol(name, c)).then_inc(*act_out.up())
                    act.wait_ge(dve_out.sem, v0 + 1)
                    nc.scalar.activation(scale[:], half[:], ACT.Exp).then_inc(*act_out.up())
                    act.wait_ge(dve_out.sem, v0 + 2)
                    if back:
                        nc.scalar.activation(flat(ex), flat(lw), ACT.Exp, scale=-1.0).then_inc(*act_out.up())
                        alink(nc.scalar.activation(flat(cc), flat(cc), ACT.Exp, scale=-1.0))
                    else:
                        alink(nc.scalar.activation(flat(ex), flat(cc), ACT.Exp, scale=-1.0))
                        nc.scalar.activation(flat(cc), flat(cc), ACT.Exp).then_inc(*act_out.up())
                    act.wait_ge(act_step.sem, act_step.n)
                    if back:
                        act.wait_ge(act_out.sem, act_out.n)
                    nc.scalar.activation(flat(lw), flat(lw), ACT.Exp).then_inc(*act_out.up())

                @block.vector
                def _(dve):
                    dve.wait_ge(act_out.sem, a0 + CT)
                    vlink(nc.vector.tensor_scalar(flat(lw), flat(lw), -math.exp(-0.5), None, ALU.mult))
                    for c in range(CT):
                        for n in range(KT):
                            at = slice(n * P, (n + 1) * P)
                            ins = nc.vector.tensor_tensor_scan(cc[:, c, at], ones, lw[:, c, at], 0.0, ALU.mult, ALU.add)
                    vlink(ins)
                    totals = chunks(cc)[:, :, P - 1:P]
                    ins = nc.vector.tensor_scalar(half[:].unsqueeze(2), totals, 0.5, None, ALU.mult)
                    ins.then_inc(*dve_out.up())
                    dve.wait_ge(dve_out.sem, v0 + 1)
                    vlink(nc.vector.tensor_tensor(chunks(cc), chunks(cc), half[:].unsqueeze(2).to_broadcast([P, CT * KT, P]), ALU.subtract))
                    nc.vector.tensor_tensor(flat(lw), flat(cc), flat(lw), ALU.subtract).then_inc(*dve_out.up())
                    dve.wait_ge(act_out.sem, a0 + 2 * CT)
                    for c in range(CT):
                        ins = nc.vector.tensor_scalar(kd[:, c, :], a_[:, c, :], -1.0, vcol("rw_k_a", c), ALU.add, ALU.mult)
                    vlink(ins)
                    nc.vector.scalar_tensor_tensor(flat(kd), flat(kd), 1.0, flat(k_), ALU.add, ALU.mult).then_inc(*dve_out.up())
                    vlink(nc.vector.tensor_tensor(flat(a_), flat(a_), flat(kk), ALU.mult))
                    dve.wait_ge(act_out.sem, a0 + 2 * CT + 3)
                    dve.wait_ge(act_step.sem, act_step.n)
                    eq, er, eb = (cc, ex, lw) if back else (lw, cc, ex)
                    nc.vector.tensor_tensor(flat(qt), flat(kk), flat(eq), ALU.mult)
                    nc.vector.tensor_tensor(flat(a_), flat(a_), flat(eb), ALU.mult)
                    dve.wait_ge(pool_out.sem, p0 + 1)
                    nc.vector.tensor_tensor(flat(kd), flat(kd), flat(eb), ALU.mult)

                @block.gpsimd
                def _(pool):
                    pool.wait_ge(dve_out.sem, v0 + 3)
                    if back:
                        nc.gpsimd.tensor_tensor(flat(kd_sum), flat(kd_sum), flat(kd), ALU.add).then_inc(*pool_out.up())
                    else:
                        nc.gpsimd.tensor_copy(flat(kd_sum), flat(kd)).then_inc(*pool_out.up())
                    pool.wait_ge(act_out.sem, a0 + 2 * CT + 3)
                    pool.wait_ge(act_step.sem, act_step.n)
                    nc.gpsimd.tensor_tensor(flat(rt), flat(r_), flat(cc if not back else ex), ALU.mult)

        def to_tokens(pairs):
            m0 = mm_done.n
            a0 = act_evac.n
            v0 = dve_evac.n
            jobs = [(src, dst, n) for src, dst in pairs for n in range(src.shape[2] // P)]
            with nc.Block() as block:
                @block.tensor
                def _(pe):
                    for j, (src, dst, n) in enumerate(jobs):
                        if j >= 8:
                            if j % 2:
                                pe.wait_ge(act_evac.sem, a0 + (j - 8) // 2 + 1)
                            else:
                                pe.wait_ge(dve_evac.sem, v0 + (j - 8) // 2 + 1)
                        n_c = src.shape[1]
                        for c in range(n_c):
                            last = nc.tensor.transpose(ps[:, j % 8, c * P:(c + 1) * P], src[:, c, n * P:(n + 1) * P], ident)
                        last.then_inc(*mm_done.up())

                @block.scalar
                def _(act):
                    for j, (src, dst, n) in enumerate(jobs):
                        if j % 2:
                            act.wait_ge(mm_done.sem, m0 + j + 1)
                            nc.scalar.activation(dst[:, n, :], ps[:, j % 8, 0:src.shape[1] * P], ACT.Copy).then_inc(*act_evac.up())

                @block.vector
                def _(dve):
                    for j, (src, dst, n) in enumerate(jobs):
                        if j % 2 == 0:
                            dve.wait_ge(mm_done.sem, m0 + j + 1)
                            nc.vector.tensor_copy(dst[:, n, :], ps[:, j % 8, 0:src.shape[1] * P]).then_inc(*dve_evac.up())

        def rwkv_scan(back, bufs, v_tok, y, masks):
            qt, rt, kt, bt = bufs["q"], bufs["r"], bufs["kd"], bufs["a"]
            b_tok, k_tok = bufs["b_tok"], bufs["k_tok"]
            scale = bufs["scale"]
            N, X, U = (bufs[n] for n in ("N", "X", "U"))
            both = {n: bufs[n] for n in ("Z", "BT", "RB", "RK")}
            rhs, sa, S, hop = bufs["rhs"], bufs["sa"], bufs["S"], bufs["hop"]
            d = 1 if back else 0
            strict = masks["strict"][:, d * P:(d + 1) * P]
            incl = masks["incl"][:, d * P:(d + 1) * P]

            def level(l, back_=back):
                at = (LEVELS * int(back_) + l) * P
                return masks["levels"][:, at:at + P]

            order = list(range(KT))[::-1] if back else list(range(KT))
            H4 = CT
            rows = (slice(0, 64), slice(64, 128))
            lower, upper = (1, 0) if back else (0, 1)

            def halves_of(ap, l, which):
                return ap.rearrange("p h (m two b) -> p h m two b", two=2, b=2 ** l)[:, :, :, which, :]

            jobs = []
            for j in range(KT + 1):
                behind = []
                if j > 0:
                    n = order[j - 1]
                    behind = [[(n, "rhs", 0, 0), (n, "rhs", 1, 0)], [(n, "sa", 0, 0)], [(n, "y", 0, 0), (n, "y", 1, 0)], [(n, "S", 0, 0)]]
                if j < KT:
                    n = order[j]
                    for par in range(2):
                        jobs += [(n, nm, par, 0) for nm in ("A", "N")]
                    others = [(n, nm, par, 0) for nm in ("RB", "BT", "RK") for par in range(2)]
                    jobs += behind.pop(0) if behind else []
                    jobs += others[0:2]
                    del others[0:2]
                    for l in range(1, LEVELS):
                        jobs += [(n, "U", par, l) for par in range(2)]
                        jobs += behind.pop(0) if behind else []
                        jobs += [others.pop(0)] if others else []
                        for par in range(2):
                            if l < LEVELS - 1:
                                jobs.append((n, "X", par, l))
                            jobs.append((n, "Z", par, l))
                for step in behind:
                    jobs += step
            number = {job: i for i, job in enumerate(jobs)}
            m0, e0 = mm_done.n, dve_evac.n

            def four(bank):
                return ps[:, bank, :].rearrange("p (h i) -> p h i", h=H4)

            with nc.Block() as block:
                @block.tensor
                def _(pe):
                    free = [0]

                    def evacuated(job):
                        need = number[job] + 1
                        if need > free[0]:
                            free[0] = need
                            pe.wait_ge(dve_evac.sem, e0 + need)

                    for i, (n, nm, par, l) in enumerate(jobs):
                        at = slice(n * P, (n + 1) * P)
                        r = rows[par]
                        bank = ps[:, i % 8, :]
                        Z, BT, RB, RK = (both[x][order.index(n) % 2] for x in ("Z", "BT", "RB", "RK"))
                        if i >= 8:
                            evacuated(jobs[i - 8])
                        mm = nc.tensor.matmul
                        if nm in ("A", "N", "RB", "BT", "RK"):
                            lhs, rhs_ = {"A": (qt, bt), "N": (bt, qt), "RB": (bt, rt), "BT": (kt, qt), "RK": (kt, rt)}[nm]
                            for h in range(H4):
                                last = mm(bank[:, h * P:(h + 1) * P], lhs[r, h, at], rhs_[r, h, at], start=True, stop=True)
                        elif nm == "U":
                            evacuated((n, "N", par, 0) if l == 1 else (n, "X", par, l - 1))
                            for h in range(H4):
                                last = mm(bank[:, h * P:(h + 1) * P], N[:, par, h, :], X[:, par, h, :], start=True, stop=True)
                        elif nm == "X":
                            evacuated((n, "U", par, l))
                            for h in range(H4):
                                last = mm(bank[:, h * P:(h + 1) * P], Z[:, par, h, :], U[:, par, h, :], start=True, stop=True)
                        elif nm == "Z":
                            evacuated((n, "U", par, l))
                            for h in range(H4):
                                last = mm(bank[:, h * P:(h + 1) * P], U[:, par, h, :], Z[:, par, h, :], start=True, stop=True)
                        elif nm == "rhs":
                            evacuated((n, "RK", 1, 0))
                            if n != order[0]:
                                evacuated((order[order.index(n) - 1], "S", 0, 0))
                            for h in range(H4):
                                o = bank[:, h * 64:(h + 1) * 64]
                                mm(o, qt[r, h, at], S[r, h, :], start=True, stop=False)
                                last = mm(o, BT[:, par, h, :], v_tok[:, n, h * P + par * 64:h * P + par * 64 + 64], start=False, stop=True)
                        elif nm == "sa":
                            evacuated((n, "Z", 1, LEVELS - 1))
                            evacuated((n, "rhs", 1, 0))
                            for h in range(H4):
                                for q in range(2):
                                    last = mm(bank[:, (2 * h + q) * 64:(2 * h + q + 1) * 64], Z[:, q, h, :], rhs[:, q, h, :], start=True, stop=True)
                        elif nm == "y":
                            evacuated((n, "sa", 0, 0))
                            for h in range(H4):
                                o = bank[r, h * P:(h + 1) * P]
                                head = slice(h * P + par * 64, h * P + par * 64 + 64)
                                mm(o, S[r, h, :], rt[r, h, at], start=True, stop=False)
                                mm(o, sa[:, head], RB[:, par, h, :], start=False, stop=False)
                                last = mm(o, v_tok[:, n, head], RK[:, par, h, :], start=False, stop=True)
                        else:
                            for h in range(H4):
                                for q in range(2):
                                    o = bank[rows[q], h * 64:(h + 1) * 64]
                                    head = slice(h * P + q * 64, h * P + q * 64 + 64)
                                    mm(o, b_tok[:, n, head], sa[:, head], start=True, stop=False)
                                    last = mm(o, k_tok[:, n, head], v_tok[:, n, head], start=False, stop=True)
                        last.then_inc(*mm_done.up())

                @block.vector
                def _(dve):
                    sc = scale[:].rearrange("p (c n) -> p c n", n=KT)
                    for j, n in enumerate(order[:-1]):
                        nc.vector.tensor_tensor(hop[:, j, :], sc[:, :, n], sc[:, :, order[j + 1]], ALU.mult)
                    vlink(nc.vector.memset(S[:], 0.0))
                    for i, (n, nm, par, l) in enumerate(jobs):
                        dve.wait_ge(mm_done.sem, m0 + i + 1)
                        at = slice(n * P, (n + 1) * P)
                        r = rows[par]
                        bank = four(i % 8)
                        Z, BT, RB, RK = (both[x][order.index(n) % 2] for x in ("Z", "BT", "RB", "RK"))
                        tt = nc.vector.tensor_tensor

                        if nm == "A":
                            vlink(tt(X[:, par], bank, bcast(level(0), H4), ALU.mult))
                            ins = tt(X[:, par], bcast(ident, H4), X[:, par], ALU.subtract)
                        elif nm == "N":
                            vlink(tt(N[:, par], bank, bcast(strict, H4), ALU.mult))
                            vlink(tt(Z[:, par], N[:, par], bcast(level(0, not back), H4), ALU.mult))
                            ins = tt(Z[:, par], bcast(ident, H4), Z[:, par], ALU.subtract)
                        elif nm in ("RB", "BT", "RK"):
                            ins = tt({"RB": RB, "BT": BT, "RK": RK}[nm][:, par], bank, bcast(strict if nm == "BT" else incl, H4), ALU.mult)
                        elif nm == "U":
                            ins = tt(U[:, par], bank, bcast(level(l), H4), ALU.mult)
                        elif nm in ("X", "Z"):
                            M = halves_of(X[:, par], l, lower) if nm == "X" else halves_of(Z[:, par], l, upper)
                            ins = tt(M, M, halves_of(bank, l, lower if nm == "X" else upper), ALU.subtract)
                        elif nm == "rhs":
                            ins = nc.vector.tensor_scalar(rhs[:, par], ps[:, i % 8, 0:256].rearrange("p (h v) -> p h v", h=H4), -1.0, None, ALU.mult)
                        elif nm == "sa":
                            ins = nc.vector.tensor_copy(sa[:], ps[:, i % 8, :])
                        elif nm == "y":
                            o = y[r, :, at]
                            if back:
                                ins = tt(o, o, bank[r], ALU.add)
                            else:
                                ins = nc.vector.tensor_copy(o, bank[r])
                        else:
                            j = order.index(n)
                            if j == KT - 1:
                                ins = nc.vector.tensor_copy(S[:], ps[:, i % 8, 0:256].rearrange("p (h v) -> p h v", h=H4))
                            else:
                                vlink(tt(S[:], S[:], ps[:, i % 8, 0:256].rearrange("p (h v) -> p h v", h=H4), ALU.add))
                                ins = tt(S[:], S[:], hop[:, j, :].unsqueeze(2).to_broadcast([P, CT, 64]), ALU.mult)
                        ins.then_inc(*dve_evac.up())
                        dve.wait_ge(dve_evac.sem, e0 + i + 1)

        def rwkv_output(proj, y, kd_sum, g2, ahead):
            r_, v_ = proj[:, 0:4, :], proj[:, 8:12, :]
            with ExitStack() as st:
                sq = sbuf(st, "gn_sq", [P, CT, T])
                m0, v0, a0 = mm_done.n, dve_out.n, act_out.n
                n_mm = 4 * CT
                with nc.Block() as block:
                    @block.sync
                    def _(sp):
                        ahead.load(sp, 0, 2)

                    @block.gpsimd
                    def _(pool):
                        ahead.split_lo(pool, 0, 2)
                        ahead.early = True

                    @block.tensor
                    def _(pe):
                        for c in range(CT):
                            nc.tensor.matmul(ps[:, c, :], head_ones, y[:, c, :], start=True, stop=True).then_inc(*mm_done.up())
                        for c in range(CT):
                            nc.tensor.matmul(ps[:, 4 + c, :], g2[:, c * P:(c + 1) * P], proj[:, 14, :], start=True, stop=True).then_inc(*mm_done.up())
                        for c in range(CT):
                            pe.wait_ge(dve_out.sem, v0 + c + 1)
                            last = nc.tensor.matmul(ps[32 * c:32 * c + 32, 0, :], head_ones[:, 0:P:4], sq[:, c, :], start=True, stop=True)
                        last.then_inc(*mm_done.up())
                        pe.wait_ge(dve_out.sem, v0 + 2 * CT + 2)
                        for c in range(CT):
                            r = slice(32 * c, 32 * c + 32)
                            nc.tensor.matmul(ps[:, c, :], spread[r, :], sq[r, 1, :], start=True, stop=True).then_inc(*mm_done.up())
                        for c in range(CT):
                            pe.wait_ge(dve_out.sem, v0 + 2 * CT + 2 + c + 1)
                            nc.tensor.matmul(ps[:, c, :], head_ones, kd_sum[:, c, :], start=True, stop=True).then_inc(*mm_done.up())

                    @block.scalar
                    def _(act):
                        ahead.split_hi(act, 0)
                        ahead.split_hi(act, 1)
                        act.wait_ge(dve_out.sem, v0 + CT + 1)
                        nc.scalar.activation(sq[:, 0, :], sq[:, 0, :], ACT.Sqrt).then_inc(*act_out.up())

                    @block.vector
                    def _(dve):
                        for c in range(CT):
                            dve.wait_ge(mm_done.sem, m0 + c + 1)
                            vlink(nc.vector.scalar_tensor_tensor(y[:, c, :], ps[:, c, :], -1.0 / RW_HD, y[:, c, :], ALU.mult, ALU.add))
                            nc.vector.tensor_tensor(sq[:, c, :], y[:, c, :], y[:, c, :], ALU.mult).then_inc(*dve_out.up())
                        dve.wait_ge(mm_done.sem, m0 + 2 * CT + 1)
                        nc.vector.tensor_scalar(sq[:, 0, :], ps[:, 0, :], 1.0 / RW_HD, RW_GN_EPS, ALU.mult, ALU.add).then_inc(*dve_out.up())
                        for c in range(CT):
                            nc.vector.scalar_tensor_tensor(kd_sum[:, c, :], r_[:, c, :], vcol("rw_r_k", c), kd_sum[:, c, :], ALU.mult, ALU.mult).then_inc(*dve_out.up())
                        dve.wait_ge(act_out.sem, a0 + 1)
                        nc.vector.reciprocal(sq[:, 1, :], sq[:, 0, :]).then_inc(*dve_out.up())
                        for c in range(CT):
                            dve.wait_ge(mm_done.sem, m0 + 2 * CT + 2 + c)
                            nc.vector.tensor_tensor(y[:, c, :], y[:, c, :], ps[:, c, :], ALU.mult).then_inc(*dve_out.up())
                        for c in range(CT):
                            dve.wait_ge(dve_out.sem, v0 + 2 * CT + 3 + c)
                            vlink(nc.vector.tensor_scalar(y[:, c, :], y[:, c, :], vcol("rw_ln_w", c), vcol("rw_ln_b", c), ALU.mult, ALU.add))
                            dve.wait_ge(mm_done.sem, m0 + 3 * CT + 2 + c)
                            vlink(nc.vector.tensor_tensor(v_[:, c, :], ps[:, c, :], v_[:, c, :], ALU.mult))
                            vlink(nc.vector.tensor_tensor(y[:, c, :], y[:, c, :], v_[:, c, :], ALU.add))
                            nc.vector.tensor_tensor(y[:, c, :], ps[:, 4 + c, :], y[:, c, :], ALU.mult)

        def gla_mixer(q, k, v_tok, gl, og, o, masks):
            n_sub = P // GLA_SUB
            NT = 2
            C8 = NT * KT

            def flat(t):
                return t[:, :, :].rearrange("p c n -> p (c n)")

            def chunks(t):
                return t[:, :, :].rearrange("p c (n i) -> p (c n) i", i=P)

            with ExitStack() as st:
                gw2 = sbuf(st, "gw2", [32, 2, 256])
                def two(name, shape):
                    return [sbuf(st, f"{name}{d}", shape) for d in range(2)]

                z2, L2, e2 = two("gz", [P, NT, T]), two("gL", [P, NT, T]), two("ge", [P, NT, T])
                qs2 = e2
                qz2 = two("g_qz", [P, NT, 2 * T])
                qc2 = two("g_qc", [P, NT, T])
                kc2 = two("g_kc", [P, NT, T])
                ks2 = two("g_ks", [P, n_sub, NT, T])
                kc_tok2 = [flat(x).rearrange("p (t c) -> p t c", t=KT) for x in L2]
                att4 = [flat(x).rearrange("p (two h i) -> p two h i", two=2, h=4) for x in z2]
                S2 = two("g_S", [P, NT, P])
                last_decay2 = two("g_last", [P, C8])
                l0 = inputs_in.n
                ways = (False, True)
                orders = (list(range(KT)), list(range(KT))[::-1])
                m0, a0, v0, p0 = mm_done.n, act_out.n, dve_out.n, pool_out.n
                PER_WAY = 3 + n_sub
                exp_z = {}
                with nc.Block() as block:
                    @block.sync
                    def _(sp):
                        sp.dma_start(gw2[:], A["gla_gw2"]).then_inc(*inputs_in.up(16))

                    @block.tensor
                    def _(pe):
                        pe.wait_ge(inputs_in.sem, l0 + 16)
                        for d in range(2):
                            for c in range(NT):
                                nc.tensor.matmul(ps[:, d * NT + c, :], gw2[:, d, c * P:(c + 1) * P], gl[:, :], start=True, stop=True).then_inc(*mm_done.up())

                    @block.scalar
                    def _(act):
                        for d in range(2):
                            act.wait_ge(dve_out.sem, v0 + d + 1)
                            ins = nc.scalar.activation(flat(e2[d]), flat(z2[d]), ACT.Abs)
                        alink(ins)
                        for d in range(2):
                            ins = nc.scalar.activation(flat(e2[d]), flat(e2[d]), ACT.Exp, scale=-1.0)
                        alink(ins)
                        for d in range(2):
                            nc.scalar.activation(flat(e2[d]), flat(e2[d]), ACT.Ln, bias=1.0).then_inc(*act_out.up())
                        for d, back in enumerate(ways):
                            z, L, qs, kc, ks, last_decay, vd = z2[d], L2[d], qs2[d], kc2[d], ks2[d], last_decay2[d], v0 + 2 + d * PER_WAY
                            act.wait_ge(dve_out.sem, vd + 1)
                            alink(nc.scalar.activation(flat(z), flat(L), ACT.Exp, scale=1.0 / GLA_TAU))
                            exp_z[d] = act_step.n
                            nc.scalar.activation(last_decay[:].unsqueeze(2), chunks(z)[:, :, 0:1] if back else chunks(z)[:, :, P - 1:P], ACT.Copy).then_inc(*act_out.up())
                            act.wait_ge(dve_out.sem, vd + 2)
                            nc.scalar.activation(flat(kc), flat(kc), ACT.Exp, scale=1.0 / GLA_TAU).then_inc(*act_out.up())
                            act.wait_ge(dve_out.sem, vd + 3)
                            nc.scalar.activation(flat(qs), flat(qs), ACT.Exp, scale=1.0 / GLA_TAU).then_inc(*act_out.up())
                            for s in range(n_sub):
                                act.wait_ge(dve_out.sem, vd + 4 + s)
                                nc.scalar.activation(flat(ks[:, s]), flat(ks[:, s]), ACT.Exp, scale=-1.0 / GLA_TAU).then_inc(*act_out.up())

                    @block.gpsimd
                    def _(pool):
                        for d in range(2):
                            nc.gpsimd.memset(qz2[d][:], 0.0).then_inc(*pool_out.up())
                        for d in range(2):
                            for s in range(n_sub):
                                pool.wait_ge(act_out.sem, a0 + 2 + d * PER_WAY + 4 + s)
                                nc.gpsimd.tensor_tensor(flat(ks2[d][:, s]), flat(k), flat(ks2[d][:, s]), ALU.mult)

                    @block.vector
                    def _(dve):
                        for d, back in enumerate(ways):
                            for c in range(NT):
                                dve.wait_ge(mm_done.sem, m0 + d * NT + c + 1)
                                ins = nc.vector.tensor_scalar(z2[d][:, c, :], ps[:, d * NT + c, :], vcol("gla_gb_b" if back else "gla_gb_f", c), None, ALU.add)
                            ins.then_inc(*dve_out.up())
                        for d, back in enumerate(ways):
                            z, L, e, qs, qc, kc, ks = z2[d], L2[d], e2[d], qs2[d], qc2[d], kc2[d], ks2[d]
                            ad, vd = a0 + 2 + d * PER_WAY, v0 + 2 + d * PER_WAY
                            dve.wait_ge(act_out.sem, a0 + d + 1)
                            vlink(nc.vector.scalar_tensor_tensor(flat(z), flat(z), 0.0, flat(e), ALU.min, ALU.subtract))
                            way = slice(None, None, -1) if back else slice(None)
                            for j in range(C8):
                                ins = nc.vector.tensor_tensor_scan(chunks(L)[:, j, way], ones, chunks(z)[:, j, way], 0.0, ALU.mult, ALU.add)
                            ins.then_inc(*dve_out.up())
                            dve.wait_ge(dve_out.sem, vd + 1)
                            total = chunks(L)[:, :, 0:1] if back else chunks(L)[:, :, P - 1:P]
                            nc.vector.tensor_tensor(chunks(kc), total.to_broadcast([P, C8, P]), chunks(L), ALU.subtract).then_inc(*dve_out.up())
                            for s in range(n_sub):
                                sub = slice(s * GLA_SUB, (s + 1) * GLA_SUB)
                                mid = s * GLA_SUB + GLA_SUB // 2
                                anchor = chunks(L)[:, :, mid:mid + 1]
                                ins = nc.vector.tensor_tensor(chunks(qs)[:, :, sub], chunks(L)[:, :, sub], anchor.to_broadcast([P, C8, GLA_SUB]), ALU.subtract)
                            vlink(ins)
                            nc.vector.tensor_scalar(flat(qs), flat(qs), GLA_CLAMP * GLA_TAU, None, ALU.min).then_inc(*dve_out.up())
                            for s in range(n_sub):
                                mid = s * GLA_SUB + GLA_SUB // 2
                                anchor = chunks(L)[:, :, mid:mid + 1]
                                vlink(nc.vector.tensor_tensor(chunks(ks[:, s]), chunks(L), anchor.to_broadcast([P, C8, P]), ALU.subtract))
                                nc.vector.tensor_scalar(flat(ks[:, s]), flat(ks[:, s]), -GLA_CLAMP * GLA_TAU, None, ALU.max).then_inc(*dve_out.up())
                            dve.wait_ge(act_out.sem, ad + 3)
                            dve.wait_ge(act_step.sem, exp_z[d])
                            nc.vector.tensor_tensor(flat(qc), flat(q), flat(z), ALU.mult)
                            nc.vector.tensor_tensor(flat(kc), flat(k), flat(kc), ALU.mult)
                            dve.wait_ge(pool_out.sem, p0 + d + 1)
                            for par in range(2):
                                r = slice(64 * par, 64 * par + 64)
                                to = qz2[d][r].rearrange("p c (b two i) -> p c b two i", two=2, i=GLA_SUB)[:, :, :, par, :]
                                by_sub = [x[r].rearrange("p c (b i) -> p c b i", i=GLA_SUB) for x in (q, qs)]
                                nc.vector.tensor_tensor(to, by_sub[0], by_sub[1], ALU.mult)
                to_tokens([(kc2[d], kc_tok2[d]) for d in range(2)])
                rows = (slice(0, 64), slice(64, 128))
                jobs = []
                for j in range(KT + 1):
                    for d in range(2):
                        if j < KT:
                            jobs += [(d, orders[d][j], "att", 0)]
                        if j > 0:
                            jobs += [(d, orders[d][j - 1], nm, q_) for nm, q_ in (("o", 0), ("o", 1), ("S", 0))]
                number = {job: i for i, job in enumerate(jobs)}
                m1, e1 = mm_done.n, dve_evac.n
                with nc.Block() as block:
                    @block.tensor
                    def _(pe):
                        for i, (d, n, nm, par) in enumerate(jobs):
                            at = slice(n * P, (n + 1) * P)
                            r = rows[par]
                            j = orders[d].index(n)
                            qz, qc, ks, kc_tok, S, att = qz2[d], qc2[d], ks2[d], kc_tok2[d], S2[d], att4[d][:, j % 2]
                            bank = ps[:, i % 8, :]
                            if i >= 8:
                                pe.wait_ge(dve_evac.sem, e1 + i - 7)
                            if nm == "att":
                                for c in range(NT):
                                    for s in range(n_sub):
                                        both = 2 * GLA_SUB
                                        b = n * n_sub + s
                                        o0 = (c * n_sub + s) * both
                                        last = nc.tensor.matmul(bank[:, o0:o0 + both], ks[:, s, c, at], qz[:, c, b * both:(b + 1) * both], start=True, stop=True)
                            elif nm == "o":
                                pe.wait_ge(dve_evac.sem, e1 + number[(d, n, "att", 0)] + 1)
                                if j > 0:
                                    pe.wait_ge(dve_evac.sem, e1 + number[(d, orders[d][j - 1], "S", 0)] + 1)
                                for c in range(NT):
                                    h = 2 * c + par
                                    nc.tensor.matmul(bank[:, c * P:(c + 1) * P], S[r, c, :], qc[r, c, at], start=True, stop=False)
                                    last = nc.tensor.matmul(bank[:, c * P:(c + 1) * P], v_tok[:, n, h * P:(h + 1) * P], att[:, h, :], start=False, stop=True)
                            else:
                                for c in range(NT):
                                    for q_ in range(2):
                                        h = 2 * c + q_
                                        last = nc.tensor.matmul(bank[rows[q_], c * P:(c + 1) * P], kc_tok[:, n, h * 64:(h + 1) * 64],
                                                                v_tok[:, n, h * P:(h + 1) * P], start=True, stop=True)
                            last.then_inc(*mm_done.up())

                    @block.vector
                    def _(dve):
                        for d in range(2):
                            vlink(nc.vector.memset(S2[d][:], 0.0))
                        for i, (d, n, nm, par) in enumerate(jobs):
                            at = slice(n * P, (n + 1) * P)
                            j = orders[d].index(n)
                            S, att = S2[d], att4[d][:, j % 2]
                            incl = masks["incl"][:, d * P:(d + 1) * P]
                            ld = last_decay2[d][:].rearrange("p (c n) -> p c n", n=KT)
                            dve.wait_ge(mm_done.sem, m1 + i + 1)
                            pair = ps[:, i % 8, 0:2 * P].rearrange("p (c i) -> p c i", c=NT)
                            if nm == "att":
                                mask = incl.rearrange("p (s i) -> p s i", i=GLA_SUB).unsqueeze(2).to_broadcast([P, n_sub, 2, GLA_SUB])
                                for c in range(NT):
                                    got = ps[:, i % 8, c * 2 * P:(c + 1) * 2 * P].rearrange("p (s h i) -> p s h i", h=2, i=GLA_SUB)
                                    ins = nc.vector.tensor_tensor(att[:, 2 * c:2 * c + 2, :].rearrange("p h (s i) -> p s h i", i=GLA_SUB), got, mask, ALU.mult)
                            elif nm == "o":
                                dst = o[:, par::2, at]
                                if 2 * j >= KT:
                                    ins = nc.vector.tensor_tensor(dst, dst, pair, ALU.add)
                                else:
                                    ins = nc.vector.tensor_copy(dst, pair)
                            else:
                                vlink(nc.vector.tensor_tensor(S[:], S[:], ld[:, :, n:n + 1].to_broadcast([P, NT, P]), ALU.mult))
                                ins = nc.vector.tensor_tensor(S[:], S[:], pair, ALU.add)
                            ins.then_inc(*dve_evac.up())
                            dve.wait_ge(dve_evac.sem, e1 + i + 1)
                ks = ks2[0]
                sq, root, scale = ks[:, :, 0, :], ks[:, 0, 1, :], ks[:, 1, 1, :]
                m2, v2, a2 = mm_done.n, dve_out.n, act_out.n
                with nc.Block() as block:
                    @block.tensor
                    def _(pe):
                        for c in range(CT):
                            pe.wait_ge(dve_out.sem, v2 + c + 1)
                            last = nc.tensor.matmul(ps[32 * c:32 * c + 32, 0, :], ones[:, 0:32], sq[:, c, :], start=True, stop=True)
                        last.then_inc(*mm_done.up())
                        pe.wait_ge(dve_out.sem, v2 + CT + 2)
                        for c in range(CT):
                            nc.tensor.matmul(ps[:, 1 + c, :], ones[32 * c:32 * c + 1, :], scale[32 * c:32 * c + 1, :], start=True, stop=True).then_inc(*mm_done.up())

                    @block.scalar
                    def _(act):
                        act.wait_ge(dve_out.sem, v2 + CT + 1)
                        nc.scalar.activation(root, root, ACT.Sqrt).then_inc(*act_out.up())

                    @block.vector
                    def _(dve):
                        for c in range(CT):
                            nc.vector.tensor_tensor(sq[:, c, :], o[:, c, :], o[:, c, :], ALU.mult).then_inc(*dve_out.up())
                        dve.wait_ge(mm_done.sem, m2 + 1)
                        nc.vector.tensor_scalar(root, ps[:, 0, :], 1.0 / P, RMS_EPS, ALU.mult, ALU.add).then_inc(*dve_out.up())
                        dve.wait_ge(act_out.sem, a2 + 1)
                        nc.vector.reciprocal(scale, root).then_inc(*dve_out.up())
                        for c in range(CT):
                            dve.wait_ge(mm_done.sem, m2 + 2 + c)
                            vlink(nc.vector.scalar_tensor_tensor(o[:, c, :], o[:, c, :], vcol("gla_norm_w", c), ps[:, 1 + c, :], ALU.mult, ALU.mult))
                            nc.vector.tensor_tensor(o[:, c, :], o[:, c, :], og[:, c, :], ALU.mult)

        def project_residual(W, src, dst, gate=None, bias=None):
            per = UNIT_COLS // P
            n_u = KD // per
            with ExitStack() as st:
                tmp = sbuf(st, "wt", [P, 2, T])
                parts = [sbuf(st, f"src_part{j}", [P, KD, T], F32R) for j in range(2)]
                m0, v0, a0, d0 = mm_done.n, dve_evac.n, act_out.n, dve_out.n
                W.unit_end = [m0 + per * (u + 1) for u in range(n_u)]
                with nc.Block() as block:
                    @block.sync
                    def _(sp):
                        W.load(sp, W.next_unit())

                    @block.gpsimd
                    def _(pool):
                        W.split_lo(pool, W.next_unit())

                    @block.scalar
                    def _(act):
                        for k in range(KD):
                            nc.scalar.activation(parts[0][:, k, :], src[:, k, :], ACT.Copy).then_inc(*act_out.up())
                        for u in range(W.next_unit(), n_u):
                            W.split_hi(act, u)

                    @block.tensor
                    def _(pe):
                        pe.wait_ge(dve_out.sem, d0 + KD)
                        for m in range(KD):
                            if m % per == 0:
                                W.ready(pe, m // per)
                            W.product(ps[:, m, :], m // per, (m % per) * P, parts, slice(0, T)).then_inc(*mm_done.up())

                    @block.vector
                    def _(dve):
                        for k in range(KD):
                            dve.wait_ge(act_out.sem, a0 + k + 1)
                            nc.vector.tensor_tensor(parts[1][:, k, :], src[:, k, :], parts[0][:, k, :].bitcast(F32), ALU.subtract).then_inc(*dve_out.up())
                        for m in range(KD):
                            dve.wait_ge(mm_done.sem, m0 + m + 1)
                            if gate is None:
                                nc.vector.tensor_tensor(dst[:, m, :], ps[:, m, :], dst[:, m, :], ALU.add)
                            elif bias is None:
                                nc.vector.scalar_tensor_tensor(dst[:, m, :], ps[:, m, :], gate(m), dst[:, m, :], ALU.mult, ALU.add)
                            else:
                                if m >= 2:
                                    dve.wait_ge(dve_evac.sem, v0 + m - 1)
                                vlink(nc.vector.tensor_scalar(tmp[:, m % 2, :], ps[:, m, :], bias(m), gate(m), ALU.add, ALU.mult))
                                nc.vector.tensor_tensor(dst[:, m, :], tmp[:, m % 2, :], dst[:, m, :], ALU.add).then_inc(*dve_evac.up())

        def rows_of(src, hi, lo):
            m0, a0 = mm_done.n, act_out.n
            jobs = [(n, half) for n in range(KT) for half in range(2)]
            with nc.Block() as block:
                @block.tensor
                def _(pe):
                    for j, (n, half) in enumerate(jobs):
                        for c in range(4):
                            last = nc.tensor.transpose(ps[:, j, c * P:(c + 1) * P], src[:, half * 4 + c, n * P:(n + 1) * P], ident)
                        last.then_inc(*mm_done.up())

                @block.scalar
                def _(act):
                    for j, (n, half) in enumerate(jobs):
                        act.wait_ge(mm_done.sem, m0 + j + 1)
                        nc.scalar.activation(hi[:, n, half * 512:(half + 1) * 512], ps[:, j, :], ACT.Copy).then_inc(*act_out.up())

                @block.vector
                def _(dve):
                    for j, (n, half) in enumerate(jobs):
                        at = slice(half * 512, (half + 1) * 512)
                        dve.wait_ge(act_out.sem, a0 + j + 1)
                        nc.vector.tensor_tensor(lo[:, n, at], ps[:, j, :], hi[:, n, at].bitcast(F32), ALU.subtract)

        def route_first(hT, rankm, wts, over_one, over_first, over_int, load_ahead):
            E, NG, NE = N_EXP1, N_GROUPS, PER_GROUP
            n_log = NG + E
            with ExitStack() as st:
                wr = sbuf(st, "w_route", [P, KD, n_log])
                br = sbuf(st, "b_route", [1, n_log])
                lg = sbuf(st, "logits", [P, KT, n_log])
                t4 = sbuf(st, "t4", [P, KT, NG])
                og = sbuf(st, "one_group", [P, KT, NG])
                prod = sbuf(st, "prod", [P, KT, NE, NG])
                fs = sbuf(st, "fine", [P, KT, NE])
                t8 = sbuf(st, "t8", [P, KT, NE])
                o1 = sbuf(st, "one_first", [P, KT, NE])
                o2 = sbuf(st, "one_second", [P, KT, NE])
                col = {n: sbuf(st, "col_" + n, [P, KT]) for n in ("m", "pg", "m1", "m2", "e2", "c1", "c2", "t")}
                E1 = sbuf(st, "E1", [P, KT, NG, NE])
                E2 = sbuf(st, "E2", [P, KT, NG, NE])
                M = sbuf(st, "Mboth", [P, KT, E])
                cnt = sbuf(st, "cnt", [P, E])
                nov = sbuf(st, "nov", [P, E])
                gt = sbuf(st, "gt", [P, E])
                cum = sbuf(st, "cum", [P, E])
                cux = sbuf(st, "cux", [P, E])
                ov = hT[:, 0, 0:N_OVER * E].rearrange("p (o e) -> p o e", e=E)
                ofl = sbuf(st, "ofl", [P, N_OVER + 1])
                m0, a0, v0, l0 = mm_done.n, act_out.n, dve_out.n, inputs_in.n
                V = nc.vector

                def tt(o, a, b, op):
                    vlink(V.tensor_tensor(o, a, b, op))

                def over(ap, n):
                    return ap.unsqueeze(len(ap.shape)).to_broadcast(list(ap.shape) + [n])

                with nc.Block() as block:
                    @block.sync
                    def _(sp):
                        sp.dma_start(wr[:], A["moe_w_route"].rearrange("(k p) n -> p k n", p=P)).then_inc(*inputs_in.up(16))
                        sp.dma_start(br[:], A["moe_b_route"]).then_inc(*inputs_in.up(16))
                        load_ahead(sp)

                    @block.tensor
                    def _(pe):
                        pe.wait_ge(inputs_in.sem, l0 + 32)
                        for t in range(KT):
                            o = ps[:, 0, t * n_log:(t + 1) * n_log]
                            for k in range(KD):
                                nc.tensor.matmul(o, hT[:, k, t * P:(t + 1) * P], wr[:, k, :], start=(k == 0), stop=False)
                            last = nc.tensor.matmul(o, ones[0:1, :], br[:], start=False, stop=True)
                        last.then_inc(*mm_done.up())
                        pe.wait_ge(dve_out.sem, v0 + 3)
                        for t in range(KT):
                            o = ps[:, 1, t * E:(t + 1) * E]
                            for s in range(t + 1):
                                nc.tensor.matmul(o, before if s == t else ones, M[:, s, :], start=(s == 0), stop=(s == t))
                        for t in range(KT):
                            last = nc.tensor.matmul(ps[:, 2, 0:E], ones, M[:, t, :], start=(t == 0), stop=(t == KT - 1))
                        last.then_inc(*mm_done.up())

                    @block.scalar
                    def _(act):
                        act.wait_ge(dve_out.sem, v0 + 1)
                        nc.scalar.activation(t4[:], t4[:], ACT.Exp).then_inc(*act_out.up())
                        act.wait_ge(dve_out.sem, v0 + 2)
                        nc.scalar.activation(col["e2"][:], col["e2"][:], ACT.Exp).then_inc(*act_out.up())

                    @block.vector
                    def _(dve):
                        dve.wait_ge(mm_done.sem, m0 + 1)
                        vlink(V.tensor_copy(lg[:], ps[:, 0, 0:KT * n_log].rearrange("p (t n) -> p t n", t=KT)))
                        coarse = lg[:, :, 0:NG]
                        fine = lg[:, :, NG:].rearrange("p t (g e) -> p t e g", g=NG)
                        vlink(V.tensor_reduce(col["m"][:], coarse, AX.X, ALU.max))
                        V.tensor_tensor(t4[:], coarse, over(col["m"][:], NG), ALU.subtract).then_inc(*dve_out.up())
                        tt(og[:], coarse, over(col["m"][:], NG), ALU.is_equal)
                        tt(og[:], og[:], bcast(first4, KT), ALU.mult)
                        vlink(V.tensor_reduce(col["t"][:], og[:], AX.X, ALU.max))
                        tt(og[:], og[:], over(col["t"][:], NG), ALU.is_equal)
                        tt(prod[:], fine, og[:].unsqueeze(2).to_broadcast([P, KT, NE, NG]), ALU.mult)
                        vlink(V.tensor_reduce(fs[:], prod[:], AX.X, ALU.add))
                        for m, o in (("m1", o1), ("m2", o2)):
                            vlink(V.tensor_reduce(col[m][:], fs[:], AX.X, ALU.max))
                            tt(o[:], fs[:], over(col[m][:], NE), ALU.is_equal)
                            tt(o[:], o[:], bcast(first8, KT), ALU.mult)
                            vlink(V.tensor_reduce(col["t"][:], o[:], AX.X, ALU.max))
                            tt(o[:], o[:], over(col["t"][:], NE), ALU.is_equal)
                            if m == "m1":
                                vlink(V.tensor_scalar(t8[:], o1[:], -3e38, None, ALU.mult))
                                tt(fs[:], fs[:], t8[:], ALU.add)
                        V.tensor_tensor(col["e2"][:], col["m2"][:], col["m1"][:], ALU.subtract).then_inc(*dve_out.up())
                        for Eo, o in ((E1, o1), (E2, o2)):
                            tt(Eo[:], over(og[:], NE), o[:].unsqueeze(2).to_broadcast([P, KT, NG, NE]), ALU.mult)
                        e1, e2 = (x[:].rearrange("p t g e -> p t (g e)") for x in (E1, E2))
                        V.tensor_tensor(M[:], e1, e2, ALU.add).then_inc(*dve_out.up())
                        dve.wait_ge(act_out.sem, a0 + 2)
                        vlink(V.tensor_reduce(col["pg"][:], t4[:], AX.X, ALU.add))
                        vlink(V.reciprocal(col["pg"][:], col["pg"][:]))
                        vlink(V.tensor_scalar(col["c1"][:], col["e2"][:], 1.0, None, ALU.add))
                        vlink(V.reciprocal(col["c1"][:], col["c1"][:]))
                        tt(col["c1"][:], col["c1"][:], col["pg"][:], ALU.mult)
                        tt(col["c2"][:], col["c1"][:], col["e2"][:], ALU.mult)
                        tt(wts[:], e1, over(col["c1"][:], E), ALU.mult)
                        tt(e2, e2, over(col["c2"][:], E), ALU.mult)
                        tt(wts[:], wts[:], e2, ALU.add)
                        dve.wait_ge(mm_done.sem, m0 + 2)
                        vlink(V.scalar_tensor_tensor(rankm[:], ps[:, 1, 0:KT * E].rearrange("p (t e) -> p t e", t=KT), 1.0, M[:], ALU.add, ALU.mult))
                        vlink(V.tensor_scalar(rankm[:], rankm[:], -1.0, None, ALU.add))
                        vlink(V.tensor_copy(cnt[:], ps[:, 2, 0:E]))
                        vlink(V.tensor_scalar(nov[:], cnt[:], float(SLOTS), None, ALU.is_gt))
                        for j in range(2, MORE1 + 1):
                            vlink(V.tensor_scalar(gt[:], cnt[:], float(j * SLOTS), None, ALU.is_gt))
                            tt(nov[:], nov[:], gt[:], ALU.add)
                        vlink(V.tensor_tensor_scan(cum[:], ones[:, 0:E], nov[:], 0.0, ALU.mult, ALU.add))
                        tt(cux[:], cum[:], nov[:], ALU.subtract)
                        o_ax = overflows.unsqueeze(2).to_broadcast([P, N_OVER, E])
                        tt(over_one[:], bcast(cux[:], N_OVER), o_ax, ALU.is_le)
                        tt(ov[:], bcast(cum[:], N_OVER), o_ax, ALU.is_gt)
                        tt(over_one[:], over_one[:], ov[:], ALU.mult)
                        tt(ov[:], over_one[:], bcast(cux[:], N_OVER), ALU.mult)
                        vlink(V.tensor_reduce(over_first[:], ov[:], AX.X, ALU.add))
                        tt(over_first[:], overflows, over_first[:], ALU.subtract)
                        vlink(V.tensor_scalar(over_first[:], over_first[:], 1.0, float(SLOTS), ALU.add, ALU.mult))
                        tt(ov[:], over_one[:], bcast(experts, N_OVER), ALU.mult)
                        vlink(V.tensor_reduce(ofl[:, 0:N_OVER], ov[:], AX.X, ALU.add))
                        vlink(V.tensor_copy(ofl[:, N_OVER:], cum[:, E - 1:E]))
                        V.tensor_copy(over_int[:], ofl[:])

        def experts_pass(moe, tag, h_hi, h_lo, rankm, wts, n_exp, w_gate, w_up, w_down, ff, out_gate):
            n_groups = n_exp // (2 * PAIRS)
            halves = ff // 512
            steps = [(p, fh) for p in range(PAIRS) for fh in range(halves)]
            S = len(steps)
            GS = 2 * PAIRS * SLOTS
            per_bank = 512 // GS
            gather_banks = [5, 6, 7, 2]
            n_gb = KD // per_bank
            scatter_banks = 3
            wg = w_gate.rearrange("e (k p) f -> e p k f", p=P)
            wu = w_up.rearrange("e (k p) f -> e p k f", p=P)
            wd = w_down.rearrange("e (f p) d -> e p f d", p=P)
            units = [(name, s, x) for s in range(S) for name in ("gate", "up", "down") for x in range(2)]
            U = len(units)
            unit_at = {u: i for i, u in enumerate(units)}
            assert U % RING == 0
            turns = U // RING

            def scattered(fh):
                n = KD // halves
                first = min(scatter_banks, n // 2)
                tiles = list(range(fh * n, (fh + 1) * n))
                return tiles[:first], tiles[first:]

            jobs, act_jobs, dve_jobs = [], [], []
            for s, (p, fh) in enumerate(steps):
                early, late = scattered(fh)
                ends = fh == halves - 1
                jobs += [("gate", s), ("up", s)] + [("scatter", p, d) for d in early] + [("turn", s)] + [("scatter", p, d) for d in late]
                jobs += [("slot_to_token", p), ("slot_weight", p)] if ends else []
                jobs += [("down", s)]
                act_jobs += [("silu", s), ("turned", s)]
                act_jobs += [("slot_to_token", p), ("hi", p, 0), ("hi", p, 1)] if ends else []
                dve_jobs += [("hidden", s)] + [("add", p, d) for d in early + late]
                dve_jobs += [("slot_weight", p)] if ends else []
                if s == S - 1:
                    jobs += [("gather", b) for b in range(n_gb)]
                    act_jobs += [("gather", b) for b in range(0, n_gb, 2)]
                    dve_jobs += [("onehot", 0), ("weighted", 0)]
                dve_jobs += [("lo", p, 0), ("lo", p, 1)] if ends else []
                if s == S - 1:
                    dve_jobs += [("gather", b) for b in range(1, n_gb, 2)]
            job_at = {j: i + 1 for i, j in enumerate(jobs)}
            act_at = {j: i + 1 for i, j in enumerate(act_jobs)}
            dve_at = {j: i + 1 for i, j in enumerate(dve_jobs)}
            NM, NA, NV = len(jobs), len(act_jobs), len(dve_jobs)
            after_last = ("onehot", "weighted", "gather")
            M0, A0, V0 = n_gb, n_gb // 2, n_gb // 2 + 2
            M_end, A_end, V_end = n_groups * NM, n_groups * NA, n_groups * NV

            ring = sbuf(moe, tag + "_ring", [P, RING, 4096])
            G = sbuf(moe, tag + "_G", [P, KT, GS], F32R)
            Gw = sbuf(moe, tag + "_Gw", [P, KT, GS])
            XG = sbuf(moe, tag + "_XG", [P, KD, GS])
            GT = sbuf(moe, tag + "_GT", [P, T], F32R)
            w_slot = sbuf(moe, tag + "_w_slot", [P, 1])
            Y_hi = sbuf(moe, tag + "_Y_hi", [P, D], F32R)
            Y_lo = sbuf(moe, tag + "_Y_lo", [P, D], F32R)
            sil = sbuf(moe, tag + "_sil", [P, 512])
            hid = sbuf(moe, tag + "_hid", [P, 512])
            hidT = sbuf(moe, tag + "_hidT", [P, 4, P])
            unit_in = [signal(f"{tag}_unit_in{j}") for j in range(RING)]
            mm = signal(tag + "_mm")
            act_did = signal(tag + "_act")
            dve_did = signal(tag + "_dve")
            zeroed = signal(tag + "_zeroed")

            def load(sp, i, first_expert):
                name, s, x = units[i]
                p, fh = steps[s]
                e = first_expert + (2 * p + x)
                unit = ring[:, i % RING, :]
                if name == "down":
                    src = wd[bass.ds(e, 1), :, fh * 4:(fh + 1) * 4, :].rearrange("e p f d -> p (e f) d")
                    dst = unit.rearrange("p (f d) -> p f d", f=4)
                else:
                    w = wg if name == "gate" else wu
                    src = w[bass.ds(e, 1), :, :, fh * 512:(fh + 1) * 512].rearrange("e p k f -> p (e k) f")
                    dst = unit.rearrange("p (k f) -> p k f", k=KD)
                sp.dma_start(dst, src).then_inc(unit_in[i % RING].sem, 16)

            def load_ahead(sp):
                for i in range(RING):
                    load(sp, i, 0)

            def one_hots(mine, written):
                r = rankm[:, :, bass.ds(mine, 2 * PAIRS)].unsqueeze(3).to_broadcast([P, KT, 2 * PAIRS, SLOTS])
                s = slots.unsqueeze(1).unsqueeze(1).to_broadcast([P, KT, 2 * PAIRS, SLOTS])
                w = wts[:, :, bass.ds(mine, 2 * PAIRS)].unsqueeze(3).to_broadcast([P, KT, 2 * PAIRS, SLOTS])
                four = [x[:].rearrange("p t (e s) -> p t e s", s=SLOTS) for x in (G, Gw)]
                for t in range(KT):
                    ins = nc.vector.tensor_tensor(four[0][:, t], s[:, t], r[:, t], ALU.is_equal)
                ins.then_inc(dve_did.sem, 1)
                written()
                for t in range(KT):
                    ins = nc.vector.tensor_tensor(four[1][:, t], four[0][:, t].bitcast(F32), w[:, t], ALU.mult)
                ins.then_inc(dve_did.sem, 1)

            def gather():
                for b in range(n_gb):
                    for i in range(per_bank):
                        d = b * per_bank + i
                        parts = [(h, t) for h in (h_hi, h_lo) for t in range(KT)]
                        for j, (h, t) in enumerate(parts):
                            last = nc.tensor.matmul(ps[:, gather_banks[b], i * GS:(i + 1) * GS], h[:, t, d * P:(d + 1) * P], G[:, t, :],
                                                    start=(j == 0), stop=(j == len(parts) - 1))
                    last.then_inc(mm.sem, 1)

            def gathered(b):
                return (XG[:, b * per_bank:(b + 1) * per_bank, :], ps[:, gather_banks[b], :].rearrange("p (d s) -> p d s", s=GS))

            def scatter(p, d):
                bank = 5 + d % scatter_banks
                nc.tensor.matmul(ps[:, bank, :], Y_hi[:, d * P:(d + 1) * P], GT[:], start=True, stop=False)
                nc.tensor.matmul(ps[:, bank, :], Y_lo[:, d * P:(d + 1) * P], GT[:], start=False, stop=True).then_inc(mm.sem, 1)

            def add_output(d):
                bank = 5 + d % scatter_banks
                if out_gate is None:
                    ins = nc.vector.tensor_tensor(xT[:, d, :], ps[:, bank, :], xT[:, d, :], ALU.add)
                else:
                    ins = nc.vector.scalar_tensor_tensor(xT[:, d, :], ps[:, bank, :], out_gate(d), xT[:, d, :], ALU.mult, ALU.add)
                ins.then_inc(dve_did.sem, 1)

            def run():
                with nc.Block() as block:
                    @block.sync
                    def _(sp):
                        def refill(j, g):
                            i, later = (j + RING) % U, (j + RING) // U
                            name, s, _ = units[j]
                            sp.wait_ge(mm.sem, M0 + g * NM + job_at[(name, s)])
                            load(sp, i, (g + later) * (2 * PAIRS))

                        with sp.Fori(0, n_groups - 1) as g:
                            for j in range(U):
                                refill(j, g)
                        for j in range(U - RING):
                            refill(j, n_groups - 1)

                    @block.gpsimd
                    def _(pool):
                        nc.gpsimd.memset(Y_hi[:].bitcast(F32), 0.0).then_inc(zeroed.sem, 1)
                        nc.gpsimd.memset(Y_lo[:].bitcast(F32), 0.0).then_inc(zeroed.sem, 1)
                        nc.gpsimd.memset(GT[:].bitcast(F32), 0.0).then_inc(zeroed.sem, 1)

                    @block.tensor
                    def _(pe):
                        pe.wait_ge(dve_did.sem, 1)
                        gather()
                        pe.wait_ge(zeroed.sem, 3)

                        def group(g, last_group):
                            def after_act(*job):
                                pe.wait_ge(act_did.sem, A0 + g * NA + act_at[job])

                            def after_dve(*job):
                                pe.wait_ge(dve_did.sem, V0 + g * NV + dve_at[job])

                            def unit(name, s, x):
                                i = unit_at[(name, s, x)]
                                pe.wait_ge(unit_in[i % RING].sem, (g * turns + (i // RING + 1)) * 16)
                                return ring[:, i % RING, :]

                            def scatter_tiles(p, tiles):
                                for d in tiles:
                                    if d == 0 and p > 0:
                                        after_act("hi", p - 1, 1)
                                        after_dve("lo", p - 1, 1)
                                    if d >= scatter_banks:
                                        after_dve("add", p, d - scatter_banks)
                                    elif p > 0:
                                        after_dve("add", p - 1, KD - 1)
                                    scatter(p, d)

                            for s, (p, fh) in enumerate(steps):
                                early, late = scattered(fh)
                                ends = fh == halves - 1
                                for bank, name in enumerate(("gate", "up")):
                                    w = [unit(name, s, x) for x in range(2)]
                                    if p > 0 and fh == 0:
                                        if name == "gate":
                                            after_dve("slot_weight", p - 1)
                                        else:
                                            after_act("slot_to_token", p - 1)
                                    for k in range(KD):
                                        if s == 0 and name == "gate" and k % per_bank == 0:
                                            b = k // per_bank
                                            if b % 2 == 0:
                                                pe.wait_ge(act_did.sem, g * NA + (b // 2 + 1))
                                            else:
                                                pe.wait_ge(dve_did.sem, g * NV + (2 + b // 2 + 1))
                                        for x in range(2):
                                            c0 = p * P + x * SLOTS
                                            last = nc.tensor.matmul(ps[x * SLOTS:(x + 1) * SLOTS, bank, :], XG[:, k, c0:c0 + SLOTS],
                                                                    w[x][:, k * 512:(k + 1) * 512], start=(k == 0), stop=(k == KD - 1))
                                    last.then_inc(mm.sem, 1)
                                scatter_tiles(p, early)
                                after_dve("hidden", s)
                                for f in range(4):
                                    last = nc.tensor.transpose(ps[:, 2, f * P:(f + 1) * P], hid[:, f * P:(f + 1) * P], ident)
                                last.then_inc(mm.sem, 1)
                                scatter_tiles(p, late)
                                if ends:
                                    for t in range(KT):
                                        last = nc.tensor.transpose(ps[:, 1, t * P:(t + 1) * P], G[:, t, p * P:(p + 1) * P].bitcast(F32), ident)
                                    last.then_inc(mm.sem, 1)
                                    for t in range(KT):
                                        last = nc.tensor.matmul(ps[:, 0, 0:1], Gw[:, t, p * P:(p + 1) * P], ones[:, 0:1], start=(t == 0), stop=(t == KT - 1))
                                    last.then_inc(mm.sem, 1)
                                w = [unit("down", s, x) for x in range(2)]
                                after_act("turned", s)
                                for x in range(2):
                                    rows = slice(x * SLOTS, (x + 1) * SLOTS)
                                    for half in range(2):
                                        for f in range(4):
                                            last = nc.tensor.matmul(ps[rows, 3 + half, :], hidT[:, f, rows], w[x][:, f * D + half * 512:f * D + half * 512 + 512],
                                                                    start=(fh == 0 and f == 0), stop=(ends and f == 3))
                                last.then_inc(mm.sem, 1)
                            if not last_group:
                                after_dve("onehot", 0)
                                gather()

                        with pe.Fori(0, n_groups - 1) as g:
                            group(g, False)
                        group(n_groups - 1, True)
                        for d in range(KD):
                            if d >= scatter_banks:
                                pe.wait_ge(dve_did.sem, V_end + d - scatter_banks + 1)
                            else:
                                pe.wait_ge(act_did.sem, A_end)
                                pe.wait_ge(dve_did.sem, V_end)
                            scatter(0, d)

                    @block.scalar
                    def _(act):
                        for b in range(0, n_gb, 2):
                            act.wait_ge(mm.sem, b + 1)
                            to, bank = gathered(b)
                            nc.scalar.activation(to, bank, ACT.Copy).then_inc(act_did.sem, 1)

                        def group(g, last_group):
                            def after_pe(*job):
                                act.wait_ge(mm.sem, M0 + g * NM + job_at[job])

                            for job in act_jobs:
                                name, j = job[0:2]
                                if last_group and name in after_last:
                                    continue
                                if name == "silu":
                                    after_pe("gate", j)
                                    ins = nc.scalar.activation(sil[:], ps[:, 0, :], ACT.Silu)
                                elif name == "turned":
                                    after_pe("turn", j)
                                    ins = nc.scalar.activation(hidT[:], ps[:, 2, :].rearrange("p (f s) -> p f s", f=4), ACT.Copy)
                                elif name == "slot_to_token":
                                    after_pe(*job)
                                    ins = nc.scalar.activation(GT[:], ps[:, 1, :], ACT.Copy)
                                elif name == "hi":
                                    half = job[2]
                                    after_pe("down", j * halves + halves - 1)
                                    act.wait_ge(dve_did.sem, V0 + g * NV + dve_at[("slot_weight", j)])
                                    ins = nc.scalar.activation(Y_hi[:, half * 512:(half + 1) * 512], ps[:, 3 + half, :], ACT.Copy, scale=w_slot[:])
                                else:
                                    after_pe(*job)
                                    to, bank = gathered(j)
                                    ins = nc.scalar.activation(to, bank, ACT.Copy)
                                ins.then_inc(act_did.sem, 1)

                        with act.Fori(0, n_groups - 1) as g:
                            group(g, False)
                        group(n_groups - 1, True)

                    @block.vector
                    def _(dve):
                        def own(n):
                            return lambda: dve.wait_ge(dve_did.sem, n)

                        one_hots(0, own(1))
                        for b in range(1, n_gb, 2):
                            dve.wait_ge(mm.sem, b + 1)
                            to, bank = gathered(b)
                            nc.vector.tensor_copy(to, bank).then_inc(dve_did.sem, 1)

                        def group(g, last_group):
                            def after_pe(*job):
                                dve.wait_ge(mm.sem, M0 + g * NM + job_at[job])

                            for job in dve_jobs:
                                name, j = job[0:2]
                                if last_group and name in after_last:
                                    continue
                                if name == "hidden":
                                    after_pe("up", j)
                                    dve.wait_ge(act_did.sem, A0 + g * NA + act_at[("silu", j)])
                                    nc.vector.tensor_tensor(hid[:], ps[:, 1, :], sil[:], ALU.mult).then_inc(dve_did.sem, 1)
                                elif name == "add":
                                    after_pe("scatter", j, job[2])
                                    add_output(job[2])
                                elif name == "slot_weight":
                                    after_pe(*job)
                                    nc.vector.tensor_copy(w_slot[:], ps[:, 0, 0:1]).then_inc(dve_did.sem, 1)
                                elif name == "onehot":
                                    one_hots(g * (2 * PAIRS) + 2 * PAIRS, own(V0 + g * NV + dve_at[job]))
                                elif name == "weighted":
                                    pass
                                elif name == "lo":
                                    half = job[2]
                                    dve.wait_ge(act_did.sem, A0 + g * NA + act_at[("hi", j, half)])
                                    at = slice(half * 512, (half + 1) * 512)
                                    nc.vector.scalar_tensor_tensor(Y_lo[:, at], ps[:, 3 + half, :], w_slot[:], Y_hi[:, at].bitcast(F32), ALU.mult, ALU.subtract).then_inc(dve_did.sem, 1)
                                else:
                                    after_pe(*job)
                                    to, bank = gathered(j)
                                    nc.vector.tensor_copy(to, bank).then_inc(dve_did.sem, 1)

                        with dve.Fori(0, n_groups - 1) as g:
                            group(g, False)
                        group(n_groups - 1, True)
                        for d in range(KD):
                            dve.wait_ge(mm.sem, M_end + d + 1)
                            add_output(d)

            return load_ahead, run

        def overflow_pass(h_hi, h_lo, rankm, wts, over_one, over_first, over_int):
            wg = A["moe_w_gate"].rearrange("e (k p) f -> e p k f", p=P)
            wu = A["moe_w_up"].rearrange("e (k p) f -> e p k f", p=P)
            wd = A["moe_w_down"].rearrange("e (f p) d -> e p f d", p=P)
            with ExitStack() as st:
                wgb = sbuf(st, "ov_wg", [P, KD, 512])
                wub = sbuf(st, "ov_wu", [P, KD, 512])
                wdb = sbuf(st, "ov_wd", [P, 4, D])
                sel = sbuf(st, "ov_sel", [P, KT, N_EXP1])
                r_o = sbuf(st, "ov_r", [P, KT])
                w_o = sbuf(st, "ov_w", [P, KT])
                G = sbuf(st, "ov_G", [P, KT, P])
                X = sbuf(st, "ov_X", [P, KD, SLOTS])
                GT = sbuf(st, "ov_GT", [SLOTS, T])
                hid = sbuf(st, "ov_hid", [P, 512])
                hidT = sbuf(st, "ov_hidT", [P, 4, SLOTS])
                Y = sbuf(st, "ov_Y", [SLOTS, D])
                w_here = signal("ov_w_here")
                mm = signal("ov_mm")
                dve_did = signal("ov_dve")
                silu = signal("ov_silu")
                v_steps = ["sel", "r", "sel2", "w", "shift", "G0", "G1", "G2", "G3", "X", "W0", "W1", "W2", "W3", "GT", "hid", "hidT", "Y0", "Y1"]
                v_steps += [f"out{d}" for d in range(KD)]
                v_at = {n: i + 1 for i, n in enumerate(v_steps)}
                p_steps = ["gather", "gt", "gate", "up", "turn", "down"] + [f"out{d}" for d in range(KD)]
                p_at = {n: i + 1 for i, n in enumerate(p_steps)}
                NV, NP = len(v_steps), len(p_steps)

                with nc.Block() as block:
                    @block.gpsimd
                    def _(pool):
                        nc.gpsimd.memset(G[:], 0.0).then_inc(dve_did.sem, 1)
                        nc.gpsimd.memset(hid[:], 0.0).then_inc(mm.sem, 1)

                def blocks(eng):
                    return eng.value_load(over_int[0:1, N_OVER:N_OVER + 1], min_val=0, max_val=N_OVER)

                with nc.Block() as block:
                    @block.sync
                    def _(sp):
                        n = blocks(sp)
                        with sp.If(n > 0):
                            with sp.Fori(0, N_OVER) as o:
                                with sp.If(o < n):
                                    e = sp.value_load(over_int[0:1, bass.ds(o, 1)], min_val=0, max_val=N_EXP1 - 1)
                                    sp.wait_ge(mm.sem, o * NP + 1)
                                    sp.dma_start(wgb[:], wg[bass.ds(e, 1)].rearrange("e p k f -> p (e k) f")).then_inc(w_here.sem, 16)
                                    sp.dma_start(wub[:], wu[bass.ds(e, 1)].rearrange("e p k f -> p (e k) f")).then_inc(w_here.sem, 16)
                                    sp.dma_start(wdb[:], wd[bass.ds(e, 1)].rearrange("e p f d -> p (e f) d")).then_inc(w_here.sem, 16)

                    @block.tensor
                    def _(pe):
                        n = blocks(pe)
                        with pe.If(n > 0):
                            with pe.Fori(0, N_OVER) as o:
                                with pe.If(o < n):
                                    def after(step):
                                        pe.wait_ge(dve_did.sem, o * NV + v_at[step] + 1)

                                    after("G3")
                                    for d in range(KD):
                                        parts = [(h, t) for h in (h_hi, h_lo) for t in range(KT)]
                                        for j, (h, t) in enumerate(parts):
                                            last = nc.tensor.matmul(ps[:, 0, d * SLOTS:(d + 1) * SLOTS], h[:, t, d * P:(d + 1) * P].bitcast(F32), G[:, t, 0:SLOTS],
                                                                    start=(j == 0), stop=(j == len(parts) - 1))
                                    last.then_inc(mm.sem, 1)
                                    after("W3")
                                    for t in range(KT):
                                        last = nc.tensor.transpose(ps[:, 1, t * P:(t + 1) * P], G[:, t, :], ident)
                                    last.then_inc(mm.sem, 1)
                                    pe.wait_ge(w_here.sem, o * 48 + 48)
                                    for bank, w in ((2, wgb), (3, wub)):
                                        for k in range(KD):
                                            last = nc.tensor.matmul(ps[0:SLOTS, bank, :], X[:, k, :], w[:, k, :], start=(k == 0), stop=(k == KD - 1))
                                        last.then_inc(mm.sem, 1)
                                    after("hid")
                                    for f in range(4):
                                        last = nc.tensor.transpose(ps[:, 4, f * P:(f + 1) * P], hid[:, f * P:(f + 1) * P], ident)
                                    last.then_inc(mm.sem, 1)
                                    after("hidT")
                                    for half in range(2):
                                        for f in range(4):
                                            last = nc.tensor.matmul(ps[0:SLOTS, 5 + half, :], hidT[:, f, :], wdb[:, f, half * 512:(half + 1) * 512], start=(f == 0), stop=(f == 3))
                                    last.then_inc(mm.sem, 1)
                                    after("Y1")
                                    for d in range(KD):
                                        nc.tensor.matmul(ps[:, d, :], Y[:, d * P:(d + 1) * P], GT[:], start=True, stop=True).then_inc(mm.sem, 1)

                    @block.scalar
                    def _(act):
                        n = blocks(act)
                        with act.If(n > 0):
                            with act.Fori(0, N_OVER) as o:
                                with act.If(o < n):
                                    act.wait_ge(mm.sem, o * NP + p_at["gate"] + 1)
                                    act.wait_ge(dve_did.sem, o * NV + 1)
                                    nc.scalar.activation(hid[0:SLOTS, :], ps[0:SLOTS, 2, :], ACT.Silu).then_inc(silu.sem, 1)

                    @block.vector
                    def _(dve):
                        n = blocks(dve)
                        with dve.If(n > 0):
                            with dve.Fori(0, N_OVER) as o:
                                with dve.If(o < n):
                                    V = nc.vector

                                    def done(step, ins):
                                        ins.then_inc(dve_did.sem, 1)
                                        if step != v_steps[-1]:
                                            dve.wait_ge(dve_did.sem, o * NV + v_at[step] + 1)

                                    def after(step):
                                        dve.wait_ge(mm.sem, o * NP + p_at[step] + 1)

                                    dve.wait_ge(dve_did.sem, o * NV + 1)
                                    one = over_one[:, bass.ds(o, 1), :].to_broadcast([P, KT, N_EXP1])
                                    done("sel", V.tensor_tensor(sel[:], rankm[:], one, ALU.mult))
                                    done("r", V.tensor_reduce(r_o[:], sel[:], AX.X, ALU.add))
                                    done("sel2", V.tensor_tensor(sel[:], wts[:], one, ALU.mult))
                                    done("w", V.tensor_reduce(w_o[:], sel[:], AX.X, ALU.add))
                                    done("shift", V.tensor_tensor(r_o[:], r_o[:], over_first[:, bass.ds(o, 1)].to_broadcast([P, KT]), ALU.subtract))
                                    for t in range(KT):
                                        done(f"G{t}", V.tensor_scalar(G[:, t, 0:SLOTS], slots, r_o[:, t:t + 1], None, ALU.is_equal))
                                    after("gather")
                                    done("X", V.tensor_copy(X[:], ps[:, 0, :].rearrange("p (k s) -> p k s", k=KD)))
                                    for t in range(KT):
                                        done(f"W{t}", V.tensor_scalar(G[:, t, 0:SLOTS], G[:, t, 0:SLOTS], w_o[:, t:t + 1], None, ALU.mult))
                                    after("gt")
                                    done("GT", V.tensor_copy(GT[:], ps[0:SLOTS, 1, :]))
                                    after("up")
                                    dve.wait_ge(silu.sem, o + 1)
                                    done("hid", V.tensor_tensor(hid[0:SLOTS, :], ps[0:SLOTS, 3, :], hid[0:SLOTS, :], ALU.mult))
                                    after("turn")
                                    done("hidT", V.tensor_copy(hidT[:], ps[:, 4, :].rearrange("p (f s) -> p f s", f=4)[:, :, 0:SLOTS]))
                                    after("down")
                                    for half in range(2):
                                        done(f"Y{half}", V.tensor_copy(Y[:, half * 512:(half + 1) * 512], ps[0:SLOTS, 5 + half, :]))
                                    for d in range(KD):
                                        after(f"out{d}")
                                        done(f"out{d}", V.tensor_tensor(xT[:, d, :], ps[:, d, :], xT[:, d, :], ALU.add))

        def even_weights(st, col_tiles):
            w, per = A["w_in_2"].rearrange("(k p) n -> p k n", p=P), UNIT_COLS // P
            return SplitWeights(st, [[(0, w[:, :, c * P:c * P + UNIT_COLS])] for c in col_tiles[::per]])

        def project_even(W, parts, n_tok, col_tiles, gate, xa, hy, side=None):
            per = UNIT_COLS // P
            n = len(col_tiles)
            n_u = n // per
            conv = [i for i in range(n) if col_tiles[i] >= 4]
            nth = {i: j for j, i in enumerate(conv)}
            with ExitStack() as st:
                pad = sbuf(st, "pad_e", [P, 3, n_tok + 3])
                m0, a0, v0, p0 = mm_done.n, act_evac.n, dve_out.n, pool_out.n
                W.unit_end = [m0 + per * (u + 1) for u in range(n_u)]
                M = Modulation(st, *side, n, lambda q: q if q < 4 else 4 + (5 * (q - 4)) // 3, lambda q: (q if q < 4 else 4 + (5 * (q - 4)) // 3) + 3) if side else None
                with nc.Block() as block:
                    @block.sync
                    def _(sp):
                        if M:
                            M.load(sp)

                    @block.gpsimd
                    def _(pool):
                        nc.gpsimd.memset(pad[:], 0.0).then_inc(*pool_out.up())
                        W.split_lo(pool, W.next_unit())

                    @block.tensor
                    def _(pe):
                        for i in range(n):
                            if i % per == 0:
                                W.ready(pe, i // per)
                            if i >= MOD_BANK:
                                pe.wait_ge(act_evac.sem, a0 + i - MOD_BANK + 1)
                            W.product(ps[:, i % MOD_BANK, 0:n_tok], i // per, (i % per) * P, parts, slice(0, n_tok)).then_inc(*mm_done.up())
                            if M:
                                M.tensor(pe, i)

                    @block.scalar
                    def _(act):
                        W.load(act, W.next_unit(), 2)
                        if M:
                            M.silu_of_c()
                        for u in range(W.next_unit(), 2):
                            W.split_hi(act, u)
                        W.load_unit(act, 2)
                        act.wait_ge(pool_out.sem, p0 + 1)
                        for i, c in enumerate(col_tiles):
                            act.wait_ge(mm_done.sem, m0 + i + 1)
                            if c < 4:
                                ins = nc.scalar.activation(gate[:, c, :], ps[:, i % MOD_BANK, 0:n_tok], ACT.Gelu_apprx_tanh)
                            else:
                                if nth[i] >= 3:
                                    act.wait_ge(dve_out.sem, v0 + nth[i] - 2)
                                ins = nc.scalar.activation(pad[:, nth[i] % 3, 1:n_tok + 1], ps[:, i % MOD_BANK, 0:n_tok], ACT.Copy)
                            ins.then_inc(*act_evac.up())
                            if i % per == per - 1:
                                W.load_unit(act, i // per + 3)
                                W.split_hi(act, i // per + 2)

                    @block.vector
                    def _(dve):
                        for i in range(n):
                            if i not in conv:
                                if M:
                                    M.vector(dve, i)
                                continue
                            c = col_tiles[i]
                            dve.wait_ge(act_evac.sem, a0 + i + 1)
                            if c < 8:
                                dst, taps, wt, bias, t0, n_t = xa[:, c - 4, :], 4, "conv_a_w_2", "conv_a_b_2", c - 4, 4
                            else:
                                dst, taps, wt, bias, t0, n_t = hy[:, c - 8, :], 3, "conv_b_w_2", "conv_b_b_2", c - 8, 12
                            b = nth[i] % 3
                            vlink(nc.vector.tensor_scalar(dst, pad[:, b, 0:n_tok], vcol(wt, t0), vcol(bias, t0), ALU.mult, ALU.add))
                            for k in range(1, taps):
                                ins = nc.vector.scalar_tensor_tensor(dst, pad[:, b, k:n_tok + k], vcol(wt, k * n_t + t0), dst, ALU.mult, ALU.add)
                                if k < taps - 1:
                                    vlink(ins)
                            ins.then_inc(*dve_out.up())
                            if M:
                                M.vector(dve, i)
                        if M:
                            M.finish(dve)

        def lru_rates(rate, gates):
            with ExitStack() as st:
                e = sbuf(st, "rate_e", [P, 8])
                lam = vcol("lru_lam_2", 0, 8)
                a0, l0 = act_out.n, inputs_in.n
                with nc.Block() as block:
                    @block.sync
                    def _(sp):
                        sp.dma_start(gates[:], A["lru_gates"]).then_inc(*inputs_in.up(16))
                        sp.wait_ge(inputs_in.sem, l0 + 16)

                    @block.scalar
                    def _(act):
                        alink(nc.scalar.activation(e[:], lam, ACT.Abs))
                        alink(nc.scalar.activation(e[:], e[:], ACT.Exp, scale=-1.0))
                        nc.scalar.activation(e[:], e[:], ACT.Ln, bias=1.0).then_inc(*act_out.up())

                    @block.vector
                    def _(dve):
                        dve.wait_ge(act_out.sem, a0 + 1)
                        vlink(nc.vector.scalar_tensor_tensor(e[:], lam, 0.0, e[:], ALU.min, ALU.subtract))
                        nc.vector.tensor_scalar(rate[:, 0, :], e[:], LRU_C, None, ALU.mult)
                        nc.vector.tensor_scalar(rate[:, 1, :], e[:], -LRU_C, None, ALU.mult)

        def lru_scan(xa, n_tok, gates, rate, start, final, total):
            n_j = 2 * CT
            with ExitStack() as st:
                r = sbuf(st, "lru_r", [P, n_j, n_tok])
                i_ = sbuf(st, "lru_i", [P, n_j, n_tok])
                th = sbuf(st, "lru_th", [P, n_j, n_tok])
                h = sbuf(st, "lru_h", [P, n_j, n_tok])
                m0, a0, v0, p0 = mm_done.n, act_out.n, dve_out.n, pool_out.n
                with nc.Block() as block:
                    @block.tensor
                    def _(pe):
                        for q in range(2):
                            for j in range(n_j):
                                if q == 1:
                                    pe.wait_ge(act_out.sem, a0 + j + 1)
                                nc.tensor.matmul(ps[:, j, 0:n_tok], gates[:, q, j // CT, j % CT, :], xa[:, j % CT, :], start=True, stop=True).then_inc(*mm_done.up())

                    @block.scalar
                    def _(act):
                        for q, (dst, bias) in enumerate(((r, "lru_br_2"), (i_, "lru_bi_2"))):
                            for j in range(n_j):
                                act.wait_ge(mm_done.sem, m0 + q * n_j + j + 1)
                                nc.scalar.activation(dst[:, j, :], ps[:, j, 0:n_tok], ACT.Sigmoid, bias=vcol(bias, j)).then_inc(*act_out.up())
                        act.wait_ge(act_out.sem, act_out.n)
                        for j in range(n_j):
                            nc.scalar.activation(th[:, j, :], r[:, j, :], ACT.Tanh, scale=rate[:, 1, j:j + 1]).then_inc(*act_out.up())
                        act.wait_ge(act_out.sem, act_out.n)
                        for j in range(n_j):
                            nc.scalar.activation(r[:, j, :], r[:, j, :], ACT.Exp, scale=rate[:, 0, j:j + 1]).then_inc(*act_out.up())
                        for j in range(n_j):
                            act.wait_ge(dve_out.sem, v0 + j + 1)
                            nc.scalar.activation(th[:, j, :], th[:, j, :], ACT.Sqrt).then_inc(*act_out.up())

                    @block.vector
                    def _(dve):
                        for j in range(n_j):
                            dve.wait_ge(act_out.sem, a0 + 3 * n_j + j + 1)
                            vlink(nc.vector.tensor_tensor(h[:, j, :], r[:, j, :], r[:, j, :], ALU.mult))
                            nc.vector.scalar_tensor_tensor(th[:, j, :], h[:, j, :], 1.0, th[:, j, :], ALU.add, ALU.mult).then_inc(*dve_out.up())
                        for j in range(n_j):
                            dve.wait_ge(pool_out.sem, p0 + j + 1)
                            dve.wait_ge(act_out.sem, a0 + 4 * n_j + j + 1)
                            vlink(nc.vector.tensor_tensor(i_[:, j, :], i_[:, j, :], th[:, j, :], ALU.mult))
                            s0 = 0.0 if start is None else start[:, j:j + 1]
                            way = slice(None, None, -1) if j >= CT else slice(None)
                            nc.vector.tensor_tensor_scan(h[:, j, way], r[:, j, way], i_[:, j, way], s0, ALU.mult, ALU.add).then_inc(*dve_out.up())
                            if final is not None:
                                end = 0 if j >= CT else n_tok - 1
                                dve.wait_ge(dve_out.sem, v0 + n_j + j + 1)
                                nc.vector.tensor_copy(final[:, j:j + 1], h[:, j, end:end + 1])

                    @block.gpsimd
                    def _(pool):
                        for j in range(n_j):
                            pool.wait_ge(act_out.sem, a0 + n_j + j + 1)
                            nc.gpsimd.tensor_tensor(i_[:, j, :], i_[:, j, :], xa[:, j % CT, :], ALU.mult).then_inc(*pool_out.up())
                        if total is not None:
                            for c in range(CT):
                                pool.wait_ge(dve_out.sem, v0 + n_j + CT + c + 1)
                                nc.gpsimd.tensor_tensor(h[:, CT + c, :], h[:, CT + c, :], h[:, c, :], ALU.add).then_inc(*pool_out.up())
                                pool.wait_ge(pool_out.sem, p0 + n_j + c + 1)
                                nc.gpsimd.tensor_tensor(total[:, c, :], total[:, c, :], h[:, CT + c, :], ALU.mult)

        HF = KT // 2

        def half_spectrum(spec, src, f, q):
            for odd in range(2):
                for t in range(HF):
                    k = odd * HF + t
                    last = nc.tensor.matmul(ps[:, 2 * (2 * f + q) + odd, :], spec[:, k, q * (T // 2) + f * P:q * (T // 2) + (f + 1) * P], src[:, k, :],
                                            start=(t == 0), stop=(t == HF - 1))
            last.then_inc(*mm_done.up())

        def whole_spectrum(low, mirror, even, odd, q):
            nc.vector.tensor_tensor(low, even, odd, ALU.add)
            if q == 0:
                return nc.vector.tensor_tensor(mirror, even, odd, ALU.subtract)
            return nc.vector.tensor_tensor(mirror, odd, even, ALU.subtract)

        def hyena_filters(spec, Kc, Ks, inv, z_first, values):
            with ExitStack() as st:
                z = sbuf(st, "f_z", [FILTER_EMB, T])
                w1 = sbuf(st, "f_w1", [FILTER_EMB, FILTER_HIDDEN])
                w2 = sbuf(st, "f_w2", [FILTER_HIDDEN, FILTER_HIDDEN])
                w3 = sbuf(st, "f_w3", [FILTER_HIDDEN + 1, 4 * HYENA_WIDTH])
                win = sbuf(st, "f_win", [P, KT, HYENA_WIDTH])
                x = sbuf(st, "f_x", [FILTER_HIDDEN, T])
                turns = sbuf(st, "f_turns", [FILTER_HIDDEN, T])
                hid = sbuf(st, "f_hid", [FILTER_HIDDEN + 1, T])
                even = sbuf(st, "f_even", [P, 2, HYENA_WIDTH])
                both = sbuf(st, "f_both", [P, KT, 2, HYENA_WIDTH])
                fsum = sbuf(st, "f_sum", [P, KT, HYENA_WIDTH])
                fdiff = sbuf(st, "f_diff", [P, KT, HYENA_WIDTH])
                m0, a0, v0, l0, e0, d0 = mm_done.n, act_out.n, dve_out.n, inputs_in.n, act_evac.n, dve_evac.n
                H = FILTER_HIDDEN
                hidden_in = signal("hidden_in")
                with nc.Block() as block:
                    @block.sync
                    def _(sp):
                        for dst, src in ((z[:], A["hy_z"]), (w1[:], A["filt_w1_2"]), (w2[:], A["filt_w2_2"])):
                            sp.dma_start(dst, src).then_inc(*hidden_in.up(16))
                        for dst, src in ((w3[:], A["filt_w3_2"]), (win[:], A["hy_window"].rearrange("(t p) c -> p t c", p=P)),
                                         (spec[:], A["hy_spectrum"].rearrange("(t p) f -> p t f", p=P))):
                            sp.dma_start(dst, src).then_inc(*inputs_in.up(16))
                        sp.dma_start(inv[:], A["hy_inverse"].rearrange("(f p) t -> p f t", p=P)).then_inc(*inputs_in.up(16))
                        sp.wait_ge(inputs_in.sem, l0 + 64)

                    @block.gpsimd
                    def _(pool):
                        nc.gpsimd.tensor_copy(z_first, values)

                    @block.tensor
                    def _(pe):
                        pe.wait_ge(hidden_in.sem, 48)
                        nc.tensor.matmul(ps[0:H, 0, :], w1[:], z[:], start=True, stop=True).then_inc(*mm_done.up())
                        pe.wait_ge(act_out.sem, a0 + 1)
                        nc.tensor.matmul(ps[0:H, 1, :], w2[:], hid[0:H, :], start=True, stop=True).then_inc(*mm_done.up())
                        pe.wait_ge(act_out.sem, a0 + 2)
                        pe.wait_ge(dve_out.sem, v0 + 3)
                        pe.wait_ge(inputs_in.sem, l0 + 64)
                        for o in range(HYENA_ORDER):
                            if o > 0:
                                pe.wait_ge(dve_evac.sem, d0 + 4 * o)
                            for t in range(KT):
                                for q in range(2):
                                    nc.tensor.matmul(ps[:, 2 * t + q, :], hid[:, t * P:(t + 1) * P], w3[:, (2 * o + q) * 512:(2 * o + q + 1) * 512],
                                                     start=True, stop=True).then_inc(*mm_done.up())
                            pe.wait_ge(dve_out.sem, v0 + 4 + o)
                            for f in range(HF):
                                for q, src in enumerate((fsum, fdiff)):
                                    half_spectrum(spec, src, f, q)

                    @block.scalar
                    def _(act):
                        for j in range(2):
                            act.wait_ge(dve_out.sem, v0 + j + 1)
                            nc.scalar.activation(hid[0:H, :], x[:], ACT.Sin).then_inc(*act_out.up())
                        for o in range(HYENA_ORDER):
                            for f in range(HF):
                                for q in range(2):
                                    i = 2 * f + q
                                    act.wait_ge(mm_done.sem, m0 + 2 + 12 * o + 8 + i + 1)
                                    if 4 * o + i >= 2:
                                        act.wait_ge(dve_evac.sem, d0 + 4 * o + i - 1)
                                    nc.scalar.activation(even[:, i % 2, :], ps[:, 2 * i, :], ACT.Copy).then_inc(*act_evac.up())

                    @block.vector
                    def _(dve):
                        V = nc.vector
                        for j, bias in enumerate(("filt_b1_2", "filt_b2_2")):
                            dve.wait_ge(mm_done.sem, m0 + j + 1)
                            vlink(V.tensor_scalar(x[:], ps[0:H, j, :], vcol(bias, 0)[0:H], vcol("filt_freq_2", j)[0:H], ALU.add, ALU.mult))
                            vlink(V.tensor_scalar(turns[:], x[:], 1.0 / (2.0 * math.pi), ROUND, ALU.mult, ALU.add))
                            vlink(V.tensor_scalar(turns[:], turns[:], -ROUND, None, ALU.add))
                            vlink(V.scalar_tensor_tensor(x[:], turns[:], -TURN_HI, x[:], ALU.mult, ALU.add))
                            vlink(V.scalar_tensor_tensor(x[:], turns[:], -TURN_LO, x[:], ALU.mult, ALU.add))
                            V.tensor_scalar(x[:], x[:], -PI_IN, PI_IN, ALU.max, ALU.min).then_inc(*dve_out.up())
                            dve.wait_ge(act_out.sem, a0 + j + 1)
                        V.memset(hid[H:H + 1, :], 1.0).then_inc(*dve_out.up())
                        for o in range(HYENA_ORDER):
                            for t in range(KT):
                                for q in range(2):
                                    dve.wait_ge(mm_done.sem, m0 + 2 + 12 * o + 2 * t + q + 1)
                                    ins = V.tensor_tensor(both[:, t, q, :], ps[:, 2 * t + q, :], win[:, t, :], ALU.mult)
                            vlink(ins)
                            vlink(V.memset(both[0:1, 0, 1, :], 0.0))
                            if o > 0:
                                dve.wait_ge(mm_done.sem, m0 + 2 + 12 * o)
                            V.tensor_tensor(fsum[:], both[:, :, 0, :], both[:, :, 1, :], ALU.add)
                            vlink_n = V.tensor_tensor(fdiff[:], both[:, :, 0, :], both[:, :, 1, :], ALU.subtract)
                            vlink_n.then_inc(*dve_out.up())
                            dve.wait_ge(dve_out.sem, v0 + 4 + o)
                            for f in range(HF):
                                for q, dst in enumerate((Kc, Ks)):
                                    i = 2 * f + q
                                    dve.wait_ge(act_evac.sem, e0 + 4 * o + i + 1)
                                    whole_spectrum(dst[:, f, o, :], dst[:, HF + f, o, :], even[:, i % 2, :], ps[:, 2 * i + 1, :], q).then_inc(*dve_evac.up())

        def hyena_conv(o, z, gates, spec, inv, Kc, Ks):
            with ExitStack() as st:
                z_tok = sbuf(st, "hz_tok", [P, KT, HYENA_WIDTH])
                even = sbuf(st, "h_even", [P, 2, HYENA_WIDTH])
                U = sbuf(st, "hU", [P, 2, KT, HYENA_WIDTH])
                Y = sbuf(st, "hY", [P, 2, KT, HYENA_WIDTH])
                t1 = sbuf(st, "ht1", [P, KT, 2, HYENA_WIDTH])
                B = sbuf(st, "hB", [P, 2, 2, HF, HYENA_WIDTH])
                to_tokens([(z[:, :, odd::2], z_tok[:, odd * HF:(odd + 1) * HF, :]) for odd in range(2)])
                m0, a0, v0, e0, p0 = mm_done.n, act_evac.n, dve_out.n, dve_evac.n, pool_out.n
                with nc.Block() as block:
                    @block.tensor
                    def _(pe):
                        for f in range(HF):
                            for q in range(2):
                                half_spectrum(spec, z_tok, f, q)
                        pe.wait_ge(dve_evac.sem, e0 + 2 * HF)
                        pe.wait_ge(dve_out.sem, v0 + HF)
                        pe.wait_ge(pool_out.sem, p0 + 2 * HF)
                        for c in range(CT):
                            for odd in range(2):
                                n = T // 2
                                for i in range(2 * HF):
                                    last = nc.tensor.matmul(ps[:, 2 * c + odd, 0:n], B[:, odd, i // HF, i % HF, c * P:(c + 1) * P], inv[:, i, odd * n:(odd + 1) * n],
                                                            start=(i == 0), stop=(i == 2 * HF - 1))
                            last.then_inc(*mm_done.up())

                    @block.scalar
                    def _(act):
                        for i in range(2 * HF):
                            act.wait_ge(mm_done.sem, m0 + i + 1)
                            if i >= 2:
                                act.wait_ge(dve_evac.sem, e0 + i - 1)
                            nc.scalar.activation(even[:, i % 2, :], ps[:, 2 * i, :], ACT.Copy).then_inc(*act_evac.up())

                    def product(eng, f):
                        eng.tensor_tensor(Y[:, 0, f, :], U[:, 0, f, :], Kc[:, f, o, :], ALU.mult)
                        eng.tensor_tensor(t1[:, f, 0, :], U[:, 1, f, :], Ks[:, f, o, :], ALU.mult)
                        eng.tensor_tensor(Y[:, 1, f, :], U[:, 0, f, :], Ks[:, f, o, :], ALU.mult)
                        return eng.tensor_tensor(t1[:, f, 1, :], U[:, 1, f, :], Kc[:, f, o, :], ALU.mult)

                    def collect(eng, f):
                        eng.tensor_tensor(Y[:, 0, f, :], Y[:, 0, f, :], t1[:, f, 0, :], ALU.subtract)
                        return eng.tensor_tensor(Y[:, 1, f, :], Y[:, 1, f, :], t1[:, f, 1, :], ALU.add)

                    @block.gpsimd
                    def _(pool):
                        for f in range(HF):
                            pool.wait_ge(dve_evac.sem, e0 + 2 * f + 2)
                            product(nc.gpsimd, HF + f).then_inc(*pool_out.up())
                            pool.wait_ge(pool_out.sem, p0 + 2 * f + 1)
                            collect(nc.gpsimd, HF + f).then_inc(*pool_out.up())

                    @block.vector
                    def _(dve):
                        V = nc.vector
                        for f in range(HF):
                            for q in range(2):
                                i = 2 * f + q
                                dve.wait_ge(act_evac.sem, a0 + i + 1)
                                whole_spectrum(U[:, q, f, :], U[:, q, HF + f, :], even[:, i % 2, :], ps[:, 2 * i + 1, :], q).then_inc(*dve_evac.up())
                            dve.wait_ge(dve_evac.sem, e0 + 2 * f + 2)
                            vlink(product(V, f))
                            vlink(collect(V, f))
                        for f in range(HF):
                            dve.wait_ge(pool_out.sem, p0 + 2 * f + 2)
                            V.tensor_tensor(B[:, 0, 0, f, :], Y[:, 0, f, :], Y[:, 0, HF + f, :], ALU.add)
                            V.tensor_tensor(B[:, 0, 1, f, :], Y[:, 1, f, :], Y[:, 1, HF + f, :], ALU.subtract)
                            V.tensor_tensor(B[:, 1, 0, f, :], Y[:, 0, f, :], Y[:, 0, HF + f, :], ALU.subtract)
                            V.tensor_tensor(B[:, 1, 1, f, :], Y[:, 1, f, :], Y[:, 1, HF + f, :], ALU.add).then_inc(*dve_out.up())
                        for c in range(CT):
                            dve.wait_ge(mm_done.sem, m0 + 2 * HF + c + 1)
                            for odd in range(2):
                                at = z[:, c, odd::2]
                                ins = V.scalar_tensor_tensor(at, at, vcol("filt_bias_2", 4 * o + c), ps[:, 2 * c + odd, 0:T // 2], ALU.mult, ALU.add)
                            vlink(ins)
                            V.tensor_tensor(z[:, c, :], z[:, c, :], gates[:, 4 * o + c, :], ALU.mult)

        def route_choice(l, hT, rankm, wts, load_ahead):
            E = N_EXP2
            with ExitStack() as st:
                wr = sbuf(st, "c_wr", [P, KD, E])
                lg = sbuf(st, "c_lg", [P, KT, E])
                col = sbuf(st, "c_col", [P, KT])
                work = [sbuf(st, f"c_work{j}", [E, T]) for j in range(2)]
                top = sbuf(st, "c_top", [E, 8])
                sel = sbuf(st, "c_sel", [E, T])
                rk = sbuf(st, "c_rk", [E, T])
                m0, a0, v0, l0 = mm_done.n, act_out.n, dve_out.n, inputs_in.n
                with nc.Block() as block:
                    @block.sync
                    def _(sp):
                        sp.dma_start(wr[:], A["router_2"][l].rearrange("(k p) e -> p k e", p=P)).then_inc(*inputs_in.up(16))
                        load_ahead(sp)

                    @block.tensor
                    def _(pe):
                        pe.wait_ge(inputs_in.sem, l0 + 16)
                        for t in range(KT):
                            for k in range(KD):
                                last = nc.tensor.matmul(ps[:, 0, t * E:(t + 1) * E], hT[:, k, t * P:(t + 1) * P], wr[:, k, :], start=(k == 0), stop=(k == KD - 1))
                        last.then_inc(*mm_done.up())
                        pe.wait_ge(dve_out.sem, v0 + 2)
                        for t in range(KT):
                            last = nc.tensor.transpose(ps[0:E, 1, t * P:(t + 1) * P], wts[:, t, :], ident)
                        last.then_inc(*mm_done.up())
                        pe.wait_ge(dve_out.sem, v0 + 3)
                        for t in range(KT):
                            last = nc.tensor.transpose(ps[:, 2, t * E:(t + 1) * E], rk[:, t * P:(t + 1) * P], ident[0:E, 0:E])
                        last.then_inc(*mm_done.up())

                    @block.scalar
                    def _(act):
                        act.wait_ge(dve_out.sem, v0 + 1)
                        nc.scalar.activation(lg[:], lg[:], ACT.Exp).then_inc(*act_out.up())

                    @block.vector
                    def _(dve):
                        V = nc.vector
                        dve.wait_ge(mm_done.sem, m0 + 1)
                        logits = ps[:, 0, 0:KT * E].rearrange("p (t e) -> p t e", t=KT)
                        vlink(V.tensor_reduce(col[:], logits, AX.X, ALU.max))
                        V.tensor_tensor(lg[:], logits, col[:].unsqueeze(2).to_broadcast([P, KT, E]), ALU.subtract).then_inc(*dve_out.up())
                        dve.wait_ge(act_out.sem, a0 + 1)
                        vlink(V.tensor_reduce(col[:], lg[:], AX.X, ALU.add))
                        vlink(V.reciprocal(col[:], col[:]))
                        V.tensor_tensor(wts[:], lg[:], col[:].unsqueeze(2).to_broadcast([P, KT, E]), ALU.mult).then_inc(*dve_out.up())
                        dve.wait_ge(mm_done.sem, m0 + 2)
                        vlink(V.tensor_copy(work[0][:], ps[0:E, 1, :]))
                        for j in range(CAP2 // 8):
                            vlink(V.max(top[:], work[j % 2][:]))
                            vlink(V.match_replace(work[(j + 1) % 2][:], top[:], work[j % 2][:], -1.0))
                        vlink(V.tensor_scalar(sel[:], work[CAP2 // 8 % 2][:], 0.0, None, ALU.is_lt))
                        vlink(V.tensor_tensor_scan(rk[:], sel[:], sel[:], 0.0, ALU.add, ALU.max))
                        vlink(V.tensor_tensor(rk[:], rk[:], sel[:], ALU.mult))
                        V.tensor_scalar(rk[:], rk[:], -1.0, None, ALU.add).then_inc(*dve_out.up())
                        dve.wait_ge(mm_done.sem, m0 + 3)
                        V.tensor_copy(rankm[:], ps[:, 2, 0:KT * E].rearrange("p (t e) -> p t e", t=KT))

        def conformer_weights(st):
            w = A["cf_w1_2"].rearrange("(k p) n -> p k n", p=P)
            return SplitWeights(st, [[(h * P, w[:, :, h * D + m * P:h * D + (m + 1) * P]) for h in range(2)] for m in range(KD)])

        def conformer_in(W, parts, u, acc):
            rows = T // GRID_W
            mid = (CONF_TAPS - 1) // 2
            with ExitStack() as st:
                sig = sbuf(st, "cf_sig", [P, 2, T])
                m0, a0, v0 = mm_done.n, act_out.n, dve_out.n
                W.unit_end = [m0 + 2 * (m + 1) for m in range(KD)]
                with nc.Block() as block:
                    @block.sync
                    def _(sp):
                        W.load(sp, W.next_unit())

                    @block.gpsimd
                    def _(pool):
                        W.split_lo(pool, W.next_unit())

                    @block.tensor
                    def _(pe):
                        for m in range(KD):
                            W.ready(pe, m)
                            if m >= 4:
                                pe.wait_ge(dve_out.sem, v0 + m - 3)
                            for half in range(2):
                                W.product(ps[:, 2 * (m % 4) + half, :], m, half * P, parts, slice(0, T)).then_inc(*mm_done.up())

                    @block.scalar
                    def _(act):
                        for i in range(W.next_unit(), 2):
                            W.split_hi(act, i)
                        for m in range(KD):
                            act.wait_ge(mm_done.sem, m0 + 2 * m + 2)
                            if m >= 2:
                                act.wait_ge(dve_out.sem, v0 + m - 1)
                            nc.scalar.activation(sig[:, m % 2, :], ps[:, 2 * (m % 4) + 1, :], ACT.Sigmoid, bias=vcol("cf_b1_2", KD + m)).then_inc(*act_out.up())
                            W.split_hi(act, m + 2)

                    @block.vector
                    def _(dve):
                        for m in range(KD):
                            dve.wait_ge(act_out.sem, a0 + m + 1)
                            nc.vector.scalar_tensor_tensor(u[:, m, :], ps[:, 2 * (m % 4), :], vcol("cf_b1_2", m), sig[:, m % 2, :], ALU.add, ALU.mult).then_inc(*dve_out.up())
                            dve.wait_ge(dve_out.sem, v0 + m + 1)
                            V = nc.vector

                            def tap(k):
                                return vcol("cf_dw_w_2", k * KD + m)

                            vlink(V.tensor_scalar(acc[:, m, :], u[:, m, :], tap(mid), vcol("cf_dw_b_2", m), ALU.mult, ALU.add))
                            for d in range(1, rows):
                                n = (rows - d) * GRID_W
                                vlink(V.scalar_tensor_tensor(acc[:, m, 0:n], u[:, m, T - n:T], tap(mid + d), acc[:, m, 0:n], ALU.mult, ALU.add))
                                ins = V.scalar_tensor_tensor(acc[:, m, T - n:T], u[:, m, 0:n], tap(mid - d), acc[:, m, T - n:T], ALU.mult, ALU.add)
                                if d < rows - 1:
                                    vlink(ins)

        def conformer_norm(u, acc, ahead):
            with ExitStack() as st:
                stat = sbuf(st, "cf_stat", [P, 2, T])
                m0, a0, v0 = mm_done.n, act_out.n, dve_out.n
                with nc.Block() as block:
                    @block.sync
                    def _(sp):
                        ahead.load(sp, 0, 2)

                    @block.gpsimd
                    def _(pool):
                        ahead.split_lo(pool, 0, 2)
                        ahead.early = True

                    @block.vector
                    def _(dve):
                        V = nc.vector
                        dve.wait_ge(mm_done.sem, m0 + 1)
                        vlink(V.tensor_scalar(stat[:, 0, :], ps[:, 0, :], 1.0 / D, None, ALU.mult))
                        for c in range(KD):
                            V.tensor_tensor(acc[:, c, :], acc[:, c, :], stat[:, 0, :], ALU.subtract).then_inc(*dve_out.up())
                        dve.wait_ge(mm_done.sem, m0 + 2)
                        V.tensor_scalar(stat[:, 1, :], ps[:, 1, :], 1.0 / D, RMS_EPS, ALU.mult, ALU.add).then_inc(*dve_out.up())
                        dve.wait_ge(act_out.sem, a0 + KD + 1)
                        vlink(V.reciprocal(stat[:, 0, :], stat[:, 0, :]))
                        for c in range(KD):
                            V.scalar_tensor_tensor(acc[:, c, :], acc[:, c, :], vcol("cf_ln_g_2", c), stat[:, 0, :], ALU.mult, ALU.mult).then_inc(*dve_out.up())

                    @block.tensor
                    def _(pe):
                        for c in range(KD):
                            last = nc.tensor.matmul(ps[:, 0, :], ones, acc[:, c, :], start=(c == 0), stop=(c == KD - 1))
                        last.then_inc(*mm_done.up())
                        for c in range(KD):
                            pe.wait_ge(act_out.sem, a0 + c + 1)
                            last = nc.tensor.matmul(ps[:, 1, :], ones, u[:, c, :], start=(c == 0), stop=(c == KD - 1))
                        last.then_inc(*mm_done.up())

                    @block.scalar
                    def _(act):
                        ahead.split_hi(act, 0)
                        ahead.split_hi(act, 1)
                        for c in range(KD):
                            act.wait_ge(dve_out.sem, v0 + c + 1)
                            nc.scalar.activation(u[:, c, :], acc[:, c, :], ACT.Square).then_inc(*act_out.up())
                        act.wait_ge(dve_out.sem, v0 + KD + 1)
                        nc.scalar.activation(stat[:, 0, :], stat[:, 1, :], ACT.Sqrt).then_inc(*act_out.up())
                        for c in range(KD):
                            act.wait_ge(dve_out.sem, v0 + KD + 2 + c)
                            nc.scalar.activation(acc[:, c, :], acc[:, c, :], ACT.Silu, bias=vcol("cf_ln_b_2", c))

        def store_result(src):
            with ExitStack() as st:
                rows = sbuf(st, "out_rows", [P, KT, D])
                m0, a0, v0, s0 = mm_done.n, act_out.n, dve_out.n, stored.n
                with nc.Block() as block:
                    @block.sync
                    def _(sp):
                        for t in range(KT):
                            sp.wait_ge(dve_out.sem, v0 + t + 1)
                            sp.wait_ge(act_out.sem, a0 + t + 1)
                            sp.dma_start(out[t * P:(t + 1) * P, :], rows[:, t, :]).then_inc(*stored.up(16))
                        sp.wait_ge(stored.sem, s0 + 16 * KT)

                    @block.tensor
                    def _(pe):
                        for t in range(KT):
                            for half in range(2):
                                for c in range(4):
                                    last = nc.tensor.transpose(ps[:, 2 * t + half, c * P:(c + 1) * P], src[:, half * 4 + c, t * P:(t + 1) * P], ident)
                                last.then_inc(*mm_done.up())

                    @block.scalar
                    def _(act):
                        for t in range(KT):
                            act.wait_ge(mm_done.sem, m0 + 2 * t + 2)
                            nc.scalar.activation(rows[:, t, 512:1024], ps[:, 2 * t + 1, :], ACT.Copy).then_inc(*act_out.up())

                    @block.vector
                    def _(dve):
                        for t in range(KT):
                            dve.wait_ge(mm_done.sem, m0 + 2 * t + 1)
                            nc.vector.tensor_copy(rows[:, t, 0:512], ps[:, 2 * t, :]).then_inc(*dve_out.up())
        mods = [sbuf(ctx, f"mod_l{l}", [P, 48]) for l in range(2)]
        mod_c = sbuf(ctx, "mod_ctx", [P, 24])
        scaled = [sbuf(ctx, f"scaled_l{l}", [P, 2, KD]) for l in range(2)]
        load_and_transpose(A["x"], xT, T, True)
        with ExitStack() as blk1:
            mix = sbuf(blk1, "mix", [P, 2 * CT, T])
            with ExitStack() as mixers:
                mk = sbuf(mixers, "masks", [P, (4 + 2 * LEVELS) * P])
                masks = {"strict": mk[:, 0:2 * P], "incl": mk[:, 2 * P:4 * P], "levels": mk[:, 4 * P:]}
                proj = sbuf(mixers, "proj", [P, 15, T])
                l0 = inputs_in.n
                with nc.Block() as block:
                    @block.sync
                    def _(sp):
                        sp.dma_start(mk[:], A["consts"][:, const_at["base_end"] + 1:]).then_inc(*inputs_in.up(16))
                        sp.wait_ge(inputs_in.sem, l0 + 16)
                with ExitStack() as gla:
                    gla_q = sbuf(gla, "gla_q", [P, 2, T])
                    gla_k = sbuf(gla, "gla_k", [P, 2, T])
                    gla_v = sbuf(gla, "gla_v", [P, KT, 512])
                    gla_gl = sbuf(gla, "gla_gl", [32, T])
                    gla_og = sbuf(gla, "gla_og", [P, CT, T])
                    with ExitStack() as first:
                        hT = mix
                        parts = [sbuf(first, f"h_part{j}", [P, KD, T], F32R) for j in range(2)]
                        W = first_weights(first)
                        rms_norm(xT, hT, T, lambda k: vcol("ln1_w", k), parts=parts, ahead=W)
                        project_first(W, hT, parts, proj, gla_q, gla_k, gla_v, gla_gl, gla_og, (0, mods[0], mod_c, scaled[0]))
                    gla_mixer(gla_q, gla_k, gla_v, gla_gl, gla_og, mix[:, CT:2 * CT, :], masks)
                with ExitStack() as rwkv:
                    w2 = sbuf(rwkv, "w2s", [P, RW])
                    a2 = sbuf(rwkv, "a2s", [P, RW])
                    g2 = sbuf(rwkv, "g2s", [P, RW])
                    kk = sbuf(rwkv, "rw_kk", [P, CT, T])
                    kd_sum = sbuf(rwkv, "rw_kd_sum", [P, CT, T])
                    v_tok = sbuf(rwkv, "rw_v_tok", [P, KT, RW])
                    rwkv_keys(proj, kk, w2, a2, g2, None)
                    to_tokens([(proj[:, 8:12, :], v_tok)])
                    with ExitStack() as scan:
                        bufs = {n: sbuf(scan, "rw_" + n, [P, CT, T]) for n in ("lw", "cc", "ex", "a", "kd", "q", "r")}
                        for n in ("half", "scale"):
                            bufs[n] = sbuf(scan, "rw_" + n, [P, CT * KT])
                        for n in ("N", "X"):
                            bufs[n] = sbuf(scan, "rw_" + n, [P, 2, CT, P])
                        for n in ("Z", "BT", "RB", "RK"):
                            bufs[n] = [sbuf(scan, "rw_" + n, [P, 2, CT, P])]
                        ex4 = bufs["ex"][:].rearrange("p (two a) (h i) -> p two a h i", two=2, i=P)
                        bufs["Z"].append(ex4[:, 0])
                        bufs["BT"].append(ex4[:, 1])
                        for n in ("RB", "RK"):
                            bufs[n].append(sbuf(scan, f"rw_{n}_2", [P, 2, CT, P]))
                        bufs["U"] = sbuf(scan, "rw_U", [P, 2, CT, P])
                        bufs["rhs"] = sbuf(scan, "rw_rhs", [P, 2, CT, 64])
                        bufs["sa"] = sbuf(scan, "rw_sa", [P, RW])
                        bufs["S"] = sbuf(scan, "rw_S", [P, CT, 64])
                        bufs["hop"] = sbuf(scan, "rw_hop", [P, KT, CT])
                        bufs["b_tok"], bufs["k_tok"] = bufs["lw"], bufs["cc"]
                        for back in (False, True):
                            rwkv_direction(back, proj, kk, w2, a2, kd_sum, bufs)
                            to_tokens([(bufs["a"], bufs["b_tok"]), (bufs["kd"], bufs["k_tok"])])
                            rwkv_scan(back, bufs, v_tok, mix[:, 0:CT, :], masks)
                    with ExitStack() as last:
                        W = square_weights(last, A["w_out"])
                        rwkv_output(proj, mix[:, 0:CT, :], kd_sum, g2, W)
                        project_residual(W, mix, xT)
        with ExitStack() as moe:
            h_hi = sbuf(moe, "h_hi1", [P, KT, D], F32R)
            h_lo = sbuf(moe, "h_lo1", [P, KT, D], F32R)
            rankm = sbuf(moe, "rankm1", [P, KT, N_EXP1])
            wts = sbuf(moe, "wts1", [P, KT, N_EXP1])
            over_one = sbuf(moe, "over_one", [P, N_OVER, N_EXP1])
            over_first = sbuf(moe, "over_first", [P, N_OVER])
            over_int = sbuf(moe, "over_int", [P, N_OVER + 1], I32)
            with ExitStack() as experts_part:
                load_ahead, run = experts_pass(experts_part, "m1", h_hi, h_lo, rankm, wts, N_EXP1, A["moe_w_gate"], A["moe_w_up"], A["moe_w_down"], 512, None)
                with ExitStack() as route:
                    hT2 = sbuf(route, "hT2", [P, KD, T])
                    rms_norm(xT, hT2, T, lambda k: vcol("ln2_w", k))
                    rows_of(hT2, h_hi, h_lo)
                    route_first(hT2, rankm, wts, over_one, over_first, over_int, load_ahead)
                run()
            overflow_pass(h_hi, h_lo, rankm, wts, over_one, over_first, over_int)
        with ExitStack() as nrm:
            sq = sbuf(nrm, "sq_f1", [P, KD, T])
            rms_norm(xT, xT, T, lambda k: vcol("ln_f_w", k), sq=sq)
        def part(l, j):
            return lambda k: mods[l][:, 8 * j + k:8 * j + k + 1]

        def weight(l, j):
            return lambda k: scaled[l][:, j, k:k + 1]

        with ExitStack() as even:
            cat = sbuf(even, "cat", [P, 2 * CT, T])
            hy = sbuf(even, "hy", [P, 3 * CT, T])
            spec = sbuf(even, "spec", [P, KT, T])
            with ExitStack() as lru:
                gates = sbuf(lru, "lru_w", [P, 2, 2, CT, P])
                rate = sbuf(lru, "lru_rate", [P, 2, 8])
                state = sbuf(lru, "lru_state", [P, 2 * CT])
                xa = sbuf(lru, "xa", [P, CT, T])
                lru_rates(rate, gates)
                with ExitStack() as ctx_part:
                    cT = sbuf(ctx_part, "cT", [P, KD, CTX])
                    hc = sbuf(ctx_part, "hc", [P, KD, CTX])
                    xc = sbuf(ctx_part, "xc", [P, CT, CTX])
                    load_and_transpose(A["ctx_2"], cT, CTX, False)
                    hc_parts = [sbuf(ctx_part, f"hc_part{j}", [P, KD, CTX], F32R) for j in range(2)]
                    rms_norm(cT, hc, CTX, lambda k: mod_c[:, 16 + k:17 + k], lambda k: mod_c[:, k:k + 1], parts=hc_parts)
                    with ExitStack() as first:
                        project_even(even_weights(first, [4, 5, 6, 7]), hc_parts, CTX, [4, 5, 6, 7], None, xc, None)
                    lru_scan(xc, CTX, gates, rate, None, state, None)
                with ExitStack() as first:
                    hT = sbuf(first, "hT_l0", [P, KD, T])
                    parts = [sbuf(first, f"h_part{j}", [P, KD, T], F32R) for j in range(2)]
                    W = even_weights(first, list(range(20)))
                    rms_norm(xT, hT, T, weight(0, 0), part(0, 0), parts=parts, ahead=W)
                    project_even(W, parts, T, list(range(20)), cat[:, 0:CT, :], xa, hy, (1, mods[1], mod_c, scaled[1]))
                lru_scan(xa, T, gates, rate, state, None, cat[:, 0:CT, :])
            with ExitStack() as hyena:
                Kc = sbuf(hyena, "Kc", [P, KT, HYENA_ORDER, HYENA_WIDTH])
                Ks = sbuf(hyena, "Ks", [P, KT, HYENA_ORDER, HYENA_WIDTH])
                inv = sbuf(hyena, "inv", [P, KT, T])
                hyena_filters(spec, Kc, Ks, inv, cat[:, CT:2 * CT, :], hy[:, 0:CT, :])
                for o in range(HYENA_ORDER):
                    hyena_conv(o, cat[:, CT:2 * CT, :], hy[:, CT:3 * CT, :], spec, inv, Kc, Ks)
            project_residual(square_weights(even, A["w_out_2"]), cat, xT, gate=part(0, 2))

        for l in range(2):
            if l == 1:
                with ExitStack() as conf:
                    hT = sbuf(conf, "hT_l1", [P, KD, T])
                    u = sbuf(conf, "cf_u", [P, KD, T])
                    with ExitStack() as first:
                        parts = [sbuf(first, f"h_part{j}", [P, KD, T], F32R) for j in range(2)]
                        W = conformer_weights(first)
                        rms_norm(xT, hT, T, weight(1, 0), part(1, 0), parts=parts, ahead=W)
                        conformer_in(W, parts, u, hT)
                    W = square_weights(conf, A["cf_w2_2"])
                    conformer_norm(u, hT, W)
                    project_residual(W, hT, xT, gate=part(1, 2), bias=lambda k: vcol("cf_b2_2", k))
            with ExitStack() as moe:
                h_hi = sbuf(moe, "h_hi_c", [P, KT, D], F32R)
                h_lo = sbuf(moe, "h_lo_c", [P, KT, D], F32R)
                rankm = sbuf(moe, "rankm_c", [P, KT, N_EXP2])
                wts = sbuf(moe, "wts_c", [P, KT, N_EXP2])
                load_ahead, run = experts_pass(moe, f"c{l}", h_hi, h_lo, rankm, wts, N_EXP2, A["exp_w1_2"][l], A["exp_w3_2"][l], A["exp_w2_2"][l], FF2, part(l, 5))
                with ExitStack() as route:
                    hT = sbuf(route, "hT_c", [P, KD, T])
                    rms_norm(xT, hT, T, weight(l, 1), part(l, 3))
                    rows_of(hT, h_hi, h_lo)
                    route_choice(l, hT, rankm, wts, load_ahead)
                run()
        with ExitStack() as last:
            fin = sbuf(last, "fin", [P, KD, T])
            rms_norm(xT, fin, T, lambda k: vcol("final_g_2", k))
            store_result(fin)


def layout(inputs):
    a = {k: np.ascontiguousarray(np.asarray(v)) for k, v in inputs.items()}
    vectors, consts = pack_vectors(a), shape_constants()
    gw2 = np.zeros((32, 2, 256), np.float32)
    gw2[0:16, 0], gw2[16:32, 1] = a["gla_gw2_f"][0], a["gla_gw2_b"][0]
    ins = {"vectors": vectors.array(), "consts": consts.array(), "gla_gw2": gw2, "x": a["x"][0], "w_in": a["w_in"][0]}
    for name in ("rw_w2_f", "rw_w2_b", "rw_a2_f", "rw_a2_b", "rw_g2", "w_out"):
        ins[name] = a[name][0]
    more_layout(a, ins)
    return ins, vectors.start, consts.start


def more_layout(a, ins):
    for name in ("moe_w_gate", "moe_w_up", "moe_w_down"):
        ins[name] = a[name][0]
    ins["moe_w_route"] = np.concatenate([a["moe_w_coarse"][0], a["moe_w_fine"][0]], axis=1)
    ins["moe_b_route"] = np.concatenate([a["moe_b_coarse"][0], a["moe_b_fine"][0]])[None]
    for name in ("ctx_2", "w_in_2", "w_out_2", "filt_w1_2", "filt_w2_2", "cf_w1_2", "cf_w2_2"):
        ins[name] = a[name][0]
    for name in ("w_mod_2", "router_2", "exp_w1_2", "exp_w3_2", "exp_w2_2"):
        ins[name] = a[name]
    ins["filt_w3_2"] = np.concatenate([a["filt_w3_2"][0], a["filt_b3_2"]], axis=0)
    gates = np.zeros((P, 2, 2, CT, P), np.float32)
    for j, name in enumerate(("lru_wr_2", "lru_wi_2")):
        for h in range(8):
            at = slice(64 * (h % 2), 64 * (h % 2) + 64)
            gates[at, j, :, h // 2, at] = a[name][0, :, h].transpose(1, 0, 2)
    ins["lru_gates"] = gates
    ins.update(hyena_tables())


def kernel(**inputs):
    import concourse.bacc as bacc
    from concourse.bass_utils import run_bass_kernel_spmd

    ins, vec_at, const_at = layout(inputs)
    nc = bacc.Bacc("TRN2", target_bir_lowering=False, num_devices=1)
    A = {name: nc.dram_tensor(f"in_{name}", v.shape, mybir.dt.from_np(v.dtype), kind="ExternalInput").ap() for name, v in ins.items()}
    out = nc.dram_tensor("out_0", (T, D), F32, kind="ExternalOutput").ap()
    build(nc, A, out, vec_at, const_at)
    result = run_bass_kernel_spmd(nc, [{f"in_{name}": v for name, v in ins.items()}], core_ids=[0])
    return result.results[0]["out_0"].reshape(1, T, D)
```
